# Optimizing a Trainium2 kernel written in Bass

```python
import math
import jax, jax.numpy as jnp
from jax import lax
import numpy as np

D_MODEL = 1024
BATCH = 1
SEQ = 512
DEPTH = 2

CHUNK = 64
MEM_LEN = 256
Q_BLOCK = 128
RMS_EPS = 1e-6
NEG_INF = -1e30

FOX_HEAD_DIM = 64
FOX_HEADS = (D_MODEL // 2) // FOX_HEAD_DIM
DIFF_QK_DIM = 64
DIFF_V_DIM = 2 * DIFF_QK_DIM
DIFF_HEADS = (D_MODEL // 2) // DIFF_V_DIM
ATTN_IN_WIDTH = 3 * FOX_HEADS * FOX_HEAD_DIM + FOX_HEADS + DIFF_HEADS * (4 * DIFF_QK_DIM + DIFF_V_DIM)
MLSTM_HEADS = 4
MLSTM_V_DIM = D_MODEL // MLSTM_HEADS
MLSTM_QK_DIM = MLSTM_V_DIM // 2
MLSTM_CONV = 4
MLSTM_IN_WIDTH = 2 * MLSTM_HEADS * MLSTM_QK_DIM + 2 * MLSTM_HEADS * MLSTM_V_DIM + 2 * MLSTM_HEADS
XATTN_HEADS = 4
XATTN_HEAD_DIM = D_MODEL // XATTN_HEADS
D_FF = 256 * math.ceil(8 * D_MODEL / 3 / 256)
FFN_CONV = 3
N_EVEN = (DEPTH + 1) // 2
N_ODD = DEPTH // 2


def rms_norm(x, gain):
    x32 = x.astype(jnp.float32)
    y = x32 * lax.rsqrt(jnp.mean(x32 * x32, axis=-1, keepdims=True) + RMS_EPS)
    return (y * gain.astype(jnp.float32)).astype(x.dtype)

def causal_depthwise_conv(x, w):
    K = w.shape[0]
    S = x.shape[1]
    xp = jnp.pad(x, ((0, 0), (K - 1, 0), (0, 0)))
    y = xp[:, 0:S, :] * w[0]
    for tap in range(1, K):
        y = y + xp[:, tap:tap + S, :] * w[tap]
    return y

def split_heads(t, n_heads):
    B, S, _ = t.shape
    return t.reshape(B, S, n_heads, -1).transpose(0, 2, 1, 3)

def merge_heads(t):
    B, H, S, d = t.shape
    return t.transpose(0, 2, 1, 3).reshape(B, S, H * d)

def to_blocks(t, size):
    B, H, S = t.shape[:3]
    return jnp.moveaxis(t.reshape(B, H, S // size, size, *t.shape[3:]), 2, 0)

def from_blocks(t):
    nb, B, H, size = t.shape[:4]
    return jnp.moveaxis(t, 0, 2).reshape(B, H, nb * size, *t.shape[4:])

def forgetting_attention(q, k, v, log_f):
    S = q.shape[2]
    scale = q.shape[-1] ** -0.5
    F = jnp.cumsum(log_f, axis=-1)
    k_pos = jnp.arange(S)
    starts = jnp.arange(S // Q_BLOCK) * Q_BLOCK

    def block(args):
        start, q_b, F_b = args
        q_pos = start + jnp.arange(Q_BLOCK)
        logits = jnp.einsum('bhqd,bhkd->bhqk', q_b, k, preferred_element_type=jnp.float32) * scale
        logits = logits + F_b[..., :, None] - F[..., None, :]
        logits = jnp.where(k_pos[None, :] <= q_pos[:, None], logits, NEG_INF)
        p = jax.nn.softmax(logits, axis=-1)
        return jnp.einsum('bhqk,bhkd->bhqd', p.astype(v.dtype), v)

    out = lax.map(block, (starts, to_blocks(q, Q_BLOCK), to_blocks(F, Q_BLOCK)))
    return from_blocks(out)

def differential_attention(q1, q2, k1, k2, v, lam):
    S = q1.shape[2]
    scale = q1.shape[-1] ** -0.5
    k_chunk = jnp.arange(S) // CHUNK
    starts = jnp.arange(S // Q_BLOCK) * Q_BLOCK

    def block(args):
        start, q1_b, q2_b = args
        q_chunk = (start + jnp.arange(Q_BLOCK)) // CHUNK
        mask = k_chunk[None, :] <= q_chunk[:, None]
        l1 = jnp.einsum('bhqd,bhkd->bhqk', q1_b, k1, preferred_element_type=jnp.float32) * scale
        l2 = jnp.einsum('bhqd,bhkd->bhqk', q2_b, k2, preferred_element_type=jnp.float32) * scale
        p1 = jax.nn.softmax(jnp.where(mask, l1, NEG_INF), axis=-1)
        p2 = jax.nn.softmax(jnp.where(mask, l2, NEG_INF), axis=-1)
        p = p1 - lam * p2
        return jnp.einsum('bhqk,bhkd->bhqd', p.astype(v.dtype), v)

    out = lax.map(block, (starts, to_blocks(q1, Q_BLOCK), to_blocks(q2, Q_BLOCK)))
    return from_blocks(out)

def fox_diff_mixer(xn, w_in, fox_bf, lq1, lk1, lq2, lk2, subln, w_out, lambda_init):
    B, S, _ = xn.shape
    proj = xn @ w_in
    fw = FOX_HEADS * FOX_HEAD_DIM
    dqk = DIFF_HEADS * 2 * DIFF_QK_DIM
    cuts = np.cumsum([fw, fw, fw, FOX_HEADS, dqk, dqk]).tolist()
    fq, fk, fv, ff, dq, dk, dv = jnp.split(proj, cuts, axis=-1)
    log_f = jax.nn.log_sigmoid((ff + fox_bf).astype(jnp.float32)).transpose(0, 2, 1)
    fox_out = forgetting_attention(split_heads(fq, FOX_HEADS), split_heads(fk, FOX_HEADS),
                                   split_heads(fv, FOX_HEADS), log_f)
    dq = dq.reshape(B, S, DIFF_HEADS, 2, DIFF_QK_DIM).transpose(0, 2, 3, 1, 4)
    dk = dk.reshape(B, S, DIFF_HEADS, 2, DIFF_QK_DIM).transpose(0, 2, 3, 1, 4)
    lam = (jnp.exp(jnp.sum(lq1.astype(jnp.float32) * lk1.astype(jnp.float32)))
           - jnp.exp(jnp.sum(lq2.astype(jnp.float32) * lk2.astype(jnp.float32))) + lambda_init)
    d_out = differential_attention(dq[:, :, 0], dq[:, :, 1], dk[:, :, 0], dk[:, :, 1],
                                   split_heads(dv, DIFF_HEADS), lam)
    d_out = rms_norm(d_out, subln) * (1.0 - lambda_init)
    mixed = jnp.concatenate([merge_heads(fox_out), merge_heads(d_out)], axis=-1)
    return mixed @ w_out

def mlstm_chunkwise(q, k, v, i_pre, log_f):
    B, H, _, dqk = q.shape
    dv = v.shape[-1]
    causal = jnp.tril(jnp.ones((CHUNK, CHUNK), dtype=bool))

    def step(carry, xs):
        C, n, m = carry
        qc, kc, vc, ic, fc = xs
        b = jnp.cumsum(fc, axis=-1)
        g = b[..., -1]
        D = jnp.where(causal, b[..., :, None] - b[..., None, :] + ic[..., None, :], NEG_INF)
        inter = b + m[..., None]
        m_t = jnp.maximum(inter, jnp.max(D, axis=-1))
        w_inter = jnp.exp(inter - m_t)
        W = jnp.exp(D - m_t[..., None])
        qk = jnp.einsum('bhtd,bhsd->bhts', qc, kc) * W
        num = w_inter[..., None] * jnp.einsum('bhtd,bhde->bhte', qc, C) + jnp.einsum('bhts,bhse->bhte', qk, vc)
        den = w_inter * jnp.einsum('bhtd,bhd->bht', qc, n) + jnp.sum(qk, axis=-1)
        h = num / jnp.maximum(jnp.abs(den), jnp.exp(-m_t))[..., None]
        a = g[..., None] - b + ic
        m_new = jnp.maximum(g + m, jnp.max(a, axis=-1))
        decay = jnp.exp(g + m - m_new)
        wk = jnp.exp(a - m_new[..., None])
        C_new = decay[..., None, None] * C + jnp.einsum('bhs,bhsd,bhse->bhde', wk, kc, vc)
        n_new = decay[..., None] * n + jnp.einsum('bhs,bhsd->bhd', wk, kc)
        return (C_new, n_new, m_new), h

    init = (jnp.zeros((B, H, dqk, dv), jnp.float32), jnp.zeros((B, H, dqk), jnp.float32),
            jnp.zeros((B, H), jnp.float32))
    xs = (to_blocks(q, CHUNK), to_blocks(k, CHUNK), to_blocks(v, CHUNK),
          to_blocks(i_pre, CHUNK), to_blocks(log_f, CHUNK))
    _, h = lax.scan(step, init, xs)
    return from_blocks(h)

def mlstm_mixer(xn, w_in, conv_qk, b_i, b_f, head_norm, w_out):
    proj = xn @ w_in
    qkw = MLSTM_HEADS * MLSTM_QK_DIM
    vw = MLSTM_HEADS * MLSTM_V_DIM
    cuts = np.cumsum([2 * qkw, vw, MLSTM_HEADS, MLSTM_HEADS]).tolist()
    qk_pre, v, ig, fg, og = jnp.split(proj, cuts, axis=-1)
    qk = jax.nn.silu(causal_depthwise_conv(qk_pre, conv_qk))
    q, k = jnp.split(qk, 2, axis=-1)
    q = split_heads(q, MLSTM_HEADS).astype(jnp.float32) * (MLSTM_QK_DIM ** -0.5)
    k = split_heads(k, MLSTM_HEADS).astype(jnp.float32)
    v = split_heads(v, MLSTM_HEADS).astype(jnp.float32)
    i_pre = (ig + b_i).astype(jnp.float32).transpose(0, 2, 1)
    log_f = jax.nn.log_sigmoid((fg + b_f).astype(jnp.float32)).transpose(0, 2, 1)
    h = mlstm_chunkwise(q, k, v, i_pre, log_f)
    h = rms_norm(h, head_norm.reshape(MLSTM_HEADS, 1, MLSTM_V_DIM))
    h = merge_heads(h).astype(xn.dtype) * jax.nn.sigmoid(og)
    return h @ w_out

def memory_cross_attention(xn, memn, wq, wkv, wo):
    q = split_heads(xn @ wq, XATTN_HEADS)
    k, v = jnp.split(memn @ wkv, 2, axis=-1)
    k = split_heads(k, XATTN_HEADS)
    v = split_heads(v, XATTN_HEADS)
    logits = jnp.einsum('bhqd,bhmd->bhqm', q, k, preferred_element_type=jnp.float32) * (XATTN_HEAD_DIM ** -0.5)
    p = jax.nn.softmax(logits, axis=-1)
    out = jnp.einsum('bhqm,bhmd->bhqd', p.astype(v.dtype), v)
    return merge_heads(out) @ wo

def conv_ffn(xn, w_up, conv_w, conv_b, w_down):
    h = causal_depthwise_conv(xn @ w_up, conv_w) + conv_b
    g, u = jnp.split(h, 2, axis=-1)
    return (jax.nn.gelu(g) * u) @ w_down

def first_inputs(seed: int = 0) -> dict:
    key = jax.random.key(seed)
    ks = iter(jax.random.split(key, 40))

    def nrm(shape, scale):
        return jax.random.normal(next(ks), shape, jnp.float32) * scale

    def gain(shape):
        return 1.0 + nrm(shape, 0.02)

    out_scale = (2.0 * D_MODEL) ** -0.5
    return {
        'x': nrm((BATCH, SEQ, D_MODEL), 1.0),
        'mem': nrm((BATCH, MEM_LEN, D_MODEL), 1.0),
        'mix_norm': gain((DEPTH, D_MODEL)),
        'xattn_norm': gain((DEPTH, D_MODEL)),
        'mem_norm': gain((DEPTH, D_MODEL)),
        'ffn_norm': gain((DEPTH, D_MODEL)),
        'attn_w_in': nrm((N_EVEN, D_MODEL, ATTN_IN_WIDTH), D_MODEL ** -0.5),
        'attn_fox_bf': jnp.linspace(1.0, 4.0, FOX_HEADS, dtype=jnp.float32) + nrm((N_EVEN, FOX_HEADS), 0.1),
        'diff_lq1': nrm((N_EVEN, DIFF_QK_DIM), 0.1),
        'diff_lk1': nrm((N_EVEN, DIFF_QK_DIM), 0.1),
        'diff_lq2': nrm((N_EVEN, DIFF_QK_DIM), 0.1),
        'diff_lk2': nrm((N_EVEN, DIFF_QK_DIM), 0.1),
        'diff_subln': gain((N_EVEN, DIFF_V_DIM)),
        'attn_w_out': nrm((N_EVEN, D_MODEL, D_MODEL), out_scale),
        'mlstm_w_in': nrm((N_ODD, D_MODEL, MLSTM_IN_WIDTH), D_MODEL ** -0.5),
        'mlstm_conv_qk': nrm((N_ODD, MLSTM_CONV, 2 * MLSTM_HEADS * MLSTM_QK_DIM), MLSTM_CONV ** -0.5),
        'mlstm_b_i': nrm((N_ODD, MLSTM_HEADS), 0.1),
        'mlstm_b_f': jnp.linspace(3.0, 6.0, MLSTM_HEADS, dtype=jnp.float32) + nrm((N_ODD, MLSTM_HEADS), 0.1),
        'mlstm_head_norm': gain((N_ODD, MLSTM_HEADS * MLSTM_V_DIM)),
        'mlstm_w_out': nrm((N_ODD, D_MODEL, D_MODEL), out_scale),
        'xattn_wq': nrm((DEPTH, D_MODEL, D_MODEL), D_MODEL ** -0.5),
        'xattn_wkv': nrm((DEPTH, D_MODEL, 2 * D_MODEL), D_MODEL ** -0.5),
        'xattn_wo': nrm((DEPTH, D_MODEL, D_MODEL), out_scale),
        'ffn_w_up': nrm((DEPTH, D_MODEL, 2 * D_FF), D_MODEL ** -0.5),
        'ffn_conv_w': nrm((DEPTH, FFN_CONV, 2 * D_FF), FFN_CONV ** -0.5),
        'ffn_conv_b': nrm((DEPTH, 2 * D_FF), 0.02),
        'ffn_w_down': nrm((DEPTH, D_FF, D_MODEL), (2.0 * D_FF) ** -0.5),
        'final_norm': gain((D_MODEL,)),
    }

def first_block(x, mem, mix_norm, xattn_norm, mem_norm, ffn_norm,
              attn_w_in, attn_fox_bf, diff_lq1, diff_lk1, diff_lq2, diff_lk2, diff_subln, attn_w_out,
              mlstm_w_in, mlstm_conv_qk, mlstm_b_i, mlstm_b_f, mlstm_head_norm, mlstm_w_out,
              xattn_wq, xattn_wkv, xattn_wo,
              ffn_w_up, ffn_conv_w, ffn_conv_b, ffn_w_down, final_norm):
    for layer in range(DEPTH):
        j = layer // 2
        xn = rms_norm(x, mix_norm[layer])
        if layer % 2 == 0:
            lambda_init = 0.8 - 0.6 * math.exp(-0.3 * layer)
            mixed = fox_diff_mixer(xn, attn_w_in[j], attn_fox_bf[j], diff_lq1[j], diff_lk1[j],
                                   diff_lq2[j], diff_lk2[j], diff_subln[j], attn_w_out[j], lambda_init)
        else:
            mixed = mlstm_mixer(xn, mlstm_w_in[j], mlstm_conv_qk[j], mlstm_b_i[j], mlstm_b_f[j],
                                mlstm_head_norm[j], mlstm_w_out[j])
        x = x + mixed
        x = x + memory_cross_attention(rms_norm(x, xattn_norm[layer]), rms_norm(mem, mem_norm[layer]),
                                       xattn_wq[layer], xattn_wkv[layer], xattn_wo[layer])
        x = x + conv_ffn(rms_norm(x, ffn_norm[layer]), ffn_w_up[layer], ffn_conv_w[layer],
                         ffn_conv_b[layer], ffn_w_down[layer])
    return rms_norm(x, final_norm)


DEPTH_2 = 1

A_WIDTH = D_MODEL // 2
A_HEAD = 64
A_HEADS = A_WIDTH // A_HEAD
A_DECAY_RANK = 64
A_ICLR_RANK = 64
A_GATE_RANK = 128
GN_EPS = 64e-5
B_WIDTH = D_MODEL // 2
B_BLOCKS = 8
B_BLOCK = B_WIDTH // B_BLOCKS
CONV_WIDTH = 4
LRU_C = 8.0
IN_COLS = 3 * A_WIDTH + 2 * B_WIDTH + 2 * D_MODEL
N_GROUPS = 4
EXPERTS_PER_GROUP = 8
N_EXPERTS = N_GROUPS * EXPERTS_PER_GROUP
TOP_K = 2
D_EXPERT = 256
EPS = 1e-6


def rmsnorm(x, g):
    xf = x.astype(jnp.float32)
    y = xf * lax.rsqrt(jnp.mean(xf * xf, axis=-1, keepdims=True) + EPS)
    return (y * g.astype(jnp.float32)).astype(x.dtype)

def modulate(h, shift, scale):
    return h * (1 + scale[:, None, :]) + shift[:, None, :]

def token_shift(t):
    return jnp.pad(t, ((0, 0), (1, 0), (0, 0)))[:, :-1]

def rwkv7_time_mix(xn, rkv, mu_rkv, mu_wag, w0, w1, w2, a0, a1, a2, g1, g2,
                   k_k, k_a, r_k, lnx_g, lnx_b):
    bsz, seq, _ = xn.shape
    f32 = jnp.float32
    rkv = rkv + (token_shift(rkv) - rkv) * mu_rkv
    r, k, v = jnp.split(rkv, 3, axis=-1)
    dx = token_shift(xn) - xn
    xw = xn + dx * mu_wag[0]
    xa = xn + dx * mu_wag[1]
    xg = xn + dx * mu_wag[2]
    w_log = -jax.nn.softplus(-(w0 + jnp.tanh(xw @ w1) @ w2)) - 0.5
    decay = jnp.exp(-jnp.exp(w_log.astype(f32)))
    a = jax.nn.sigmoid(a0 + (xa @ a1) @ a2)
    g = jax.nn.sigmoid(xg @ g1) @ g2
    heads = lambda t: t.reshape(bsz, seq, A_HEADS, A_HEAD)
    kk = heads((k * k_k).astype(f32))
    kk = kk * lax.rsqrt(jnp.sum(kk * kk, axis=-1, keepdims=True) + 1e-12)
    k = k * (1 + (a - 1) * k_a)
    r_h, k_h, v_h, a_h = (heads(t.astype(f32)) for t in (r, k, v, a))
    w_h = heads(decay)
    seq_first = lambda t: jnp.moveaxis(t, 1, 0)
    xs = tuple(seq_first(t) for t in (r_h, w_h, k_h, v_h, -kk, kk * a_h))

    def step(state, inp):
        r_t, w_t, k_t, v_t, a_t, b_t = inp
        sa = jnp.einsum('bhvk,bhk->bhv', state, a_t)
        state = (state * w_t[:, :, None, :] + sa[..., None] * b_t[:, :, None, :]
                 + v_t[..., None] * k_t[:, :, None, :])
        y_t = jnp.einsum('bhvk,bhk->bhv', state, r_t)
        return state, y_t

    state0 = jnp.zeros((bsz, A_HEADS, A_HEAD, A_HEAD), f32)
    _, y = lax.scan(step, state0, xs)
    y = jnp.moveaxis(y, 0, 1)
    mean = jnp.mean(y, axis=-1, keepdims=True)
    var = jnp.mean(jnp.square(y - mean), axis=-1, keepdims=True)
    y = ((y - mean) * lax.rsqrt(var + GN_EPS)).reshape(bsz, seq, A_WIDTH)
    y = y * lnx_g.astype(f32) + lnx_b.astype(f32)
    bonus = jnp.sum(r_h * k_h * r_k.astype(f32), axis=-1, keepdims=True) * v_h
    y = y + bonus.reshape(bsz, seq, A_WIDTH)
    return (y * g.astype(f32)).astype(xn.dtype)

def rglru_branch(xb, gb, conv_w, conv_b, w_rgate, b_rgate, w_igate, b_igate, lam):
    bsz, seq, _ = xb.shape
    f32 = jnp.float32
    xc = lax.conv_general_dilated(
        xb, conv_w, window_strides=(1,), padding=((CONV_WIDTH - 1, 0),),
        dimension_numbers=('NWC', 'WIO', 'NWC'), feature_group_count=B_WIDTH) + conv_b
    xblk = xc.reshape(bsz, seq, B_BLOCKS, B_BLOCK)
    gate_r = jax.nn.sigmoid((jnp.einsum('bsgi,gij->bsgj', xblk, w_rgate)
                             .reshape(bsz, seq, B_WIDTH) + b_rgate).astype(f32))
    gate_i = jax.nn.sigmoid((jnp.einsum('bsgi,gij->bsgj', xblk, w_igate)
                             .reshape(bsz, seq, B_WIDTH) + b_igate).astype(f32))
    log_a = -LRU_C * gate_r * jax.nn.softplus(-lam.astype(f32))
    a = jnp.exp(log_a)
    u = jnp.sqrt(-jnp.expm1(2.0 * log_a)) * (gate_i * xc.astype(f32))

    def combine(left, right):
        a_l, u_l = left
        a_r, u_r = right
        return a_l * a_r, a_r * u_l + u_r

    _, h = lax.associative_scan(combine, (a, u), axis=1)
    return (h * jax.nn.gelu(gb.astype(f32))).astype(xb.dtype)

def hier_moe(h, w_rg, b_rg, w_re, b_re, w1e, w3e, w2e):
    bsz, seq, d = h.shape
    f32 = jnp.float32
    t = h.reshape(-1, d)
    pg = jax.nn.softmax((t @ w_rg + b_rg).astype(f32), axis=-1)
    pg_top, g_idx = lax.top_k(pg, 1)
    le = (t @ w_re + b_re).astype(f32).reshape(-1, N_GROUPS, EXPERTS_PER_GROUP)
    le_sel = jnp.take_along_axis(le, g_idx[:, :, None], axis=1)[:, 0]
    pe = jax.nn.softmax(le_sel, axis=-1)
    pe_top, e_idx = lax.top_k(pe, TOP_K)
    pe_top = pe_top / jnp.sum(pe_top, axis=-1, keepdims=True)
    wts = pg_top * pe_top
    flat_idx = g_idx * EXPERTS_PER_GROUP + e_idx
    cw = jnp.sum(jax.nn.one_hot(flat_idx, N_EXPERTS, dtype=f32) * wts[..., None], axis=1)
    cw = cw.astype(h.dtype)
    out = jnp.zeros_like(t)
    for e in range(N_EXPERTS):
        he = jax.nn.silu(t @ w1e[e]) * (t @ w3e[e])
        out = out + cw[:, e:e + 1] * (he @ w2e[e])
    return out.reshape(bsz, seq, d)

def second_inputs(seed: int = 0) -> dict:
    key = jax.random.key(seed)
    ks = iter(jax.random.split(key, 64))
    nrm = lambda shape, s: jax.random.normal(next(ks), shape, jnp.float32) * s
    uni = lambda shape, lo, hi: jax.random.uniform(next(ks), shape, jnp.float32, lo, hi)
    L, D, A, Bw, F = DEPTH_2, D_MODEL, A_WIDTH, B_WIDTH, D_EXPERT
    x = nrm((BATCH, SEQ, D), 1.0)
    c = nrm((BATCH, D), 1.0)
    w_ada = nrm((L, D, 6 * D), D ** -0.5)
    b_ada = nrm((L, 6 * D), 0.02)
    g_mix = 1.0 + nrm((L, D), 0.02)
    w_in = nrm((L, D, IN_COLS), D ** -0.5)
    mu_rkv = uni((L, 3 * A), 0.0, 1.0)
    mu_wag = uni((L, 3, D), 0.0, 1.0)
    w0 = uni((L, A), -6.0, -1.0)
    w1 = nrm((L, D, A_DECAY_RANK), D ** -0.5)
    w2 = nrm((L, A_DECAY_RANK, A), 0.5 * A_DECAY_RANK ** -0.5)
    a0 = nrm((L, A), 0.1)
    a1 = nrm((L, D, A_ICLR_RANK), D ** -0.5)
    a2 = nrm((L, A_ICLR_RANK, A), 0.5 * A_ICLR_RANK ** -0.5)
    g1 = nrm((L, D, A_GATE_RANK), D ** -0.5)
    g2 = nrm((L, A_GATE_RANK, A), A_GATE_RANK ** -0.5)
    k_k = 0.85 + nrm((L, A), 0.02)
    k_a = 1.0 + nrm((L, A), 0.02)
    r_k = nrm((L, A_HEADS, A_HEAD), 0.1)
    lnx_g = 1.0 + nrm((L, A), 0.02)
    lnx_b = nrm((L, A), 0.02)
    conv_w = nrm((L, CONV_WIDTH, 1, Bw), CONV_WIDTH ** -0.5)
    conv_b = nrm((L, Bw), 0.02)
    w_rgate = nrm((L, B_BLOCKS, B_BLOCK, B_BLOCK), B_BLOCK ** -0.5)
    b_rgate = nrm((L, Bw), 0.02)
    w_igate = nrm((L, B_BLOCKS, B_BLOCK, B_BLOCK), B_BLOCK ** -0.5)
    b_igate = nrm((L, Bw), 0.02)
    s = uni((L, Bw), 0.9, 0.999) ** (1.0 / LRU_C)
    lam = jnp.log(s) - jnp.log1p(-s)
    p_a = nrm((L, A, D), A ** -0.5)
    p_b = nrm((L, Bw, D), Bw ** -0.5)
    w_out = nrm((L, D, D), D ** -0.5)
    g_ffn = 1.0 + nrm((L, D), 0.02)
    w_rg = nrm((L, D, N_GROUPS), D ** -0.5)
    b_rg = nrm((L, N_GROUPS), 0.01)
    w_re = nrm((L, D, N_EXPERTS), D ** -0.5)
    b_re = nrm((L, N_EXPERTS), 0.01)
    w1e = nrm((L, N_EXPERTS, D, F), D ** -0.5)
    w3e = nrm((L, N_EXPERTS, D, F), D ** -0.5)
    w2e = nrm((L, N_EXPERTS, F, D), F ** -0.5)
    g_final = 1.0 + nrm((D,), 0.02)
    w_ada_f = nrm((D, 2 * D), D ** -0.5)
    b_ada_f = nrm((2 * D,), 0.02)
    return {'x': x, 'c': c, 'w_ada': w_ada, 'b_ada': b_ada, 'g_mix': g_mix, 'w_in': w_in,
            'mu_rkv': mu_rkv, 'mu_wag': mu_wag, 'w0': w0, 'w1': w1, 'w2': w2,
            'a0': a0, 'a1': a1, 'a2': a2, 'g1': g1, 'g2': g2, 'k_k': k_k, 'k_a': k_a,
            'r_k': r_k, 'lnx_g': lnx_g, 'lnx_b': lnx_b, 'conv_w': conv_w, 'conv_b': conv_b,
            'w_rgate': w_rgate, 'b_rgate': b_rgate, 'w_igate': w_igate, 'b_igate': b_igate,
            'lam': lam, 'p_a': p_a, 'p_b': p_b, 'w_out': w_out, 'g_ffn': g_ffn,
            'w_rg': w_rg, 'b_rg': b_rg, 'w_re': w_re, 'b_re': b_re,
            'w1e': w1e, 'w3e': w3e, 'w2e': w2e,
            'g_final': g_final, 'w_ada_f': w_ada_f, 'b_ada_f': b_ada_f}

def second_block(x, c, w_ada, b_ada, g_mix, w_in, mu_rkv, mu_wag, w0, w1, w2, a0, a1, a2,
              g1, g2, k_k, k_a, r_k, lnx_g, lnx_b, conv_w, conv_b, w_rgate, b_rgate,
              w_igate, b_igate, lam, p_a, p_b, w_out, g_ffn, w_rg, b_rg, w_re, b_re,
              w1e, w3e, w2e, g_final, w_ada_f, b_ada_f):
    c_act = jax.nn.silu(c)
    o1 = 3 * A_WIDTH
    o2 = o1 + B_WIDTH
    o3 = o2 + B_WIDTH
    o4 = o3 + D_MODEL
    for l in range(DEPTH_2):
        mod = c_act @ w_ada[l] + b_ada[l]
        sh1, sc1, gt1, sh2, sc2, gt2 = jnp.split(mod, 6, axis=-1)
        h = modulate(rmsnorm(x, g_mix[l]), sh1, sc1)
        proj = h @ w_in[l]
        y_a = rwkv7_time_mix(h, proj[..., :o1], mu_rkv[l], mu_wag[l], w0[l], w1[l], w2[l],
                             a0[l], a1[l], a2[l], g1[l], g2[l], k_k[l], k_a[l], r_k[l],
                             lnx_g[l], lnx_b[l])
        y_b = rglru_branch(proj[..., o1:o2], proj[..., o2:o3], conv_w[l], conv_b[l],
                           w_rgate[l], b_rgate[l], w_igate[l], b_igate[l], lam[l])
        merged = (jax.nn.sigmoid(proj[..., o3:o4]) * (y_a @ p_a[l])
                  + jax.nn.sigmoid(proj[..., o4:]) * (y_b @ p_b[l]))
        x = x + gt1[:, None, :] * (merged @ w_out[l])
        h2 = modulate(rmsnorm(x, g_ffn[l]), sh2, sc2)
        x = x + gt2[:, None, :] * hier_moe(h2, w_rg[l], b_rg[l], w_re[l], b_re[l],
                                           w1e[l], w3e[l], w2e[l])
    shf, scf = jnp.split(c_act @ w_ada_f + b_ada_f, 2, axis=-1)
    return modulate(rmsnorm(x, g_final), shf, scf)


def setup_inputs(seed=0):
    out = dict(first_inputs(seed))
    for name, value in second_inputs(seed + 1).items():
        if name != "x":
            out[name + "_2"] = value
    return out


def reference(
    x, mem, mix_norm, xattn_norm, mem_norm, ffn_norm, attn_w_in, attn_fox_bf, diff_lq1,
    diff_lk1, diff_lq2, diff_lk2, diff_subln, attn_w_out, mlstm_w_in, mlstm_conv_qk, mlstm_b_i,
    mlstm_b_f, mlstm_head_norm, mlstm_w_out, xattn_wq, xattn_wkv, xattn_wo, ffn_w_up,
    ffn_conv_w, ffn_conv_b, ffn_w_down, final_norm, c_2, w_ada_2, b_ada_2, g_mix_2, w_in_2,
    mu_rkv_2, mu_wag_2, w0_2, w1_2, w2_2, a0_2, a1_2, a2_2, g1_2, g2_2, k_k_2, k_a_2, r_k_2,
    lnx_g_2, lnx_b_2, conv_w_2, conv_b_2, w_rgate_2, b_rgate_2, w_igate_2, b_igate_2, lam_2,
    p_a_2, p_b_2, w_out_2, g_ffn_2, w_rg_2, b_rg_2, w_re_2, b_re_2, w1e_2, w3e_2, w2e_2,
    g_final_2, w_ada_f_2, b_ada_f_2,
):
    x = first_block(
        x, mem, mix_norm, xattn_norm, mem_norm, ffn_norm, attn_w_in, attn_fox_bf, diff_lq1,
        diff_lk1, diff_lq2, diff_lk2, diff_subln, attn_w_out, mlstm_w_in, mlstm_conv_qk,
        mlstm_b_i, mlstm_b_f, mlstm_head_norm, mlstm_w_out, xattn_wq, xattn_wkv, xattn_wo,
        ffn_w_up, ffn_conv_w, ffn_conv_b, ffn_w_down, final_norm,
    )
    return second_block(
        x, c_2, w_ada_2, b_ada_2, g_mix_2, w_in_2, mu_rkv_2, mu_wag_2, w0_2, w1_2, w2_2, a0_2,
        a1_2, a2_2, g1_2, g2_2, k_k_2, k_a_2, r_k_2, lnx_g_2, lnx_b_2, conv_w_2, conv_b_2,
        w_rgate_2, b_rgate_2, w_igate_2, b_igate_2, lam_2, p_a_2, p_b_2, w_out_2, g_ffn_2,
        w_rg_2, b_rg_2, w_re_2, b_re_2, w1e_2, w3e_2, w2e_2, g_final_2, w_ada_f_2, b_ada_f_2,
    )


_drawn_inputs = setup_inputs


def setup_inputs(seed=0):
    import zlib

    import numpy as np

    out = dict(_drawn_inputs(seed))
    spreads = {}
    factors = {'xattn_norm': 8.0,
     'mem_norm': 3.641,
     'diff_lk1': 4.104,
     'diff_lq2': 4.137,
     'mlstm_b_i': 62.53,
     'mlstm_head_norm': 3.059,
     'w2_2': 2.888,
     'a0_2': 3.747,
     'lnx_g_2': 8.0,
     'lnx_b_2': 18.074,
     'b_rgate_2': 26.23,
     'b_igate_2': 6.768,
     'b_rg_2': 8.49,
     'b_re_2': 10.85,
     'g_final_2': 9.606,
     'conv_b_2': 2.695,
     'g_ffn_2': 2.857,
     'b_ada_f_2': 3.122}
    for name, (base, spread) in spreads.items():
        noise = np.random.default_rng([zlib.crc32(name.encode()), seed]).standard_normal(out[name].shape)
        drawn = base * np.exp(spread * noise) if base else spread * noise
        out[name] = __import__('jax').numpy.asarray(drawn.astype(out[name].dtype))
    for name, factor in factors.items():
        out[name] = (out[name] * factor).astype(out[name].dtype)
    return out
```

```python
import math
from contextlib import ExitStack

import concourse.bass as bass
import numpy as np
from concourse import mybir

ACT = mybir.ActivationFunctionType
ALU = mybir.AluOpType
AX = mybir.AxisListType
F32 = mybir.dt.float32
I32 = mybir.dt.int32

P = 128
T = 512
D = 1024
KT = D // P
TT = T // P
MEM = 256
HALF = P // 2
FF = 2816
FT = FF // P
SLOT = 3072
SLOTS = 3
RMS_EPS = 1e-6
NEG = -1e30
LAMBDA_INIT = 0.2
MASKED = -1e30

FOX_PAIRS = 4
DIFF_HEADS = 4
FOX_HEADS = 8
ML_HEADS = 4
X_HEADS = 4
AW = 512
AT = AW // P
CHUNK = 64
NCHUNK = T // CHUNK
GROUPS, PER_GROUP, EXPERTS, FE = 4, 8, 32, 256
IN_FLIGHT = 4
MORE = (2 * T - 1) // P
MOE_TILES = EXPERTS + MORE


class WeightRing:

    def __init__(self, slots, ready):
        self.slots, self.ready, self.loads = slots, ready, [0] * len(slots)


class Units:

    def __init__(self, ring, ap):
        self.ring, self.ap = ring, ap
        self.n, self.per, _, self.width = ap.shape
        self.base = None

    def begin(self):
        self.base = list(self.ring.loads)
        for s in range(self.per):
            self.ring.loads[s] += self.n

    def load(self, sp, i, s):
        sp.dma_start(self.ring.slots[s][:, 0:self.width], self.ap[i, s]).then_inc(self.ring.ready[s], 16)

    def wait(self, pe, i, s):
        pe.wait_ge(self.ring.ready[s], 16 * (self.base[s] + 1) + 16 * i)

    def tile(self, s, k, m, w):
        return self.ring.slots[s][:, k * w + m * P:k * w + (m + 1) * P]

    def rows(self, s, k, w, c0, c1):
        return self.ring.slots[s][:, k * w + c0:k * w + c1]


def first_loads(sp, units):
    if units is not None:
        for s in range(units.per):
            units.load(sp, 0, s)


class Own:

    def __init__(self, eng, sem, i=0, per=0):
        self.eng, self.sem, self.base, self.n = eng, sem, i * per, 0

    def did(self, ins):
        self.n += 1
        return ins.then_inc(self.sem, 1)

    def wait(self):
        self.eng.wait_ge(self.sem, self.base + self.n)


class Core:

    def __init__(self, nc, ctx, A, where):
        self.nc, self.A, self.where = nc, A, where
        self.signals_of = None

        def sb(name, shape, dt=F32):
            return ctx.enter_context(nc.sbuf_tensor(name, shape, dt))

        self.x = sb("x", [P, KT, T])
        self.xn = sb("xn", [P, KT, T])
        self.mix = sb("mix", [P, KT, T])
        self.memn = sb("memn", [P, KT, MEM])
        self.square = sb("square", [P, 2, T])
        self.std = sb("std", [P, T])
        self.rstd = sb("rstd", [P, T])
        self.vecs = sb("vecs", [P, where["width"]])
        self.mod = sb("mod", [P, 64])
        self.gains = sb("gains", [P, 3, KT])
        self.ident = sb("ident", [P, P])
        self.mean_all = sb("mean_all", [P, P])
        self.mean_256 = sb("mean_256", [P, P])
        self.mean_128 = sb("mean_128", [P, P])
        self.ones = sb("ones", [P, P])
        self.head_sum = sb("head_sum", [P, P])
        self.causal = sb("causal", [P, P])
        self.causal_T = sb("causal_T", [P, P])
        self.chunked = sb("chunked", [P, P])
        self.eps = sb("eps", [P, 3])
        self.neg_lam = sb("neg_lam", [P, 1])
        self.ring = WeightRing([sb(f"weights{s}", [P, SLOT]) for s in range(SLOTS)],
                               [ctx.enter_context(nc.semaphore(f"weights_ready{s}")) for s in range(SLOTS)])
        self.bank = [ctx.enter_context(nc.psum_tensor(f"bank{b}", [P, 512], F32)) for b in range(8)]

    def flag(self, ctx, name):
        s = ctx.enter_context(self.nc.semaphore(name))
        if self.signals_of is not ctx:
            self.signals_of, self.signals = ctx, []
            ctx.callback(self.clear, self.signals)
        self.signals.append(s.num)
        return s

    def clear(self, numbers):
        numbers = sorted(numbers)
        first = numbers[0]
        for a, b in zip(numbers, numbers[1:] + [None]):
            if b != a + 1:
                self.nc.gpsimd.sem_clear(range(first, a + 1))
                first = b

    def stage(self, ctx, tag):
        nc = self.nc
        sem = lambda name: self.flag(ctx, name)
        sb = lambda name, shape, dt=F32: ctx.enter_context(nc.sbuf_tensor(f"{tag}_{name}", shape, dt))
        return sem, sb

    def col(self, name, j=0, rows=P):
        c = self.where[name] + j
        return self.vecs[0:rows, c:c + 1]

    def cols(self, name, n, rows=P):
        c = self.where[name]
        return self.vecs[0:rows, c:c + n]

    def col_at(self, name, j, rows=P):
        return self.vecs[0:rows, bass.ds(j + self.where[name], 1)]


class Norm:

    def __init__(self, g, ctx, gain, shift=None, out=None):
        nc = g.nc
        self.g, self.gain, self.shift, self.bank = g, gain, shift, g.bank[7]
        self.out = g.xn if out is None else out
        self.squared = g.flag(ctx, "squared")
        self.summed = g.flag(ctx, "summed")
        self.std_ready = g.flag(ctx, "std_ready")
        self.rstd_ready = g.flag(ctx, "rstd_ready")
        self.scaled = g.flag(ctx, "scaled")
        self.xn_ready = g.flag(ctx, "xn_ready") if shift is not None else self.scaled

    def scalar(self, act):
        g = self.g
        for k in range(KT):
            if k >= 2:
                act.wait_ge(self.summed, k - 1)
            g.nc.scalar.activation(g.square[:, k % 2, :], g.x[:, k, :], ACT.Square).then_inc(self.squared, 1)
        act.wait_ge(self.summed, KT)
        g.nc.scalar.activation(g.std[:, :], self.bank[:, :], ACT.Sqrt, bias=g.eps[:, 0:1]).then_inc(self.std_ready, 1)
        if self.shift is not None:
            for k in range(KT):
                act.wait_ge(self.scaled, k + 1)
                g.nc.scalar.activation(self.out[:, k, :], self.out[:, k, :], ACT.Identity,
                                       bias=self.shift[:, k:k + 1]).then_inc(self.xn_ready, 1)

    def tensor(self, pe):
        g = self.g
        for k in range(KT):
            pe.wait_ge(self.squared, k + 1)
            g.nc.tensor.matmul(self.bank[:, :], g.mean_all[:, :], g.square[:, k % 2, :],
                               start=(k == 0), stop=(k == KT - 1)).then_inc(self.summed, 1)

    def vector(self, dve):
        g = self.g
        dve.wait_ge(self.std_ready, 1)
        g.nc.vector.reciprocal(g.rstd[:, :], g.std[:, :]).then_inc(self.rstd_ready, 1)
        dve.wait_ge(self.rstd_ready, 1)
        for k in range(KT):
            g.nc.vector.scalar_tensor_tensor(self.out[:, k, :], g.x[:, k, :], self.gain[:, k:k + 1], g.rstd[:, :],
                                             ALU.mult, ALU.mult).then_inc(self.scaled, 1)

    def wait(self, eng):
        eng.wait_ge(self.xn_ready, KT)


def log1p_half(dve, own, nc, e, s, s2, p):
    own.did(nc.vector.tensor_scalar(s, e, 2.0, None, ALU.add))
    own.wait()
    own.did(nc.vector.reciprocal(s2, s))
    own.wait()
    own.did(nc.vector.tensor_tensor(s, e, s2, ALU.mult))
    own.wait()
    own.did(nc.vector.tensor_tensor(s2, s, s, ALU.mult))
    own.wait()
    own.did(nc.vector.tensor_scalar(p, s2, 1.0 / 15.0, None, ALU.mult))
    for odd in (13, 11, 9, 7, 5, 3):
        own.wait()
        own.did(nc.vector.scalar_tensor_tensor(p, p, 1.0 / odd, s2, ALU.add, ALU.mult))
    own.wait()
    own.did(nc.vector.scalar_tensor_tensor(p, p, 1.0, s, ALU.add, ALU.mult))
    own.wait()


def stage_setup(g, coming):
    nc = g.nc
    with ExitStack() as ctx:
        x_in, mem_in, vecs_in = (g.flag(ctx, n) for n in ("x_in", "mem_in", "vecs_in"))
        made, filled = g.flag(ctx, "made"), g.flag(ctx, "filled")
        squared, summed = g.flag(ctx, "squared"), g.flag(ctx, "summed")
        std_ready = g.flag(ctx, "std_ready")
        step = g.flag(ctx, "step")
        dots, dots_summed, dots_exp = (g.flag(ctx, n) for n in ("dots", "dots_summed", "dots_exp"))
        prod = ctx.enter_context(nc.sbuf_tensor("prod", [P, 2], F32))
        lam = ctx.enter_context(nc.sbuf_tensor("lam", [P, 2], F32))
        block = ctx.enter_context(nc.Block())

        @block.sync
        def _(sp):
            sp.dma_start(g.vecs[:, :], g.A["vecs"]).then_inc(vecs_in, 16)
            sp.dma_start(g.memn[:, :, :], g.A["mem"]).then_inc(mem_in, 16)
            sp.dma_start(g.x[:, :, :], g.A["x"]).then_inc(x_in, 16)
            first_loads(sp, coming)
            sp.wait_ge(x_in, 16)

        @block.gpsimd
        def _(pool):
            for t, value in ((g.ident, 0.0), (g.mean_all, 1.0 / D), (g.mean_256, 1.0 / 256), (g.mean_128, 1.0 / 128),
                             (g.ones, 1.0), (g.head_sum, 0.0), (g.causal, 0.0), (g.causal_T, 0.0), (g.chunked, 0.0)):
                nc.gpsimd.memset(t[:, :], value).then_inc(made, 1)
            for j, value in enumerate((RMS_EPS, 1e-12, 64e-5)):
                nc.gpsimd.memset(g.eps[:, j:j + 1], value).then_inc(made, 1)
            pool.wait_ge(made, 12)
            nc.gpsimd.affine_select(out=g.ident[:, :], in_=g.ident[:, :], compare_op=ALU.not_equal, fill=1.0, base=0,
                                    pattern=[[-1, P]], channel_multiplier=1).then_inc(made, 1)
            nc.gpsimd.affine_select(out=g.causal[:, :], in_=g.causal[:, :], compare_op=ALU.is_ge, fill=MASKED, base=0,
                                    pattern=[[-1, P]], channel_multiplier=1).then_inc(made, 1)
            nc.gpsimd.affine_select(out=g.causal_T[:, :], in_=g.causal_T[:, :], compare_op=ALU.is_ge, fill=MASKED, base=0,
                                    pattern=[[1, P]], channel_multiplier=-1).then_inc(made, 1)
            pool.wait_ge(made, 15)
            nc.gpsimd.memset(g.chunked[0:HALF, HALF:P], MASKED).then_inc(made, 1)
            for h in range(2):
                pool.wait_ge(made, 16 + h)
                nc.gpsimd.memset(g.head_sum[h * HALF:(h + 1) * HALF, h * HALF:(h + 1) * HALF], 1.0).then_inc(made, 1)
            pool.wait_ge(made, 18)
            nc.gpsimd.engine_nop().then_inc(filled, 1)

        @block.scalar
        def _(act):
            act.wait_ge(mem_in, 16)
            for k in range(KT):
                if k >= 2:
                    act.wait_ge(summed, k - 1)
                nc.scalar.activation(g.square[:, k % 2, 0:MEM], g.memn[:, k, :], ACT.Square).then_inc(squared, 1)
            act.wait_ge(summed, KT)
            nc.scalar.activation(g.std[:, 0:MEM], g.bank[0][:, 0:MEM], ACT.Sqrt, bias=g.eps[:, 0:1]).then_inc(std_ready, 1)
            act.wait_ge(dots_summed, 1)
            nc.scalar.activation(lam[:, :], g.bank[1][:, 0:2], ACT.Exp).then_inc(dots_exp, 1)

        @block.tensor
        def _(pe):
            pe.wait_ge(filled, 1)
            for k in range(KT):
                pe.wait_ge(squared, k + 1)
                nc.tensor.matmul(g.bank[0][:, 0:MEM], g.mean_all[:, :], g.square[:, k % 2, 0:MEM],
                                 start=(k == 0), stop=(k == KT - 1)).then_inc(summed, 1)
            pe.wait_ge(dots, 2)
            nc.tensor.matmul(g.bank[1][:, 0:2], g.ones[:, :], prod[:, :], start=True, stop=True).then_inc(dots_summed, 1)

        @block.vector
        def _(dve):
            dve.wait_ge(vecs_in, 16)
            for j in range(2):
                nc.vector.tensor_tensor(prod[:, j:j + 1], g.col("diff_l", 2 * j), g.col("diff_l", 2 * j + 1),
                                        ALU.mult).then_inc(dots, 1)
            own = Own(dve, step)
            dve.wait_ge(std_ready, 1)
            own.did(nc.vector.reciprocal(g.rstd[:, 0:MEM], g.std[:, 0:MEM]))
            own.wait()
            for k in range(KT):
                own.did(nc.vector.tensor_tensor(g.memn[:, k, :], g.memn[:, k, :], g.rstd[:, 0:MEM], ALU.mult))
            dve.wait_ge(dots_exp, 1)
            own.did(nc.vector.scalar_tensor_tensor(g.neg_lam[:, :], lam[:, 1:2], -LAMBDA_INIT, lam[:, 0:1],
                                                   ALU.add, ALU.subtract))


def stage_dense_residual(g, units, coming, src, kt, wide, gate=None):
    nc = g.nc
    units.begin()
    w = wide * P
    per = units.per * wide
    with ExitStack() as ctx:
        done = g.flag(ctx, "product_done")
        free = g.flag(ctx, "bank_free")
        block = ctx.enter_context(nc.Block())

        @block.sync
        def _(sp):
            if units.n > 1:
                with sp.Fori(1, units.n) as i:
                    for s in range(units.per):
                        sp.wait_ge(done, per * i - per + (s + 1) * wide)
                        units.load(sp, i, s)
            sp.wait_ge(done, per * units.n)
            first_loads(sp, coming)

        @block.tensor
        def _(pe):
            with pe.Fori(0, units.n) as i:
                for s in range(units.per):
                    units.wait(pe, i, s)
                    for m in range(wide):
                        b = s * wide + m
                        pe.wait_ge(free, per * i + b + 1)
                        for k in range(kt):
                            mm = nc.tensor.matmul(g.bank[b][:, :], units.tile(s, k, m, w), src[:, k, :],
                                                  start=(k == 0), stop=(k == kt - 1))
                        mm.then_inc(done, 1)

        @block.vector
        def _(dve):
            dve.sem_inc(free, per)
            with dve.Fori(0, units.n) as i:
                for b in range(per):
                    dve.wait_ge(done, per * i + b + 1)
                    here = g.x[:, bass.ds(per * i + b, 1), :]
                    if gate is None:
                        nc.vector.tensor_tensor(here, g.bank[b][:, :], here, ALU.add).then_inc(free, 1)
                    else:
                        nc.vector.scalar_tensor_tensor(here, g.bank[b][:, :], gate[:, bass.ds(per * i + b, 1)], here,
                                                       ALU.mult, ALU.add).then_inc(free, 1)


LOGITS = {3: [(0, 3, 0)], 4: [(0, 2, 0), (0, 0, 384)], 5: [(1, 3, 0)], 6: [(1, 2, 0), (1, 0, 384)],
          7: [(0, 1, 0)], 1: [(1, 1, 0)]}
NLOG = len(LOGITS)


def stage_attention(g, units, coming, fox):
    nc = g.nc
    units.begin()
    scale = HALF ** -0.5
    maps = 2 if fox else 1
    first = 0 if fox else FOX_PAIRS
    turned = 4 * maps
    with ExitStack() as ctx:
        sem, sb = g.stage(ctx, "fox" if fox else "diff")
        proj_done, q_ready, k_ready, vT_ready, vt_done, v_ready = (
            sem(n) for n in ("proj_done", "q_ready", "k_ready", "vT_ready", "vt_done", "v_ready"))
        logits_done, max_done, exp_done, p_ready = (sem(n) for n in ("logits_done", "max_done", "exp_done", "p_ready"))
        turned_done, turned_even, turned_odd = (sem(n) for n in ("turned_done", "turned_even", "turned_odd"))
        values_done, mixed = sem("values_done"), sem("mixed")
        step, rows_ready = sem("step"), sem("rows_ready")
        gate_done, gate_abs, gate_exp, forget_ready = (sem(n) for n in ("gate_done", "gate_abs", "gate_exp", "forget_ready"))
        head_squared, head_summed, head_std, head_rstd = (sem(n) for n in ("head_squared", "head_summed", "head_std", "head_rstd"))
        qT, kT, vT = sb("qT", [P, T]), sb("kT", [P, T]), sb("vT", [P, T])
        v = sb("v", [P, TT, P])
        probs = sb("probs", [P, 2, TT, T])
        probs_T = sb("probs_T", [P, 2, TT, T])
        neg_max, total, inv = sb("neg_max", [P, 8]), sb("total", [P, 8]), sb("inv", [P, 8])
        if fox:
            norm = Norm(g, ctx, g.cols("mix_norm0", KT))
            F = sb("F", [FOX_HEADS, T])
            tmp = [sb(f"gate_tmp{j}", [FOX_HEADS, T]) for j in range(5)]
            rows = sb("rows", [FOX_HEADS, 2, T])
            minus = sb("minus", [FOX_HEADS, P])
        else:
            sub_gain = sb("sub_gain", [P, 1])
        block = ctx.enter_context(nc.Block())

        @block.sync
        def _(sp):
            with sp.Fori(1, units.n) as i:
                sp.wait_ge(proj_done, 3 * i)
                units.load(sp, i, 0)
            sp.wait_ge(proj_done, 3 * units.n)
            first_loads(sp, coming)

        @block.tensor
        def _(pe):
            pe.sem_inc(turned_even, 1)
            pe.sem_inc(turned_odd, 1)
            pe.sem_inc(mixed, 1)
            pe.sem_inc(exp_done, 1)
            if fox:
                norm.tensor(pe)
                norm.wait(pe)
                for k in range(KT):
                    mm = nc.tensor.matmul(g.bank[6][0:FOX_HEADS, :], g.cols("w_forget", KT * FOX_HEADS)[:, k * FOX_HEADS:(k + 1) * FOX_HEADS],
                                          g.xn[:, k, :], start=(k == 0), stop=(k == KT - 1))
                mm.then_inc(gate_done, 1)
                pe.wait_ge(forget_ready, 1)
            with pe.Fori(0, units.n) as i:
                units.wait(pe, i, 0)
                pe.wait_ge(turned_even, turned // 2 * i + 1)
                pe.wait_ge(turned_odd, turned // 2 * i + 1)
                pe.wait_ge(mixed, i + 1)
                for j in range(3):
                    for k in range(KT):
                        mm = nc.tensor.matmul(g.bank[j][:, :], units.tile(0, k, j, 3 * P), g.xn[:, k, :],
                                              start=(k == 0), stop=(k == KT - 1))
                    mm.then_inc(proj_done, 1)
                pe.wait_ge(q_ready, i + 1)
                pe.wait_ge(k_ready, i + 1)
                pe.wait_ge(exp_done, NLOG * i + 1)
                if fox:
                    pe.wait_ge(rows_ready, 2 * i + 2)
                for b, places in LOGITS.items():
                    for m, qb, c in places:
                        keys = (qb + 1) * P
                        half = slice(m * HALF, (m + 1) * HALF)
                        out = g.bank[b][:, c:c + keys]
                        nc.tensor.matmul(out, qT[half, qb * P:(qb + 1) * P], kT[half, 0:keys], start=True, stop=False)
                        if fox:
                            nc.tensor.matmul(out, minus[:, :], rows[:, m, 0:keys], start=False, stop=False)
                        mm = nc.tensor.matmul(g.bank[b][:, c + keys - P:c + keys], g.ident[:, :],
                                              (g.causal if fox else g.chunked)[:, :], start=False, stop=True)
                    mm.then_inc(logits_done, 1)
                pe.wait_ge(vT_ready, i + 1)
                for t in range(TT):
                    mm = nc.tensor.transpose(g.bank[0][:, t * P:(t + 1) * P], vT[:, t * P:(t + 1) * P], g.ident[:, :])
                mm.then_inc(vt_done, 1)
                pe.wait_ge(v_ready, i + 1)
                for m in range(maps):
                    for n, qb in enumerate((3, 2, 1, 0)):
                        pe.wait_ge(p_ready, 4 * maps * i + 4 * m + n + 1)
                        count = turned // 2 * i + (4 * m + n) // 2
                        if 4 * m + n >= 2:
                            pe.wait_ge((turned_even, turned_odd)[n % 2], count + 1)
                        for kb in range(qb + 1):
                            mm = nc.tensor.transpose(g.bank[n % 2][:, kb * P:(kb + 1) * P],
                                                     probs[:, m, qb, kb * P:(kb + 1) * P], g.ident[:, :])
                        mm.then_inc(turned_done, 1)
                    pe.wait_ge(turned_even, turned // 2 * i + 2 * (m + 1) + 1)
                    pe.wait_ge(turned_odd, turned // 2 * i + 2 * (m + 1) + 1)
                    own = slice(m * HALF, (m + 1) * HALF) if fox else slice(0, P)
                    for kb in range(TT):
                        mm = nc.tensor.matmul(g.bank[2][own, kb * P:T], v[:, kb, own], probs_T[:, m, kb, kb * P:T],
                                              start=(kb == 0), stop=(kb == TT - 1), skip_group_check=True)
                mm.then_inc(values_done, 1)
                if not fox:
                    pe.wait_ge(head_squared, i + 1)
                    nc.tensor.matmul(g.bank[0][:, :], g.mean_128[:, :], g.square[:, 0, :], start=True, stop=True)\
                      .then_inc(head_summed, 1)
                    pe.wait_ge(head_std, i + 1)

        @block.scalar
        def _(act):
            if fox:
                norm.scalar(act)
                act.wait_ge(gate_abs, 1)
                nc.scalar.activation(tmp[1][:, :], tmp[1][:, :], ACT.Exp, scale=-1.0).then_inc(gate_exp, 1)
            with act.Fori(0, units.n) as i:
                act.wait_ge(proj_done, 3 * i + 1)
                nc.scalar.activation(qT[:, :], g.bank[0][:, :], ACT.Copy, scale=scale).then_inc(q_ready, 1)
                act.wait_ge(proj_done, 3 * i + 3)
                nc.scalar.activation(vT[:, :], g.bank[2][:, :], ACT.Copy).then_inc(vT_ready, 1)
                for j, (b, places) in enumerate(LOGITS.items()):
                    act.wait_ge(max_done, NLOG * i + j + 1)
                    for m, qb, c in places:
                        keys, n = (qb + 1) * P, 4 * m + qb
                        e = nc.scalar.activation(probs[:, m, qb, 0:keys], g.bank[b][:, c:c + keys], ACT.Exp,
                                                 bias=neg_max[:, n:n + 1], accum_out=total[:, n:n + 1])
                    e.then_inc(exp_done, 1)
                for m in range(maps):
                    for n, qb in ((0, 3), (2, 1)):
                        act.wait_ge(turned_done, turned * i + 4 * m + n + 1)
                        nc.scalar.activation(probs_T[:, m, 0:qb + 1, qb * P:(qb + 1) * P],
                                             g.bank[0][:, 0:(qb + 1) * P].rearrange("p (a b) -> p a b", b=P),
                                             ACT.Copy).then_inc(turned_even, 1)
                act.wait_ge(values_done, i + 1)
                if fox:
                    nc.scalar.activation(g.mix[:, bass.ds(i + first, 1), :], g.bank[2][:, :], ACT.Copy).then_inc(mixed, 1)
                else:
                    nc.scalar.activation(g.square[:, 0, :], g.bank[2][:, :], ACT.Square).then_inc(head_squared, 1)
                    act.wait_ge(head_summed, i + 1)
                    nc.scalar.activation(g.std[:, :], g.bank[0][:, :], ACT.Sqrt, bias=g.eps[:, 0:1]).then_inc(head_std, 1)

        @block.vector
        def _(dve):
            if fox:
                norm.vector(dve)
                z, e = tmp[0], tmp[1]
                own = Own(dve, step)
                dve.wait_ge(gate_done, 1)
                own.did(nc.vector.tensor_scalar(z[:, :], g.bank[6][0:FOX_HEADS, :], g.col("fox_bf", rows=FOX_HEADS), None, ALU.add))
                own.wait()
                nc.vector.scalar_tensor_tensor(e[:, :], z[:, :], -1.0, z[:, :], ALU.mult, ALU.max).then_inc(gate_abs, 1)
                own.did(nc.vector.memset(minus[:, :], -1.0))
                own.did(nc.vector.tensor_scalar(z[:, :], z[:, :], 0.0, None, ALU.min))
                dve.wait_ge(gate_exp, 1)
                log1p_half(dve, own, nc, e[:, :], tmp[2][:, :], tmp[3][:, :], tmp[4][:, :])
                own.did(nc.vector.scalar_tensor_tensor(z[:, :], tmp[4][:, :], -2.0, z[:, :], ALU.mult, ALU.add))
                own.did(nc.vector.memset(e[:, :], 1.0))
                own.wait()
                nc.vector.tensor_tensor_scan(F[:, :], e[:, :], z[:, :], 0.0, ALU.mult, ALU.add).then_inc(forget_ready, 1)
                dve.wait_ge(forget_ready, 1)
                opening = own.n
            else:
                own = Own(dve, step)
                own.did(nc.vector.tensor_scalar(sub_gain[:, :], g.col("subln"), 1.0 - LAMBDA_INIT, None, ALU.mult))
                own.wait()
                opening = own.n
            per = 1 if fox else 6
            with dve.Fori(0, units.n) as i:
                own = Own(dve, step, i, per)
                own.base = own.base + opening
                if fox:
                    for m in range(2):
                        nc.vector.tensor_scalar(rows[:, m, :], F[:, :], g.ident[0:FOX_HEADS, bass.ds(2 * i + m, 1)],
                                                None, ALU.mult).then_inc(rows_ready, 1)
                dve.wait_ge(proj_done, 3 * i + 2)
                nc.vector.tensor_copy(kT[:, :], g.bank[1][:, :]).then_inc(k_ready, 1)
                for j, (b, places) in enumerate(LOGITS.items()):
                    dve.wait_ge(logits_done, NLOG * i + j + 1)
                    for m, qb, c in places:
                        keys, n = (qb + 1) * P, 4 * m + qb
                        r = nc.vector.tensor_reduce(neg_max[:, n:n + 1], g.bank[b][:, c:c + keys], AX.X, ALU.max, negate=True)
                    r.then_inc(max_done, 1)
                dve.wait_ge(vt_done, i + 1)
                nc.vector.tensor_copy(v[:, :, :], g.bank[0][:, :].rearrange("p (a b) -> p a b", b=P)).then_inc(v_ready, 1)
                dve.wait_ge(exp_done, NLOG * i + NLOG + 1)
                own.did(nc.vector.reciprocal(inv[:, :], total[:, :]))
                own.wait()
                if fox:
                    for m in range(2):
                        for qb in (3, 2, 1, 0):
                            here, n = probs[:, m, qb, 0:(qb + 1) * P], 4 * m + qb
                            nc.vector.tensor_scalar(here, here, inv[:, n:n + 1], None, ALU.mult).then_inc(p_ready, 1)
                else:
                    own.did(nc.vector.tensor_scalar(inv[:, 4:8], inv[:, 4:8], g.neg_lam[:, 0:1], None, ALU.mult))
                    for qb in (3, 2, 1, 0):
                        here = probs[:, 0, qb, 0:(qb + 1) * P]
                        own.did(nc.vector.tensor_scalar(here, here, inv[:, qb:qb + 1], None, ALU.mult))
                        own.wait()
                        nc.vector.scalar_tensor_tensor(here, probs[:, 1, qb, 0:(qb + 1) * P], inv[:, 4 + qb:5 + qb], here,
                                                       ALU.mult, ALU.add).then_inc(p_ready, 1)
                for m in range(maps):
                    for n, qb in ((1, 2), (3, 0)):
                        dve.wait_ge(turned_done, turned * i + 4 * m + n + 1)
                        nc.vector.tensor_copy(probs_T[:, m, 0:qb + 1, qb * P:(qb + 1) * P],
                                              g.bank[1][:, 0:(qb + 1) * P].rearrange("p (a b) -> p a b", b=P))\
                          .then_inc(turned_odd, 1)
                if not fox:
                    dve.wait_ge(head_std, i + 1)
                    nc.vector.reciprocal(g.rstd[:, :], g.std[:, :]).then_inc(head_rstd, 1)
                    dve.wait_ge(head_rstd, i + 1)
                    nc.vector.scalar_tensor_tensor(g.mix[:, bass.ds(i + first, 1), :], g.bank[2][:, :], sub_gain[:, 0:1],
                                                   g.rstd[:, :], ALU.mult, ALU.mult).then_inc(mixed, 1)


def stage_cross_attention(g, units, coming, layer):
    nc = g.nc
    units.begin()
    HD = D // X_HEADS
    scale = HD ** -0.5
    with ExitStack() as ctx:
        sem, sb = g.stage(ctx, f"cross{layer}")
        norm = Norm(g, ctx, g.cols(f"xattn_norm{layer}", KT))
        mem_ready, proj_done, q_ready, k_ready, v_ready = (sem(n) for n in ("mem_ready", "proj_done", "q_ready", "k_ready", "v_ready"))
        logits_done, max_done, exp_done, inv_ready, p_ready = (
            sem(n) for n in ("logits_done", "max_done", "exp_done", "inv_ready", "p_ready"))
        turned_done, pT_ready, values_done, mixed = (sem(n) for n in ("turned_done", "pT_ready", "values_done", "mixed"))
        memg = sb("memg", [P, KT, MEM])
        qT, kT = sb("qT", [P, 2, T]), sb("kT", [P, 2, MEM])
        v = sb("v", [P, 2, HD])
        probs, probs_T = sb("probs", [P, TT, MEM]), sb("probs_T", [P, 2, T])
        neg_max, total, inv = sb("neg_max", [P, TT]), sb("total", [P, TT]), sb("inv", [P, TT])
        block = ctx.enter_context(nc.Block())

        @block.sync
        def _(sp):
            with sp.Fori(1, units.n) as i:
                for s in range(units.per):
                    sp.wait_ge(proj_done, 4 * i - 4 + (2, 3, 4)[s])
                    units.load(sp, i, s)
            sp.wait_ge(proj_done, 4 * units.n)
            first_loads(sp, coming)

        @block.tensor
        def _(pe):
            pe.sem_inc(mixed, 1)
            pe.sem_inc(k_ready, 1)
            pe.sem_inc(v_ready, 1)
            pe.sem_inc(exp_done, 1)
            pe.sem_inc(pT_ready, 1)
            norm.tensor(pe)
            norm.wait(pe)
            pe.wait_ge(mem_ready, KT)
            with pe.Fori(0, units.n) as i:
                units.wait(pe, i, 0)
                pe.wait_ge(mixed, 2 * i + 1)
                for m in range(2):
                    for k in range(KT):
                        mm = nc.tensor.matmul(g.bank[m][:, :], units.tile(0, k, m, HD), g.xn[:, k, :],
                                              start=(k == 0), stop=(k == KT - 1))
                    mm.then_inc(proj_done, 1)
                units.wait(pe, i, 1)
                pe.wait_ge(k_ready, i + 1)
                for m in range(2):
                    for k in range(KT):
                        mm = nc.tensor.matmul(g.bank[2][:, m * MEM:(m + 1) * MEM], units.tile(1, k, m, HD), memg[:, k, :],
                                              start=(k == 0), stop=(k == KT - 1))
                mm.then_inc(proj_done, 1)
                units.wait(pe, i, 2)
                pe.wait_ge(v_ready, i + 1)
                for t in range(2):
                    for k in range(KT):
                        mm = nc.tensor.matmul(g.bank[3][:, t * HD:(t + 1) * HD], memg[:, k, t * P:(t + 1) * P],
                                              units.rows(2, k, HD, 0, HD), start=(k == 0), stop=(k == KT - 1))
                mm.then_inc(proj_done, 1)
                pe.wait_ge(q_ready, 2 * i + 2)
                pe.wait_ge(k_ready, i + 2)
                pe.wait_ge(exp_done, 2 * i + 1)
                for b in range(2):
                    for j in range(2):
                        qb = 2 * b + j
                        for m in range(2):
                            mm = nc.tensor.matmul(g.bank[4 + b][:, j * MEM:(j + 1) * MEM], qT[:, m, qb * P:(qb + 1) * P],
                                                  kT[:, m, :], start=(m == 0), stop=(m == 1))
                    mm.then_inc(logits_done, 1)
                pe.wait_ge(p_ready, i + 1)
                pe.wait_ge(pT_ready, 2 * i + 1)
                for t in range(2):
                    for qb in range(TT):
                        mm = nc.tensor.transpose(g.bank[6 + t][:, qb * P:(qb + 1) * P], probs[:, qb, t * P:(t + 1) * P], g.ident[:, :])
                    mm.then_inc(turned_done, 1)
                pe.wait_ge(pT_ready, 2 * i + 3)
                pe.wait_ge(v_ready, i + 2)
                for m in range(2):
                    for t in range(2):
                        mm = nc.tensor.matmul(g.bank[m][:, :], v[:, t, m * P:(m + 1) * P], probs_T[:, t, :],
                                              start=(t == 0), stop=(t == 1))
                    mm.then_inc(values_done, 1)

        @block.scalar
        def _(act):
            norm.scalar(act)
            with act.Fori(0, units.n) as i:
                for m in range(2):
                    act.wait_ge(proj_done, 4 * i + m + 1)
                    nc.scalar.activation(qT[:, m, :], g.bank[m][:, :], ACT.Copy, scale=scale).then_inc(q_ready, 1)
                for b in range(2):
                    act.wait_ge(max_done, 2 * i + b + 1)
                    for j in range(2):
                        qb = 2 * b + j
                        e = nc.scalar.activation(probs[:, qb, :], g.bank[4 + b][:, j * MEM:(j + 1) * MEM], ACT.Exp,
                                                 bias=neg_max[:, qb:qb + 1], accum_out=total[:, qb:qb + 1])
                    e.then_inc(exp_done, 1)
                for m in range(2):
                    act.wait_ge(values_done, 2 * i + m + 1)
                    nc.scalar.activation(g.mix[:, bass.ds(2 * i + m, 1), :], g.bank[m][:, :], ACT.Copy).then_inc(mixed, 1)

        @block.vector
        def _(dve):
            for k in range(KT):
                nc.vector.tensor_scalar(memg[:, k, :], g.memn[:, k, :], g.col(f"mem_norm{layer}", k), None,
                                        ALU.mult).then_inc(mem_ready, 1)
            norm.vector(dve)
            with dve.Fori(0, units.n) as i:
                dve.wait_ge(proj_done, 4 * i + 3)
                nc.vector.tensor_copy(kT[:, :, :], g.bank[2][:, :].rearrange("p (a b) -> p a b", b=MEM)).then_inc(k_ready, 1)
                dve.wait_ge(proj_done, 4 * i + 4)
                nc.vector.tensor_copy(v[:, :, :], g.bank[3][:, :].rearrange("p (a b) -> p a b", b=HD)).then_inc(v_ready, 1)
                for b in range(2):
                    dve.wait_ge(logits_done, 2 * i + b + 1)
                    nc.vector.tensor_reduce(neg_max[:, 2 * b:2 * b + 2], g.bank[4 + b][:, :].rearrange("p (a b) -> p a b", b=MEM),
                                            AX.X, ALU.max, negate=True).then_inc(max_done, 1)
                dve.wait_ge(exp_done, 2 * i + 3)
                nc.vector.reciprocal(inv[:, :], total[:, :]).then_inc(inv_ready, 1)
                dve.wait_ge(inv_ready, i + 1)
                for qb in range(TT):
                    p = nc.vector.tensor_scalar(probs[:, qb, :], probs[:, qb, :], inv[:, qb:qb + 1], None, ALU.mult)
                p.then_inc(p_ready, 1)
                for t in range(2):
                    dve.wait_ge(turned_done, 2 * i + t + 1)
                    nc.vector.tensor_copy(probs_T[:, t, :], g.bank[6 + t][:, :]).then_inc(pT_ready, 1)


def stage_ffn_up(g, units, coming, layer, h):
    nc = g.nc
    units.begin()
    W = 2 * P
    with ExitStack() as ctx:
        sem, sb = g.stage(ctx, f"up{layer}")
        norm = Norm(g, ctx, g.cols(f"ffn_norm{layer}", KT))
        done, now_done, tap1_done, conv_done, gelu_done, h_done = (
            sem(n) for n in ("product_done", "now_done", "tap1_done", "conv_done", "gelu_done", "h_done"))
        y = sb("y", [P, 4, T])
        block = ctx.enter_context(nc.Block())

        def tap(j, i, b):
            return g.col_at(f"ffn_conv{layer}", 2 * i + b // 2 + (b % 2) * FT + j * 2 * FT)

        @block.sync
        def _(sp):
            with sp.Fori(1, units.n) as i:
                for s in range(2):
                    sp.wait_ge(done, 4 * i - 4 + 2 * s + 2)
                    units.load(sp, i, s)
            sp.wait_ge(done, 4 * units.n)
            first_loads(sp, coming)

        @block.tensor
        def _(pe):
            norm.tensor(pe)
            norm.wait(pe)
            with pe.Fori(0, units.n) as i:
                for b in range(4):
                    if b % 2 == 0:
                        units.wait(pe, i, b // 2)
                    pe.wait_ge(conv_done, 4 * i - 4 + b + 1 + 4)
                    for k in range(KT):
                        mm = nc.tensor.matmul(g.bank[b][:, :], units.tile(b // 2, k, b % 2, W), g.xn[:, k, :],
                                              start=(k == 0), stop=(k == KT - 1))
                    mm.then_inc(done, 1)

        @block.scalar
        def _(act):
            act.sem_inc(h_done, 1)
            norm.scalar(act)
            with act.Fori(0, units.n) as i:
                for b in range(4):
                    act.wait_ge(done, 4 * i + b + 1)
                    act.wait_ge(h_done, 2 * i + 1)
                    nc.scalar.activation(y[:, b, :], g.bank[b][:, :], ACT.Identity, scale=tap(2, i, b),
                                         bias=tap(3, i, b)).then_inc(now_done, 1)
                    if b % 2 == 1:
                        act.wait_ge(conv_done, 4 * i + b + 4)
                        nc.scalar.activation(y[:, b - 1, :], y[:, b - 1, :], ACT.Gelu_apprx_tanh).then_inc(gelu_done, 1)

        @block.vector
        def _(dve):
            norm.vector(dve)
            dve.sem_inc(conv_done, 4)
            with dve.Fori(0, units.n) as i:
                for b in range(4):
                    dve.wait_ge(now_done, 4 * i + b + 1)
                    nc.vector.scalar_tensor_tensor(y[:, b, 1:T], g.bank[b][:, 0:T - 1], tap(1, i, b), y[:, b, 1:T],
                                                   ALU.mult, ALU.add).then_inc(tap1_done, 1)
                    dve.wait_ge(tap1_done, 4 * i + b + 1)
                    nc.vector.scalar_tensor_tensor(y[:, b, 2:T], g.bank[b][:, 0:T - 2], tap(0, i, b), y[:, b, 2:T],
                                                   ALU.mult, ALU.add).then_inc(conv_done, 1)
                    if b % 2 == 1:
                        dve.wait_ge(gelu_done, 2 * i + b // 2 + 1)
                        dve.wait_ge(conv_done, 4 * i + b + 5)
                        nc.vector.tensor_tensor(h[:, bass.ds(2 * i + b // 2, 1), :], y[:, b - 1, :], y[:, b, :],
                                                ALU.mult).then_inc(h_done, 1)


def stage_mlstm(g, units, coming):
    nc = g.nc
    units.begin()
    H, VD, W = ML_HEADS, 2 * P, 2 * P
    scale = P ** -0.5
    with ExitStack() as ctx:
        sem, sb = g.stage(ctx, "mlstm")
        norm = Norm(g, ctx, g.cols("mix_norm1", KT))
        gate_done, gate_abs, gate_exp, neg_m_ready, em_ready, G_ready, G_turned, Gc_ready = (
            sem(n) for n in ("gate_done", "gate_abs", "gate_exp", "neg_m_ready", "em_ready", "G_ready", "G_turned", "Gc_ready"))
        proj_done, now_done, conv_done, qk_ready, og_ready, v_ready, rows_ready = (
            sem(n) for n in ("proj_done", "now_done", "conv_done", "qk_ready", "og_ready", "v_ready", "rows_ready"))
        scores_done, weights_done, p_ready, sums_done, den_abs, h_ready = (
            sem(n) for n in ("scores_done", "weights_done", "p_ready", "sums_done", "den_abs", "h_ready"))
        squared, mean_done, std_ready, mixed, step = (sem(n) for n in ("head_squared", "mean_done", "head_std", "mixed", "step"))
        tmp = [sb(f"tmp{j}", [H, T]) for j in range(5)]
        ig, G, top = sb("ig", [H, T]), sb("G", [H, T]), sb("top", [H, T])
        em = sb("em", [H, T])
        rows = sb("rows", [H, 2, T])
        Gc = sb("Gc", [P, TT, H])
        y = sb("y", [P, 2, T])
        qk = sb("qk", [P, 2, T])
        og, h = sb("og", [P, 2, T]), sb("h", [P, 2, T])
        v = sb("v", [P, TT, VD])
        wts = sb("wts", [P, 2, T])
        probs_T = sb("probs_T", [P, TT, T])
        den = sb("den", [P, T])
        sq = sb("sq", [P, 2, T])
        block = ctx.enter_context(nc.Block())

        @block.sync
        def _(sp):
            with sp.Fori(1, units.n) as i:
                for s in range(3):
                    sp.wait_ge(proj_done, 6 * i - 6 + 2 * s + 2)
                    units.load(sp, i, s)
            sp.wait_ge(proj_done, 6 * units.n)
            first_loads(sp, coming)

        @block.tensor
        def _(pe):
            pe.sem_inc(h_ready, 1)
            pe.sem_inc(std_ready, 1)
            pe.sem_inc(p_ready, 1)
            norm.tensor(pe)
            norm.wait(pe)
            for j in range(2):
                for k in range(KT):
                    c = k * 2 * H + j * H
                    mm = nc.tensor.matmul(g.bank[6 - j][0:H, :], g.cols("w_gates", KT * 2 * H)[:, c:c + H], g.xn[:, k, :],
                                          start=(k == 0), stop=(k == KT - 1))
                mm.then_inc(gate_done, 1)
            pe.wait_ge(G_ready, 1)
            for t in range(TT):
                mm = nc.tensor.transpose(g.bank[4][:, t * H:(t + 1) * H], G[:, t * P:(t + 1) * P], g.ident[0:H, 0:H])
            mm.then_inc(G_turned, 1)
            pe.wait_ge(Gc_ready, 1)
            with pe.Fori(0, units.n) as i:
                pe.wait_ge(h_ready, 2 * i + 1)
                for j in range(2):
                    if j == 0:
                        units.wait(pe, i, 0)
                    for k in range(KT):
                        mm = nc.tensor.matmul(g.bank[j][:, :], units.tile(0, k, j, W), g.xn[:, k, :],
                                              start=(k == 0), stop=(k == KT - 1))
                    mm.then_inc(proj_done, 1)
                units.wait(pe, i, 1)
                pe.wait_ge(std_ready, i + 1)
                for t in range(TT):
                    for k in range(KT):
                        mm = nc.tensor.matmul(g.bank[2 + t // 2][:, t % 2 * VD:(t % 2 + 1) * VD], g.xn[:, k, t * P:(t + 1) * P],
                                              units.rows(1, k, W, 0, VD), start=(k == 0), stop=(k == KT - 1))
                    if t % 2 == 1:
                        mm.then_inc(proj_done, 1)
                units.wait(pe, i, 2)
                pe.wait_ge(p_ready, 4 * i + 1)
                for j in range(2):
                    for k in range(KT):
                        mm = nc.tensor.matmul(g.bank[4 + j][:, :], units.tile(2, k, j, W), g.xn[:, k, :],
                                              start=(k == 0), stop=(k == KT - 1))
                    mm.then_inc(proj_done, 1)
                pe.wait_ge(qk_ready, 2 * i + 2)
                pe.wait_ge(rows_ready, 2 * i + 2)
                for kb in range(TT):
                    A, B = (g.bank[6], g.bank[7]) if kb % 2 == 0 else (g.bank[4], g.bank[5])
                    n = T - kb * P
                    if kb == 1:
                        pe.wait_ge(og_ready, 2 * i + 2)
                    if kb >= 2:
                        pe.wait_ge(p_ready, 4 * i + kb)
                    nc.tensor.matmul(A[:, 0:n], qk[:, 1, kb * P:(kb + 1) * P], qk[:, 0, kb * P:T], start=True, stop=True)
                    nc.tensor.matmul(B[:, 0:n], g.ones[0:H, :], rows[:, 0, kb * P:T], start=True, stop=False)
                    nc.tensor.matmul(B[:, 0:P], g.ident[:, :], g.causal_T[:, :], start=False, stop=True)\
                      .then_inc(scores_done, 1)
                pe.wait_ge(v_ready, 2 * i + 2)
                nc.tensor.matmul(g.bank[3][:, :], g.ones[0:H, :], rows[:, 1, :], start=True, stop=True)
                for kb in range(TT):
                    pe.wait_ge(p_ready, 4 * i + kb + 2)
                    for j in range(3):
                        left = v[:, kb, j * P:(j + 1) * P] if j < 2 else g.ones[:, :]
                        mm = nc.tensor.matmul(g.bank[j][:, kb * P:T], left, probs_T[:, kb, kb * P:T], start=(kb == 0),
                                              stop=(kb == TT - 1), skip_group_check=True)
                mm.then_inc(sums_done, 1)
                for j in range(2):
                    pe.wait_ge(squared, 2 * i + j + 1)
                    mm = nc.tensor.matmul(g.bank[3][:, :], g.mean_256[:, :], sq[:, j, :], start=(j == 0), stop=(j == 1))
                mm.then_inc(mean_done, 1)

        @block.scalar
        def _(act):
            act.sem_inc(mixed, 1)
            norm.scalar(act)
            act.wait_ge(gate_abs, 1)
            nc.scalar.activation(tmp[1][:, :], tmp[1][:, :], ACT.Exp, scale=-1.0).then_inc(gate_exp, 1)
            act.wait_ge(neg_m_ready, 1)
            nc.scalar.activation(em[:, :], tmp[0][:, :], ACT.Exp).then_inc(em_ready, 1)
            with act.Fori(0, units.n) as i:
                for j in range(2):
                    act.wait_ge(proj_done, 6 * i + j + 1)
                    nc.scalar.activation(y[:, j, :], g.bank[j][:, :], ACT.Copy,
                                         scale=g.col_at("conv_qk", i + 3 * 2 * H + j * H)).then_inc(now_done, 1)
                for j in range(2):
                    act.wait_ge(conv_done, 2 * i + j + 1)
                    nc.scalar.activation(qk[:, j, :], y[:, j, :], ACT.Silu).then_inc(qk_ready, 1)
                act.wait_ge(mixed, 2 * i + 1)
                for j in range(2):
                    act.wait_ge(proj_done, 6 * i + 5 + j)
                    nc.scalar.activation(og[:, j, :], g.bank[4 + j][:, :], ACT.Sigmoid).then_inc(og_ready, 1)
                for kb in range(TT):
                    act.wait_ge(scores_done, 4 * i + kb + 1)
                    if kb >= 2:
                        act.wait_ge(p_ready, 4 * i + kb)
                    nc.scalar.activation(wts[:, kb % 2, 0:T - kb * P], (g.bank[7] if kb % 2 == 0 else g.bank[5])[:, 0:T - kb * P],
                                         ACT.Exp, bias=Gc[:, kb, bass.ds(i, 1)]).then_inc(weights_done, 1)
                act.wait_ge(sums_done, i + 1)
                nc.scalar.activation(den[:, :], g.bank[2][:, :], ACT.Abs).then_inc(den_abs, 1)
                for j in range(2):
                    act.wait_ge(h_ready, 2 * i + j + 2)
                    nc.scalar.activation(sq[:, j, :], h[:, j, :], ACT.Square).then_inc(squared, 1)
                act.wait_ge(mean_done, i + 1)
                nc.scalar.activation(g.std[:, :], g.bank[3][:, :], ACT.Sqrt, bias=g.eps[:, 0:1]).then_inc(std_ready, 1)

        @block.vector
        def _(dve):
            norm.vector(dve)
            z, e = tmp[0], tmp[1]
            own = Own(dve, step)
            dve.wait_ge(gate_done, 2)
            own.did(nc.vector.tensor_scalar(ig[:, :], g.bank[6][0:H, :], g.col("mlstm_b_i", rows=H), None, ALU.add))
            own.did(nc.vector.tensor_scalar(z[:, :], g.bank[5][0:H, :], g.col("mlstm_b_f", rows=H), None, ALU.add))
            own.wait()
            nc.vector.scalar_tensor_tensor(e[:, :], z[:, :], -1.0, z[:, :], ALU.mult, ALU.max).then_inc(gate_abs, 1)
            own.did(nc.vector.tensor_scalar(z[:, :], z[:, :], 0.0, None, ALU.min))
            dve.wait_ge(gate_exp, 1)
            log1p_half(dve, own, nc, e[:, :], tmp[2][:, :], tmp[3][:, :], tmp[4][:, :])
            own.did(nc.vector.scalar_tensor_tensor(z[:, :], tmp[4][:, :], -2.0, z[:, :], ALU.mult, ALU.add))
            own.did(nc.vector.memset(e[:, :], 1.0))
            own.wait()
            F = tmp[2]
            own.did(nc.vector.tensor_tensor_scan(F[:, :], e[:, :], z[:, :], 0.0, ALU.mult, ALU.add))
            own.wait()
            nc.vector.tensor_tensor(G[:, :], ig[:, :], F[:, :], ALU.subtract).then_inc(G_ready, 1)
            dve.wait_ge(G_ready, 1)
            own.did(nc.vector.tensor_tensor_scan(top[:, :], G[:, :], G[:, :], 0.0, ALU.max, ALU.max))
            own.wait()
            nc.vector.scalar_tensor_tensor(z[:, :], top[:, :], -1.0, F[:, :], ALU.mult, ALU.subtract).then_inc(neg_m_ready, 1)
            own.did(nc.vector.tensor_scalar(top[:, :], top[:, :], -1.0, None, ALU.mult))
            dve.wait_ge(G_turned, 1)
            nc.vector.tensor_copy(Gc[:, :, :], g.bank[4][:, 0:TT * H].rearrange("p (a b) -> p a b", b=H)).then_inc(Gc_ready, 1)
            dve.wait_ge(em_ready, 1)
            own.wait()
            opening = own.n
            per = 2 * 2 + 2 + 1 + 2
            with dve.Fori(0, units.n) as i:
                own = Own(dve, step, i, per)
                own.base = own.base + opening
                for j, row in enumerate((top, em)):
                    nc.vector.tensor_scalar(rows[:, j, :], row[:, :], g.ident[0:H, bass.ds(i, 1)], None,
                                            ALU.mult).then_inc(rows_ready, 1)
                for j in range(2):
                    dve.wait_ge(now_done, 2 * i + j + 1)
                    for back in (1, 2, 3):
                        tap = nc.vector.scalar_tensor_tensor(y[:, j, back:T], g.bank[j][:, 0:T - back],
                                                             g.col_at("conv_qk", i + (3 - back) * 2 * H + j * H), y[:, j, back:T],
                                                             ALU.mult, ALU.add)
                        if back < 3:
                            own.did(tap)
                            own.wait()
                        else:
                            tap.then_inc(conv_done, 1)
                for j in range(2):
                    dve.wait_ge(proj_done, 6 * i + 3 + j)
                    nc.vector.tensor_copy(v[:, 2 * j:2 * j + 2, :], g.bank[2 + j][:, :].rearrange("p (a b) -> p a b", b=VD))\
                      .then_inc(v_ready, 1)
                for kb in range(TT):
                    dve.wait_ge(weights_done, 4 * i + kb + 1)
                    n = T - kb * P
                    nc.vector.scalar_tensor_tensor(probs_T[:, kb, kb * P:T], (g.bank[6] if kb % 2 == 0 else g.bank[4])[:, 0:n],
                                                   scale, wts[:, kb % 2, 0:n], ALU.mult, ALU.mult).then_inc(p_ready, 1)
                dve.wait_ge(den_abs, i + 1)
                own.did(nc.vector.tensor_tensor(den[:, :], den[:, :], g.bank[3][:, :], ALU.max))
                own.wait()
                own.did(nc.vector.reciprocal(den[:, :], den[:, :]))
                own.wait()
                for j in range(2):
                    nc.vector.tensor_tensor(h[:, j, :], g.bank[j][:, :], den[:, :], ALU.mult).then_inc(h_ready, 1)
                dve.wait_ge(std_ready, i + 2)
                own.did(nc.vector.reciprocal(g.rstd[:, :], g.std[:, :]))
                own.wait()
                for j in range(2):
                    own.did(nc.vector.scalar_tensor_tensor(h[:, j, :], h[:, j, :], g.col_at("head_norm", 2 * i + j), g.rstd[:, :],
                                                           ALU.mult, ALU.mult))
                    own.wait()
                    nc.vector.tensor_tensor(g.mix[:, bass.ds(2 * i + j, 1), :], h[:, j, :], og[:, j, :], ALU.mult)\
                      .then_inc(mixed, 1)


def stage_norm(g, gain, coming, shift=None, out=None):
    nc = g.nc
    with ExitStack() as ctx:
        norm = Norm(g, ctx, gain, shift, out)
        block = ctx.enter_context(nc.Block())

        @block.sync
        def _(sp):
            first_loads(sp, coming)

        @block.tensor
        def _(pe):
            norm.tensor(pe)

        @block.scalar
        def _(act):
            norm.scalar(act)

        @block.vector
        def _(dve):
            norm.vector(dve)


def stage_modulation(g, units, coming):
    nc = g.nc
    units.begin()
    W, HALVES = units.width, 2
    with ExitStack() as ctx:
        sem, sb = g.stage(ctx, "modulation")
        silu_ready, zeroed, used, summed, step = (sem(n) for n in ("silu_ready", "zeroed", "used", "summed", "step"))
        c = sb("c", [P, KT])
        acc = sb("acc", [P, HALVES, 2, W])
        block = ctx.enter_context(nc.Block())

        @block.sync
        def _(sp):
            with sp.Fori(1, units.n) as i:
                for s in range(2):
                    sp.wait_ge(used, 2 * i + s)
                    units.load(sp, i, s)
            sp.wait_ge(used, 2 * units.n + 1)
            first_loads(sp, coming)

        @block.scalar
        def _(act):
            nc.scalar.activation(c[:, :], g.cols("c", KT), ACT.Silu).then_inc(silu_ready, 1)

        @block.vector
        def _(dve):
            dve.sem_inc(used, 1)
            nc.vector.memset(acc[:, :, :, :], 0.0).then_inc(zeroed, 1)
            dve.wait_ge(zeroed, 1)
            dve.wait_ge(silu_ready, 1)
            for half in range(HALVES):
                with dve.Fori(0, KT) as k:
                    dve.wait_ge(used, 2 * k + 2 * KT * half + 1)
                    for s in range(2):
                        units.wait(dve, k + half * KT, s)
                        here = acc[:, half, s, :]
                        nc.vector.scalar_tensor_tensor(here, g.ring.slots[s][:, 0:W], c[:, bass.ds(k, 1)], here,
                                                       ALU.mult, ALU.add).then_inc(used, 1)
            own = Own(dve, step)
            dve.wait_ge(summed, 1)
            own.did(nc.vector.tensor_tensor(g.mod[:, :], g.bank[0][:, 0:64], g.cols("b_ada", 64), ALU.add))
            own.wait()
            for j, (name, scale) in enumerate((("g_mix", 8), ("g_ffn", 32), ("g_final", 56))):
                own.did(nc.vector.scalar_tensor_tensor(g.gains[:, j, :], g.mod[:, scale:scale + KT], 1.0, g.cols(name, KT),
                                                       ALU.add, ALU.mult))

        @block.tensor
        def _(pe):
            pe.wait_ge(used, 2 * units.n + 1)
            flat = acc[:, :, :, :].rearrange("p a b n -> p (a b n)")
            for j in range(64):
                mm = nc.tensor.matmul(g.bank[0][:, j:j + 1], flat[:, j * P:(j + 1) * P], g.ones[:, 0:1], start=True, stop=True)
            mm.then_inc(summed, 1)


class Recurrent:

    def __init__(self, nc, ctx):
        sb = lambda name, shape: ctx.enter_context(nc.sbuf_tensor(f"rec_{name}", shape, F32))
        self.rkv = sb("rkv", [P, 3 * AT, T])
        self.r, self.k, self.v = (self.rkv[:, j * AT:(j + 1) * AT, :] for j in range(3))
        self.xc = sb("xc", [P, AT, T])
        self.gelu_gate = sb("gelu_gate", [P, AT, T])
        self.ell = sb("ell", [P, AT, T])
        self.a = sb("a", [P, AT, T])
        self.gate = sb("gate", [P, AT, T])
        self.gate_r, self.gate_i = sb("gate_r", [P, AT, T]), sb("gate_i", [P, AT, T])
        self.keep = sb("keep", [P, 3 * AT])


def stage_recurrent_in(g, rec, units, coming):
    nc = g.nc
    units.begin()
    W = 2 * P
    with ExitStack() as ctx:
        sem, sb = g.stage(ctx, "recurrent_in")
        norm = Norm(g, ctx, g.gains[:, 0, :], g.mod[:, 0:KT])
        done, now_done, free, keep_ready, step = (sem(n) for n in ("product_done", "now_done", "bank_free", "keep_ready", "step"))
        block = ctx.enter_context(nc.Block())

        @block.sync
        def _(sp):
            with sp.Fori(1, units.n) as i:
                for s in range(2):
                    sp.wait_ge(done, 4 * i - 4 + 2 * s + 2)
                    units.load(sp, i, s)
            sp.wait_ge(done, 4 * units.n)
            first_loads(sp, coming)

        @block.tensor
        def _(pe):
            norm.tensor(pe)
            norm.wait(pe)
            with pe.Fori(0, units.n) as i:
                for b in range(4):
                    if b % 2 == 0:
                        units.wait(pe, i, b // 2)
                    pe.wait_ge(free, 4 * i + b + 1)
                    for k in range(KT):
                        mm = nc.tensor.matmul(g.bank[b][:, :], units.tile(b // 2, k, b % 2, W), g.xn[:, k, :],
                                              start=(k == 0), stop=(k == KT - 1))
                    mm.then_inc(done, 1)

        @block.scalar
        def _(act):
            norm.scalar(act)
            act.wait_ge(keep_ready, 1)
            with act.Fori(0, 3) as i:
                for b in range(4):
                    act.wait_ge(done, 4 * i + b + 1)
                    nc.scalar.activation(rec.rkv[:, bass.ds(4 * i + b, 1), :], g.bank[b][:, :], ACT.Copy,
                                         scale=rec.keep[:, bass.ds(4 * i + b, 1)]).then_inc(now_done, 1)
            for b in range(4):
                act.wait_ge(done, 12 + b + 1)
                nc.scalar.activation(rec.xc[:, b, :], g.bank[b][:, :], ACT.Identity, scale=g.col("conv_w", 3 * AT + b),
                                     bias=g.col("conv_b", b)).then_inc(now_done, 1)
            for b in range(4):
                act.wait_ge(done, 16 + b + 1)
                nc.scalar.activation(rec.gelu_gate[:, b, :], g.bank[b][:, :], ACT.Gelu_apprx_tanh)

        @block.vector
        def _(dve):
            nc.vector.tensor_scalar(rec.keep[:, :], g.cols("mu_rkv", 3 * AT), -1.0, 1.0, ALU.mult, ALU.add).then_inc(keep_ready, 1)
            norm.vector(dve)
            dve.sem_inc(free, 4)
            with dve.Fori(0, 3) as i:
                for b in range(4):
                    dve.wait_ge(now_done, 4 * i + b + 1)
                    here = rec.rkv[:, bass.ds(4 * i + b, 1), 1:T]
                    nc.vector.scalar_tensor_tensor(here, g.bank[b][:, 0:T - 1], g.col_at("mu_rkv", 4 * i + b), here,
                                                   ALU.mult, ALU.add).then_inc(free, 1)
            own = Own(dve, step)
            for b in range(4):
                dve.wait_ge(now_done, 12 + b + 1)
                for back in (1, 2, 3):
                    here = rec.xc[:, b, back:T]
                    tap = nc.vector.scalar_tensor_tensor(here, g.bank[b][:, 0:T - back], g.col("conv_w", (3 - back) * AT + b), here,
                                                         ALU.mult, ALU.add)
                    if back < 3:
                        own.did(tap)
                        own.wait()
                    else:
                        tap.then_inc(free, 1)


def stage_low_rank(g, rec, units, coming):
    nc = g.nc
    units.begin()
    W = 2 * P
    RANK = (HALF, HALF, P)
    START = (0, HALF, P)
    with ExitStack() as ctx:
        sem, sb = g.stage(ctx, "low_rank")
        shifted, mixed, used, low_done, low_ready, up_done, up_read = (
            sem(n) for n in ("shifted", "mixed", "used", "low_done", "low_ready", "up_done", "up_read"))
        dx = g.mix
        mixes = sb("mixes", [P, 4, T])
        low = [sb(f"low{j}", [RANK[j], T]) for j in range(3)]
        block = ctx.enter_context(nc.Block())
        small = g.ring.slots[1]
        ups = [(rec.ell, m, small[0:HALF, m * P:(m + 1) * P], low[0][:, :], ACT.Sigmoid, "w0") for m in range(AT)]
        ups += [(rec.a, m, small[0:HALF, AW + m * P:AW + (m + 1) * P], low[1][:, :], ACT.Sigmoid, "a0") for m in range(AT)]
        ups += [(rec.gate, m, small[:, 2 * AW + m * P:2 * AW + (m + 1) * P], low[2][:, :], ACT.Copy, None) for m in range(AT)]
        ups += [(rec.gate_r, m, small[:, 3 * AW + m * P:3 * AW + (m + 1) * P], rec.xc[:, m, :], ACT.Sigmoid, "b_rgate") for m in range(AT)]
        ups += [(rec.gate_i, m, small[:, 4 * AW + m * P:4 * AW + (m + 1) * P], rec.xc[:, m, :], ACT.Sigmoid, "b_igate") for m in range(AT)]

        @block.sync
        def _(sp):
            sp.wait_ge(up_done, len(ups))
            first_loads(sp, coming)

        @block.vector
        def _(dve):
            nc.vector.tensor_scalar(dx[:, :, 0:1], g.xn[:, :, 0:1], -1.0, None, ALU.mult).then_inc(shifted, 1)
            for k in range(KT):
                nc.vector.tensor_tensor(dx[:, k, 1:T], g.xn[:, k, 0:T - 1], g.xn[:, k, 1:T], ALU.subtract).then_inc(shifted, 1)
            for j in range(3):
                for k in range(KT):
                    n = j * KT + k
                    if j == 0:
                        dve.wait_ge(shifted, k + 2)
                    if n >= 4:
                        dve.wait_ge(used, n - 3)
                    nc.vector.scalar_tensor_tensor(mixes[:, n % 4, :], dx[:, k, :], g.col("mu_wag", n), g.xn[:, k, :],
                                                   ALU.mult, ALU.add).then_inc(mixed, 1)

        @block.tensor
        def _(pe):
            units.wait(pe, 0, 0)
            units.wait(pe, 0, 1)
            for j in range(3):
                for k in range(KT):
                    pe.wait_ge(mixed, j * KT + k + 1)
                    mm = nc.tensor.matmul(g.bank[j][0:RANK[j], :], g.ring.slots[0][:, k * W + START[j]:k * W + START[j] + RANK[j]],
                                          mixes[:, (j * KT + k) % 4, :], start=(k == 0), stop=(k == KT - 1))
                    mm.then_inc(used, 1)
            for n, (_, _, weights, source, _, _) in enumerate(ups):
                if n % AT == 0 and n < 3 * AT:
                    pe.wait_ge(low_ready, n // AT + 1)
                if n >= 4:
                    pe.wait_ge(up_read, n - 3)
                nc.tensor.matmul(g.bank[3 + n % 4][:, :], weights, source, start=True, stop=True).then_inc(up_done, 1)

        @block.scalar
        def _(act):
            for j, f in enumerate((ACT.Tanh, ACT.Copy, ACT.Sigmoid)):
                act.wait_ge(used, (j + 1) * KT)
                nc.scalar.activation(low[j][:, :], g.bank[j][0:RANK[j], :], f).then_inc(low_ready, 1)
            for n, (out, m, _, _, f, bias) in enumerate(ups):
                act.wait_ge(up_done, n + 1)
                more = {} if bias is None else {"bias": g.col(bias, m)}
                nc.scalar.activation(out[:, m, :], g.bank[3 + n % 4][:, :], f, **more).then_inc(up_read, 1)


def stage_rg_lru(g, rec):
    nc = g.nc
    with ExitStack() as ctx:
        sem, sb = g.stage(ctx, "rg_lru")
        lam_abs, lam_exp, rate_ready, tanh_done, root_in, root_done, input_ready, h_ready, step = (
            sem(n) for n in ("lam_abs", "lam_exp", "rate_ready", "tanh_done", "root_in", "root_done", "input_ready", "h_ready", "step"))
        small = [sb(f"small{j}", [P, AT]) for j in range(5)]
        t = rec.gate_r
        u = g.mix[:, 0:AT, :]
        d = sb("d", [P, AT, T])
        block = ctx.enter_context(nc.Block())
        lam = g.cols("lam", AT)
        all_of = lambda b: b[:, :, :].rearrange("p a b -> p (a b)")

        @block.scalar
        def _(act):
            act.wait_ge(lam_abs, 1)
            nc.scalar.activation(small[0][:, :], small[0][:, :], ACT.Exp, scale=-1.0).then_inc(lam_exp, 1)
            act.wait_ge(rate_ready, 1)
            for m in range(AT):
                nc.scalar.activation(t[:, m, :], rec.gate_r[:, m, :], ACT.Tanh, scale=small[4][:, m:m + 1]).then_inc(tanh_done, 1)
            act.wait_ge(root_in, 1)
            nc.scalar.activation(all_of(d), all_of(d), ACT.Sqrt).then_inc(root_done, 1)

        @block.gpsimd
        def _(pool):
            nc.gpsimd.tensor_tensor(all_of(u), all_of(rec.gate_i), all_of(rec.xc), ALU.mult).then_inc(input_ready, 1)

        @block.vector
        def _(dve):
            own = Own(dve, step)
            nc.vector.scalar_tensor_tensor(small[0][:, :], lam, -1.0, lam, ALU.mult, ALU.max).then_inc(lam_abs, 1)
            dve.wait_ge(lam_exp, 1)
            log1p_half(dve, own, nc, *(s[:, :] for s in small[0:4]))
            own.did(nc.vector.tensor_scalar(small[1][:, :], lam, 0.0, -4.0, ALU.min, ALU.mult))
            own.wait()
            nc.vector.scalar_tensor_tensor(small[4][:, :], small[3][:, :], 8.0, small[1][:, :], ALU.mult, ALU.add).then_inc(rate_ready, 1)
            dve.wait_ge(tanh_done, AT)
            own.did(nc.vector.tensor_scalar(all_of(d), all_of(t), 1.0, None, ALU.add))
            own.wait()
            own.did(nc.vector.reciprocal(all_of(d), all_of(d)))
            own.wait()
            own.did(nc.vector.scalar_tensor_tensor(all_of(d), all_of(t), 2.0, all_of(d), ALU.mult, ALU.mult))
            own.wait()
            own.did(nc.vector.tensor_scalar(all_of(t), all_of(d), -1.0, 1.0, ALU.mult, ALU.add))
            own.wait()
            nc.vector.scalar_tensor_tensor(all_of(d), all_of(t), 1.0, all_of(d), ALU.add, ALU.mult).then_inc(root_in, 1)
            dve.wait_ge(root_done, 1)
            dve.wait_ge(input_ready, 1)
            own.did(nc.vector.tensor_tensor(all_of(u), all_of(u), all_of(d), ALU.mult))
            own.wait()
            for m in range(AT):
                own.did(nc.vector.tensor_tensor_scan(d[:, m, :], t[:, m, :], u[:, m, :], 0.0, ALU.mult, ALU.add))
            own.wait()
            nc.vector.tensor_tensor(g.mix[:, AT:2 * AT, :].rearrange("p a b -> p (a b)"), all_of(d), all_of(rec.gelu_gate),
                                    ALU.mult).then_inc(h_ready, 1)


class Rwkv:

    def __init__(self, rec):
        self.nkk = rec.xc
        self.b = rec.gelu_gate
        self.L = rec.gate_r
        self.y = rec.gate_i


def stage_rwkv_prepare(g, rec, rw):
    nc = g.nc
    with ExitStack() as ctx:
        sem, sb = g.stage(ctx, "prepare")
        kk_ready, squared, summed, norm_ready, step, rates_ready = (
            sem(n) for n in ("kk_ready", "squared", "summed", "norm_ready", "step", "rates_ready"))
        kk = rw.nkk
        sq, one = sb("sq", [P, AT, T]), sb("one", [P, T])
        inv = sq
        block = ctx.enter_context(nc.Block())

        @block.vector
        def _(dve):
            own = Own(dve, step)
            for m in range(AT):
                nc.vector.tensor_scalar(kk[:, m, :], rec.k[:, m, :], g.col("k_k", m), None, ALU.mult).then_inc(kk_ready, 1)
            own.did(nc.vector.memset(one[:, :], 1.0))
            own.wait()
            own.did(nc.vector.memset(one[:, 0:T:CHUNK], 0.0))
            own.wait()
            decay = -math.exp(-0.5)
            for m in range(AT):
                own.did(nc.vector.tensor_scalar(rec.ell[:, m, :], rec.ell[:, m, :], decay, None, ALU.mult))
            own.wait()
            for m in range(AT):
                own.did(nc.vector.tensor_tensor_scan(rw.L[:, m, :], one[:, :], rec.ell[:, m, :], 0.0, ALU.mult, ALU.add))
            dve.wait_ge(rates_ready, AT)
            for m in range(AT):
                own.did(nc.vector.scalar_tensor_tensor(rec.k[:, m, :], rw.y[:, m, :], 1.0, rec.k[:, m, :], ALU.add, ALU.mult))
            for m in range(AT):
                dve.wait_ge(norm_ready, m + 1)
                own.did(nc.vector.reciprocal(inv[:, m, :], inv[:, m, :]))
                own.wait()
                own.did(nc.vector.scalar_tensor_tensor(rw.nkk[:, m, :], kk[:, m, :], -1.0, inv[:, m, :], ALU.mult, ALU.mult))
                own.wait()
                own.did(nc.vector.scalar_tensor_tensor(rw.b[:, m, :], rw.nkk[:, m, :], -1.0, rec.a[:, m, :], ALU.mult, ALU.mult))

        @block.gpsimd
        def _(pool):
            pool.wait_ge(kk_ready, AT)
            for m in range(AT):
                nc.gpsimd.tensor_scalar(rw.y[:, m, :], rec.a[:, m, :], -1.0, g.col("k_a", m), ALU.add, ALU.mult).then_inc(rates_ready, 1)

        @block.scalar
        def _(act):
            for m in range(AT):
                act.wait_ge(kk_ready, m + 1)
                nc.scalar.activation(sq[:, m, :], kk[:, m, :], ACT.Square).then_inc(squared, 1)
            for m in range(AT):
                act.wait_ge(summed, m + 1)
                nc.scalar.activation(inv[:, m, :], g.bank[m][:, :], ACT.Sqrt, bias=g.eps[:, 1:2]).then_inc(norm_ready, 1)

        @block.tensor
        def _(pe):
            for m in range(AT):
                pe.wait_ge(squared, m + 1)
                nc.tensor.matmul(g.bank[m][:, :], g.head_sum[:, :], sq[:, m, :], start=True, stop=True).then_inc(summed, 1)


def stage_rwkv_chunks(g, rec, rw):
    nc = g.nc
    LEVELS = int(math.log2(CHUNK))
    PAIRS = AT
    both = [slice(h * HALF, (h + 1) * HALF) for h in range(2)]
    with ExitStack() as ctx:
        sem, sb = g.stage(ctx, "chunks")
        diff_ready, exps_ready, scaled, v_copied, pairs_done, pairs_read, tokens_read = (
            sem(n) for n in ("diff_ready", "exps_ready", "scaled", "v_copied", "pairs_done", "pairs_read", "tokens_read"))
        level_ready, w_done, w_ready, z_done, zt_done, inverse_step = (
            sem(n) for n in ("level_ready", "w_done", "w_ready", "z_done", "zt_done", "inverse_step"))
        rhs_done, rhs_ready, u_done, u_ready, y_done, y_ready, s_done, s_added, s_ready, passed = (
            sem(n) for n in ("rhs_done", "rhs_ready", "u_done", "u_ready", "y_done", "y_ready", "s_done", "s_added", "s_ready", "passed"))
        C = CHUNK
        dl, en, ep, epv = (sb(n, [P, PAIRS, C]) for n in ("dl", "en", "ep", "epv"))
        ar = sb("ar", [P, PAIRS, 2, C])
        bt, kt, vt = (sb(n, [P, PAIRS, C]) for n in ("bt", "kt", "vt"))
        Mb, Mk = (g.square[:, j, :].rearrange("p (a b n) -> p a b n", b=2, n=C) for j in range(2))
        bk = sb("bk", [P, 2, PAIRS, C])
        vs = sb("vs", [P, PAIRS, C])
        al = g.memn[:, 0:LEVELS, :].rearrange("p l (a n) -> p l a n", n=C)
        M, MT = (g.memn[:, LEVELS + j, :].rearrange("p (a n) -> p a n", n=C) for j in range(2))
        Wt = sb("Wt", [P, PAIRS, C])
        rhs, U = (g.std[:, j * PAIRS * C:(j + 1) * PAIRS * C].rearrange("p (a n) -> p a n", n=C) for j in range(2))
        S = sb("S", [P, PAIRS, C])
        block = ctx.enter_context(nc.Block())
        eye = g.cols("eye", C)
        tri = g.cols("tri", 2 * C).rearrange("p (a b) -> p a b", b=C)
        level = lambda l: g.cols("levels", LEVELS * C)[:, l * C:(l + 1) * C]
        spread = lambda m: m.unsqueeze(1).broadcast_to([P, PAIRS, *m.shape[1:]])
        wide = lambda b: g.bank[b][:, 0:PAIRS * C].rearrange("p (a b) -> p a b", b=C)
        now = lambda a, c: a[:, :, bass.ds(c * C, C)]
        steps = 2 * LEVELS - 1

        @block.scalar
        def _(act):
            with act.Fori(0, NCHUNK) as c:
                act.wait_ge(s_ready, c + 1)
                nc.scalar.activation(en[:, :, :], now(rw.L, c), ACT.Exp, scale=-1.0).then_inc(exps_ready, 1)
                nc.scalar.activation(ep[:, :, :], now(rw.L, c), ACT.Exp).then_inc(exps_ready, 1)
                act.wait_ge(diff_ready, c + 1)
                nc.scalar.activation(epv[:, :, :], dl[:, :, :], ACT.Exp).then_inc(exps_ready, 1)
                act.wait_ge(pairs_done, 4 * c + 3)
                nc.scalar.activation(bk[:, :, :, :].rearrange("p a b n -> p (a b n)"), g.bank[2][:, :], ACT.Copy).then_inc(tokens_read, 1)
                act.wait_ge(pairs_done, 4 * c + 4)
                nc.scalar.activation(vs[:, :, :], wide(3), ACT.Copy).then_inc(tokens_read, 1)
                for l in range(1, LEVELS):
                    act.wait_ge(w_done, LEVELS * c + l + 1)
                    nc.scalar.activation(Wt[:, :, :], wide(4), ACT.Copy).then_inc(w_ready, 1)
                act.wait_ge(rhs_done, c + 1)
                nc.scalar.activation(rhs[:, :, :], wide(7), ACT.Copy).then_inc(rhs_ready, 1)
                act.wait_ge(u_done, c + 1)
                nc.scalar.activation(U[:, :, :], wide(4), ACT.Copy).then_inc(u_ready, 1)
                act.wait_ge(y_done, c + 1)
                nc.scalar.activation(now(rw.y, c), wide(5), ACT.Copy).then_inc(y_ready, 1)

        @block.gpsimd
        def _(pool):
            with pool.Fori(0, NCHUNK) as c:
                pool.wait_ge(s_ready, c + 1)
                nc.gpsimd.tensor_copy(vt[:, :, :], now(rec.v, c)).then_inc(v_copied, 1)
                pool.wait_ge(pairs_read, 2 * c + 1)
                for l in range(LEVELS):
                    nc.gpsimd.tensor_tensor(al[:, l, :, :], Mb[:, :, 0, :], spread(level(l)), ALU.mult).then_inc(level_ready, 1)

        @block.vector
        def _(dve):
            dve.sem_inc(s_ready, 1)
            nc.vector.memset(S[:, :, :], 0.0).then_inc(s_added, 1)
            with dve.Fori(0, NCHUNK) as c:
                dve.wait_ge(s_ready, c + 1)
                nc.vector.tensor_tensor(dl[:, :, :], now(rw.L, c), now(rec.ell, c), ALU.subtract).then_inc(diff_ready, 1)
                dve.wait_ge(exps_ready, 3 * c + 2)
                nc.vector.tensor_tensor(bt[:, :, :], now(rw.b, c), en[:, :, :], ALU.mult).then_inc(scaled, 1)
                nc.vector.tensor_tensor(kt[:, :, :], now(rec.k, c), en[:, :, :], ALU.mult).then_inc(scaled, 1)
                nc.vector.tensor_tensor(ar[:, :, 1, :], now(rec.r, c), ep[:, :, :], ALU.mult).then_inc(scaled, 1)
                dve.wait_ge(exps_ready, 3 * c + 3)
                nc.vector.tensor_tensor(ar[:, :, 0, :], now(rw.nkk, c), epv[:, :, :], ALU.mult).then_inc(scaled, 1)
                for b, m in enumerate((Mb, Mk)):
                    dve.wait_ge(pairs_done, 4 * c + b + 1)
                    nc.vector.tensor_tensor(m[:, :, :, :], g.bank[b][:, :].rearrange("p (a b n) -> p a b n", b=2, n=C),
                                            spread(tri), ALU.mult).then_inc(pairs_read, 1)
                dve.wait_ge(level_ready, LEVELS * c + 1)
                nc.vector.tensor_tensor(MT[:, :, :], al[:, 0, :, :], spread(eye), ALU.add).then_inc(inverse_step, 1)
                dve.wait_ge(w_done, LEVELS * c + 1)
                nc.vector.tensor_tensor(M[:, :, :], wide(4), spread(eye), ALU.add).then_inc(inverse_step, 1)
                for l in range(1, LEVELS):
                    if l < LEVELS - 1:
                        dve.wait_ge(z_done, (LEVELS - 2) * c + l)
                        dve.wait_ge(inverse_step, steps * c + 2 * l)
                        nc.vector.tensor_tensor(M[:, :, :], wide(5), M[:, :, :], ALU.add).then_inc(inverse_step, 1)
                    dve.wait_ge(zt_done, (LEVELS - 1) * c + l)
                    nc.vector.tensor_tensor(MT[:, :, :], wide(6), MT[:, :, :], ALU.add).then_inc(inverse_step, 1)
                dve.wait_ge(s_done, c + 1)
                dve.wait_ge(s_added, c + 1)
                nc.vector.tensor_tensor(S[:, :, :], wide(6), S[:, :, :], ALU.add).then_inc(s_added, 1)
                dve.wait_ge(s_added, c + 2)
                dve.wait_ge(y_ready, c + 1)
                nc.vector.tensor_tensor(S[:, :, :], S[:, :, :], ep[:, :, C - 1:C].broadcast_to([P, PAIRS, C]), ALU.mult).then_inc(s_ready, 1)

        @block.tensor
        def _(pe):
            def product(bank, left, right, width=C):
                for n in range(PAIRS):
                    for h in both:
                        mm = nc.tensor.matmul(g.bank[bank][h, n * width:(n + 1) * width], left(h, n), right(h, n), start=True, stop=True)
                return mm

            with pe.Fori(0, NCHUNK) as c:
                pe.wait_ge(scaled, 4 * c + 4)
                pe.wait_ge(v_copied, c + 1)
                pe.wait_ge(s_added, c + 1)
                pe.sem_inc(passed, 1)
                product(0, lambda h, n: bt[h, n, :], lambda h, n: ar[h, n, :, :].rearrange("p a b -> p (a b)"), 2 * C).then_inc(pairs_done, 1)
                product(1, lambda h, n: kt[h, n, :], lambda h, n: ar[h, n, :, :].rearrange("p a b -> p (a b)"), 2 * C).then_inc(pairs_done, 1)
                for j, src in enumerate((bt, kt)):
                    for n in range(PAIRS):
                        for h in both:
                            mm = nc.tensor.matmul(g.bank[2][h, (j * PAIRS + n) * C:(j * PAIRS + n + 1) * C], src[h, n, :], g.ident[h, h],
                                                  start=True, stop=True)
                mm.then_inc(pairs_done, 1)
                product(3, lambda h, n: vt[h, n, :], lambda h, n: g.ident[h, h]).then_inc(pairs_done, 1)
                pe.wait_ge(level_ready, LEVELS * c + 1)
                pe.sem_inc(passed, 1)
                product(4, lambda h, n: al[h, 0, n, :], lambda h, n: eye[h, :]).then_inc(w_done, 1)
                for l in range(1, LEVELS):
                    pe.wait_ge(level_ready, LEVELS * c + l + 1)
                    pe.wait_ge(inverse_step, steps * c + 2 * l)
                    pe.sem_inc(passed, 1)
                    product(4, lambda h, n: al[h, l, n, :], lambda h, n: M[h, n, :]).then_inc(w_done, 1)
                    pe.wait_ge(w_ready, (LEVELS - 1) * c + l)
                    pe.sem_inc(passed, 1)
                    if l < LEVELS - 1:
                        product(5, lambda h, n: MT[h, n, :], lambda h, n: Wt[h, n, :]).then_inc(z_done, 1)
                    product(6, lambda h, n: Wt[h, n, :], lambda h, n: MT[h, n, :]).then_inc(zt_done, 1)
                pe.wait_ge(tokens_read, 2 * c + 2)
                pe.wait_ge(pairs_read, 2 * c + 2)
                pe.sem_inc(passed, 1)
                for n in range(PAIRS):
                    for h in both:
                        out = g.bank[7][h, n * C:(n + 1) * C]
                        nc.tensor.matmul(out, Mk[h, n, 0, :], vs[h, n, :], start=True, stop=False)
                        mm = nc.tensor.matmul(out, ar[h, n, 0, :], S[h, n, :], start=False, stop=True)
                mm.then_inc(rhs_done, 1)
                pe.wait_ge(rhs_ready, c + 1)
                pe.wait_ge(inverse_step, steps * (c + 1))
                pe.sem_inc(passed, 1)
                product(4, lambda h, n: MT[h, n, :], lambda h, n: rhs[h, n, :]).then_inc(u_done, 1)
                pe.wait_ge(u_ready, c + 1)
                pe.sem_inc(passed, 1)
                for n in range(PAIRS):
                    for h in both:
                        out = g.bank[5][h, n * C:(n + 1) * C]
                        nc.tensor.matmul(out, S[h, n, :], ar[h, n, 1, :], start=True, stop=False)
                        nc.tensor.matmul(out, U[h, n, :], Mb[h, n, 1, :], start=False, stop=False)
                        mm = nc.tensor.matmul(out, vs[h, n, :], Mk[h, n, 1, :], start=False, stop=True)
                mm.then_inc(y_done, 1)
                for n in range(PAIRS):
                    for h in both:
                        out = g.bank[6][h, n * C:(n + 1) * C]
                        nc.tensor.matmul(out, bk[h, 0, n, :], U[h, n, :], start=True, stop=False)
                        mm = nc.tensor.matmul(out, bk[h, 1, n, :], vs[h, n, :], start=False, stop=True)
                mm.then_inc(s_done, 1)
                pe.wait_ge(s_ready, c + 2)
                pe.sem_inc(passed, 1)


def stage_rwkv_finish(g, rec, rw, coming):
    nc = g.nc
    with ExitStack() as ctx:
        sem, sb = g.stage(ctx, "finish")
        rk_ready, bonus_done, mean_done, centred, squared, var_done, std_ready, step = (
            sem(n) for n in ("rk_ready", "bonus_done", "mean_done", "centred", "squared", "var_done", "std_ready", "step"))
        rk, sq, std = rw.nkk, rw.b, rw.L
        block = ctx.enter_context(nc.Block())

        @block.sync
        def _(sp):
            first_loads(sp, coming)

        @block.vector
        def _(dve):
            own = Own(dve, step)
            for m in range(AT):
                nc.vector.scalar_tensor_tensor(rk[:, m, :], rec.r[:, m, :], g.col("r_k", m), rec.k[:, m, :],
                                               ALU.mult, ALU.mult).then_inc(rk_ready, 1)
            for m in range(AT):
                dve.wait_ge(mean_done, m + 1)
                nc.vector.scalar_tensor_tensor(rw.y[:, m, :], g.bank[m][:, :], -1.0 / HALF, rw.y[:, m, :], ALU.mult, ALU.add)\
                  .then_inc(centred, 1)
            dve.wait_ge(bonus_done, AT)
            for m in range(AT):
                own.did(nc.vector.tensor_tensor(rk[:, m, :], g.bank[4 + m][:, :], rec.v[:, m, :], ALU.mult))
            for m in range(AT):
                dve.wait_ge(std_ready, m + 1)
                own.did(nc.vector.reciprocal(std[:, m, :], std[:, m, :]))
                own.wait()
                own.did(nc.vector.scalar_tensor_tensor(rw.y[:, m, :], rw.y[:, m, :], g.col("lnx_g", m), std[:, m, :], ALU.mult, ALU.mult))
                own.wait()
                own.did(nc.vector.scalar_tensor_tensor(rw.y[:, m, :], rw.y[:, m, :], g.col("lnx_b", m), rk[:, m, :], ALU.add, ALU.add))
                own.wait()
                own.did(nc.vector.tensor_tensor(g.mix[:, m, :], rw.y[:, m, :], rec.gate[:, m, :], ALU.mult))

        @block.scalar
        def _(act):
            for m in range(AT):
                act.wait_ge(centred, m + 1)
                nc.scalar.activation(sq[:, m, :], rw.y[:, m, :], ACT.Square).then_inc(squared, 1)
            for m in range(AT):
                act.wait_ge(var_done, m + 1)
                nc.scalar.activation(std[:, m, :], g.bank[m][:, :], ACT.Sqrt, scale=1.0 / HALF, bias=g.eps[:, 2:3]).then_inc(std_ready, 1)

        @block.tensor
        def _(pe):
            for m in range(AT):
                nc.tensor.matmul(g.bank[m][:, :], g.head_sum[:, :], rw.y[:, m, :], start=True, stop=True).then_inc(mean_done, 1)
            for m in range(AT):
                pe.wait_ge(rk_ready, m + 1)
                nc.tensor.matmul(g.bank[4 + m][:, :], g.head_sum[:, :], rk[:, m, :], start=True, stop=True).then_inc(bonus_done, 1)
            for m in range(AT):
                pe.wait_ge(squared, m + 1)
                nc.tensor.matmul(g.bank[m][:, :], g.head_sum[:, :], sq[:, m, :], start=True, stop=True).then_inc(var_done, 1)


def stage_merge(g, units, coming, merged):
    nc = g.nc
    units.begin()
    W = 2 * P
    with ExitStack() as ctx:
        sem, sb = g.stage(ctx, "merge")
        done, gated, read, merged_done, step = (sem(n) for n in ("product_done", "gated", "read", "merged_done", "step"))
        sig = sb("sig", [P, 4, T])
        block = ctx.enter_context(nc.Block())

        @block.sync
        def _(sp):
            with sp.Fori(1, units.n) as i:
                for s, last in enumerate((2, 4, 8)):
                    sp.wait_ge(done, 8 * i - 8 + last)
                    units.load(sp, i, s)
            sp.wait_ge(done, 8 * units.n)
            first_loads(sp, coming)

        @block.tensor
        def _(pe):
            pe.sem_inc(gated, 1)
            pe.sem_inc(read, 1)
            with pe.Fori(0, units.n) as i:
                pe.wait_ge(gated, 4 * i + 1)
                for b in range(4):
                    if b % 2 == 0:
                        units.wait(pe, i, b // 2)
                    for k in range(KT):
                        mm = nc.tensor.matmul(g.bank[b][:, :], units.tile(b // 2, k, b % 2, W), g.xn[:, k, :],
                                              start=(k == 0), stop=(k == KT - 1))
                    mm.then_inc(done, 1)
                units.wait(pe, i, 2)
                pe.wait_ge(read, 4 * i + 1)
                for b in range(4):
                    for k in range(AT):
                        mm = nc.tensor.matmul(g.bank[4 + b][:, :], units.tile(2, b // 2 * AT + k, b % 2, W),
                                              g.mix[:, b // 2 * AT + k, :], start=(k == 0), stop=(k == AT - 1))
                    mm.then_inc(done, 1)

        @block.scalar
        def _(act):
            act.sem_inc(merged_done, 1)
            with act.Fori(0, units.n) as i:
                act.wait_ge(merged_done, 2 * i + 1)
                for b in range(4):
                    act.wait_ge(done, 8 * i + b + 1)
                    nc.scalar.activation(sig[:, b, :], g.bank[b][:, :], ACT.Sigmoid).then_inc(gated, 1)

        @block.vector
        def _(dve):
            with dve.Fori(0, units.n) as i:
                for b in range(4):
                    dve.wait_ge(done, 8 * i + 4 + b + 1)
                    dve.wait_ge(gated, 4 * i + b + 2)
                    nc.vector.tensor_tensor(sig[:, b, :], g.bank[4 + b][:, :], sig[:, b, :], ALU.mult).then_inc(read, 1)
                    if b >= 2:
                        dve.wait_ge(read, 4 * i + b + 2)
                        nc.vector.tensor_tensor(merged[:, bass.ds(2 * i + b - 2, 1), :], sig[:, b - 2, :], sig[:, b, :], ALU.add)\
                          .then_inc(merged_done, 1)


class Experts:

    def __init__(self, nc, ctx, ring):
        sb = lambda name, shape, dt=F32: ctx.enter_context(nc.sbuf_tensor(f"moe_{name}", shape, dt))
        dram = lambda name, rows: nc.dram_tensor(name, [rows, D], F32, kind="Internal").ap()
        self.weight = sb("weight", [P, 2, TT])
        self.pair = sb("pair", [P, MOE_TILES], I32)
        self.token = sb("token", [P, MOE_TILES], I32)
        self.more_expert = sb("more_expert", [1, MORE], I32)
        self.more_tiles = sb("more_tiles", [1, 1], I32)
        self.rows = dram("moe_rows", T)
        self.pair_rows = dram("moe_pair_rows", 2 * T)
        extra = 2 * IN_FLIGHT - SLOTS
        self.ring = WeightRing(ring.slots + [sb(f"weights{s}", [P, SLOT]) for s in range(extra)],
                               ring.ready + [ctx.enter_context(nc.semaphore(f"expert_ready{s}")) for s in range(extra)])
        self.ring.loads = ring.loads + [0] * extra


def stage_router(g, moe, units):
    nc = g.nc
    LOGITS = GROUPS + EXPERTS
    with ExitStack() as ctx:
        sem, sb = g.stage(ctx, "router")
        norm = Norm(g, ctx, g.gains[:, 1, :], g.mod[:, 24:24 + KT])
        turned, row_read, stored, logits_done, step, to_exp, exp_done = (
            sem(n) for n in ("turned", "row_read", "stored", "logits_done", "step", "to_exp", "exp_done"))
        chosen, counted, sorted_, placed, table_done = (sem(n) for n in ("chosen", "counted", "sorted", "placed", "table_done"))
        rows = g.mix[:, :, :].rearrange("p (t h) n -> p t (h n)", h=2)
        logits = sb("logits", [P, TT, LOGITS])
        top, first, total = sb("top", [P, TT]), sb("first", [P, TT]), sb("total", [P, TT])
        exps = sb("exps", [P, TT, GROUPS])
        group, group_weight = sb("group", [P, TT, GROUPS]), sb("group_weight", [P, TT])
        parts = sb("parts", [P, TT, GROUPS, PER_GROUP])
        inside = sb("inside", [P, TT, PER_GROUP])
        best = sb("best", [P, 2, TT])
        here = sb("here", [P, 2, TT, PER_GROUP])
        second = sb("second", [P, TT])
        hot = sb("hot", [P, 2, TT, EXPERTS])
        both = sb("both", [P, TT, EXPERTS])
        earlier = sb("earlier", [P, P])
        rank, count = sb("rank", [P, TT, EXPERTS]), sb("count", [P, EXPERTS])
        more, more_end, more_start = sb("more", [P, EXPERTS]), sb("more_end", [P, EXPERTS]), sb("more_start", [P, EXPERTS])
        picked = sb("picked", [P, 2, TT, EXPERTS])
        slot, expert, start, past = (sb(n, [P, 2, TT]) for n in ("slot", "expert", "start", "past"))
        by_slot = sb("by_slot", [P, 2 * TT, P])
        by_tile = sb("by_tile", [P, 2 * TT, MOE_TILES])
        place = sb("place", [P, MOE_TILES])
        empty = sb("empty", [P, MOE_TILES])
        ended = sb("ended", [1, MORE, EXPERTS])
        which = sb("which", [1, MORE])
        block = ctx.enter_context(nc.Block())
        iota = lambda n, rows=P: g.cols("iota", n, rows)
        w_router = g.cols("w_router", KT * LOGITS)

        @block.sync
        def _(sp):
            for s in range(units.per):
                units.load(sp, 0, s)
            for t in range(TT):
                sp.wait_ge(row_read, 2 * t + 2)
                sp.dma_start(moe.rows[t * P:(t + 1) * P, :], rows[:, t, :]).then_inc(stored, 16)
            sp.wait_ge(stored, 16 * TT)

        @block.tensor
        def _(pe):
            norm.tensor(pe)
            norm.wait(pe)
            for t in range(TT):
                for k in range(KT):
                    mm = nc.tensor.matmul(g.bank[0][:, t * LOGITS:(t + 1) * LOGITS], g.xn[:, k, t * P:(t + 1) * P],
                                          w_router[:, k * LOGITS:(k + 1) * LOGITS], start=(k == 0), stop=(k == KT - 1))
            mm.then_inc(logits_done, 1)
            for t in range(TT):
                for h in range(2):
                    n = 2 * t + h
                    if n >= 4:
                        pe.wait_ge(row_read, n - 3)
                    for j in range(TT):
                        mm = nc.tensor.matmul(g.bank[2 + n % 4][:, j * P:(j + 1) * P], g.xn[:, h * 4 + j, t * P:(t + 1) * P],
                                              g.ident[:, :], start=True, stop=True)
                    mm.then_inc(turned, 1)
            pe.wait_ge(chosen, 1)
            for t in range(TT):
                for s in range(t + 1):
                    nc.tensor.matmul(g.bank[1][:, t * EXPERTS:(t + 1) * EXPERTS], (earlier if s == t else g.ones)[:, :],
                                     both[:, s, :], start=(s == 0), stop=(s == t))
            for t in range(TT):
                mm = nc.tensor.matmul(g.bank[1][:, TT * EXPERTS:(TT + 1) * EXPERTS], g.ones[:, :], both[:, t, :],
                                      start=(t == 0), stop=(t == TT - 1))
            mm.then_inc(counted, 1)
            pe.wait_ge(placed, 1)
            for n in range(2 * TT):
                mm = nc.tensor.matmul(g.bank[6][:, 0:MOE_TILES], by_slot[:, n, :], by_tile[:, n, :],
                                      start=(n == 0), stop=(n == 2 * TT - 1))
            mm.then_inc(table_done, 1)

        @block.scalar
        def _(act):
            norm.scalar(act)
            for n in range(2 * TT):
                act.wait_ge(turned, n + 1)
                nc.scalar.activation(rows[:, n // 2, n % 2 * T:(n % 2 + 1) * T], g.bank[2 + n % 4][:, :], ACT.Copy).then_inc(row_read, 1)
            act.wait_ge(to_exp, 1)
            nc.scalar.activation(exps[:, :, :], exps[:, :, :], ACT.Exp).then_inc(exp_done, 1)
            act.wait_ge(to_exp, 2)
            nc.scalar.activation(second[:, :], second[:, :], ACT.Exp).then_inc(exp_done, 1)

        @block.vector
        def _(dve):
            norm.vector(dve)
            own = Own(dve, step)
            v = nc.vector

            def do(ins):
                own.did(ins)
                own.wait()

            def last(a, n):
                return a.unsqueeze(len(a.shape)).broadcast_to([*a.shape, n])

            def one_hot_max(values, top, out, n):
                do(v.tensor_reduce(top, values, AX.X, ALU.max))
                do(v.tensor_tensor(out, values, last(top, n), ALU.is_ge))
                do(v.tensor_scalar(out, out, -float(n), float(n), ALU.mult, ALU.add))
                do(v.tensor_tensor(out, out, iota(n).unsqueeze(1).broadcast_to([P, TT, n]), ALU.add))
                do(v.tensor_reduce(first[:, :], out, AX.X, ALU.min))
                do(v.tensor_tensor(out, iota(n).unsqueeze(1).broadcast_to([P, TT, n]), last(first[:, :], n), ALU.is_equal))

            do(v.scalar_tensor_tensor(earlier[:, :], g.causal_T[:, :], 0.0, g.ident[:, :], ALU.is_equal, ALU.subtract))
            dve.wait_ge(logits_done, 1)
            do(v.tensor_tensor(logits[:, :, :], g.bank[0][:, 0:TT * LOGITS].rearrange("p (t n) -> p t n", n=LOGITS),
                               g.cols("b_router", LOGITS).unsqueeze(1).broadcast_to([P, TT, LOGITS]), ALU.add))
            groups = logits[:, :, 0:GROUPS]
            one_hot_max(groups, top[:, :], group[:, :, :], GROUPS)
            v.tensor_tensor(exps[:, :, :], groups, last(top[:, :], GROUPS), ALU.subtract).then_inc(to_exp, 1)
            do(v.tensor_tensor(parts[:, :, :, :], logits[:, :, GROUPS:LOGITS].rearrange("p t (g e) -> p t g e", e=PER_GROUP),
                               last(group[:, :, :], PER_GROUP), ALU.mult))
            do(v.tensor_reduce(inside[:, :, :], parts[:, :, :, :].rearrange("p t g e -> p t e g"), AX.X, ALU.add))
            one_hot_max(inside[:, :, :], best[:, 0, :], here[:, 0, :, :], PER_GROUP)
            do(v.scalar_tensor_tensor(inside[:, :, :], here[:, 0, :, :], -3e38, inside[:, :, :], ALU.mult, ALU.add))
            one_hot_max(inside[:, :, :], best[:, 1, :], here[:, 1, :, :], PER_GROUP)
            v.tensor_tensor(second[:, :], best[:, 1, :], best[:, 0, :], ALU.subtract).then_inc(to_exp, 1)
            for c in range(2):
                do(v.tensor_tensor(hot[:, c, :, :].rearrange("p t (g e) -> p t g e", e=PER_GROUP), last(group[:, :, :], PER_GROUP),
                                   here[:, c, :, :].unsqueeze(2).broadcast_to([P, TT, GROUPS, PER_GROUP]), ALU.mult))
            v.tensor_tensor(both[:, :, :], hot[:, 0, :, :], hot[:, 1, :, :], ALU.add).then_inc(chosen, 1)
            dve.wait_ge(exp_done, 2)
            do(v.tensor_reduce(total[:, :], exps[:, :, :], AX.X, ALU.add))
            do(v.scalar_tensor_tensor(total[:, :], second[:, :], 1.0, total[:, :], ALU.add, ALU.mult))
            do(v.reciprocal(moe.weight[:, 0, :], total[:, :]))
            do(v.tensor_tensor(moe.weight[:, 1, :], moe.weight[:, 0, :], second[:, :], ALU.mult))
            dve.wait_ge(counted, 1)
            do(v.tensor_copy(rank[:, :, :], g.bank[1][:, 0:TT * EXPERTS].rearrange("p (t e) -> p t e", e=EXPERTS)))
            do(v.tensor_copy(count[:, :], g.bank[1][:, TT * EXPERTS:(TT + 1) * EXPERTS]))
            do(v.tensor_scalar(more[:, :], count[:, :], float(P), None, ALU.is_gt))
            for j in range(2, TT):
                do(v.scalar_tensor_tensor(more[:, :], count[:, :], float(j * P), more[:, :], ALU.is_gt, ALU.add))
            do(v.tensor_tensor_scan(more_end[:, :], g.ones[:, 0:EXPERTS], more[:, :], 0.0, ALU.mult, ALU.add))
            do(v.tensor_tensor(more_start[:, :], more_end[:, :], more[:, :], ALU.subtract))
            over_pairs = lambda a: a.unsqueeze(1).broadcast_to([P, 2, TT, EXPERTS])
            spread = lambda a: a.unsqueeze(1).broadcast_to([P, TT, EXPERTS])
            for out, of in ((slot, rank[:, :, :]), (expert, spread(iota(EXPERTS))), (start, spread(more_start[:, :]))):
                for c in range(2):
                    do(v.tensor_tensor(picked[:, c, :, :], hot[:, c, :, :], of, ALU.mult))
                do(v.tensor_reduce(out[:, :, :], picked[:, :, :, :], AX.X, ALU.add))
            do(v.tensor_scalar(past[:, :, :], slot[:, :, :], float(P), None, ALU.is_ge))
            for j in range(2, TT):
                do(v.scalar_tensor_tensor(past[:, :, :], slot[:, :, :], float(j * P), past[:, :, :], ALU.is_ge, ALU.add))
            do(v.scalar_tensor_tensor(slot[:, :, :], past[:, :, :], -float(P), slot[:, :, :], ALU.mult, ALU.add))
            do(v.scalar_tensor_tensor(start[:, :, :], start[:, :, :], EXPERTS - 1.0, past[:, :, :], ALU.add, ALU.add))
            do(v.tensor_tensor(start[:, :, :], start[:, :, :], expert[:, :, :], ALU.subtract))
            do(v.scalar_tensor_tensor(start[:, :, :], past[:, :, :], 0.0, start[:, :, :], ALU.is_gt, ALU.mult))
            do(v.tensor_tensor(expert[:, :, :], expert[:, :, :], start[:, :, :], ALU.add))
            for c in range(2):
                for t in range(TT):
                    n = c * TT + t
                    own.did(v.tensor_scalar(by_slot[:, n, :], iota(P), slot[:, c, t:t + 1], None, ALU.is_equal))
                    own.did(v.tensor_scalar(by_tile[:, n, :], iota(MOE_TILES), expert[:, c, t:t + 1], g.col("pair_number", n),
                                            ALU.is_equal, ALU.mult))
            own.wait()
            dve.sem_inc(placed, 1)
            do(v.tensor_tensor(ended[:, :, :], more_end[0:1, :].unsqueeze(1).broadcast_to([1, MORE, EXPERTS]),
                               last(iota(MORE, 1), EXPERTS), ALU.is_le))
            do(v.tensor_reduce(which[:, :], ended[:, :, :], AX.X, ALU.add))
            do(v.tensor_scalar(which[:, :], which[:, :], EXPERTS - 1.0, None, ALU.min))
            do(v.tensor_copy(moe.more_expert[:, :], which[:, :]))
            do(v.tensor_copy(moe.more_tiles[:, :], more_end[0:1, EXPERTS - 1:EXPERTS]))
            dve.wait_ge(table_done, 1)
            do(v.tensor_scalar(empty[:, :], g.bank[6][:, 0:MOE_TILES], 0.0, g.col("beyond"), ALU.is_equal, ALU.mult))
            do(v.scalar_tensor_tensor(place[:, :], g.bank[6][:, 0:MOE_TILES], -1.0, empty[:, :], ALU.add, ALU.add))
            do(v.tensor_copy(moe.pair[:, :], place[:, :]))
            do(v.tensor_scalar(moe.token[:, :], moe.pair[:, :], 1, None, ALU.logical_shift_right))



def after(eng, semaphore, count):
    if not isinstance(count, int) or count > 0:
        eng.wait_ge(semaphore, count)


class Tile:

    def __init__(self, g, ctx, moe, tag):
        sem, sb = g.stage(ctx, tag)
        self.g, self.moe = g, moe
        self.cleared, self.passed = sem("cleared"), sem("passed")
        self.token_copied, self.pair_copied = sem("token_copied"), sem("pair_copied")
        self.gathered, self.scattered = [sem("gathered0"), sem("gathered1")], [sem("scattered0"), sem("scattered1")]
        self.turned, self.turn_read_act, self.turn_read_dve = sem("turned"), sem("turn_read_act"), sem("turn_read_dve")
        self.up_done, self.silu_done, self.product_done = sem("up_done"), sem("silu_done"), sem("product_done")
        self.back_turned, self.back_read = sem("back_turned"), sem("back_read")
        self.down_done, self.out_read_act, self.out_read_dve = sem("down_done"), sem("out_read_act"), sem("out_read_dve")
        self.rows = [g.mix[:, 2 * b:2 * b + 2, :].rearrange("p a n -> p (a n)") for b in range(2)]
        self.xt = g.mix[:, 4:6, :].rearrange("p a (k n) -> p (a k) n", n=P)
        self.out = [g.memn[:, 4 * b:4 * b + 4, :].rearrange("p a n -> p (a n)") for b in range(2)]
        self.silu, self.act, self.back = sb("silu", [P, FE]), sb("act", [P, FE]), sb("back", [P, 2, P])
        self.token, self.pair = sb("token", [P, 2], I32), sb("pair", [P, 2], I32)


    def clear(self, pool):
        for b in range(2):
            self.g.nc.gpsimd.memset(self.rows[b], 0.0).then_inc(self.cleared, 1)
        pool.wait_ge(self.cleared, 2)

    def gather(self, pool, n, tile, b):
        nc, moe, here = self.g.nc, self.moe, slice(b, b + 1)
        nc.gpsimd.tensor_copy(self.token[:, here], moe.token[:, tile]).then_inc(self.token_copied, 1)
        pool.wait_ge(self.token_copied, n + 1)
        pool.sem_inc(self.passed, 1)
        nc.gpsimd.indirect_dma_start(out=self.rows[b], out_offset=None, in_=moe.rows,
                                     in_offset=bass.IndirectOffsetOnAxis(ap=self.token[:, here], axis=0),
                                     bounds_check=T - 1, oob_is_err=False).then_inc(self.gathered[b], 16)

    def scatter(self, pool, n, tile, b):
        nc, moe, here = self.g.nc, self.moe, slice(b, b + 1)
        pool.wait_ge(self.out_read_act, n + 1)
        pool.wait_ge(self.out_read_dve, n + 1)
        pool.sem_inc(self.passed, 1)
        nc.gpsimd.tensor_copy(self.pair[:, here], moe.pair[:, tile]).then_inc(self.pair_copied, 1)
        pool.wait_ge(self.pair_copied, n + 1)
        pool.sem_inc(self.passed, 1)
        nc.gpsimd.indirect_dma_start(out=moe.pair_rows, out_offset=bass.IndirectOffsetOnAxis(ap=self.pair[:, here], axis=0),
                                     in_=self.out[b], in_offset=None,
                                     bounds_check=2 * T - 1, oob_is_err=False).then_inc(self.scattered[b], 16)


    def turn(self, pe, n, b, uses):
        pe.wait_ge(self.gathered[b], 16 * uses + 16)
        after(pe, self.turn_read_act, n)
        after(pe, self.turn_read_dve, n)
        for k in range(KT):
            mm = self.g.nc.tensor.matmul(self.g.bank[k // 4][:, k % 4 * P:(k % 4 + 1) * P], self.rows[b][:, k * P:(k + 1) * P],
                                         self.g.ident[:, :], start=True, stop=True)
            if k % 4 == 3:
                mm.then_inc(self.turned, 1)

    def up(self, pe, n, b, weights):
        pe.wait_ge(self.turn_read_act, n + 1)
        pe.wait_ge(self.turn_read_dve, n + 1)
        for k in range(KT):
            mm = self.g.nc.tensor.matmul(self.g.bank[2 + b][:, :], self.xt[:, k, :], weights[k // 4][:, k % 4 * 2 * FE:(k % 4 + 1) * 2 * FE],
                                         start=(k == 0), stop=(k == KT - 1))
        mm.then_inc(self.up_done, 1)

    def turn_back(self, pe, n):
        pe.wait_ge(self.product_done, n + 1)
        for j in range(2):
            mm = self.g.nc.tensor.matmul(self.g.bank[4][:, j * P:(j + 1) * P], self.act[:, j * P:(j + 1) * P], self.g.ident[:, :],
                                         start=True, stop=True)
        mm.then_inc(self.back_turned, 1)

    def down(self, pe, n, weights):
        pe.wait_ge(self.back_read, n + 1)
        after(pe, self.out_read_act, n)
        after(pe, self.out_read_dve, n)
        for h in range(2):
            for j in range(2):
                c = 4 * 2 * FE + h * T
                mm = self.g.nc.tensor.matmul(self.g.bank[5 + h][:, :], self.back[:, j, :], weights[j][:, c:c + T],
                                             start=(j == 0), stop=(j == 1))
            mm.then_inc(self.down_done, 1)


    def act_turn(self, act, n):
        act.wait_ge(self.turned, 2 * n + 1)
        self.g.nc.scalar.activation(self.xt[:, 0:4, :].rearrange("p k n -> p (k n)"), self.g.bank[0][:, :], ACT.Copy)\
            .then_inc(self.turn_read_act, 1)

    def act_silu(self, act, n, b):
        act.wait_ge(self.up_done, n + 1)
        after(act, self.product_done, n)
        self.g.nc.scalar.activation(self.silu[:, :], self.g.bank[2 + b][:, 0:FE], ACT.Silu).then_inc(self.silu_done, 1)

    def act_out(self, act, n, b, uses):
        act.wait_ge(self.down_done, 2 * n + 1)
        after(act, self.scattered[b], 16 * uses)
        self.g.nc.scalar.activation(self.out[b][:, 0:T], self.g.bank[5][:, :], ACT.Copy).then_inc(self.out_read_act, 1)


    def dve_turn(self, dve, n):
        dve.wait_ge(self.turned, 2 * n + 2)
        self.g.nc.vector.tensor_copy(self.xt[:, 4:8, :].rearrange("p k n -> p (k n)"), self.g.bank[1][:, :])\
            .then_inc(self.turn_read_dve, 1)

    def dve_product(self, dve, n, b):
        dve.wait_ge(self.silu_done, n + 1)
        after(dve, self.back_turned, n)
        self.g.nc.vector.tensor_tensor(self.act[:, :], self.silu[:, :], self.g.bank[2 + b][:, FE:2 * FE], ALU.mult)\
            .then_inc(self.product_done, 1)

    def dve_back(self, dve, n):
        dve.wait_ge(self.back_turned, n + 1)
        after(dve, self.down_done, 2 * n)
        self.g.nc.vector.tensor_copy(self.back[:, :, :].rearrange("p a n -> p (a n)"), self.g.bank[4][:, 0:2 * P])\
            .then_inc(self.back_read, 1)

    def dve_out(self, dve, n, b, uses):
        dve.wait_ge(self.down_done, 2 * n + 2)
        after(dve, self.scattered[b], 16 * uses)
        self.g.nc.vector.tensor_copy(self.out[b][:, T:D], self.g.bank[6][:, :]).then_inc(self.out_read_dve, 1)


def stage_experts(g, moe, units):
    nc = g.nc
    units.begin()
    ROUNDS = EXPERTS // IN_FLIGHT
    weights = [[moe.ring.slots[2 * u], moe.ring.slots[2 * u + 1]] for u in range(IN_FLIGHT)]
    with ExitStack() as ctx:
        w = Tile(g, ctx, moe, "experts")
        block = ctx.enter_context(nc.Block())

        def rounds(eng, step):
            for u in range(IN_FLIGHT):
                step(0, u, IN_FLIGHT)
            with eng.Fori(1, ROUNDS - 1) as i:
                for u in range(IN_FLIGHT):
                    step(i, u, IN_FLIGHT)
            for u in range(IN_FLIGHT):
                step(ROUNDS - 1, u, IN_FLIGHT - 1 - u)

        @block.sync
        def _(sp):
            with sp.Fori(1, ROUNDS) as i:
                for u in range(IN_FLIGHT):
                    sp.wait_ge(w.down_done, 2 * IN_FLIGHT * i - 2 * IN_FLIGHT + 2 * u + 2)
                    units.load(sp, i, 2 * u)
                    units.load(sp, i, 2 * u + 1)

        @block.gpsimd
        def _(pool):
            w.clear(pool)
            w.gather(pool, 0, slice(0, 1), 0)
            w.gather(pool, 1, slice(1, 2), 1)

            def step(i, u, later):
                n, b = IN_FLIGHT * i + u, u % 2
                if later >= 2:
                    pool.wait_ge(w.turned, 2 * n + 2)
                    pool.sem_inc(w.passed, 1)
                    w.gather(pool, n + 2, bass.ds(n + 2, 1), b)
                w.scatter(pool, n, bass.ds(n, 1), b)
            rounds(pool, step)
            for b in range(2):
                pool.wait_ge(w.scattered[b], 16 * EXPERTS // 2)

        @block.tensor
        def _(pe):
            def load_up(i, u):
                n, v = IN_FLIGHT * i + u, u % IN_FLIGHT
                for s in range(2):
                    units.wait(pe, i + u // IN_FLIGHT, 2 * v + s)
                w.up(pe, n, u % 2, weights[v])

            def step(i, u, later):
                n = IN_FLIGHT * i + u
                if later >= 1:
                    w.turn(pe, n + 1, (u + 1) % 2, IN_FLIGHT // 2 * i + (u + 1) // 2)
                w.turn_back(pe, n)
                if later >= 1:
                    load_up(i, u + 1)
                w.down(pe, n, weights[u])
            w.turn(pe, 0, 0, 0)
            load_up(0, 0)
            rounds(pe, step)

        @block.scalar
        def _(act):
            def step(i, u, later):
                n = IN_FLIGHT * i + u
                if later >= 1:
                    w.act_turn(act, n + 1)
                    w.act_silu(act, n + 1, (u + 1) % 2)
                w.act_out(act, n, u % 2, IN_FLIGHT // 2 * i + u // 2)
            w.act_turn(act, 0)
            w.act_silu(act, 0, 0)
            rounds(act, step)

        @block.vector
        def _(dve):
            def step(i, u, later):
                n = IN_FLIGHT * i + u
                if later >= 1:
                    w.dve_turn(dve, n + 1)
                w.dve_back(dve, n)
                if later >= 1:
                    w.dve_product(dve, n + 1, (u + 1) % 2)
                w.dve_out(dve, n, u % 2, IN_FLIGHT // 2 * i + u // 2)
            w.dve_turn(dve, 0)
            w.dve_product(dve, 0, 0)
            rounds(dve, step)


def stage_more_experts(g, moe, units):
    nc = g.nc
    of_expert = units.ap.rearrange("i (u s) p n -> (i u) s p n", s=2)
    weights = moe.ring.slots[0:2]
    with ExitStack() as ctx:
        w = Tile(g, ctx, moe, "more")
        ready = [g.flag(ctx, f"more_ready{s}") for s in range(2)]
        block = ctx.enter_context(nc.Block())

        def any_more(eng):
            return eng.If(eng.value_load(moe.more_tiles[0:1, 0:1], min_val=0, max_val=MORE) > 0)

        def tiles(eng, tile):
            tile(0)
            with eng.Fori(1, MORE) as n:
                tile(n)

        @block.sync
        def _(sp):
            with any_more(sp):
                def tile(n):
                    expert = sp.value_load(moe.more_expert[0:1, bass.ds(n, 1)], min_val=0, max_val=EXPERTS - 1)
                    after(sp, w.down_done, 2 * n)
                    sp.sem_inc(w.passed, 1)
                    for s in range(2):
                        sp.dma_start(weights[s][:, :], of_expert[expert, s]).then_inc(ready[s], 16)
                tiles(sp, tile)

        @block.gpsimd
        def _(pool):
            with any_more(pool):
                def tile(n):
                    after(pool, w.turned, 2 * n)
                    pool.sem_inc(w.passed, 1)
                    w.gather(pool, n, bass.ds(n + EXPERTS, 1), 0)
                    w.scatter(pool, n, bass.ds(n + EXPERTS, 1), 0)
                tiles(pool, tile)
                pool.wait_ge(w.scattered[0], 16 * MORE)

        @block.tensor
        def _(pe):
            with any_more(pe):
                def tile(n):
                    w.turn(pe, n, 0, n)
                    for s in range(2):
                        pe.wait_ge(ready[s], 16 * n + 16)
                    w.up(pe, n, 0, weights)
                    w.turn_back(pe, n)
                    w.down(pe, n, weights)
                tiles(pe, tile)

        @block.scalar
        def _(act):
            with any_more(act):
                def tile(n):
                    w.act_turn(act, n)
                    w.act_silu(act, n, 0)
                    w.act_out(act, n, 0, n)
                tiles(act, tile)

        @block.vector
        def _(dve):
            with any_more(dve):
                def tile(n):
                    w.dve_turn(dve, n)
                    w.dve_product(dve, n, 0)
                    w.dve_back(dve, n)
                    w.dve_out(dve, n, 0, n)
                tiles(dve, tile)


def stage_combine(g, moe):
    nc = g.nc
    with ExitStack() as ctx:
        sem, sb = g.stage(ctx, "combine")
        loaded = [sem("loaded0"), sem("loaded1")]
        weighed, summed, turned, added = (sem(n) for n in ("weighed", "summed", "turned", "added"))
        two = [sb(f"two{b}", [P, 2, D]) for b in range(2)]
        out = [sb(f"sum{b}", [P, D]) for b in range(2)]
        block = ctx.enter_context(nc.Block())
        pairs = moe.pair_rows.rearrange("(t p c) n -> t p (c n)", p=P, c=2)

        @block.sync
        def _(sp):
            for t in range(TT):
                if t >= 2:
                    sp.wait_ge(summed, t - 1)
                sp.dma_start(two[t % 2][:, :, :].rearrange("p c n -> p (c n)"), pairs[t]).then_inc(loaded[t % 2], 16)
            sp.wait_ge(loaded[0], 32)
            sp.wait_ge(loaded[1], 32)

        @block.scalar
        def _(act):
            for t in range(TT):
                act.wait_ge(loaded[t % 2], 16 * (t // 2 + 1))
                if t >= 2:
                    act.wait_ge(turned, 2 * t - 2)
                nc.scalar.activation(out[t % 2][:, :], two[t % 2][:, 0, :], ACT.Copy, scale=moe.weight[:, 0, t:t + 1]).then_inc(weighed, 1)

        @block.vector
        def _(dve):
            def add(t):
                for h in range(2):
                    dve.wait_ge(turned, 2 * t + h + 1)
                    for j in range(4):
                        here = g.x[:, 4 * h + j, t * P:(t + 1) * P]
                        ins = nc.vector.scalar_tensor_tensor(here, g.bank[2 * (t % 2) + h][:, j * P:(j + 1) * P],
                                                             g.mod[:, 40 + 4 * h + j:41 + 4 * h + j], here, ALU.mult, ALU.add)
                    ins.then_inc(added, 1)
            for t in range(TT):
                dve.wait_ge(weighed, t + 1)
                nc.vector.scalar_tensor_tensor(out[t % 2][:, :], two[t % 2][:, 1, :], moe.weight[:, 1, t:t + 1], out[t % 2][:, :],
                                               ALU.mult, ALU.add).then_inc(summed, 1)
                if t > 0:
                    add(t - 1)
            add(TT - 1)

        @block.tensor
        def _(pe):
            for t in range(TT):
                pe.wait_ge(summed, t + 1)
                for h in range(2):
                    if t >= 2:
                        pe.wait_ge(added, 2 * (t - 2) + h + 1)
                    for j in range(4):
                        k = 4 * h + j
                        mm = nc.tensor.matmul(g.bank[2 * (t % 2) + h][:, j * P:(j + 1) * P], out[t % 2][:, k * P:(k + 1) * P],
                                              g.ident[:, :], start=True, stop=True)
                    mm.then_inc(turned, 1)


def stage_store(g, out):
    nc = g.nc
    with ExitStack() as ctx:
        norm = Norm(g, ctx, g.gains[:, 2, :], g.mod[:, 48:48 + KT])
        stored = g.flag(ctx, "stored")
        block = ctx.enter_context(nc.Block())

        @block.sync
        def _(sp):
            for k in range(KT):
                sp.wait_ge(norm.xn_ready, k + 1)
                sp.dma_start(out[:, k, :], g.xn[:, k, :]).then_inc(stored, 16)
            sp.wait_ge(stored, 16 * KT)

        @block.tensor
        def _(pe):
            norm.tensor(pe)

        @block.scalar
        def _(act):
            norm.scalar(act)

        @block.vector
        def _(dve):
            norm.vector(dve)



def as_columns(a):
    return np.asarray(a).reshape(-1, P).T


def padded_column(a):
    a = np.asarray(a).reshape(-1)
    return np.pad(a, (0, P - a.size)).reshape(P, 1)


def by_partition(w):
    w = np.asarray(w)
    return w.reshape(-1, P, w.shape[1]).transpose(1, 0, 2).reshape(P, -1)


def units_of(pieces):
    return np.stack([np.stack([by_partition(p) for p in one]) for one in pieces])


def columns_of(w, width, per):
    w = np.asarray(w)
    cut = [w[:, c:c + width] for c in range(0, w.shape[1], width)]
    return units_of([cut[n:n + per] for n in range(0, len(cut), per)])


def side(*pieces):
    return np.concatenate([np.asarray(p) for p in pieces], axis=1)


def lay_out(v):
    a, table = {}, []
    v = {k: np.asarray(x) for k, x in v.items()}
    feature_major = lambda t: t.reshape(-1, KT, P).transpose(2, 1, 0)
    a["x"], a["mem"] = feature_major(v["x"][0]), feature_major(v["mem"][0])
    for l in range(2):
        for n in ("mix", "xattn", "mem", "ffn"):
            table.append((f"{n}_norm{l}", as_columns(v[f"{n}_norm"][l])))
        table.append((f"ffn_conv{l}", as_columns(np.concatenate([v["ffn_conv_w"][l].reshape(-1), v["ffn_conv_b"][l]]))))
    w = v["attn_w_in"][0]
    table.append(("w_forget", by_partition(w[:, 1536:1544])))
    table.append(("fox_bf", padded_column(v["attn_fox_bf"][0])))
    table.append(("diff_l", np.concatenate([padded_column(v[n][0]) for n in ("diff_lq1", "diff_lk1", "diff_lq2", "diff_lk2")], 1)))
    table.append(("subln", as_columns(v["diff_subln"][0])))
    a["w_fox"] = units_of([[side(*(w[:, c + P * h:c + P * h + P] for c in (0, 512, 1024)))] for h in range(4)])
    a["w_diff"] = units_of([[side(*(w[:, 1544 + c + P * h:1544 + c + P * h + P] for c in (0, 512, 1024)))] for h in range(4)])
    a["w_attn_out"] = columns_of(v["attn_w_out"][0], 256, 2)
    for l in range(2):
        q, kv = v["xattn_wq"][l], v["xattn_wkv"][l]
        a[f"w_xattn{l}"] = units_of([[m[:, c + 256 * h:c + 256 * h + 256] for m, c in ((q, 0), (kv, 0), (kv, D))] for h in range(X_HEADS)])
        a[f"w_xattn_out{l}"] = columns_of(v["xattn_wo"][l], 256, 2)
        up = v["ffn_w_up"][l]
        cut = [side(up[:, P * u:P * u + P], up[:, FF + P * u:FF + P * u + P]) for u in range(FT)]
        a[f"w_up{l}"] = units_of([cut[n:n + 2] for n in range(0, FT, 2)])
        a[f"w_down{l}"] = columns_of(v["ffn_w_down"][l], P, 2)
    lay_out_more(v, a, table)
    where, at = {}, 0
    for name, c in table:
        where[name], at = at, at + c.shape[1]
    where["width"] = at
    a["vecs"] = np.concatenate([c for _, c in table], axis=1)
    return {k: np.ascontiguousarray(x) for k, x in a.items()}, where


def lay_out_mlstm(v, a, table):
    w = v["mlstm_w_in"][0]
    table.append(("w_gates", by_partition(w[:, 2048:2056])))
    table.append(("mlstm_b_i", padded_column(v["mlstm_b_i"][0])))
    table.append(("mlstm_b_f", padded_column(v["mlstm_b_f"][0])))
    table.append(("conv_qk", as_columns(v["mlstm_conv_qk"][0])))
    table.append(("head_norm", as_columns(v["mlstm_head_norm"][0])))
    a["w_mlstm"] = units_of([[side(w[:, P * h:P * h + P], w[:, 512 + P * h:512 + P * h + P]),
                              w[:, 1024 + 256 * h:1024 + 256 * h + 256], w[:, 2056 + 256 * h:2056 + 256 * h + 256]]
                             for h in range(ML_HEADS)])
    a["w_mlstm_out"] = columns_of(v["mlstm_w_out"][0], 256, 2)


def lay_out_second(v, a, table):
    for name in ("mu_rkv", "w0", "a0", "k_k", "k_a", "lnx_g", "lnx_b", "conv_b", "b_rgate", "b_igate", "lam",
                 "g_mix", "g_ffn", "mu_wag", "r_k"):
        table.append((name, as_columns(v[f"{name}_2"][0])))
    table.append(("final_norm", as_columns(v["final_norm"])))
    table.append(("g_final", as_columns(v["g_final_2"])))
    table.append(("c", as_columns(v["c_2"])))
    table.append(("b_ada", np.concatenate([as_columns(v["b_ada_2"][0]), as_columns(v["b_ada_f_2"])], 1)))
    table.append(("conv_w", as_columns(v["conv_w_2"][0])))
    s, t = np.arange(CHUNK)[:, None], np.arange(CHUNK)[None, :]
    twice = lambda m: np.concatenate([m, m], 0).astype(np.float32)
    table.append(("eye", twice(s == t)))
    table.append(("tri", np.concatenate([twice(s < t), twice(s <= t)], 1)))
    table.append(("levels", np.concatenate([twice((s >> l + 1 == t >> l + 1) & (t >> l & 1 == 1) & (s >> l & 1 == 0))
                                            for l in range(6)], 1)))
    ada = side(v["w_ada_2"][0], v["w_ada_f_2"])
    rows = ada.reshape(KT, P, 2, 2, 2048).transpose(2, 0, 3, 1, 4)
    a["w_modulation"] = rows.reshape(2 * KT, 2, P, 2048)
    w = v["w_in_2"][0]
    a["w_rec_in"] = columns_of(w[:, 0:2560], 256, 2)
    first = by_partition(side(v["w1_2"][0], v["a1_2"][0], v["g1_2"][0]))
    lower = lambda m: np.pad(m, ((0, P - m.shape[0]), (0, 0)))

    def diagonal(blocks):
        z = np.zeros((HALF, HALF), blocks.dtype)
        return side(*(np.block([[blocks[2 * m], z], [z, blocks[2 * m + 1]]]) for m in range(AT)))

    second = side(lower(v["w2_2"][0]), lower(v["a2_2"][0]), v["g2_2"][0], diagonal(v["w_rgate_2"][0]), diagonal(v["w_igate_2"][0]))
    a["w_low"] = np.stack([np.pad(first, ((0, 0), (0, second.shape[1] - first.shape[1]))), second])[None]
    a["w_merge"] = units_of([[w[:, 2560 + c:2560 + c + 256], w[:, 2560 + D + c:2560 + D + c + 256],
                              np.concatenate([v["p_a_2"][0][:, c:c + 256], v["p_b_2"][0][:, c:c + 256]], 0)]
                             for c in range(0, D, 256)])
    a["w_mix_out"] = columns_of(v["w_out_2"][0], 256, 2)


def lay_out_experts(v, a, table):
    table.append(("w_router", by_partition(side(v["w_rg_2"][0], v["w_re_2"][0]))))
    bias = np.concatenate([v["b_rg_2"][0], v["b_re_2"][0]])
    table.append(("b_router", np.broadcast_to(bias, (P, bias.size))))
    p = np.arange(P, dtype=np.float32)[:, None]
    table.append(("iota", np.broadcast_to(np.arange(P, dtype=np.float32), (P, P))))
    table.append(("pair_number", np.concatenate([2 * (P * t + p) + c + 1 for c in range(2) for t in range(TT)], 1)))
    table.append(("beyond", 8 * T + 2 * p))
    up = [side(v["w1e_2"][0][e], v["w3e_2"][0][e]) for e in range(EXPERTS)]
    down = v["w2e_2"][0]
    half = lambda e, s: np.concatenate([by_partition(up[e][s * T:(s + 1) * T]), down[e][s * P:(s + 1) * P]], 1)
    a["w_experts"] = np.stack([half(e, s) for e in range(EXPERTS) for s in range(2)]).reshape(
        EXPERTS // IN_FLIGHT, 2 * IN_FLIGHT, P, SLOT)


def lay_out_more(v, a, table):
    lay_out_mlstm(v, a, table)
    lay_out_second(v, a, table)
    lay_out_experts(v, a, table)


def build(nc, A, where, out):
    with ExitStack() as ctx:
        g = Core(nc, ctx, A, where)
        U = {name: Units(g.ring, A[name]) for name in A if name.startswith("w_") and name != "w_experts"}
        stage_setup(g, U["w_modulation"])
        stage_modulation(g, U["w_modulation"], U["w_fox"])

        stage_attention(g, U["w_fox"], U["w_diff"], True)
        stage_attention(g, U["w_diff"], U["w_attn_out"], False)
        stage_dense_residual(g, U["w_attn_out"], U["w_xattn0"], g.mix, KT, 2)
        for layer in range(2):
            if layer == 1:
                stage_mlstm(g, U["w_mlstm"], U["w_mlstm_out"])
                stage_dense_residual(g, U["w_mlstm_out"], U["w_xattn1"], g.mix, KT, 2)
            stage_cross_attention(g, U[f"w_xattn{layer}"], U[f"w_xattn_out{layer}"], layer)
            stage_dense_residual(g, U[f"w_xattn_out{layer}"], U[f"w_up{layer}"], g.mix, KT, 2)
            with nc.sbuf_tensor(f"hidden{layer}", [P, FT, T], F32) as hidden:
                stage_ffn_up(g, U[f"w_up{layer}"], U[f"w_down{layer}"], layer, hidden)
                stage_dense_residual(g, U[f"w_down{layer}"], U[("w_mlstm", "w_rec_in")[layer]], hidden, FT, 1)
        stage_norm(g, g.cols("final_norm", KT), None, out=g.x)

        with ExitStack() as inner:
            rec = Recurrent(nc, inner)
            stage_recurrent_in(g, rec, U["w_rec_in"], U["w_low"])
            stage_low_rank(g, rec, U["w_low"], None)
            stage_rg_lru(g, rec)
            rw = Rwkv(rec)
            stage_rwkv_prepare(g, rec, rw)
            stage_rwkv_chunks(g, rec, rw)
            stage_rwkv_finish(g, rec, rw, U["w_merge"])
        with nc.sbuf_tensor("merged", [P, KT, T], F32) as merged:
            stage_merge(g, U["w_merge"], U["w_mix_out"], merged)
            stage_dense_residual(g, U["w_mix_out"], None, merged, KT, 2, gate=g.mod[:, 16:24])
        with ExitStack() as inner:
            moe = Experts(nc, inner, g.ring)
            experts = Units(moe.ring, A["w_experts"])
            stage_router(g, moe, experts)
            stage_experts(g, moe, experts)
            stage_more_experts(g, moe, experts)
            stage_combine(g, moe)
        stage_store(g, out)


def kernel(**inputs):
    import concourse.bacc as bacc
    from concourse.bass_utils import run_bass_kernel_spmd

    arrays, where = lay_out(inputs)
    nc = bacc.Bacc("TRN2", target_bir_lowering=False, num_devices=1)
    A = {name: nc.dram_tensor(f"in_{name}", a.shape, mybir.dt.from_np(a.dtype), kind="ExternalInput").ap()
         for name, a in arrays.items()}
    out = nc.dram_tensor("out", [P, KT, T], F32, kind="ExternalOutput").ap()
    build(nc, A, where, out)
    if not nc.is_finalized():
        nc.finalize()
    r = run_bass_kernel_spmd(nc, [{f"in_{name}": a for name, a in arrays.items()}], core_ids=[0])
    return np.ascontiguousarray(np.asarray(r.results[0]["out"]).transpose(2, 1, 0).reshape(1, T, D))
```

```python
import math
from contextlib import ExitStack

import concourse.bass as bass
import numpy as np
from concourse import mybir

ACT = mybir.ActivationFunctionType
ALU = mybir.AluOpType
AX = mybir.AxisListType
F32 = mybir.dt.float32
F32R = mybir.dt.float32r
I32 = mybir.dt.int32

P = 128
T = 512
D = 1024
KT = D // P
TT = T // P
MEM = 256
HALF = P // 2
FF = 2816
FT = FF // P
SLOT = 3072
SLOTS = 3
RMS_EPS = 1e-6
NEG = -1e30
LAMBDA_INIT = 0.2
MASKED = -1e30

FOX_PAIRS = 4
DIFF_HEADS = 4
FOX_HEADS = 8
ML_HEADS = 4
X_HEADS = 4
AW = 512
AT = AW // P
CHUNK = 64
NCHUNK = T // CHUNK
GROUPS, PER_GROUP, EXPERTS, FE = 4, 8, 32, 256
IN_FLIGHT = 4
MORE = (2 * T - 1) // P
MOE_TILES = EXPERTS + MORE


class WeightRing:

    def __init__(self, slots, ready):
        self.slots, self.ready, self.loads = slots, ready, [0] * len(slots)


class Units:

    def __init__(self, ring, ap):
        self.ring, self.ap = ring, ap
        self.n, self.per, _, self.width = ap.shape
        self.base = None

    def begin(self):
        self.base = list(self.ring.loads)
        for s in range(self.per):
            self.ring.loads[s] += self.n

    def load(self, sp, i, s):
        sp.dma_start(self.ring.slots[s][:, 0:self.width], self.ap[i, s]).then_inc(self.ring.ready[s], 16)

    def wait(self, pe, i, s):
        pe.wait_ge(self.ring.ready[s], 16 * (self.base[s] + 1) + 16 * i)

    def tile(self, s, k, m, w):
        return self.ring.slots[s][:, k * w + m * P:k * w + (m + 1) * P]

    def rows(self, s, k, w, c0, c1):
        return self.ring.slots[s][:, k * w + c0:k * w + c1]


def first_loads(sp, units):
    if units is not None:
        for s in range(units.per):
            units.load(sp, 0, s)


class Own:

    def __init__(self, eng, sem, i=0, per=0):
        self.eng, self.sem, self.base, self.n = eng, sem, i * per, 0

    def did(self, ins):
        self.n += 1
        return ins.then_inc(self.sem, 1)

    def wait(self):
        self.eng.wait_ge(self.sem, self.base + self.n)


class Core:

    def __init__(self, nc, ctx, A, where):
        self.nc, self.A, self.where = nc, A, where
        self.signals_of = None

        def sb(name, shape, dt=F32):
            return ctx.enter_context(nc.sbuf_tensor(name, shape, dt))

        self.x = sb("x", [P, KT, T])
        self.xn = sb("xn", [P, KT, T])
        self.mix = sb("mix", [P, KT, T])
        self.memn = sb("memn", [P, KT, MEM])
        self.square = sb("square", [P, 2, T])
        self.std = sb("std", [P, T])
        self.rstd = sb("rstd", [P, T])
        self.vecs = sb("vecs", [P, where["width"]])
        self.mod = sb("mod", [P, 64])
        self.gains = sb("gains", [P, 3, KT])
        self.ident = sb("ident", [P, P])
        self.mean_all = sb("mean_all", [P, P])
        self.mean_256 = sb("mean_256", [P, P])
        self.mean_128 = sb("mean_128", [P, P])
        self.ones = sb("ones", [P, P])
        self.head_sum = sb("head_sum", [P, P])
        self.causal = sb("causal", [P, P])
        self.causal_T = sb("causal_T", [P, P])
        self.chunked = sb("chunked", [P, P])
        self.eps = sb("eps", [P, 3])
        self.neg_lam = sb("neg_lam", [P, 1])
        self.ring = WeightRing([sb(f"weights{s}", [P, SLOT]) for s in range(SLOTS)],
                               [ctx.enter_context(nc.semaphore(f"weights_ready{s}")) for s in range(SLOTS)])
        self.bank = [ctx.enter_context(nc.psum_tensor(f"bank{b}", [P, 512], F32)) for b in range(8)]

    def flag(self, ctx, name):
        s = ctx.enter_context(self.nc.semaphore(name))
        if self.signals_of is not ctx:
            self.signals_of, self.signals = ctx, []
            ctx.callback(self.clear, self.signals)
        self.signals.append(s.num)
        return s

    def clear(self, numbers):
        numbers = sorted(numbers)
        first = numbers[0]
        for a, b in zip(numbers, numbers[1:] + [None]):
            if b != a + 1:
                self.nc.gpsimd.sem_clear(range(first, a + 1))
                first = b

    def stage(self, ctx, tag):
        nc = self.nc
        sem = lambda name: self.flag(ctx, name)
        sb = lambda name, shape, dt=F32: ctx.enter_context(nc.sbuf_tensor(f"{tag}_{name}", shape, dt))
        return sem, sb

    def col(self, name, j=0, rows=P):
        c = self.where[name] + j
        return self.vecs[0:rows, c:c + 1]

    def cols(self, name, n, rows=P):
        c = self.where[name]
        return self.vecs[0:rows, c:c + n]

    def col_at(self, name, j, rows=P):
        return self.vecs[0:rows, bass.ds(j + self.where[name], 1)]


class Norm:

    def __init__(self, g, ctx, gain, shift=None, out=None):
        nc = g.nc
        self.g, self.gain, self.shift, self.bank = g, gain, shift, g.bank[7]
        self.out = g.xn if out is None else out
        self.squared = g.flag(ctx, "squared")
        self.summed = g.flag(ctx, "summed")
        self.std_ready = g.flag(ctx, "std_ready")
        self.rstd_ready = g.flag(ctx, "rstd_ready")
        self.scaled = g.flag(ctx, "scaled")
        self.xn_ready = g.flag(ctx, "xn_ready") if shift is not None else self.scaled

    def scalar(self, act):
        g = self.g
        for k in range(KT):
            if k >= 2:
                act.wait_ge(self.summed, k - 1)
            g.nc.scalar.activation(g.square[:, k % 2, :], g.x[:, k, :], ACT.Square).then_inc(self.squared, 1)
        act.wait_ge(self.summed, KT)
        g.nc.scalar.activation(g.std[:, :], self.bank[:, :], ACT.Sqrt, bias=g.eps[:, 0:1]).then_inc(self.std_ready, 1)
        if self.shift is not None:
            for k in range(KT):
                act.wait_ge(self.scaled, k + 1)
                g.nc.scalar.activation(self.out[:, k, :], self.out[:, k, :], ACT.Identity,
                                       bias=self.shift[:, k:k + 1]).then_inc(self.xn_ready, 1)

    def tensor(self, pe):
        g = self.g
        for k in range(KT):
            pe.wait_ge(self.squared, k + 1)
            g.nc.tensor.matmul(self.bank[:, :], g.mean_all[:, :], g.square[:, k % 2, :],
                               start=(k == 0), stop=(k == KT - 1)).then_inc(self.summed, 1)

    def vector(self, dve):
        g = self.g
        dve.wait_ge(self.std_ready, 1)
        g.nc.vector.reciprocal(g.rstd[:, :], g.std[:, :]).then_inc(self.rstd_ready, 1)
        dve.wait_ge(self.rstd_ready, 1)
        for k in range(KT):
            g.nc.vector.scalar_tensor_tensor(self.out[:, k, :], g.x[:, k, :], self.gain[:, k:k + 1], g.rstd[:, :],
                                             ALU.mult, ALU.mult).then_inc(self.scaled, 1)

    def wait(self, eng):
        eng.wait_ge(self.xn_ready, KT)


def log1p_half(dve, own, nc, e, s, s2, p):
    own.did(nc.vector.tensor_scalar(s, e, 2.0, None, ALU.add))
    own.wait()
    own.did(nc.vector.reciprocal(s2, s))
    own.wait()
    own.did(nc.vector.tensor_tensor(s, e, s2, ALU.mult))
    own.wait()
    own.did(nc.vector.tensor_tensor(s2, s, s, ALU.mult))
    own.wait()
    own.did(nc.vector.tensor_scalar(p, s2, 1.0 / 15.0, None, ALU.mult))
    for odd in (13, 11, 9, 7, 5, 3):
        own.wait()
        own.did(nc.vector.scalar_tensor_tensor(p, p, 1.0 / odd, s2, ALU.add, ALU.mult))
    own.wait()
    own.did(nc.vector.scalar_tensor_tensor(p, p, 1.0, s, ALU.add, ALU.mult))
    own.wait()


def stage_setup(g, coming):
    nc = g.nc
    with ExitStack() as ctx:
        x_in, mem_in, vecs_in = (g.flag(ctx, n) for n in ("x_in", "mem_in", "vecs_in"))
        made, filled = g.flag(ctx, "made"), g.flag(ctx, "filled")
        squared, summed = g.flag(ctx, "squared"), g.flag(ctx, "summed")
        std_ready = g.flag(ctx, "std_ready")
        step = g.flag(ctx, "step")
        dots, dots_summed, dots_exp = (g.flag(ctx, n) for n in ("dots", "dots_summed", "dots_exp"))
        prod = ctx.enter_context(nc.sbuf_tensor("prod", [P, 2], F32))
        lam = ctx.enter_context(nc.sbuf_tensor("lam", [P, 2], F32))
        block = ctx.enter_context(nc.Block())

        @block.sync
        def _(sp):
            sp.dma_start(g.vecs[:, :], g.A["vecs"]).then_inc(vecs_in, 16)
            sp.dma_start(g.memn[:, :, :], g.A["mem"]).then_inc(mem_in, 16)
            sp.dma_start(g.x[:, :, :], g.A["x"]).then_inc(x_in, 16)
            first_loads(sp, coming)
            sp.wait_ge(x_in, 16)

        @block.gpsimd
        def _(pool):
            for t, value in ((g.ident, 0.0), (g.mean_all, 1.0 / D), (g.mean_256, 1.0 / 256), (g.mean_128, 1.0 / 128),
                             (g.ones, 1.0), (g.head_sum, 0.0), (g.causal, 0.0), (g.causal_T, 0.0), (g.chunked, 0.0)):
                nc.gpsimd.memset(t[:, :], value).then_inc(made, 1)
            for j, value in enumerate((RMS_EPS, 1e-12, 64e-5)):
                nc.gpsimd.memset(g.eps[:, j:j + 1], value).then_inc(made, 1)
            pool.wait_ge(made, 12)
            nc.gpsimd.affine_select(out=g.ident[:, :], in_=g.ident[:, :], compare_op=ALU.not_equal, fill=1.0, base=0,
                                    pattern=[[-1, P]], channel_multiplier=1).then_inc(made, 1)
            nc.gpsimd.affine_select(out=g.causal[:, :], in_=g.causal[:, :], compare_op=ALU.is_ge, fill=MASKED, base=0,
                                    pattern=[[-1, P]], channel_multiplier=1).then_inc(made, 1)
            nc.gpsimd.affine_select(out=g.causal_T[:, :], in_=g.causal_T[:, :], compare_op=ALU.is_ge, fill=MASKED, base=0,
                                    pattern=[[1, P]], channel_multiplier=-1).then_inc(made, 1)
            pool.wait_ge(made, 15)
            nc.gpsimd.memset(g.chunked[0:HALF, HALF:P], MASKED).then_inc(made, 1)
            for h in range(2):
                pool.wait_ge(made, 16 + h)
                nc.gpsimd.memset(g.head_sum[h * HALF:(h + 1) * HALF, h * HALF:(h + 1) * HALF], 1.0).then_inc(made, 1)
            pool.wait_ge(made, 18)
            nc.gpsimd.engine_nop().then_inc(filled, 1)

        @block.scalar
        def _(act):
            act.wait_ge(mem_in, 16)
            for k in range(KT):
                if k >= 2:
                    act.wait_ge(summed, k - 1)
                nc.scalar.activation(g.square[:, k % 2, 0:MEM], g.memn[:, k, :], ACT.Square).then_inc(squared, 1)
            act.wait_ge(summed, KT)
            nc.scalar.activation(g.std[:, 0:MEM], g.bank[0][:, 0:MEM], ACT.Sqrt, bias=g.eps[:, 0:1]).then_inc(std_ready, 1)
            act.wait_ge(dots_summed, 1)
            nc.scalar.activation(lam[:, :], g.bank[1][:, 0:2], ACT.Exp).then_inc(dots_exp, 1)

        @block.tensor
        def _(pe):
            pe.wait_ge(filled, 1)
            for k in range(KT):
                pe.wait_ge(squared, k + 1)
                nc.tensor.matmul(g.bank[0][:, 0:MEM], g.mean_all[:, :], g.square[:, k % 2, 0:MEM],
                                 start=(k == 0), stop=(k == KT - 1)).then_inc(summed, 1)
            pe.wait_ge(dots, 2)
            nc.tensor.matmul(g.bank[1][:, 0:2], g.ones[:, :], prod[:, :], start=True, stop=True).then_inc(dots_summed, 1)

        @block.vector
        def _(dve):
            dve.wait_ge(vecs_in, 16)
            for j in range(2):
                nc.vector.tensor_tensor(prod[:, j:j + 1], g.col("diff_l", 2 * j), g.col("diff_l", 2 * j + 1),
                                        ALU.mult).then_inc(dots, 1)
            own = Own(dve, step)
            dve.wait_ge(std_ready, 1)
            own.did(nc.vector.reciprocal(g.rstd[:, 0:MEM], g.std[:, 0:MEM]))
            own.wait()
            for k in range(KT):
                own.did(nc.vector.tensor_tensor(g.memn[:, k, :], g.memn[:, k, :], g.rstd[:, 0:MEM], ALU.mult))
            dve.wait_ge(dots_exp, 1)
            own.did(nc.vector.scalar_tensor_tensor(g.neg_lam[:, :], lam[:, 1:2], -LAMBDA_INIT, lam[:, 0:1],
                                                   ALU.add, ALU.subtract))


class Split:

    def __init__(self, hi, lo):
        self.hi, self.lo = hi, lo


def split_products(nc, out, left, right, first, last):
    nc.tensor.matmul(out, left.hi, right.hi, start=first, stop=False)
    nc.tensor.matmul(out, left.hi, right.lo, start=False, stop=False)
    return nc.tensor.matmul(out, left.lo, right.hi, start=False, stop=last)


def stage_dense_residual(g, units, coming, src, gate=None, modulation=False):
    nc = g.nc
    units.begin()
    rounds = units.n
    with ExitStack() as ctx:
        sem, sb = g.stage(ctx, f"dense{units.base[0]}")
        w_rounded, s_rounded, w_split, s_split, used, done, read, passed = (
            sem(n) for n in ("w_rounded", "s_rounded", "w_split", "s_split", "used", "product_done", "bank_read", "passed"))
        w = [Split(sb(f"w_hi{b}", [P, D], F32R), sb(f"w_lo{b}", [P, D], F32R)) for b in range(2)]
        s = [Split(sb(f"s_hi{b}", [P, T], F32R), sb(f"s_lo{b}", [P, T], F32R)) for b in range(2)]
        beside = Modulation(g, ctx) if modulation else None
        block = ctx.enter_context(nc.Block())

        def steps(eng, step, cut=0):
            def alone(i):
                for b in range(2):
                    step(i, b, 2 * i + b, slice(2 * i + b, 2 * i + b + 1), i < cut or (i == cut and b == 0))

            def loop(start, end):
                with eng.Fori(start, end) as i:
                    for b in range(2):
                        step(i, b, 2 * i + b, bass.ds(2 * i + b, 1), start < cut)
            alone(0)
            if cut:
                loop(1, cut)
                alone(cut)
                loop(cut + 1, rounds - 1)
            else:
                loop(1, rounds - 1)
            alone(rounds - 1)

        @block.sync
        def _(sp):
            with sp.Fori(1, rounds) as i:
                for b in range(2):
                    sp.wait_ge(w_split, 2 * i + b - 1)
                    units.load(sp, i, b)
            sp.wait_ge(w_split, 2 * rounds)
            first_loads(sp, coming)

        @block.scalar
        def _(act):
            if beside:
                beside.scalar(act)

            def step(i, b, k, tile, early):
                if not isinstance(i, int) or i > 0:
                    act.wait_ge(used, k - 1)
                units.wait(act, i, b)
                nc.scalar.activation(w[b].hi[:, :], units.rows(b, 0, D, 0, D), ACT.Copy).then_inc(w_rounded, 1)
                nc.scalar.activation(s[b].hi[:, :], src[:, tile, :].rearrange("p a n -> p (a n)"), ACT.Copy).then_inc(s_rounded, 1)
                if beside and early:
                    beside.load(act, beside.PLACES * k + beside.PLACES)
            steps(act, step, beside.steps // 2 if beside else 0)

        @block.gpsimd
        def _(pool):
            def step(i, b, k, tile, early):
                pool.wait_ge(w_rounded, k + 1)
                pool.sem_inc(passed, 1)
                nc.gpsimd.tensor_tensor(w[b].lo[:, :], units.rows(b, 0, D, 0, D), w[b].hi[:, :], ALU.subtract).then_inc(w_split, 1)
                pool.wait_ge(s_rounded, k + 1)
                pool.sem_inc(passed, 1)
                nc.gpsimd.tensor_tensor(s[b].lo[:, :], src[:, tile, :].rearrange("p a n -> p (a n)"), s[b].hi[:, :],
                                        ALU.subtract).then_inc(s_split, 1)
            steps(pool, step)

        @block.tensor
        def _(pe):
            def step(i, b, k, tile, early):
                first = isinstance(i, int) and k == 0
                last = isinstance(i, int) and k == 2 * rounds - 1
                pe.wait_ge(w_split, k + 1)
                pe.wait_ge(s_split, k + 1)
                for m in range(KT):
                    cut = slice(m * P, (m + 1) * P)
                    left = Split(w[b].hi[:, cut], w[b].lo[:, cut])
                    mm = split_products(nc, g.bank[m][:, :], left, Split(s[b].hi[:, :], s[b].lo[:, :]), first, last)
                    if last:
                        mm.then_inc(done, 1)
                if not last:
                    mm.then_inc(used, 1)
            steps(pe, step)
            if beside:
                pe.wait_ge(read, KT)
                beside.tensor(pe)

        @block.vector
        def _(dve):
            if beside:
                beside.vector(dve)
            for m in range(KT):
                dve.wait_ge(done, m + 1)
                here = g.x[:, m, :]
                if gate is None:
                    nc.vector.tensor_tensor(here, g.bank[m][:, :], here, ALU.add).then_inc(read, 1)
                else:
                    nc.vector.scalar_tensor_tensor(here, g.bank[m][:, :], gate[:, m:m + 1], here, ALU.mult, ALU.add).then_inc(read, 1)
            if beside:
                beside.end(dve)


LOGITS = {3: [(0, 3, 0)], 4: [(0, 2, 0), (0, 0, 384)], 5: [(1, 3, 0)], 6: [(1, 2, 0), (1, 0, 384)],
          7: [(0, 1, 0)], 1: [(1, 1, 0)]}
NLOG = len(LOGITS)


def stage_attention(g, units, coming, fox):
    nc = g.nc
    units.begin()
    scale = HALF ** -0.5
    maps = 2 if fox else 1
    first = 0 if fox else FOX_PAIRS
    turned = 4 * maps
    with ExitStack() as ctx:
        sem, sb = g.stage(ctx, "fox" if fox else "diff")
        proj_done, q_ready, k_ready, vT_ready, vt_done, v_ready = (
            sem(n) for n in ("proj_done", "q_ready", "k_ready", "vT_ready", "vt_done", "v_ready"))
        logits_done, max_done, exp_done, p_ready = (sem(n) for n in ("logits_done", "max_done", "exp_done", "p_ready"))
        turned_done, turned_even, turned_odd = (sem(n) for n in ("turned_done", "turned_even", "turned_odd"))
        values_done, mixed = sem("values_done"), sem("mixed")
        step, rows_ready = sem("step"), sem("rows_ready")
        gate_done, gate_abs, gate_exp, forget_ready = (sem(n) for n in ("gate_done", "gate_abs", "gate_exp", "forget_ready"))
        head_squared, head_summed, head_std, head_rstd = (sem(n) for n in ("head_squared", "head_summed", "head_std", "head_rstd"))
        qT, kT, vT = sb("qT", [P, T]), sb("kT", [P, T]), sb("vT", [P, T])
        v = sb("v", [P, TT, P])
        probs = sb("probs", [P, 2, TT, T])
        probs_T = sb("probs_T", [P, 2, TT, T])
        neg_max, total, inv = sb("neg_max", [P, 8]), sb("total", [P, 8]), sb("inv", [P, 8])
        if fox:
            norm = Norm(g, ctx, g.cols("mix_norm0", KT))
            F = sb("F", [FOX_HEADS, T])
            tmp = [sb(f"gate_tmp{j}", [FOX_HEADS, T]) for j in range(5)]
            rows = sb("rows", [FOX_HEADS, 2, T])
            minus = sb("minus", [FOX_HEADS, P])
        else:
            sub_gain = sb("sub_gain", [P, 1])
        block = ctx.enter_context(nc.Block())

        @block.sync
        def _(sp):
            with sp.Fori(1, units.n) as i:
                sp.wait_ge(proj_done, 3 * i)
                units.load(sp, i, 0)
            sp.wait_ge(proj_done, 3 * units.n)
            first_loads(sp, coming)

        @block.tensor
        def _(pe):
            pe.sem_inc(turned_even, 1)
            pe.sem_inc(turned_odd, 1)
            pe.sem_inc(mixed, 1)
            pe.sem_inc(exp_done, 1)
            if fox:
                norm.tensor(pe)
                norm.wait(pe)
                for k in range(KT):
                    mm = nc.tensor.matmul(g.bank[6][0:FOX_HEADS, :], g.cols("w_forget", KT * FOX_HEADS)[:, k * FOX_HEADS:(k + 1) * FOX_HEADS],
                                          g.xn[:, k, :], start=(k == 0), stop=(k == KT - 1))
                mm.then_inc(gate_done, 1)
                pe.wait_ge(forget_ready, 1)
            with pe.Fori(0, units.n) as i:
                units.wait(pe, i, 0)
                pe.wait_ge(turned_even, turned // 2 * i + 1)
                pe.wait_ge(turned_odd, turned // 2 * i + 1)
                pe.wait_ge(mixed, i + 1)
                for j in range(3):
                    for k in range(KT):
                        mm = nc.tensor.matmul(g.bank[j][:, :], units.tile(0, k, j, 3 * P), g.xn[:, k, :],
                                              start=(k == 0), stop=(k == KT - 1))
                    mm.then_inc(proj_done, 1)
                pe.wait_ge(q_ready, i + 1)
                pe.wait_ge(k_ready, i + 1)
                pe.wait_ge(exp_done, NLOG * i + 1)
                if fox:
                    pe.wait_ge(rows_ready, 2 * i + 2)
                for b, places in LOGITS.items():
                    for m, qb, c in places:
                        keys = (qb + 1) * P
                        half = slice(m * HALF, (m + 1) * HALF)
                        out = g.bank[b][:, c:c + keys]
                        nc.tensor.matmul(out, qT[half, qb * P:(qb + 1) * P], kT[half, 0:keys], start=True, stop=False)
                        if fox:
                            nc.tensor.matmul(out, minus[:, :], rows[:, m, 0:keys], start=False, stop=False)
                        mm = nc.tensor.matmul(g.bank[b][:, c + keys - P:c + keys], g.ident[:, :],
                                              (g.causal if fox else g.chunked)[:, :], start=False, stop=True)
                    mm.then_inc(logits_done, 1)
                pe.wait_ge(vT_ready, i + 1)
                for t in range(TT):
                    mm = nc.tensor.transpose(g.bank[0][:, t * P:(t + 1) * P], vT[:, t * P:(t + 1) * P], g.ident[:, :])
                mm.then_inc(vt_done, 1)
                pe.wait_ge(v_ready, i + 1)
                for m in range(maps):
                    for n, qb in enumerate((3, 2, 1, 0)):
                        pe.wait_ge(p_ready, 4 * maps * i + 4 * m + n + 1)
                        count = turned // 2 * i + (4 * m + n) // 2
                        if 4 * m + n >= 2:
                            pe.wait_ge((turned_even, turned_odd)[n % 2], count + 1)
                        for kb in range(qb + 1):
                            mm = nc.tensor.transpose(g.bank[n % 2][:, kb * P:(kb + 1) * P],
                                                     probs[:, m, qb, kb * P:(kb + 1) * P], g.ident[:, :])
                        mm.then_inc(turned_done, 1)
                    pe.wait_ge(turned_even, turned // 2 * i + 2 * (m + 1) + 1)
                    pe.wait_ge(turned_odd, turned // 2 * i + 2 * (m + 1) + 1)
                    own = slice(m * HALF, (m + 1) * HALF) if fox else slice(0, P)
                    for kb in range(TT):
                        mm = nc.tensor.matmul(g.bank[2][own, kb * P:T], v[:, kb, own], probs_T[:, m, kb, kb * P:T],
                                              start=(kb == 0), stop=(kb == TT - 1), skip_group_check=True)
                mm.then_inc(values_done, 1)
                if not fox:
                    pe.wait_ge(head_squared, i + 1)
                    nc.tensor.matmul(g.bank[0][:, :], g.mean_128[:, :], g.square[:, 0, :], start=True, stop=True)\
                      .then_inc(head_summed, 1)
                    pe.wait_ge(head_std, i + 1)

        @block.scalar
        def _(act):
            if fox:
                norm.scalar(act)
                act.wait_ge(gate_abs, 1)
                nc.scalar.activation(tmp[1][:, :], tmp[1][:, :], ACT.Exp, scale=-1.0).then_inc(gate_exp, 1)
            with act.Fori(0, units.n) as i:
                act.wait_ge(proj_done, 3 * i + 1)
                nc.scalar.activation(qT[:, :], g.bank[0][:, :], ACT.Copy, scale=scale).then_inc(q_ready, 1)
                act.wait_ge(proj_done, 3 * i + 3)
                nc.scalar.activation(vT[:, :], g.bank[2][:, :], ACT.Copy).then_inc(vT_ready, 1)
                for j, (b, places) in enumerate(LOGITS.items()):
                    act.wait_ge(max_done, NLOG * i + j + 1)
                    for m, qb, c in places:
                        keys, n = (qb + 1) * P, 4 * m + qb
                        e = nc.scalar.activation(probs[:, m, qb, 0:keys], g.bank[b][:, c:c + keys], ACT.Exp,
                                                 bias=neg_max[:, n:n + 1], accum_out=total[:, n:n + 1])
                    e.then_inc(exp_done, 1)
                for m in range(maps):
                    for n, qb in ((0, 3), (2, 1)):
                        act.wait_ge(turned_done, turned * i + 4 * m + n + 1)
                        nc.scalar.activation(probs_T[:, m, 0:qb + 1, qb * P:(qb + 1) * P],
                                             g.bank[0][:, 0:(qb + 1) * P].rearrange("p (a b) -> p a b", b=P),
                                             ACT.Copy).then_inc(turned_even, 1)
                act.wait_ge(values_done, i + 1)
                if fox:
                    nc.scalar.activation(g.mix[:, bass.ds(i + first, 1), :], g.bank[2][:, :], ACT.Copy).then_inc(mixed, 1)
                else:
                    nc.scalar.activation(g.square[:, 0, :], g.bank[2][:, :], ACT.Square).then_inc(head_squared, 1)
                    act.wait_ge(head_summed, i + 1)
                    nc.scalar.activation(g.std[:, :], g.bank[0][:, :], ACT.Sqrt, bias=g.eps[:, 0:1]).then_inc(head_std, 1)

        @block.vector
        def _(dve):
            if fox:
                norm.vector(dve)
                z, e = tmp[0], tmp[1]
                own = Own(dve, step)
                dve.wait_ge(gate_done, 1)
                own.did(nc.vector.tensor_scalar(z[:, :], g.bank[6][0:FOX_HEADS, :], g.col("fox_bf", rows=FOX_HEADS), None, ALU.add))
                own.wait()
                nc.vector.scalar_tensor_tensor(e[:, :], z[:, :], -1.0, z[:, :], ALU.mult, ALU.max).then_inc(gate_abs, 1)
                own.did(nc.vector.memset(minus[:, :], -1.0))
                own.did(nc.vector.tensor_scalar(z[:, :], z[:, :], 0.0, None, ALU.min))
                dve.wait_ge(gate_exp, 1)
                log1p_half(dve, own, nc, e[:, :], tmp[2][:, :], tmp[3][:, :], tmp[4][:, :])
                own.did(nc.vector.scalar_tensor_tensor(z[:, :], tmp[4][:, :], -2.0, z[:, :], ALU.mult, ALU.add))
                own.did(nc.vector.memset(e[:, :], 1.0))
                own.wait()
                nc.vector.tensor_tensor_scan(F[:, :], e[:, :], z[:, :], 0.0, ALU.mult, ALU.add).then_inc(forget_ready, 1)
                dve.wait_ge(forget_ready, 1)
                opening = own.n
            else:
                own = Own(dve, step)
                own.did(nc.vector.tensor_scalar(sub_gain[:, :], g.col("subln"), 1.0 - LAMBDA_INIT, None, ALU.mult))
                own.wait()
                opening = own.n
            per = 1 if fox else 6
            with dve.Fori(0, units.n) as i:
                own = Own(dve, step, i, per)
                own.base = own.base + opening
                if fox:
                    for m in range(2):
                        nc.vector.tensor_scalar(rows[:, m, :], F[:, :], g.ident[0:FOX_HEADS, bass.ds(2 * i + m, 1)],
                                                None, ALU.mult).then_inc(rows_ready, 1)
                dve.wait_ge(proj_done, 3 * i + 2)
                nc.vector.tensor_copy(kT[:, :], g.bank[1][:, :]).then_inc(k_ready, 1)
                for j, (b, places) in enumerate(LOGITS.items()):
                    dve.wait_ge(logits_done, NLOG * i + j + 1)
                    for m, qb, c in places:
                        keys, n = (qb + 1) * P, 4 * m + qb
                        r = nc.vector.tensor_reduce(neg_max[:, n:n + 1], g.bank[b][:, c:c + keys], AX.X, ALU.max, negate=True)
                    r.then_inc(max_done, 1)
                dve.wait_ge(vt_done, i + 1)
                nc.vector.tensor_copy(v[:, :, :], g.bank[0][:, :].rearrange("p (a b) -> p a b", b=P)).then_inc(v_ready, 1)
                dve.wait_ge(exp_done, NLOG * i + NLOG + 1)
                own.did(nc.vector.reciprocal(inv[:, :], total[:, :]))
                own.wait()
                if fox:
                    for m in range(2):
                        for qb in (3, 2, 1, 0):
                            here, n = probs[:, m, qb, 0:(qb + 1) * P], 4 * m + qb
                            nc.vector.tensor_scalar(here, here, inv[:, n:n + 1], None, ALU.mult).then_inc(p_ready, 1)
                else:
                    own.did(nc.vector.tensor_scalar(inv[:, 4:8], inv[:, 4:8], g.neg_lam[:, 0:1], None, ALU.mult))
                    for qb in (3, 2, 1, 0):
                        here = probs[:, 0, qb, 0:(qb + 1) * P]
                        own.did(nc.vector.tensor_scalar(here, here, inv[:, qb:qb + 1], None, ALU.mult))
                        own.wait()
                        nc.vector.scalar_tensor_tensor(here, probs[:, 1, qb, 0:(qb + 1) * P], inv[:, 4 + qb:5 + qb], here,
                                                       ALU.mult, ALU.add).then_inc(p_ready, 1)
                for m in range(maps):
                    for n, qb in ((1, 2), (3, 0)):
                        dve.wait_ge(turned_done, turned * i + 4 * m + n + 1)
                        nc.vector.tensor_copy(probs_T[:, m, 0:qb + 1, qb * P:(qb + 1) * P],
                                              g.bank[1][:, 0:(qb + 1) * P].rearrange("p (a b) -> p a b", b=P))\
                          .then_inc(turned_odd, 1)
                if not fox:
                    dve.wait_ge(head_std, i + 1)
                    nc.vector.reciprocal(g.rstd[:, :], g.std[:, :]).then_inc(head_rstd, 1)
                    dve.wait_ge(head_rstd, i + 1)
                    nc.vector.scalar_tensor_tensor(g.mix[:, bass.ds(i + first, 1), :], g.bank[2][:, :], sub_gain[:, 0:1],
                                                   g.rstd[:, :], ALU.mult, ALU.mult).then_inc(mixed, 1)


def stage_cross_attention(g, units, coming, layer):
    nc = g.nc
    units.begin()
    HD = D // X_HEADS
    scale = HD ** -0.5
    with ExitStack() as ctx:
        sem, sb = g.stage(ctx, f"cross{layer}")
        norm = Norm(g, ctx, g.cols(f"xattn_norm{layer}", KT))
        mem_ready, proj_done, q_ready, k_ready, v_ready = (sem(n) for n in ("mem_ready", "proj_done", "q_ready", "k_ready", "v_ready"))
        logits_done, max_done, exp_done, inv_ready, p_ready = (
            sem(n) for n in ("logits_done", "max_done", "exp_done", "inv_ready", "p_ready"))
        turned_done, pT_ready, values_done, mixed = (sem(n) for n in ("turned_done", "pT_ready", "values_done", "mixed"))
        memg = sb("memg", [P, KT, MEM])
        qT, kT = sb("qT", [P, 2, T]), sb("kT", [P, 2, MEM])
        v = sb("v", [P, 2, HD])
        probs, probs_T = sb("probs", [P, TT, MEM]), sb("probs_T", [P, 2, T])
        neg_max, total, inv = sb("neg_max", [P, TT]), sb("total", [P, TT]), sb("inv", [P, TT])
        block = ctx.enter_context(nc.Block())

        @block.sync
        def _(sp):
            with sp.Fori(1, units.n) as i:
                for s in range(units.per):
                    sp.wait_ge(proj_done, 4 * i - 4 + (2, 3, 4)[s])
                    units.load(sp, i, s)
            sp.wait_ge(proj_done, 4 * units.n)
            first_loads(sp, coming)

        @block.tensor
        def _(pe):
            pe.sem_inc(mixed, 1)
            pe.sem_inc(k_ready, 1)
            pe.sem_inc(v_ready, 1)
            pe.sem_inc(exp_done, 1)
            pe.sem_inc(pT_ready, 1)
            norm.tensor(pe)
            norm.wait(pe)
            pe.wait_ge(mem_ready, KT)
            with pe.Fori(0, units.n) as i:
                units.wait(pe, i, 0)
                pe.wait_ge(mixed, 2 * i + 1)
                for m in range(2):
                    for k in range(KT):
                        mm = nc.tensor.matmul(g.bank[m][:, :], units.tile(0, k, m, HD), g.xn[:, k, :],
                                              start=(k == 0), stop=(k == KT - 1))
                    mm.then_inc(proj_done, 1)
                units.wait(pe, i, 1)
                pe.wait_ge(k_ready, i + 1)
                for m in range(2):
                    for k in range(KT):
                        mm = nc.tensor.matmul(g.bank[2][:, m * MEM:(m + 1) * MEM], units.tile(1, k, m, HD), memg[:, k, :],
                                              start=(k == 0), stop=(k == KT - 1))
                mm.then_inc(proj_done, 1)
                units.wait(pe, i, 2)
                pe.wait_ge(v_ready, i + 1)
                for t in range(2):
                    for k in range(KT):
                        mm = nc.tensor.matmul(g.bank[3][:, t * HD:(t + 1) * HD], memg[:, k, t * P:(t + 1) * P],
                                              units.rows(2, k, HD, 0, HD), start=(k == 0), stop=(k == KT - 1))
                mm.then_inc(proj_done, 1)
                pe.wait_ge(q_ready, 2 * i + 2)
                pe.wait_ge(k_ready, i + 2)
                pe.wait_ge(exp_done, 2 * i + 1)
                for b in range(2):
                    for j in range(2):
                        qb = 2 * b + j
                        for m in range(2):
                            mm = nc.tensor.matmul(g.bank[4 + b][:, j * MEM:(j + 1) * MEM], qT[:, m, qb * P:(qb + 1) * P],
                                                  kT[:, m, :], start=(m == 0), stop=(m == 1))
                    mm.then_inc(logits_done, 1)
                pe.wait_ge(p_ready, i + 1)
                pe.wait_ge(pT_ready, 2 * i + 1)
                for t in range(2):
                    for qb in range(TT):
                        mm = nc.tensor.transpose(g.bank[6 + t][:, qb * P:(qb + 1) * P], probs[:, qb, t * P:(t + 1) * P], g.ident[:, :])
                    mm.then_inc(turned_done, 1)
                pe.wait_ge(pT_ready, 2 * i + 3)
                pe.wait_ge(v_ready, i + 2)
                for m in range(2):
                    for t in range(2):
                        mm = nc.tensor.matmul(g.bank[m][:, :], v[:, t, m * P:(m + 1) * P], probs_T[:, t, :],
                                              start=(t == 0), stop=(t == 1))
                    mm.then_inc(values_done, 1)

        @block.scalar
        def _(act):
            norm.scalar(act)
            with act.Fori(0, units.n) as i:
                for m in range(2):
                    act.wait_ge(proj_done, 4 * i + m + 1)
                    nc.scalar.activation(qT[:, m, :], g.bank[m][:, :], ACT.Copy, scale=scale).then_inc(q_ready, 1)
                for b in range(2):
                    act.wait_ge(max_done, 2 * i + b + 1)
                    for j in range(2):
                        qb = 2 * b + j
                        e = nc.scalar.activation(probs[:, qb, :], g.bank[4 + b][:, j * MEM:(j + 1) * MEM], ACT.Exp,
                                                 bias=neg_max[:, qb:qb + 1], accum_out=total[:, qb:qb + 1])
                    e.then_inc(exp_done, 1)
                for m in range(2):
                    act.wait_ge(values_done, 2 * i + m + 1)
                    nc.scalar.activation(g.mix[:, bass.ds(2 * i + m, 1), :], g.bank[m][:, :], ACT.Copy).then_inc(mixed, 1)

        @block.vector
        def _(dve):
            for k in range(KT):
                nc.vector.tensor_scalar(memg[:, k, :], g.memn[:, k, :], g.col(f"mem_norm{layer}", k), None,
                                        ALU.mult).then_inc(mem_ready, 1)
            norm.vector(dve)
            with dve.Fori(0, units.n) as i:
                dve.wait_ge(proj_done, 4 * i + 3)
                nc.vector.tensor_copy(kT[:, :, :], g.bank[2][:, :].rearrange("p (a b) -> p a b", b=MEM)).then_inc(k_ready, 1)
                dve.wait_ge(proj_done, 4 * i + 4)
                nc.vector.tensor_copy(v[:, :, :], g.bank[3][:, :].rearrange("p (a b) -> p a b", b=HD)).then_inc(v_ready, 1)
                for b in range(2):
                    dve.wait_ge(logits_done, 2 * i + b + 1)
                    nc.vector.tensor_reduce(neg_max[:, 2 * b:2 * b + 2], g.bank[4 + b][:, :].rearrange("p (a b) -> p a b", b=MEM),
                                            AX.X, ALU.max, negate=True).then_inc(max_done, 1)
                dve.wait_ge(exp_done, 2 * i + 3)
                nc.vector.reciprocal(inv[:, :], total[:, :]).then_inc(inv_ready, 1)
                dve.wait_ge(inv_ready, i + 1)
                for qb in range(TT):
                    p = nc.vector.tensor_scalar(probs[:, qb, :], probs[:, qb, :], inv[:, qb:qb + 1], None, ALU.mult)
                p.then_inc(p_ready, 1)
                for t in range(2):
                    dve.wait_ge(turned_done, 2 * i + t + 1)
                    nc.vector.tensor_copy(probs_T[:, t, :], g.bank[6 + t][:, :]).then_inc(pT_ready, 1)


def stage_ffn_up(g, units, coming, layer, h):
    nc = g.nc
    units.begin()
    W = 2 * P
    with ExitStack() as ctx:
        sem, sb = g.stage(ctx, f"up{layer}")
        norm = Norm(g, ctx, g.cols(f"ffn_norm{layer}", KT))
        done, now_done, tap1_done, conv_done, gelu_done, h_done = (
            sem(n) for n in ("product_done", "now_done", "tap1_done", "conv_done", "gelu_done", "h_done"))
        y = sb("y", [P, 4, T])
        block = ctx.enter_context(nc.Block())

        def tap(j, i, b):
            return g.col_at(f"ffn_conv{layer}", 2 * i + b // 2 + (b % 2) * FT + j * 2 * FT)

        @block.sync
        def _(sp):
            with sp.Fori(1, units.n) as i:
                for s in range(2):
                    sp.wait_ge(done, 4 * i - 4 + 2 * s + 2)
                    units.load(sp, i, s)
            sp.wait_ge(done, 4 * units.n)
            first_loads(sp, coming)

        @block.tensor
        def _(pe):
            norm.tensor(pe)
            norm.wait(pe)
            with pe.Fori(0, units.n) as i:
                for b in range(4):
                    if b % 2 == 0:
                        units.wait(pe, i, b // 2)
                    pe.wait_ge(conv_done, 4 * i - 4 + b + 1 + 4)
                    for k in range(KT):
                        mm = nc.tensor.matmul(g.bank[b][:, :], units.tile(b // 2, k, b % 2, W), g.xn[:, k, :],
                                              start=(k == 0), stop=(k == KT - 1))
                    mm.then_inc(done, 1)

        @block.scalar
        def _(act):
            act.sem_inc(h_done, 1)
            norm.scalar(act)
            with act.Fori(0, units.n) as i:
                for b in range(4):
                    act.wait_ge(done, 4 * i + b + 1)
                    act.wait_ge(h_done, 2 * i + 1)
                    nc.scalar.activation(y[:, b, :], g.bank[b][:, :], ACT.Identity, scale=tap(2, i, b),
                                         bias=tap(3, i, b)).then_inc(now_done, 1)
                    if b % 2 == 1:
                        act.wait_ge(conv_done, 4 * i + b + 4)
                        nc.scalar.activation(y[:, b - 1, :], y[:, b - 1, :], ACT.Gelu_apprx_tanh).then_inc(gelu_done, 1)

        @block.vector
        def _(dve):
            norm.vector(dve)
            dve.sem_inc(conv_done, 4)
            with dve.Fori(0, units.n) as i:
                for b in range(4):
                    dve.wait_ge(now_done, 4 * i + b + 1)
                    nc.vector.scalar_tensor_tensor(y[:, b, 1:T], g.bank[b][:, 0:T - 1], tap(1, i, b), y[:, b, 1:T],
                                                   ALU.mult, ALU.add).then_inc(tap1_done, 1)
                    dve.wait_ge(tap1_done, 4 * i + b + 1)
                    nc.vector.scalar_tensor_tensor(y[:, b, 2:T], g.bank[b][:, 0:T - 2], tap(0, i, b), y[:, b, 2:T],
                                                   ALU.mult, ALU.add).then_inc(conv_done, 1)
                    if b % 2 == 1:
                        dve.wait_ge(gelu_done, 2 * i + b // 2 + 1)
                        dve.wait_ge(conv_done, 4 * i + b + 5)
                        nc.vector.tensor_tensor(h[:, bass.ds(2 * i + b // 2, 1), :], y[:, b - 1, :], y[:, b, :],
                                                ALU.mult).then_inc(h_done, 1)


def stage_mlstm(g, units, coming):
    nc = g.nc
    units.begin()
    H, VD, W = ML_HEADS, 2 * P, 2 * P
    scale = P ** -0.5
    with ExitStack() as ctx:
        sem, sb = g.stage(ctx, "mlstm")
        norm = Norm(g, ctx, g.cols("mix_norm1", KT))
        gate_done, gate_abs, gate_exp, neg_m_ready, em_ready, G_ready, G_turned, Gc_ready = (
            sem(n) for n in ("gate_done", "gate_abs", "gate_exp", "neg_m_ready", "em_ready", "G_ready", "G_turned", "Gc_ready"))
        proj_done, now_done, conv_done, qk_ready, og_ready, v_ready, rows_ready = (
            sem(n) for n in ("proj_done", "now_done", "conv_done", "qk_ready", "og_ready", "v_ready", "rows_ready"))
        scores_done, weights_done, p_ready, sums_done, den_abs, h_ready = (
            sem(n) for n in ("scores_done", "weights_done", "p_ready", "sums_done", "den_abs", "h_ready"))
        squared, mean_done, std_ready, mixed, step = (sem(n) for n in ("head_squared", "mean_done", "head_std", "mixed", "step"))
        tmp = [sb(f"tmp{j}", [H, T]) for j in range(5)]
        ig, G, top = sb("ig", [H, T]), sb("G", [H, T]), sb("top", [H, T])
        em = sb("em", [H, T])
        rows = sb("rows", [H, 2, T])
        Gc = sb("Gc", [P, TT, H])
        y = sb("y", [P, 2, T])
        qk = sb("qk", [P, 2, T])
        og, h = sb("og", [P, 2, T]), sb("h", [P, 2, T])
        v = sb("v", [P, TT, VD])
        wts = sb("wts", [P, 2, T])
        probs_T = sb("probs_T", [P, TT, T])
        den = sb("den", [P, T])
        sq = sb("sq", [P, 2, T])
        block = ctx.enter_context(nc.Block())

        @block.sync
        def _(sp):
            with sp.Fori(1, units.n) as i:
                for s in range(3):
                    sp.wait_ge(proj_done, 6 * i - 6 + 2 * s + 2)
                    units.load(sp, i, s)
            sp.wait_ge(proj_done, 6 * units.n)
            first_loads(sp, coming)

        @block.tensor
        def _(pe):
            pe.sem_inc(h_ready, 1)
            pe.sem_inc(std_ready, 1)
            pe.sem_inc(p_ready, 1)
            norm.tensor(pe)
            norm.wait(pe)
            for j in range(2):
                for k in range(KT):
                    c = k * 2 * H + j * H
                    mm = nc.tensor.matmul(g.bank[6 - j][0:H, :], g.cols("w_gates", KT * 2 * H)[:, c:c + H], g.xn[:, k, :],
                                          start=(k == 0), stop=(k == KT - 1))
                mm.then_inc(gate_done, 1)
            pe.wait_ge(G_ready, 1)
            for t in range(TT):
                mm = nc.tensor.transpose(g.bank[4][:, t * H:(t + 1) * H], G[:, t * P:(t + 1) * P], g.ident[0:H, 0:H])
            mm.then_inc(G_turned, 1)
            pe.wait_ge(Gc_ready, 1)
            with pe.Fori(0, units.n) as i:
                pe.wait_ge(h_ready, 2 * i + 1)
                for j in range(2):
                    if j == 0:
                        units.wait(pe, i, 0)
                    for k in range(KT):
                        mm = nc.tensor.matmul(g.bank[j][:, :], units.tile(0, k, j, W), g.xn[:, k, :],
                                              start=(k == 0), stop=(k == KT - 1))
                    mm.then_inc(proj_done, 1)
                units.wait(pe, i, 1)
                pe.wait_ge(std_ready, i + 1)
                for t in range(TT):
                    for k in range(KT):
                        mm = nc.tensor.matmul(g.bank[2 + t // 2][:, t % 2 * VD:(t % 2 + 1) * VD], g.xn[:, k, t * P:(t + 1) * P],
                                              units.rows(1, k, W, 0, VD), start=(k == 0), stop=(k == KT - 1))
                    if t % 2 == 1:
                        mm.then_inc(proj_done, 1)
                units.wait(pe, i, 2)
                pe.wait_ge(p_ready, 4 * i + 1)
                for j in range(2):
                    for k in range(KT):
                        mm = nc.tensor.matmul(g.bank[4 + j][:, :], units.tile(2, k, j, W), g.xn[:, k, :],
                                              start=(k == 0), stop=(k == KT - 1))
                    mm.then_inc(proj_done, 1)
                pe.wait_ge(qk_ready, 2 * i + 2)
                pe.wait_ge(rows_ready, 2 * i + 2)
                for kb in range(TT):
                    A, B = (g.bank[6], g.bank[7]) if kb % 2 == 0 else (g.bank[4], g.bank[5])
                    n = T - kb * P
                    if kb == 1:
                        pe.wait_ge(og_ready, 2 * i + 2)
                    if kb >= 2:
                        pe.wait_ge(p_ready, 4 * i + kb)
                    nc.tensor.matmul(A[:, 0:n], qk[:, 1, kb * P:(kb + 1) * P], qk[:, 0, kb * P:T], start=True, stop=True)
                    nc.tensor.matmul(B[:, 0:n], g.ones[0:H, :], rows[:, 0, kb * P:T], start=True, stop=False)
                    nc.tensor.matmul(B[:, 0:P], g.ident[:, :], g.causal_T[:, :], start=False, stop=True)\
                      .then_inc(scores_done, 1)
                pe.wait_ge(v_ready, 2 * i + 2)
                nc.tensor.matmul(g.bank[3][:, :], g.ones[0:H, :], rows[:, 1, :], start=True, stop=True)
                for kb in range(TT):
                    pe.wait_ge(p_ready, 4 * i + kb + 2)
                    for j in range(3):
                        left = v[:, kb, j * P:(j + 1) * P] if j < 2 else g.ones[:, :]
                        mm = nc.tensor.matmul(g.bank[j][:, kb * P:T], left, probs_T[:, kb, kb * P:T], start=(kb == 0),
                                              stop=(kb == TT - 1), skip_group_check=True)
                mm.then_inc(sums_done, 1)
                for j in range(2):
                    pe.wait_ge(squared, 2 * i + j + 1)
                    mm = nc.tensor.matmul(g.bank[3][:, :], g.mean_256[:, :], sq[:, j, :], start=(j == 0), stop=(j == 1))
                mm.then_inc(mean_done, 1)

        @block.scalar
        def _(act):
            act.sem_inc(mixed, 1)
            norm.scalar(act)
            act.wait_ge(gate_abs, 1)
            nc.scalar.activation(tmp[1][:, :], tmp[1][:, :], ACT.Exp, scale=-1.0).then_inc(gate_exp, 1)
            act.wait_ge(neg_m_ready, 1)
            nc.scalar.activation(em[:, :], tmp[0][:, :], ACT.Exp).then_inc(em_ready, 1)
            with act.Fori(0, units.n) as i:
                for j in range(2):
                    act.wait_ge(proj_done, 6 * i + j + 1)
                    nc.scalar.activation(y[:, j, :], g.bank[j][:, :], ACT.Copy,
                                         scale=g.col_at("conv_qk", i + 3 * 2 * H + j * H)).then_inc(now_done, 1)
                for j in range(2):
                    act.wait_ge(conv_done, 2 * i + j + 1)
                    nc.scalar.activation(qk[:, j, :], y[:, j, :], ACT.Silu).then_inc(qk_ready, 1)
                act.wait_ge(mixed, 2 * i + 1)
                for j in range(2):
                    act.wait_ge(proj_done, 6 * i + 5 + j)
                    nc.scalar.activation(og[:, j, :], g.bank[4 + j][:, :], ACT.Sigmoid).then_inc(og_ready, 1)
                for kb in range(TT):
                    act.wait_ge(scores_done, 4 * i + kb + 1)
                    if kb >= 2:
                        act.wait_ge(p_ready, 4 * i + kb)
                    nc.scalar.activation(wts[:, kb % 2, 0:T - kb * P], (g.bank[7] if kb % 2 == 0 else g.bank[5])[:, 0:T - kb * P],
                                         ACT.Exp, bias=Gc[:, kb, bass.ds(i, 1)]).then_inc(weights_done, 1)
                act.wait_ge(sums_done, i + 1)
                nc.scalar.activation(den[:, :], g.bank[2][:, :], ACT.Abs).then_inc(den_abs, 1)
                for j in range(2):
                    act.wait_ge(h_ready, 2 * i + j + 2)
                    nc.scalar.activation(sq[:, j, :], h[:, j, :], ACT.Square).then_inc(squared, 1)
                act.wait_ge(mean_done, i + 1)
                nc.scalar.activation(g.std[:, :], g.bank[3][:, :], ACT.Sqrt, bias=g.eps[:, 0:1]).then_inc(std_ready, 1)

        @block.vector
        def _(dve):
            norm.vector(dve)
            z, e = tmp[0], tmp[1]
            own = Own(dve, step)
            dve.wait_ge(gate_done, 2)
            own.did(nc.vector.tensor_scalar(ig[:, :], g.bank[6][0:H, :], g.col("mlstm_b_i", rows=H), None, ALU.add))
            own.did(nc.vector.tensor_scalar(z[:, :], g.bank[5][0:H, :], g.col("mlstm_b_f", rows=H), None, ALU.add))
            own.wait()
            nc.vector.scalar_tensor_tensor(e[:, :], z[:, :], -1.0, z[:, :], ALU.mult, ALU.max).then_inc(gate_abs, 1)
            own.did(nc.vector.tensor_scalar(z[:, :], z[:, :], 0.0, None, ALU.min))
            dve.wait_ge(gate_exp, 1)
            log1p_half(dve, own, nc, e[:, :], tmp[2][:, :], tmp[3][:, :], tmp[4][:, :])
            own.did(nc.vector.scalar_tensor_tensor(z[:, :], tmp[4][:, :], -2.0, z[:, :], ALU.mult, ALU.add))
            own.did(nc.vector.memset(e[:, :], 1.0))
            own.wait()
            F = tmp[2]
            own.did(nc.vector.tensor_tensor_scan(F[:, :], e[:, :], z[:, :], 0.0, ALU.mult, ALU.add))
            own.wait()
            nc.vector.tensor_tensor(G[:, :], ig[:, :], F[:, :], ALU.subtract).then_inc(G_ready, 1)
            dve.wait_ge(G_ready, 1)
            own.did(nc.vector.tensor_tensor_scan(top[:, :], G[:, :], G[:, :], 0.0, ALU.max, ALU.max))
            own.wait()
            nc.vector.scalar_tensor_tensor(z[:, :], top[:, :], -1.0, F[:, :], ALU.mult, ALU.subtract).then_inc(neg_m_ready, 1)
            own.did(nc.vector.tensor_scalar(top[:, :], top[:, :], -1.0, None, ALU.mult))
            dve.wait_ge(G_turned, 1)
            nc.vector.tensor_copy(Gc[:, :, :], g.bank[4][:, 0:TT * H].rearrange("p (a b) -> p a b", b=H)).then_inc(Gc_ready, 1)
            dve.wait_ge(em_ready, 1)
            own.wait()
            opening = own.n
            per = 2 * 2 + 2 + 1 + 2
            with dve.Fori(0, units.n) as i:
                own = Own(dve, step, i, per)
                own.base = own.base + opening
                for j, row in enumerate((top, em)):
                    nc.vector.tensor_scalar(rows[:, j, :], row[:, :], g.ident[0:H, bass.ds(i, 1)], None,
                                            ALU.mult).then_inc(rows_ready, 1)
                for j in range(2):
                    dve.wait_ge(now_done, 2 * i + j + 1)
                    for back in (1, 2, 3):
                        tap = nc.vector.scalar_tensor_tensor(y[:, j, back:T], g.bank[j][:, 0:T - back],
                                                             g.col_at("conv_qk", i + (3 - back) * 2 * H + j * H), y[:, j, back:T],
                                                             ALU.mult, ALU.add)
                        if back < 3:
                            own.did(tap)
                            own.wait()
                        else:
                            tap.then_inc(conv_done, 1)
                for j in range(2):
                    dve.wait_ge(proj_done, 6 * i + 3 + j)
                    nc.vector.tensor_copy(v[:, 2 * j:2 * j + 2, :], g.bank[2 + j][:, :].rearrange("p (a b) -> p a b", b=VD))\
                      .then_inc(v_ready, 1)
                for kb in range(TT):
                    dve.wait_ge(weights_done, 4 * i + kb + 1)
                    n = T - kb * P
                    nc.vector.scalar_tensor_tensor(probs_T[:, kb, kb * P:T], (g.bank[6] if kb % 2 == 0 else g.bank[4])[:, 0:n],
                                                   scale, wts[:, kb % 2, 0:n], ALU.mult, ALU.mult).then_inc(p_ready, 1)
                dve.wait_ge(den_abs, i + 1)
                own.did(nc.vector.tensor_tensor(den[:, :], den[:, :], g.bank[3][:, :], ALU.max))
                own.wait()
                own.did(nc.vector.reciprocal(den[:, :], den[:, :]))
                own.wait()
                for j in range(2):
                    nc.vector.tensor_tensor(h[:, j, :], g.bank[j][:, :], den[:, :], ALU.mult).then_inc(h_ready, 1)
                dve.wait_ge(std_ready, i + 2)
                own.did(nc.vector.reciprocal(g.rstd[:, :], g.std[:, :]))
                own.wait()
                for j in range(2):
                    own.did(nc.vector.scalar_tensor_tensor(h[:, j, :], h[:, j, :], g.col_at("head_norm", 2 * i + j), g.rstd[:, :],
                                                           ALU.mult, ALU.mult))
                    own.wait()
                    nc.vector.tensor_tensor(g.mix[:, bass.ds(2 * i + j, 1), :], h[:, j, :], og[:, j, :], ALU.mult)\
                      .then_inc(mixed, 1)


def stage_norm(g, gain, coming, shift=None, out=None):
    nc = g.nc
    with ExitStack() as ctx:
        norm = Norm(g, ctx, gain, shift, out)
        block = ctx.enter_context(nc.Block())

        @block.sync
        def _(sp):
            first_loads(sp, coming)

        @block.tensor
        def _(pe):
            norm.tensor(pe)

        @block.scalar
        def _(act):
            norm.scalar(act)

        @block.vector
        def _(dve):
            norm.vector(dve)


class Modulation:
    PARTS, PLACES = 8, 4

    def __init__(self, g, ctx):
        sem, sb = g.stage(ctx, "modulation")
        self.g, self.ap = g, g.A["modulation"]
        self.W = self.ap.shape[3]
        self.units = self.ap.rearrange("k q p n -> (k q) p n")
        self.steps = self.PARTS * KT // self.PLACES - 1
        self.silu_ready, self.zeroed, self.used, self.summed, self.step = (
            sem(n) for n in ("silu_ready", "zeroed", "weighed", "summed", "modulation_step"))
        self.ready = [sem(f"rows_ready{s}") for s in range(self.PLACES)]
        pairs = lambda t: [t[:, 2 * s:2 * s + 2, :].rearrange("p a n -> p (a n)") for s in range(KT // 2)]
        more = sb("sums", [P, KT, T])
        self.rows, self.sums = pairs(g.mix), pairs(g.xn) + pairs(more)
        self.c = sb("c", [P, KT])

    def load(self, act, n):
        for b in range(self.PLACES):
            if not isinstance(n, int) or n > 0:
                act.wait_ge(self.used, n + b - self.PLACES + 1)
            act.dma_start(self.rows[b], self.units[bass.ds(n + b, 1)].rearrange("a p n -> (a p) n")).then_inc(self.ready[b], 16)

    def scalar(self, act):
        self.load(act, 0)
        self.g.nc.scalar.activation(self.c[:, :], self.g.cols("c", KT), ACT.Silu).then_inc(self.silu_ready, 1)

    def vector(self, dve):
        n, places = self.PARTS, self.PLACES
        for q in range(n):
            self.g.nc.vector.memset(self.sums[q], 0.0).then_inc(self.zeroed, 1)
        dve.wait_ge(self.zeroed, n)
        dve.wait_ge(self.silu_ready, 1)
        with dve.Fori(0, KT) as k:
            for q in range(n):
                dve.wait_ge(self.ready[q % places], 16 * (n // places) * k + 16 * (q // places) + 16)
                if q > 0:
                    dve.wait_ge(self.used, n * k + q)
                self.g.nc.vector.scalar_tensor_tensor(self.sums[q], self.rows[q % places], self.c[:, bass.ds(k, 1)], self.sums[q],
                                                      ALU.mult, ALU.add).then_inc(self.used, 1)

    def end(self, dve):
        g, own = self.g, Own(dve, self.step)
        dve.wait_ge(self.summed, 1)
        own.did(g.nc.vector.tensor_tensor(g.mod[:, :], g.bank[7][:, 0:64], g.cols("b_ada", 64), ALU.add))
        own.wait()
        for j, (name, scale) in enumerate((("g_mix", 8), ("g_ffn", 32), ("g_final", 56))):
            own.did(g.nc.vector.scalar_tensor_tensor(g.gains[:, j, :], g.mod[:, scale:scale + KT], 1.0, g.cols(name, KT),
                                                     ALU.add, ALU.mult))

    def tensor(self, pe):
        pe.wait_ge(self.used, self.PARTS * KT)
        for j in range(64):
            q, c = divmod(j * P, self.W)
            mm = self.g.nc.tensor.matmul(self.g.bank[7][:, j:j + 1], self.sums[q][:, c:c + P], self.g.ones[:, 0:1], start=True, stop=True)
        mm.then_inc(self.summed, 1)


class Recurrent:

    def __init__(self, nc, ctx):
        sb = lambda name, shape: ctx.enter_context(nc.sbuf_tensor(f"rec_{name}", shape, F32))
        self.rkv = sb("rkv", [P, 3 * AT, T])
        self.r, self.k, self.v = (self.rkv[:, j * AT:(j + 1) * AT, :] for j in range(3))
        self.xc = sb("xc", [P, AT, T])
        self.gelu_gate = sb("gelu_gate", [P, AT, T])
        self.ell = sb("ell", [P, AT, T])
        self.a = sb("a", [P, AT, T])
        self.gate = sb("gate", [P, AT, T])
        self.gate_r, self.gate_i = sb("gate_r", [P, AT, T]), sb("gate_i", [P, AT, T])
        self.keep = sb("keep", [P, 3 * AT])


def stage_recurrent_in(g, rec, units, coming):
    nc = g.nc
    units.begin()
    W = 2 * P
    with ExitStack() as ctx:
        sem, sb = g.stage(ctx, "recurrent_in")
        norm = Norm(g, ctx, g.gains[:, 0, :], g.mod[:, 0:KT])
        done, now_done, free, keep_ready, step = (sem(n) for n in ("product_done", "now_done", "bank_free", "keep_ready", "step"))
        block = ctx.enter_context(nc.Block())

        @block.sync
        def _(sp):
            with sp.Fori(1, units.n) as i:
                for s in range(2):
                    sp.wait_ge(done, 4 * i - 4 + 2 * s + 2)
                    units.load(sp, i, s)
            sp.wait_ge(done, 4 * units.n)
            first_loads(sp, coming)

        @block.tensor
        def _(pe):
            norm.tensor(pe)
            norm.wait(pe)
            with pe.Fori(0, units.n) as i:
                for b in range(4):
                    if b % 2 == 0:
                        units.wait(pe, i, b // 2)
                    pe.wait_ge(free, 4 * i + b + 1)
                    for k in range(KT):
                        mm = nc.tensor.matmul(g.bank[b][:, :], units.tile(b // 2, k, b % 2, W), g.xn[:, k, :],
                                              start=(k == 0), stop=(k == KT - 1))
                    mm.then_inc(done, 1)

        @block.scalar
        def _(act):
            norm.scalar(act)
            act.wait_ge(keep_ready, 1)
            with act.Fori(0, 3) as i:
                for b in range(4):
                    act.wait_ge(done, 4 * i + b + 1)
                    nc.scalar.activation(rec.rkv[:, bass.ds(4 * i + b, 1), :], g.bank[b][:, :], ACT.Copy,
                                         scale=rec.keep[:, bass.ds(4 * i + b, 1)]).then_inc(now_done, 1)
            for b in range(4):
                act.wait_ge(done, 12 + b + 1)
                nc.scalar.activation(rec.xc[:, b, :], g.bank[b][:, :], ACT.Identity, scale=g.col("conv_w", 3 * AT + b),
                                     bias=g.col("conv_b", b)).then_inc(now_done, 1)
            for b in range(4):
                act.wait_ge(done, 16 + b + 1)
                nc.scalar.activation(rec.gelu_gate[:, b, :], g.bank[b][:, :], ACT.Gelu_apprx_tanh)

        @block.vector
        def _(dve):
            nc.vector.tensor_scalar(rec.keep[:, :], g.cols("mu_rkv", 3 * AT), -1.0, 1.0, ALU.mult, ALU.add).then_inc(keep_ready, 1)
            norm.vector(dve)
            dve.sem_inc(free, 4)
            with dve.Fori(0, 3) as i:
                for b in range(4):
                    dve.wait_ge(now_done, 4 * i + b + 1)
                    here = rec.rkv[:, bass.ds(4 * i + b, 1), 1:T]
                    nc.vector.scalar_tensor_tensor(here, g.bank[b][:, 0:T - 1], g.col_at("mu_rkv", 4 * i + b), here,
                                                   ALU.mult, ALU.add).then_inc(free, 1)
            own = Own(dve, step)
            for b in range(4):
                dve.wait_ge(now_done, 12 + b + 1)
                for back in (1, 2, 3):
                    here = rec.xc[:, b, back:T]
                    tap = nc.vector.scalar_tensor_tensor(here, g.bank[b][:, 0:T - back], g.col("conv_w", (3 - back) * AT + b), here,
                                                         ALU.mult, ALU.add)
                    if back < 3:
                        own.did(tap)
                        own.wait()
                    else:
                        tap.then_inc(free, 1)


def stage_low_rank(g, rec, units, coming):
    nc = g.nc
    units.begin()
    W = 2 * P
    RANK = (HALF, HALF, P)
    START = (0, HALF, P)
    with ExitStack() as ctx:
        sem, sb = g.stage(ctx, "low_rank")
        shifted, mixed, used, low_done, low_ready, up_done, up_read = (
            sem(n) for n in ("shifted", "mixed", "used", "low_done", "low_ready", "up_done", "up_read"))
        dx = g.mix
        mixes = sb("mixes", [P, 4, T])
        low = [sb(f"low{j}", [RANK[j], T]) for j in range(3)]
        block = ctx.enter_context(nc.Block())
        small = g.ring.slots[1]
        ups = [(rec.ell, m, small[0:HALF, m * P:(m + 1) * P], low[0][:, :], ACT.Sigmoid, "w0") for m in range(AT)]
        ups += [(rec.a, m, small[0:HALF, AW + m * P:AW + (m + 1) * P], low[1][:, :], ACT.Sigmoid, "a0") for m in range(AT)]
        ups += [(rec.gate, m, small[:, 2 * AW + m * P:2 * AW + (m + 1) * P], low[2][:, :], ACT.Copy, None) for m in range(AT)]
        ups += [(rec.gate_r, m, small[:, 3 * AW + m * P:3 * AW + (m + 1) * P], rec.xc[:, m, :], ACT.Sigmoid, "b_rgate") for m in range(AT)]
        ups += [(rec.gate_i, m, small[:, 4 * AW + m * P:4 * AW + (m + 1) * P], rec.xc[:, m, :], ACT.Sigmoid, "b_igate") for m in range(AT)]

        @block.sync
        def _(sp):
            sp.wait_ge(up_done, len(ups))
            first_loads(sp, coming)

        @block.vector
        def _(dve):
            nc.vector.tensor_scalar(dx[:, :, 0:1], g.xn[:, :, 0:1], -1.0, None, ALU.mult).then_inc(shifted, 1)
            for k in range(KT):
                nc.vector.tensor_tensor(dx[:, k, 1:T], g.xn[:, k, 0:T - 1], g.xn[:, k, 1:T], ALU.subtract).then_inc(shifted, 1)
            for j in range(3):
                for k in range(KT):
                    n = j * KT + k
                    if j == 0:
                        dve.wait_ge(shifted, k + 2)
                    if n >= 4:
                        dve.wait_ge(used, n - 3)
                    nc.vector.scalar_tensor_tensor(mixes[:, n % 4, :], dx[:, k, :], g.col("mu_wag", n), g.xn[:, k, :],
                                                   ALU.mult, ALU.add).then_inc(mixed, 1)

        @block.tensor
        def _(pe):
            units.wait(pe, 0, 0)
            units.wait(pe, 0, 1)
            for j in range(3):
                for k in range(KT):
                    pe.wait_ge(mixed, j * KT + k + 1)
                    mm = nc.tensor.matmul(g.bank[j][0:RANK[j], :], g.ring.slots[0][:, k * W + START[j]:k * W + START[j] + RANK[j]],
                                          mixes[:, (j * KT + k) % 4, :], start=(k == 0), stop=(k == KT - 1))
                    mm.then_inc(used, 1)
            for n, (_, _, weights, source, _, _) in enumerate(ups):
                if n % AT == 0 and n < 3 * AT:
                    pe.wait_ge(low_ready, n // AT + 1)
                if n >= 4:
                    pe.wait_ge(up_read, n - 3)
                nc.tensor.matmul(g.bank[3 + n % 4][:, :], weights, source, start=True, stop=True).then_inc(up_done, 1)

        @block.scalar
        def _(act):
            for j, f in enumerate((ACT.Tanh, ACT.Copy, ACT.Sigmoid)):
                act.wait_ge(used, (j + 1) * KT)
                nc.scalar.activation(low[j][:, :], g.bank[j][0:RANK[j], :], f).then_inc(low_ready, 1)
            for n, (out, m, _, _, f, bias) in enumerate(ups):
                act.wait_ge(up_done, n + 1)
                more = {} if bias is None else {"bias": g.col(bias, m)}
                nc.scalar.activation(out[:, m, :], g.bank[3 + n % 4][:, :], f, **more).then_inc(up_read, 1)


def stage_rg_lru(g, rec):
    nc = g.nc
    with ExitStack() as ctx:
        sem, sb = g.stage(ctx, "rg_lru")
        lam_abs, lam_exp, rate_ready, tanh_done, root_in, root_done, input_ready, h_ready, step = (
            sem(n) for n in ("lam_abs", "lam_exp", "rate_ready", "tanh_done", "root_in", "root_done", "input_ready", "h_ready", "step"))
        small = [sb(f"small{j}", [P, AT]) for j in range(5)]
        t = rec.gate_r
        u = g.mix[:, 0:AT, :]
        d = sb("d", [P, AT, T])
        block = ctx.enter_context(nc.Block())
        lam = g.cols("lam", AT)
        all_of = lambda b: b[:, :, :].rearrange("p a b -> p (a b)")

        @block.scalar
        def _(act):
            act.wait_ge(lam_abs, 1)
            nc.scalar.activation(small[0][:, :], small[0][:, :], ACT.Exp, scale=-1.0).then_inc(lam_exp, 1)
            act.wait_ge(rate_ready, 1)
            for m in range(AT):
                nc.scalar.activation(t[:, m, :], rec.gate_r[:, m, :], ACT.Tanh, scale=small[4][:, m:m + 1]).then_inc(tanh_done, 1)
            act.wait_ge(root_in, 1)
            nc.scalar.activation(all_of(d), all_of(d), ACT.Sqrt).then_inc(root_done, 1)

        @block.gpsimd
        def _(pool):
            nc.gpsimd.tensor_tensor(all_of(u), all_of(rec.gate_i), all_of(rec.xc), ALU.mult).then_inc(input_ready, 1)

        @block.vector
        def _(dve):
            own = Own(dve, step)
            nc.vector.scalar_tensor_tensor(small[0][:, :], lam, -1.0, lam, ALU.mult, ALU.max).then_inc(lam_abs, 1)
            dve.wait_ge(lam_exp, 1)
            log1p_half(dve, own, nc, *(s[:, :] for s in small[0:4]))
            own.did(nc.vector.tensor_scalar(small[1][:, :], lam, 0.0, -4.0, ALU.min, ALU.mult))
            own.wait()
            nc.vector.scalar_tensor_tensor(small[4][:, :], small[3][:, :], 8.0, small[1][:, :], ALU.mult, ALU.add).then_inc(rate_ready, 1)
            dve.wait_ge(tanh_done, AT)
            own.did(nc.vector.tensor_scalar(all_of(d), all_of(t), 1.0, None, ALU.add))
            own.wait()
            own.did(nc.vector.reciprocal(all_of(d), all_of(d)))
            own.wait()
            own.did(nc.vector.scalar_tensor_tensor(all_of(d), all_of(t), 2.0, all_of(d), ALU.mult, ALU.mult))
            own.wait()
            own.did(nc.vector.tensor_scalar(all_of(t), all_of(d), -1.0, 1.0, ALU.mult, ALU.add))
            own.wait()
            nc.vector.scalar_tensor_tensor(all_of(d), all_of(t), 1.0, all_of(d), ALU.add, ALU.mult).then_inc(root_in, 1)
            dve.wait_ge(root_done, 1)
            dve.wait_ge(input_ready, 1)
            own.did(nc.vector.tensor_tensor(all_of(u), all_of(u), all_of(d), ALU.mult))
            own.wait()
            for m in range(AT):
                own.did(nc.vector.tensor_tensor_scan(d[:, m, :], t[:, m, :], u[:, m, :], 0.0, ALU.mult, ALU.add))
            own.wait()
            nc.vector.tensor_tensor(g.mix[:, AT:2 * AT, :].rearrange("p a b -> p (a b)"), all_of(d), all_of(rec.gelu_gate),
                                    ALU.mult).then_inc(h_ready, 1)


class Rwkv:

    def __init__(self, rec):
        self.nkk = rec.xc
        self.b = rec.gelu_gate
        self.L = rec.gate_r
        self.y = rec.gate_i


def stage_rwkv_prepare(g, rec, rw):
    nc = g.nc
    with ExitStack() as ctx:
        sem, sb = g.stage(ctx, "prepare")
        kk_ready, squared, summed, norm_ready, step, rates_ready = (
            sem(n) for n in ("kk_ready", "squared", "summed", "norm_ready", "step", "rates_ready"))
        kk = rw.nkk
        sq, one = sb("sq", [P, AT, T]), sb("one", [P, T])
        inv = sq
        block = ctx.enter_context(nc.Block())

        @block.vector
        def _(dve):
            own = Own(dve, step)
            for m in range(AT):
                nc.vector.tensor_scalar(kk[:, m, :], rec.k[:, m, :], g.col("k_k", m), None, ALU.mult).then_inc(kk_ready, 1)
            own.did(nc.vector.memset(one[:, :], 1.0))
            own.wait()
            own.did(nc.vector.memset(one[:, 0:T:CHUNK], 0.0))
            own.wait()
            decay = -math.exp(-0.5)
            for m in range(AT):
                own.did(nc.vector.tensor_scalar(rec.ell[:, m, :], rec.ell[:, m, :], decay, None, ALU.mult))
            own.wait()
            for m in range(AT):
                own.did(nc.vector.tensor_tensor_scan(rw.L[:, m, :], one[:, :], rec.ell[:, m, :], 0.0, ALU.mult, ALU.add))
            dve.wait_ge(rates_ready, AT)
            for m in range(AT):
                own.did(nc.vector.scalar_tensor_tensor(rec.k[:, m, :], rw.y[:, m, :], 1.0, rec.k[:, m, :], ALU.add, ALU.mult))
            for m in range(AT):
                dve.wait_ge(norm_ready, m + 1)
                own.did(nc.vector.reciprocal(inv[:, m, :], inv[:, m, :]))
                own.wait()
                own.did(nc.vector.scalar_tensor_tensor(rw.nkk[:, m, :], kk[:, m, :], -1.0, inv[:, m, :], ALU.mult, ALU.mult))
                own.wait()
                own.did(nc.vector.scalar_tensor_tensor(rw.b[:, m, :], rw.nkk[:, m, :], -1.0, rec.a[:, m, :], ALU.mult, ALU.mult))

        @block.gpsimd
        def _(pool):
            pool.wait_ge(kk_ready, AT)
            for m in range(AT):
                nc.gpsimd.tensor_scalar(rw.y[:, m, :], rec.a[:, m, :], -1.0, g.col("k_a", m), ALU.add, ALU.mult).then_inc(rates_ready, 1)

        @block.scalar
        def _(act):
            for m in range(AT):
                act.wait_ge(kk_ready, m + 1)
                nc.scalar.activation(sq[:, m, :], kk[:, m, :], ACT.Square).then_inc(squared, 1)
            for m in range(AT):
                act.wait_ge(summed, m + 1)
                nc.scalar.activation(inv[:, m, :], g.bank[m][:, :], ACT.Sqrt, bias=g.eps[:, 1:2]).then_inc(norm_ready, 1)

        @block.tensor
        def _(pe):
            for m in range(AT):
                pe.wait_ge(squared, m + 1)
                nc.tensor.matmul(g.bank[m][:, :], g.head_sum[:, :], sq[:, m, :], start=True, stop=True).then_inc(summed, 1)


def stage_rwkv_chunks(g, rec, rw):
    nc = g.nc
    C, PAIRS = CHUNK, AT
    LEVELS = int(math.log2(C))
    UNIT = PAIRS * C
    TWO = range(2)
    ROUNDS = NCHUNK // 2
    both = [slice(h * HALF, (h + 1) * HALF) for h in range(2)]
    with ExitStack() as ctx:
        sem, sb = g.stage(ctx, "chunks")
        S = [sb(f"S{p}", [P, PAIRS, C]) for p in TWO]
        flat = lambda t: t[:, :, :].rearrange("p a n -> p (a n)")
        places = [slot[:, :] for slot in g.ring.slots] + [flat(g.memn), flat(g.square), g.std[:, :], g.rstd[:, :],
                                                          sb("own", [P, 6 * UNIT])[:, :]]

        class Chunk:
            pass

        def carve(*shape):
            n = int(np.prod(shape))
            i = next(i for i, place in enumerate(places) if place.shape[1] >= n)
            here, places[i] = places[i][:, 0:n], places[i][:, n:]
            if len(shape) == 2:
                return here.rearrange("p (a n) -> p a n", n=C)
            return here.rearrange("p (a b n) -> p a b n", b=shape[1], n=C)

        chunks = []
        for p in TWO:
            w = Chunk()
            w.al = carve(LEVELS, PAIRS, C)
            w.ar = carve(PAIRS, 2, C)
            w.Mb, w.Mk = carve(PAIRS, 2, C), carve(PAIRS, 2, C)
            w.bk = carve(2, PAIRS, C)
            w.dl, w.en, w.ep, w.epv = (carve(PAIRS, C) for _ in range(4))
            w.bt, w.kt, w.vt = (carve(PAIRS, C) for _ in range(3))
            w.vs = carve(PAIRS, C)
            w.M, w.MT, w.Wt = (carve(PAIRS, C) for _ in range(3))
            w.rhs, w.U = (carve(PAIRS, C) for _ in range(2))
            w.w_bank, w.z_bank, w.zt_bank = ((4, 5, 6), (0, 1, 2))[p]
            w.diff_ready, w.exps_ready, w.scaled, w.v_copied, w.pairs_done, w.pairs_read, w.tokens_read = (
                sem(f"{n}{p}") for n in ("diff_ready", "exps_ready", "scaled", "v_copied", "pairs_done", "pairs_read", "tokens_read"))
            w.level_ready, w.w_done, w.w_ready, w.z_done, w.zt_done, w.inverse_step = (
                sem(f"{n}{p}") for n in ("level_ready", "w_done", "w_ready", "z_done", "zt_done", "inverse_step"))
            w.rhs_done, w.rhs_ready, w.u_done, w.u_ready, w.y_done, w.y_ready, w.s_done = (
                sem(f"{n}{p}") for n in ("rhs_done", "rhs_ready", "u_done", "u_ready", "y_done", "y_ready", "s_done"))
            chunks.append(w)
        s_added, s_ready, passed = sem("s_added"), sem("s_ready"), sem("passed")
        block = ctx.enter_context(nc.Block())
        eye = g.cols("eye", C)
        tri = g.cols("tri", 2 * C).rearrange("p (a b) -> p a b", b=C)
        level = lambda l: g.cols("levels", LEVELS * C)[:, l * C:(l + 1) * C]
        spread = lambda m: m.unsqueeze(1).broadcast_to([P, PAIRS, *m.shape[1:]])
        wide = lambda b: g.bank[b][:, 0:UNIT].rearrange("p (a b) -> p a b", b=C)
        now = lambda a, i, p: a[:, :, bass.ds(i * 2 * C + p * C, C)]
        steps = 2 * LEVELS - 1

        @block.scalar
        def _(act):
            with act.Fori(0, ROUNDS) as i:
                for p, w in enumerate(chunks):
                    act.wait_ge(s_ready, 2 * i + p)
                    nc.scalar.activation(w.en, now(rw.L, i, p), ACT.Exp, scale=-1.0).then_inc(w.exps_ready, 1)
                    nc.scalar.activation(w.ep, now(rw.L, i, p), ACT.Exp).then_inc(w.exps_ready, 1)
                    act.wait_ge(w.diff_ready, i + 1)
                    nc.scalar.activation(w.epv, w.dl, ACT.Exp).then_inc(w.exps_ready, 1)
                for p, w in enumerate(chunks):
                    act.wait_ge(w.pairs_done, 4 * i + 3)
                    nc.scalar.activation(w.bk.rearrange("p a b n -> p (a b n)"), g.bank[(2, 7)[p]][:, :], ACT.Copy).then_inc(w.tokens_read, 1)
                    act.wait_ge(w.pairs_done, 4 * i + 4)
                    nc.scalar.activation(w.vs, wide(3), ACT.Copy).then_inc(w.tokens_read, 1)
                for l in range(1, LEVELS):
                    for w in chunks:
                        act.wait_ge(w.w_done, LEVELS * i + l + 1)
                        nc.scalar.activation(w.Wt, wide(w.w_bank), ACT.Copy).then_inc(w.w_ready, 1)
                for p, w in enumerate(chunks):
                    act.wait_ge(w.rhs_done, i + 1)
                    nc.scalar.activation(w.rhs, wide(7), ACT.Copy).then_inc(w.rhs_ready, 1)
                    act.wait_ge(w.u_done, i + 1)
                    nc.scalar.activation(w.U, wide(4), ACT.Copy).then_inc(w.u_ready, 1)
                    act.wait_ge(w.y_done, i + 2)
                    nc.scalar.activation(now(rw.y, i, p), wide((5, 3)[p]), ACT.Copy).then_inc(w.y_ready, 1)

        @block.gpsimd
        def _(pool):
            with pool.Fori(0, ROUNDS) as i:
                for p, w in enumerate(chunks):
                    pool.wait_ge(s_ready, 2 * i + p)
                    nc.gpsimd.tensor_copy(w.vt, now(rec.v, i, p)).then_inc(w.v_copied, 1)
                for w in chunks:
                    pool.wait_ge(w.pairs_read, 2 * i + 1)
                    nc.gpsimd.tensor_tensor(w.al[:, 0, :, :], w.Mb[:, :, 0, :], spread(level(0)), ALU.mult).then_inc(w.level_ready, 1)
                for l in range(1, LEVELS):
                    for w in chunks:
                        nc.gpsimd.tensor_tensor(w.al[:, l, :, :], w.Mb[:, :, 0, :], spread(level(l)), ALU.mult).then_inc(w.level_ready, 1)

        @block.vector
        def _(dve):
            nc.vector.memset(S[0][:, :, :], 0.0).then_inc(s_added, 1)
            dve.sem_inc(s_ready, 1)
            for w in chunks:
                dve.sem_inc(w.y_done, 1)
                dve.sem_inc(w.y_ready, 1)
            with dve.Fori(0, ROUNDS) as i:
                for p, w in enumerate(chunks):
                    dve.wait_ge(s_ready, 2 * i + p)
                    nc.vector.tensor_tensor(w.dl, now(rw.L, i, p), now(rec.ell, i, p), ALU.subtract).then_inc(w.diff_ready, 1)
                for p, w in enumerate(chunks):
                    dve.wait_ge(w.exps_ready, 3 * i + 2)
                    dve.wait_ge(w.y_done, i + 1)
                    nc.vector.tensor_tensor(w.bt, now(rw.b, i, p), w.en, ALU.mult).then_inc(w.scaled, 1)
                    nc.vector.tensor_tensor(w.kt, now(rec.k, i, p), w.en, ALU.mult).then_inc(w.scaled, 1)
                    nc.vector.tensor_tensor(w.ar[:, :, 1, :], now(rec.r, i, p), w.ep, ALU.mult).then_inc(w.scaled, 1)
                    dve.wait_ge(w.exps_ready, 3 * i + 3)
                    nc.vector.tensor_tensor(w.ar[:, :, 0, :], now(rw.nkk, i, p), w.epv, ALU.mult).then_inc(w.scaled, 1)
                for w in chunks:
                    for j, m in enumerate((w.Mb, w.Mk)):
                        dve.wait_ge(w.pairs_done, 4 * i + j + 1)
                        nc.vector.tensor_tensor(m, g.bank[j][:, :].rearrange("p (a b n) -> p a b n", b=2, n=C),
                                                spread(tri), ALU.mult).then_inc(w.pairs_read, 1)
                for w in chunks:
                    dve.wait_ge(w.level_ready, LEVELS * i + 1)
                    nc.vector.tensor_tensor(w.MT, w.al[:, 0, :, :], spread(eye), ALU.add).then_inc(w.inverse_step, 1)
                    dve.wait_ge(w.w_done, LEVELS * i + 1)
                    nc.vector.tensor_tensor(w.M, wide(w.w_bank), spread(eye), ALU.add).then_inc(w.inverse_step, 1)
                for l in range(1, LEVELS):
                    for w in chunks:
                        if l < LEVELS - 1:
                            dve.wait_ge(w.z_done, (LEVELS - 2) * i + l)
                            dve.wait_ge(w.inverse_step, steps * i + 2 * l)
                            nc.vector.tensor_tensor(w.M, wide(w.z_bank), w.M, ALU.add).then_inc(w.inverse_step, 1)
                        dve.wait_ge(w.zt_done, (LEVELS - 1) * i + l)
                        nc.vector.tensor_tensor(w.MT, wide(w.zt_bank), w.MT, ALU.add).then_inc(w.inverse_step, 1)
                for p, w in enumerate(chunks):
                    dve.wait_ge(w.s_done, i + 1)
                    dve.wait_ge(s_added, 2 * i + p + 1)
                    after = S[1 - p][:, :, :]
                    nc.vector.tensor_tensor(after, wide(6), S[p][:, :, :], ALU.add).then_inc(s_added, 1)
                    dve.wait_ge(s_added, 2 * i + p + 2)
                    nc.vector.tensor_tensor(after, after, w.ep[:, :, C - 1:C].broadcast_to([P, PAIRS, C]), ALU.mult).then_inc(s_ready, 1)

        @block.tensor
        def _(pe):
            def product(bank, left, right, width=C):
                for n in range(PAIRS):
                    for h in both:
                        mm = nc.tensor.matmul(g.bank[bank][h, n * width:(n + 1) * width], left(h, n), right(h, n), start=True, stop=True)
                return mm

            with pe.Fori(0, ROUNDS) as i:
                for w in chunks:
                    pe.wait_ge(w.y_ready, i + 1)
                for p, w in enumerate(chunks):
                    pe.wait_ge(w.scaled, 4 * i + 4)
                    pe.wait_ge(w.v_copied, i + 1)
                    pe.wait_ge(s_added, 2 * i + 1)
                    pe.sem_inc(passed, 1)
                    for j, left in enumerate((w.bt, w.kt)):
                        if p == 1:
                            pe.wait_ge(chunks[0].pairs_read, 2 * i + j + 1)
                            pe.sem_inc(passed, 1)
                        product(j, lambda h, n: left[h, n, :], lambda h, n: w.ar[h, n, :, :].rearrange("p a b -> p (a b)"), 2 * C)\
                            .then_inc(w.pairs_done, 1)
                    for j, src in enumerate((w.bt, w.kt)):
                        for n in range(PAIRS):
                            for h in both:
                                mm = nc.tensor.matmul(g.bank[(2, 7)[p]][h, (j * PAIRS + n) * C:(j * PAIRS + n + 1) * C], src[h, n, :],
                                                      g.ident[h, h], start=True, stop=True)
                    mm.then_inc(w.pairs_done, 1)
                    if p == 1:
                        pe.wait_ge(chunks[0].tokens_read, 2 * i + 2)
                        pe.sem_inc(passed, 1)
                    product(3, lambda h, n: w.vt[h, n, :], lambda h, n: g.ident[h, h]).then_inc(w.pairs_done, 1)
                for p, w in enumerate(chunks):
                    pe.wait_ge(w.level_ready, LEVELS * i + 1)
                    if p == 1:
                        pe.wait_ge(w.pairs_read, 2 * i + 2)
                        pe.wait_ge(w.tokens_read, 2 * i + 2)
                    pe.sem_inc(passed, 1)
                    product(w.w_bank, lambda h, n: w.al[h, 0, n, :], lambda h, n: eye[h, :]).then_inc(w.w_done, 1)
                for l in range(1, LEVELS):
                    for w in chunks:
                        pe.wait_ge(w.level_ready, LEVELS * i + l + 1)
                        pe.wait_ge(w.inverse_step, steps * i + 2 * l)
                        pe.sem_inc(passed, 1)
                        product(w.w_bank, lambda h, n: w.al[h, l, n, :], lambda h, n: w.M[h, n, :]).then_inc(w.w_done, 1)
                    for w in chunks:
                        pe.wait_ge(w.w_ready, (LEVELS - 1) * i + l)
                        pe.sem_inc(passed, 1)
                        if l < LEVELS - 1:
                            product(w.z_bank, lambda h, n: w.MT[h, n, :], lambda h, n: w.Wt[h, n, :]).then_inc(w.z_done, 1)
                        product(w.zt_bank, lambda h, n: w.Wt[h, n, :], lambda h, n: w.MT[h, n, :]).then_inc(w.zt_done, 1)
                for p, w in enumerate(chunks):
                    pe.wait_ge(w.tokens_read, 2 * i + 2)
                    pe.wait_ge(w.pairs_read, 2 * i + 2)
                    pe.wait_ge(s_ready, 2 * i + p + 1)
                    pe.sem_inc(passed, 1)
                    for n in range(PAIRS):
                        for h in both:
                            out = g.bank[7][h, n * C:(n + 1) * C]
                            nc.tensor.matmul(out, w.Mk[h, n, 0, :], w.vs[h, n, :], start=True, stop=False)
                            mm = nc.tensor.matmul(out, w.ar[h, n, 0, :], S[p][h, n, :], start=False, stop=True)
                    mm.then_inc(w.rhs_done, 1)
                    pe.wait_ge(w.rhs_ready, i + 1)
                    pe.wait_ge(w.inverse_step, steps * (i + 1))
                    pe.sem_inc(passed, 1)
                    product(4, lambda h, n: w.MT[h, n, :], lambda h, n: w.rhs[h, n, :]).then_inc(w.u_done, 1)
                    pe.wait_ge(w.u_ready, i + 1)
                    pe.sem_inc(passed, 1)
                    for n in range(PAIRS):
                        for h in both:
                            out = g.bank[6][h, n * C:(n + 1) * C]
                            nc.tensor.matmul(out, w.bk[h, 0, n, :], w.U[h, n, :], start=True, stop=False)
                            mm = nc.tensor.matmul(out, w.bk[h, 1, n, :], w.vs[h, n, :], start=False, stop=True)
                    mm.then_inc(w.s_done, 1)
                    for n in range(PAIRS):
                        for h in both:
                            out = g.bank[(5, 3)[p]][h, n * C:(n + 1) * C]
                            nc.tensor.matmul(out, S[p][h, n, :], w.ar[h, n, 1, :], start=True, stop=False)
                            nc.tensor.matmul(out, w.U[h, n, :], w.Mb[h, n, 1, :], start=False, stop=False)
                            mm = nc.tensor.matmul(out, w.vs[h, n, :], w.Mk[h, n, 1, :], start=False, stop=True)
                    mm.then_inc(w.y_done, 1)


def stage_rwkv_finish(g, rec, rw, coming):
    nc = g.nc
    with ExitStack() as ctx:
        sem, sb = g.stage(ctx, "finish")
        rk_ready, bonus_done, mean_done, centred, squared, var_done, std_ready, step = (
            sem(n) for n in ("rk_ready", "bonus_done", "mean_done", "centred", "squared", "var_done", "std_ready", "step"))
        rk, sq, std = rw.nkk, rw.b, rw.L
        block = ctx.enter_context(nc.Block())

        @block.sync
        def _(sp):
            first_loads(sp, coming)

        @block.vector
        def _(dve):
            own = Own(dve, step)
            for m in range(AT):
                nc.vector.scalar_tensor_tensor(rk[:, m, :], rec.r[:, m, :], g.col("r_k", m), rec.k[:, m, :],
                                               ALU.mult, ALU.mult).then_inc(rk_ready, 1)
            for m in range(AT):
                dve.wait_ge(mean_done, m + 1)
                nc.vector.scalar_tensor_tensor(rw.y[:, m, :], g.bank[m][:, :], -1.0 / HALF, rw.y[:, m, :], ALU.mult, ALU.add)\
                  .then_inc(centred, 1)
            dve.wait_ge(bonus_done, AT)
            for m in range(AT):
                own.did(nc.vector.tensor_tensor(rk[:, m, :], g.bank[4 + m][:, :], rec.v[:, m, :], ALU.mult))
            for m in range(AT):
                dve.wait_ge(std_ready, m + 1)
                own.did(nc.vector.reciprocal(std[:, m, :], std[:, m, :]))
                own.wait()
                own.did(nc.vector.scalar_tensor_tensor(rw.y[:, m, :], rw.y[:, m, :], g.col("lnx_g", m), std[:, m, :], ALU.mult, ALU.mult))
                own.wait()
                own.did(nc.vector.scalar_tensor_tensor(rw.y[:, m, :], rw.y[:, m, :], g.col("lnx_b", m), rk[:, m, :], ALU.add, ALU.add))
                own.wait()
                own.did(nc.vector.tensor_tensor(g.mix[:, m, :], rw.y[:, m, :], rec.gate[:, m, :], ALU.mult))

        @block.scalar
        def _(act):
            for m in range(AT):
                act.wait_ge(centred, m + 1)
                nc.scalar.activation(sq[:, m, :], rw.y[:, m, :], ACT.Square).then_inc(squared, 1)
            for m in range(AT):
                act.wait_ge(var_done, m + 1)
                nc.scalar.activation(std[:, m, :], g.bank[m][:, :], ACT.Sqrt, scale=1.0 / HALF, bias=g.eps[:, 2:3]).then_inc(std_ready, 1)

        @block.tensor
        def _(pe):
            for m in range(AT):
                nc.tensor.matmul(g.bank[m][:, :], g.head_sum[:, :], rw.y[:, m, :], start=True, stop=True).then_inc(mean_done, 1)
            for m in range(AT):
                pe.wait_ge(rk_ready, m + 1)
                nc.tensor.matmul(g.bank[4 + m][:, :], g.head_sum[:, :], rk[:, m, :], start=True, stop=True).then_inc(bonus_done, 1)
            for m in range(AT):
                pe.wait_ge(squared, m + 1)
                nc.tensor.matmul(g.bank[m][:, :], g.head_sum[:, :], sq[:, m, :], start=True, stop=True).then_inc(var_done, 1)


def stage_merge(g, units, coming, merged):
    nc = g.nc
    units.begin()
    W = 2 * P
    with ExitStack() as ctx:
        sem, sb = g.stage(ctx, "merge")
        done, gated, read, merged_done, step = (sem(n) for n in ("product_done", "gated", "read", "merged_done", "step"))
        sig = sb("sig", [P, 4, T])
        block = ctx.enter_context(nc.Block())

        @block.sync
        def _(sp):
            with sp.Fori(1, units.n) as i:
                for s, last in enumerate((2, 4, 8)):
                    sp.wait_ge(done, 8 * i - 8 + last)
                    units.load(sp, i, s)
            sp.wait_ge(done, 8 * units.n)
            first_loads(sp, coming)

        @block.tensor
        def _(pe):
            pe.sem_inc(gated, 1)
            pe.sem_inc(read, 1)
            with pe.Fori(0, units.n) as i:
                pe.wait_ge(gated, 4 * i + 1)
                for b in range(4):
                    if b % 2 == 0:
                        units.wait(pe, i, b // 2)
                    for k in range(KT):
                        mm = nc.tensor.matmul(g.bank[b][:, :], units.tile(b // 2, k, b % 2, W), g.xn[:, k, :],
                                              start=(k == 0), stop=(k == KT - 1))
                    mm.then_inc(done, 1)
                units.wait(pe, i, 2)
                pe.wait_ge(read, 4 * i + 1)
                for b in range(4):
                    for k in range(AT):
                        mm = nc.tensor.matmul(g.bank[4 + b][:, :], units.tile(2, b // 2 * AT + k, b % 2, W),
                                              g.mix[:, b // 2 * AT + k, :], start=(k == 0), stop=(k == AT - 1))
                    mm.then_inc(done, 1)

        @block.scalar
        def _(act):
            act.sem_inc(merged_done, 1)
            with act.Fori(0, units.n) as i:
                act.wait_ge(merged_done, 2 * i + 1)
                for b in range(4):
                    act.wait_ge(done, 8 * i + b + 1)
                    nc.scalar.activation(sig[:, b, :], g.bank[b][:, :], ACT.Sigmoid).then_inc(gated, 1)

        @block.vector
        def _(dve):
            with dve.Fori(0, units.n) as i:
                for b in range(4):
                    dve.wait_ge(done, 8 * i + 4 + b + 1)
                    dve.wait_ge(gated, 4 * i + b + 2)
                    nc.vector.tensor_tensor(sig[:, b, :], g.bank[4 + b][:, :], sig[:, b, :], ALU.mult).then_inc(read, 1)
                    if b >= 2:
                        dve.wait_ge(read, 4 * i + b + 2)
                        nc.vector.tensor_tensor(merged[:, bass.ds(2 * i + b - 2, 1), :], sig[:, b - 2, :], sig[:, b, :], ALU.add)\
                          .then_inc(merged_done, 1)


class Experts:

    def __init__(self, nc, ctx, ring):
        sb = lambda name, shape, dt=F32: ctx.enter_context(nc.sbuf_tensor(f"moe_{name}", shape, dt))
        dram = lambda name, rows: nc.dram_tensor(name, [rows, D], F32, kind="Internal").ap()
        self.weight = sb("weight", [P, 2, TT])
        self.pair = sb("pair", [P, MOE_TILES], I32)
        self.token = sb("token", [P, MOE_TILES], I32)
        self.more_expert = sb("more_expert", [1, MORE], I32)
        self.more_tiles = sb("more_tiles", [1, 1], I32)
        self.rows = dram("moe_rows", T)
        self.pair_rows = dram("moe_pair_rows", 2 * T)
        extra = 2 * IN_FLIGHT - SLOTS
        self.ring = WeightRing(ring.slots + [sb(f"weights{s}", [P, SLOT]) for s in range(extra)],
                               ring.ready + [ctx.enter_context(nc.semaphore(f"expert_ready{s}")) for s in range(extra)])
        self.ring.loads = ring.loads + [0] * extra


def stage_router(g, moe, units):
    nc = g.nc
    LOGITS = GROUPS + EXPERTS
    with ExitStack() as ctx:
        sem, sb = g.stage(ctx, "router")
        norm = Norm(g, ctx, g.gains[:, 1, :], g.mod[:, 24:24 + KT])
        turned, row_read, stored, logits_done, step, to_exp, exp_done = (
            sem(n) for n in ("turned", "row_read", "stored", "logits_done", "step", "to_exp", "exp_done"))
        chosen, counted, sorted_, placed, table_done = (sem(n) for n in ("chosen", "counted", "sorted", "placed", "table_done"))
        rows = g.mix[:, :, :].rearrange("p (t h) n -> p t (h n)", h=2)
        logits = sb("logits", [P, TT, LOGITS])
        top, first, total = sb("top", [P, TT]), sb("first", [P, TT]), sb("total", [P, TT])
        exps = sb("exps", [P, TT, GROUPS])
        group, group_weight = sb("group", [P, TT, GROUPS]), sb("group_weight", [P, TT])
        parts = sb("parts", [P, TT, GROUPS, PER_GROUP])
        inside = sb("inside", [P, TT, PER_GROUP])
        best = sb("best", [P, 2, TT])
        here = sb("here", [P, 2, TT, PER_GROUP])
        second = sb("second", [P, TT])
        hot = sb("hot", [P, 2, TT, EXPERTS])
        both = sb("both", [P, TT, EXPERTS])
        earlier = sb("earlier", [P, P])
        rank, count = sb("rank", [P, TT, EXPERTS]), sb("count", [P, EXPERTS])
        more, more_end, more_start = sb("more", [P, EXPERTS]), sb("more_end", [P, EXPERTS]), sb("more_start", [P, EXPERTS])
        picked = sb("picked", [P, 2, TT, EXPERTS])
        slot, expert, start, past = (sb(n, [P, 2, TT]) for n in ("slot", "expert", "start", "past"))
        by_slot = sb("by_slot", [P, 2 * TT, P])
        by_tile = sb("by_tile", [P, 2 * TT, MOE_TILES])
        place = sb("place", [P, MOE_TILES])
        empty = sb("empty", [P, MOE_TILES])
        ended = sb("ended", [1, MORE, EXPERTS])
        which = sb("which", [1, MORE])
        block = ctx.enter_context(nc.Block())
        iota = lambda n, rows=P: g.cols("iota", n, rows)
        w_router = g.cols("w_router", KT * LOGITS)

        @block.sync
        def _(sp):
            for s in range(units.per):
                units.load(sp, 0, s)
            for t in range(TT):
                sp.wait_ge(row_read, 2 * t + 2)
                sp.dma_start(moe.rows[t * P:(t + 1) * P, :], rows[:, t, :]).then_inc(stored, 16)
            sp.wait_ge(stored, 16 * TT)

        @block.tensor
        def _(pe):
            norm.tensor(pe)
            norm.wait(pe)
            for t in range(TT):
                for k in range(KT):
                    mm = nc.tensor.matmul(g.bank[0][:, t * LOGITS:(t + 1) * LOGITS], g.xn[:, k, t * P:(t + 1) * P],
                                          w_router[:, k * LOGITS:(k + 1) * LOGITS], start=(k == 0), stop=(k == KT - 1))
            mm.then_inc(logits_done, 1)
            for t in range(TT):
                for h in range(2):
                    n = 2 * t + h
                    if n >= 4:
                        pe.wait_ge(row_read, n - 3)
                    for j in range(TT):
                        mm = nc.tensor.matmul(g.bank[2 + n % 4][:, j * P:(j + 1) * P], g.xn[:, h * 4 + j, t * P:(t + 1) * P],
                                              g.ident[:, :], start=True, stop=True)
                    mm.then_inc(turned, 1)
            pe.wait_ge(chosen, 1)
            for t in range(TT):
                for s in range(t + 1):
                    nc.tensor.matmul(g.bank[1][:, t * EXPERTS:(t + 1) * EXPERTS], (earlier if s == t else g.ones)[:, :],
                                     both[:, s, :], start=(s == 0), stop=(s == t))
            for t in range(TT):
                mm = nc.tensor.matmul(g.bank[1][:, TT * EXPERTS:(TT + 1) * EXPERTS], g.ones[:, :], both[:, t, :],
                                      start=(t == 0), stop=(t == TT - 1))
            mm.then_inc(counted, 1)
            pe.wait_ge(placed, 1)
            for n in range(2 * TT):
                mm = nc.tensor.matmul(g.bank[6][:, 0:MOE_TILES], by_slot[:, n, :], by_tile[:, n, :],
                                      start=(n == 0), stop=(n == 2 * TT - 1))
            mm.then_inc(table_done, 1)

        @block.scalar
        def _(act):
            norm.scalar(act)
            for n in range(2 * TT):
                act.wait_ge(turned, n + 1)
                nc.scalar.activation(rows[:, n // 2, n % 2 * T:(n % 2 + 1) * T], g.bank[2 + n % 4][:, :], ACT.Copy).then_inc(row_read, 1)
            act.wait_ge(to_exp, 1)
            nc.scalar.activation(exps[:, :, :], exps[:, :, :], ACT.Exp).then_inc(exp_done, 1)
            act.wait_ge(to_exp, 2)
            nc.scalar.activation(second[:, :], second[:, :], ACT.Exp).then_inc(exp_done, 1)

        @block.vector
        def _(dve):
            norm.vector(dve)
            own = Own(dve, step)
            v = nc.vector

            def do(ins):
                own.did(ins)
                own.wait()

            def last(a, n):
                return a.unsqueeze(len(a.shape)).broadcast_to([*a.shape, n])

            def one_hot_max(values, top, out, n):
                do(v.tensor_reduce(top, values, AX.X, ALU.max))
                do(v.tensor_tensor(out, values, last(top, n), ALU.is_ge))
                do(v.tensor_scalar(out, out, -float(n), float(n), ALU.mult, ALU.add))
                do(v.tensor_tensor(out, out, iota(n).unsqueeze(1).broadcast_to([P, TT, n]), ALU.add))
                do(v.tensor_reduce(first[:, :], out, AX.X, ALU.min))
                do(v.tensor_tensor(out, iota(n).unsqueeze(1).broadcast_to([P, TT, n]), last(first[:, :], n), ALU.is_equal))

            do(v.scalar_tensor_tensor(earlier[:, :], g.causal_T[:, :], 0.0, g.ident[:, :], ALU.is_equal, ALU.subtract))
            dve.wait_ge(logits_done, 1)
            do(v.tensor_tensor(logits[:, :, :], g.bank[0][:, 0:TT * LOGITS].rearrange("p (t n) -> p t n", n=LOGITS),
                               g.cols("b_router", LOGITS).unsqueeze(1).broadcast_to([P, TT, LOGITS]), ALU.add))
            groups = logits[:, :, 0:GROUPS]
            one_hot_max(groups, top[:, :], group[:, :, :], GROUPS)
            v.tensor_tensor(exps[:, :, :], groups, last(top[:, :], GROUPS), ALU.subtract).then_inc(to_exp, 1)
            do(v.tensor_tensor(parts[:, :, :, :], logits[:, :, GROUPS:LOGITS].rearrange("p t (g e) -> p t g e", e=PER_GROUP),
                               last(group[:, :, :], PER_GROUP), ALU.mult))
            do(v.tensor_reduce(inside[:, :, :], parts[:, :, :, :].rearrange("p t g e -> p t e g"), AX.X, ALU.add))
            one_hot_max(inside[:, :, :], best[:, 0, :], here[:, 0, :, :], PER_GROUP)
            do(v.scalar_tensor_tensor(inside[:, :, :], here[:, 0, :, :], -3e38, inside[:, :, :], ALU.mult, ALU.add))
            one_hot_max(inside[:, :, :], best[:, 1, :], here[:, 1, :, :], PER_GROUP)
            v.tensor_tensor(second[:, :], best[:, 1, :], best[:, 0, :], ALU.subtract).then_inc(to_exp, 1)
            for c in range(2):
                do(v.tensor_tensor(hot[:, c, :, :].rearrange("p t (g e) -> p t g e", e=PER_GROUP), last(group[:, :, :], PER_GROUP),
                                   here[:, c, :, :].unsqueeze(2).broadcast_to([P, TT, GROUPS, PER_GROUP]), ALU.mult))
            v.tensor_tensor(both[:, :, :], hot[:, 0, :, :], hot[:, 1, :, :], ALU.add).then_inc(chosen, 1)
            dve.wait_ge(exp_done, 2)
            do(v.tensor_reduce(total[:, :], exps[:, :, :], AX.X, ALU.add))
            do(v.scalar_tensor_tensor(total[:, :], second[:, :], 1.0, total[:, :], ALU.add, ALU.mult))
            do(v.reciprocal(moe.weight[:, 0, :], total[:, :]))
            do(v.tensor_tensor(moe.weight[:, 1, :], moe.weight[:, 0, :], second[:, :], ALU.mult))
            dve.wait_ge(counted, 1)
            do(v.tensor_copy(rank[:, :, :], g.bank[1][:, 0:TT * EXPERTS].rearrange("p (t e) -> p t e", e=EXPERTS)))
            do(v.tensor_copy(count[:, :], g.bank[1][:, TT * EXPERTS:(TT + 1) * EXPERTS]))
            do(v.tensor_scalar(more[:, :], count[:, :], float(P), None, ALU.is_gt))
            for j in range(2, TT):
                do(v.scalar_tensor_tensor(more[:, :], count[:, :], float(j * P), more[:, :], ALU.is_gt, ALU.add))
            do(v.tensor_tensor_scan(more_end[:, :], g.ones[:, 0:EXPERTS], more[:, :], 0.0, ALU.mult, ALU.add))
            do(v.tensor_tensor(more_start[:, :], more_end[:, :], more[:, :], ALU.subtract))
            over_pairs = lambda a: a.unsqueeze(1).broadcast_to([P, 2, TT, EXPERTS])
            spread = lambda a: a.unsqueeze(1).broadcast_to([P, TT, EXPERTS])
            for out, of in ((slot, rank[:, :, :]), (expert, spread(iota(EXPERTS))), (start, spread(more_start[:, :]))):
                for c in range(2):
                    do(v.tensor_tensor(picked[:, c, :, :], hot[:, c, :, :], of, ALU.mult))
                do(v.tensor_reduce(out[:, :, :], picked[:, :, :, :], AX.X, ALU.add))
            do(v.tensor_scalar(past[:, :, :], slot[:, :, :], float(P), None, ALU.is_ge))
            for j in range(2, TT):
                do(v.scalar_tensor_tensor(past[:, :, :], slot[:, :, :], float(j * P), past[:, :, :], ALU.is_ge, ALU.add))
            do(v.scalar_tensor_tensor(slot[:, :, :], past[:, :, :], -float(P), slot[:, :, :], ALU.mult, ALU.add))
            do(v.scalar_tensor_tensor(start[:, :, :], start[:, :, :], EXPERTS - 1.0, past[:, :, :], ALU.add, ALU.add))
            do(v.tensor_tensor(start[:, :, :], start[:, :, :], expert[:, :, :], ALU.subtract))
            do(v.scalar_tensor_tensor(start[:, :, :], past[:, :, :], 0.0, start[:, :, :], ALU.is_gt, ALU.mult))
            do(v.tensor_tensor(expert[:, :, :], expert[:, :, :], start[:, :, :], ALU.add))
            for c in range(2):
                for t in range(TT):
                    n = c * TT + t
                    own.did(v.tensor_scalar(by_slot[:, n, :], iota(P), slot[:, c, t:t + 1], None, ALU.is_equal))
                    own.did(v.tensor_scalar(by_tile[:, n, :], iota(MOE_TILES), expert[:, c, t:t + 1], g.col("pair_number", n),
                                            ALU.is_equal, ALU.mult))
            own.wait()
            dve.sem_inc(placed, 1)
            do(v.tensor_tensor(ended[:, :, :], more_end[0:1, :].unsqueeze(1).broadcast_to([1, MORE, EXPERTS]),
                               last(iota(MORE, 1), EXPERTS), ALU.is_le))
            do(v.tensor_reduce(which[:, :], ended[:, :, :], AX.X, ALU.add))
            do(v.tensor_scalar(which[:, :], which[:, :], EXPERTS - 1.0, None, ALU.min))
            do(v.tensor_copy(moe.more_expert[:, :], which[:, :]))
            do(v.tensor_copy(moe.more_tiles[:, :], more_end[0:1, EXPERTS - 1:EXPERTS]))
            dve.wait_ge(table_done, 1)
            do(v.tensor_scalar(empty[:, :], g.bank[6][:, 0:MOE_TILES], 0.0, g.col("beyond"), ALU.is_equal, ALU.mult))
            do(v.scalar_tensor_tensor(place[:, :], g.bank[6][:, 0:MOE_TILES], -1.0, empty[:, :], ALU.add, ALU.add))
            do(v.tensor_copy(moe.pair[:, :], place[:, :]))
            do(v.tensor_scalar(moe.token[:, :], moe.pair[:, :], 1, None, ALU.logical_shift_right))



def after(eng, semaphore, count):
    if not isinstance(count, int) or count > 0:
        eng.wait_ge(semaphore, count)


class Tile:

    def __init__(self, g, ctx, moe, tag):
        sem, sb = g.stage(ctx, tag)
        self.g, self.moe = g, moe
        self.cleared, self.passed = sem("cleared"), sem("passed")
        self.token_copied, self.pair_copied = sem("token_copied"), sem("pair_copied")
        self.gathered, self.scattered = [sem("gathered0"), sem("gathered1")], [sem("scattered0"), sem("scattered1")]
        self.turned, self.turn_read_act, self.turn_read_dve = sem("turned"), sem("turn_read_act"), sem("turn_read_dve")
        self.up_done, self.silu_done, self.product_done = sem("up_done"), sem("silu_done"), sem("product_done")
        self.back_turned, self.back_read = sem("back_turned"), sem("back_read")
        self.down_done, self.out_read_act, self.out_read_dve = sem("down_done"), sem("out_read_act"), sem("out_read_dve")
        self.rows = [g.mix[:, 2 * b:2 * b + 2, :].rearrange("p a n -> p (a n)") for b in range(2)]
        self.xt = g.mix[:, 4:6, :].rearrange("p a (k n) -> p (a k) n", n=P)
        self.out = [g.memn[:, 4 * b:4 * b + 4, :].rearrange("p a n -> p (a n)") for b in range(2)]
        self.silu, self.act, self.back = sb("silu", [P, FE]), sb("act", [P, FE]), sb("back", [P, 2, P])
        self.token, self.pair = sb("token", [P, 2], I32), sb("pair", [P, 2], I32)


    def clear(self, pool):
        for b in range(2):
            self.g.nc.gpsimd.memset(self.rows[b], 0.0).then_inc(self.cleared, 1)
        pool.wait_ge(self.cleared, 2)

    def gather(self, pool, n, tile, b):
        nc, moe, here = self.g.nc, self.moe, slice(b, b + 1)
        nc.gpsimd.tensor_copy(self.token[:, here], moe.token[:, tile]).then_inc(self.token_copied, 1)
        pool.wait_ge(self.token_copied, n + 1)
        pool.sem_inc(self.passed, 1)
        nc.gpsimd.indirect_dma_start(out=self.rows[b], out_offset=None, in_=moe.rows,
                                     in_offset=bass.IndirectOffsetOnAxis(ap=self.token[:, here], axis=0),
                                     bounds_check=T - 1, oob_is_err=False).then_inc(self.gathered[b], 16)

    def scatter(self, pool, n, tile, b):
        nc, moe, here = self.g.nc, self.moe, slice(b, b + 1)
        pool.wait_ge(self.out_read_act, n + 1)
        pool.wait_ge(self.out_read_dve, n + 1)
        pool.sem_inc(self.passed, 1)
        nc.gpsimd.tensor_copy(self.pair[:, here], moe.pair[:, tile]).then_inc(self.pair_copied, 1)
        pool.wait_ge(self.pair_copied, n + 1)
        pool.sem_inc(self.passed, 1)
        nc.gpsimd.indirect_dma_start(out=moe.pair_rows, out_offset=bass.IndirectOffsetOnAxis(ap=self.pair[:, here], axis=0),
                                     in_=self.out[b], in_offset=None,
                                     bounds_check=2 * T - 1, oob_is_err=False).then_inc(self.scattered[b], 16)


    def turn(self, pe, n, b, uses):
        pe.wait_ge(self.gathered[b], 16 * uses + 16)
        after(pe, self.turn_read_act, n)
        after(pe, self.turn_read_dve, n)
        for k in range(KT):
            mm = self.g.nc.tensor.matmul(self.g.bank[k // 4][:, k % 4 * P:(k % 4 + 1) * P], self.rows[b][:, k * P:(k + 1) * P],
                                         self.g.ident[:, :], start=True, stop=True)
            if k % 4 == 3:
                mm.then_inc(self.turned, 1)

    def up(self, pe, n, b, weights):
        pe.wait_ge(self.turn_read_act, n + 1)
        pe.wait_ge(self.turn_read_dve, n + 1)
        for k in range(KT):
            mm = self.g.nc.tensor.matmul(self.g.bank[2 + b][:, :], self.xt[:, k, :], weights[k // 4][:, k % 4 * 2 * FE:(k % 4 + 1) * 2 * FE],
                                         start=(k == 0), stop=(k == KT - 1))
        mm.then_inc(self.up_done, 1)

    def turn_back(self, pe, n):
        pe.wait_ge(self.product_done, n + 1)
        for j in range(2):
            mm = self.g.nc.tensor.matmul(self.g.bank[4][:, j * P:(j + 1) * P], self.act[:, j * P:(j + 1) * P], self.g.ident[:, :],
                                         start=True, stop=True)
        mm.then_inc(self.back_turned, 1)

    def down(self, pe, n, weights):
        pe.wait_ge(self.back_read, n + 1)
        after(pe, self.out_read_act, n)
        after(pe, self.out_read_dve, n)
        for h in range(2):
            for j in range(2):
                c = 4 * 2 * FE + h * T
                mm = self.g.nc.tensor.matmul(self.g.bank[5 + h][:, :], self.back[:, j, :], weights[j][:, c:c + T],
                                             start=(j == 0), stop=(j == 1))
            mm.then_inc(self.down_done, 1)


    def act_turn(self, act, n):
        act.wait_ge(self.turned, 2 * n + 1)
        self.g.nc.scalar.activation(self.xt[:, 0:4, :].rearrange("p k n -> p (k n)"), self.g.bank[0][:, :], ACT.Copy)\
            .then_inc(self.turn_read_act, 1)

    def act_silu(self, act, n, b):
        act.wait_ge(self.up_done, n + 1)
        after(act, self.product_done, n)
        self.g.nc.scalar.activation(self.silu[:, :], self.g.bank[2 + b][:, 0:FE], ACT.Silu).then_inc(self.silu_done, 1)

    def act_out(self, act, n, b, uses):
        act.wait_ge(self.down_done, 2 * n + 1)
        after(act, self.scattered[b], 16 * uses)
        self.g.nc.scalar.activation(self.out[b][:, 0:T], self.g.bank[5][:, :], ACT.Copy).then_inc(self.out_read_act, 1)


    def dve_turn(self, dve, n):
        dve.wait_ge(self.turned, 2 * n + 2)
        self.g.nc.vector.tensor_copy(self.xt[:, 4:8, :].rearrange("p k n -> p (k n)"), self.g.bank[1][:, :])\
            .then_inc(self.turn_read_dve, 1)

    def dve_product(self, dve, n, b):
        dve.wait_ge(self.silu_done, n + 1)
        after(dve, self.back_turned, n)
        self.g.nc.vector.tensor_tensor(self.act[:, :], self.silu[:, :], self.g.bank[2 + b][:, FE:2 * FE], ALU.mult)\
            .then_inc(self.product_done, 1)

    def dve_back(self, dve, n):
        dve.wait_ge(self.back_turned, n + 1)
        after(dve, self.down_done, 2 * n)
        self.g.nc.vector.tensor_copy(self.back[:, :, :].rearrange("p a n -> p (a n)"), self.g.bank[4][:, 0:2 * P])\
            .then_inc(self.back_read, 1)

    def dve_out(self, dve, n, b, uses):
        dve.wait_ge(self.down_done, 2 * n + 2)
        after(dve, self.scattered[b], 16 * uses)
        self.g.nc.vector.tensor_copy(self.out[b][:, T:D], self.g.bank[6][:, :]).then_inc(self.out_read_dve, 1)


def stage_experts(g, moe, units):
    nc = g.nc
    units.begin()
    ROUNDS = EXPERTS // IN_FLIGHT
    weights = [[moe.ring.slots[2 * u], moe.ring.slots[2 * u + 1]] for u in range(IN_FLIGHT)]
    with ExitStack() as ctx:
        w = Tile(g, ctx, moe, "experts")
        block = ctx.enter_context(nc.Block())

        def rounds(eng, step):
            for u in range(IN_FLIGHT):
                step(0, u, IN_FLIGHT)
            with eng.Fori(1, ROUNDS - 1) as i:
                for u in range(IN_FLIGHT):
                    step(i, u, IN_FLIGHT)
            for u in range(IN_FLIGHT):
                step(ROUNDS - 1, u, IN_FLIGHT - 1 - u)

        @block.sync
        def _(sp):
            with sp.Fori(1, ROUNDS) as i:
                for u in range(IN_FLIGHT):
                    sp.wait_ge(w.down_done, 2 * IN_FLIGHT * i - 2 * IN_FLIGHT + 2 * u + 2)
                    units.load(sp, i, 2 * u)
                    units.load(sp, i, 2 * u + 1)

        @block.gpsimd
        def _(pool):
            w.clear(pool)
            w.gather(pool, 0, slice(0, 1), 0)
            w.gather(pool, 1, slice(1, 2), 1)

            def step(i, u, later):
                n, b = IN_FLIGHT * i + u, u % 2
                if later >= 2:
                    pool.wait_ge(w.turned, 2 * n + 2)
                    pool.sem_inc(w.passed, 1)
                    w.gather(pool, n + 2, bass.ds(n + 2, 1), b)
                w.scatter(pool, n, bass.ds(n, 1), b)
            rounds(pool, step)
            for b in range(2):
                pool.wait_ge(w.scattered[b], 16 * EXPERTS // 2)

        @block.tensor
        def _(pe):
            def load_up(i, u):
                n, v = IN_FLIGHT * i + u, u % IN_FLIGHT
                for s in range(2):
                    units.wait(pe, i + u // IN_FLIGHT, 2 * v + s)
                w.up(pe, n, u % 2, weights[v])

            def step(i, u, later):
                n = IN_FLIGHT * i + u
                if later >= 1:
                    w.turn(pe, n + 1, (u + 1) % 2, IN_FLIGHT // 2 * i + (u + 1) // 2)
                w.turn_back(pe, n)
                if later >= 1:
                    load_up(i, u + 1)
                w.down(pe, n, weights[u])
            w.turn(pe, 0, 0, 0)
            load_up(0, 0)
            rounds(pe, step)

        @block.scalar
        def _(act):
            def step(i, u, later):
                n = IN_FLIGHT * i + u
                if later >= 1:
                    w.act_turn(act, n + 1)
                    w.act_silu(act, n + 1, (u + 1) % 2)
                w.act_out(act, n, u % 2, IN_FLIGHT // 2 * i + u // 2)
            w.act_turn(act, 0)
            w.act_silu(act, 0, 0)
            rounds(act, step)

        @block.vector
        def _(dve):
            def step(i, u, later):
                n = IN_FLIGHT * i + u
                if later >= 1:
                    w.dve_turn(dve, n + 1)
                w.dve_back(dve, n)
                if later >= 1:
                    w.dve_product(dve, n + 1, (u + 1) % 2)
                w.dve_out(dve, n, u % 2, IN_FLIGHT // 2 * i + u // 2)
            w.dve_turn(dve, 0)
            w.dve_product(dve, 0, 0)
            rounds(dve, step)


def stage_more_experts(g, moe, units):
    nc = g.nc
    of_expert = units.ap.rearrange("i (u s) p n -> (i u) s p n", s=2)
    weights = moe.ring.slots[0:2]
    with ExitStack() as ctx:
        w = Tile(g, ctx, moe, "more")
        ready = [g.flag(ctx, f"more_ready{s}") for s in range(2)]
        block = ctx.enter_context(nc.Block())

        def any_more(eng):
            return eng.If(eng.value_load(moe.more_tiles[0:1, 0:1], min_val=0, max_val=MORE) > 0)

        def tiles(eng, tile):
            tile(0)
            with eng.Fori(1, MORE) as n:
                tile(n)

        @block.sync
        def _(sp):
            with any_more(sp):
                def tile(n):
                    expert = sp.value_load(moe.more_expert[0:1, bass.ds(n, 1)], min_val=0, max_val=EXPERTS - 1)
                    after(sp, w.down_done, 2 * n)
                    sp.sem_inc(w.passed, 1)
                    for s in range(2):
                        sp.dma_start(weights[s][:, :], of_expert[expert, s]).then_inc(ready[s], 16)
                tiles(sp, tile)

        @block.gpsimd
        def _(pool):
            with any_more(pool):
                def tile(n):
                    after(pool, w.turned, 2 * n)
                    pool.sem_inc(w.passed, 1)
                    w.gather(pool, n, bass.ds(n + EXPERTS, 1), 0)
                    w.scatter(pool, n, bass.ds(n + EXPERTS, 1), 0)
                tiles(pool, tile)
                pool.wait_ge(w.scattered[0], 16 * MORE)

        @block.tensor
        def _(pe):
            with any_more(pe):
                def tile(n):
                    w.turn(pe, n, 0, n)
                    for s in range(2):
                        pe.wait_ge(ready[s], 16 * n + 16)
                    w.up(pe, n, 0, weights)
                    w.turn_back(pe, n)
                    w.down(pe, n, weights)
                tiles(pe, tile)

        @block.scalar
        def _(act):
            with any_more(act):
                def tile(n):
                    w.act_turn(act, n)
                    w.act_silu(act, n, 0)
                    w.act_out(act, n, 0, n)
                tiles(act, tile)

        @block.vector
        def _(dve):
            with any_more(dve):
                def tile(n):
                    w.dve_turn(dve, n)
                    w.dve_product(dve, n, 0)
                    w.dve_back(dve, n)
                    w.dve_out(dve, n, 0, n)
                tiles(dve, tile)


def stage_combine(g, moe):
    nc = g.nc
    with ExitStack() as ctx:
        sem, sb = g.stage(ctx, "combine")
        loaded = [sem("loaded0"), sem("loaded1")]
        weighed, summed, turned, added = (sem(n) for n in ("weighed", "summed", "turned", "added"))
        two = [sb(f"two{b}", [P, 2, D]) for b in range(2)]
        out = [sb(f"sum{b}", [P, D]) for b in range(2)]
        block = ctx.enter_context(nc.Block())
        pairs = moe.pair_rows.rearrange("(t p c) n -> t p (c n)", p=P, c=2)

        @block.sync
        def _(sp):
            for t in range(TT):
                if t >= 2:
                    sp.wait_ge(summed, t - 1)
                sp.dma_start(two[t % 2][:, :, :].rearrange("p c n -> p (c n)"), pairs[t]).then_inc(loaded[t % 2], 16)
            sp.wait_ge(loaded[0], 32)
            sp.wait_ge(loaded[1], 32)

        @block.scalar
        def _(act):
            for t in range(TT):
                act.wait_ge(loaded[t % 2], 16 * (t // 2 + 1))
                if t >= 2:
                    act.wait_ge(turned, 2 * t - 2)
                nc.scalar.activation(out[t % 2][:, :], two[t % 2][:, 0, :], ACT.Copy, scale=moe.weight[:, 0, t:t + 1]).then_inc(weighed, 1)

        @block.vector
        def _(dve):
            def add(t):
                for h in range(2):
                    dve.wait_ge(turned, 2 * t + h + 1)
                    for j in range(4):
                        here = g.x[:, 4 * h + j, t * P:(t + 1) * P]
                        ins = nc.vector.scalar_tensor_tensor(here, g.bank[2 * (t % 2) + h][:, j * P:(j + 1) * P],
                                                             g.mod[:, 40 + 4 * h + j:41 + 4 * h + j], here, ALU.mult, ALU.add)
                    ins.then_inc(added, 1)
            for t in range(TT):
                dve.wait_ge(weighed, t + 1)
                nc.vector.scalar_tensor_tensor(out[t % 2][:, :], two[t % 2][:, 1, :], moe.weight[:, 1, t:t + 1], out[t % 2][:, :],
                                               ALU.mult, ALU.add).then_inc(summed, 1)
                if t > 0:
                    add(t - 1)
            add(TT - 1)

        @block.tensor
        def _(pe):
            for t in range(TT):
                pe.wait_ge(summed, t + 1)
                for h in range(2):
                    if t >= 2:
                        pe.wait_ge(added, 2 * (t - 2) + h + 1)
                    for j in range(4):
                        k = 4 * h + j
                        mm = nc.tensor.matmul(g.bank[2 * (t % 2) + h][:, j * P:(j + 1) * P], out[t % 2][:, k * P:(k + 1) * P],
                                              g.ident[:, :], start=True, stop=True)
                    mm.then_inc(turned, 1)


def stage_store(g, out):
    nc = g.nc
    with ExitStack() as ctx:
        norm = Norm(g, ctx, g.gains[:, 2, :], g.mod[:, 48:48 + KT])
        stored = g.flag(ctx, "stored")
        block = ctx.enter_context(nc.Block())

        @block.sync
        def _(sp):
            for k in range(KT):
                sp.wait_ge(norm.xn_ready, k + 1)
                sp.dma_start(out[:, k, :], g.xn[:, k, :]).then_inc(stored, 16)
            sp.wait_ge(stored, 16 * KT)

        @block.tensor
        def _(pe):
            norm.tensor(pe)

        @block.scalar
        def _(act):
            norm.scalar(act)

        @block.vector
        def _(dve):
            norm.vector(dve)



def as_columns(a):
    return np.asarray(a).reshape(-1, P).T


def padded_column(a):
    a = np.asarray(a).reshape(-1)
    return np.pad(a, (0, P - a.size)).reshape(P, 1)


def by_partition(w):
    w = np.asarray(w)
    return w.reshape(-1, P, w.shape[1]).transpose(1, 0, 2).reshape(P, -1)


def units_of(pieces):
    return np.stack([np.stack([by_partition(p) for p in one]) for one in pieces])


def columns_of(w, width, per):
    w = np.asarray(w)
    cut = [w[:, c:c + width] for c in range(0, w.shape[1], width)]
    return units_of([cut[n:n + per] for n in range(0, len(cut), per)])


def rows_of(w):
    w = np.asarray(w)
    return w.reshape(-1, 2, P, w.shape[1])


def side(*pieces):
    return np.concatenate([np.asarray(p) for p in pieces], axis=1)


def lay_out(v):
    a, table = {}, []
    v = {k: np.asarray(x) for k, x in v.items()}
    feature_major = lambda t: t.reshape(-1, KT, P).transpose(2, 1, 0)
    a["x"], a["mem"] = feature_major(v["x"][0]), feature_major(v["mem"][0])
    for l in range(2):
        for n in ("mix", "xattn", "mem", "ffn"):
            table.append((f"{n}_norm{l}", as_columns(v[f"{n}_norm"][l])))
        table.append((f"ffn_conv{l}", as_columns(np.concatenate([v["ffn_conv_w"][l].reshape(-1), v["ffn_conv_b"][l]]))))
    w = v["attn_w_in"][0]
    table.append(("w_forget", by_partition(w[:, 1536:1544])))
    table.append(("fox_bf", padded_column(v["attn_fox_bf"][0])))
    table.append(("diff_l", np.concatenate([padded_column(v[n][0]) for n in ("diff_lq1", "diff_lk1", "diff_lq2", "diff_lk2")], 1)))
    table.append(("subln", as_columns(v["diff_subln"][0])))
    a["w_fox"] = units_of([[side(*(w[:, c + P * h:c + P * h + P] for c in (0, 512, 1024)))] for h in range(4)])
    a["w_diff"] = units_of([[side(*(w[:, 1544 + c + P * h:1544 + c + P * h + P] for c in (0, 512, 1024)))] for h in range(4)])
    a["w_attn_out"] = rows_of(v["attn_w_out"][0])
    for l in range(2):
        q, kv = v["xattn_wq"][l], v["xattn_wkv"][l]
        a[f"w_xattn{l}"] = units_of([[m[:, c + 256 * h:c + 256 * h + 256] for m, c in ((q, 0), (kv, 0), (kv, D))] for h in range(X_HEADS)])
        a[f"w_xattn_out{l}"] = rows_of(v["xattn_wo"][l])
        up = v["ffn_w_up"][l]
        cut = [side(up[:, P * u:P * u + P], up[:, FF + P * u:FF + P * u + P]) for u in range(FT)]
        a[f"w_up{l}"] = units_of([cut[n:n + 2] for n in range(0, FT, 2)])
        a[f"w_down{l}"] = rows_of(v["ffn_w_down"][l])
    lay_out_more(v, a, table)
    where, at = {}, 0
    for name, c in table:
        where[name], at = at, at + c.shape[1]
    where["width"] = at
    a["vecs"] = np.concatenate([c for _, c in table], axis=1)
    return {k: np.ascontiguousarray(x) for k, x in a.items()}, where


def lay_out_mlstm(v, a, table):
    w = v["mlstm_w_in"][0]
    table.append(("w_gates", by_partition(w[:, 2048:2056])))
    table.append(("mlstm_b_i", padded_column(v["mlstm_b_i"][0])))
    table.append(("mlstm_b_f", padded_column(v["mlstm_b_f"][0])))
    table.append(("conv_qk", as_columns(v["mlstm_conv_qk"][0])))
    table.append(("head_norm", as_columns(v["mlstm_head_norm"][0])))
    a["w_mlstm"] = units_of([[side(w[:, P * h:P * h + P], w[:, 512 + P * h:512 + P * h + P]),
                              w[:, 1024 + 256 * h:1024 + 256 * h + 256], w[:, 2056 + 256 * h:2056 + 256 * h + 256]]
                             for h in range(ML_HEADS)])
    a["w_mlstm_out"] = rows_of(v["mlstm_w_out"][0])


def lay_out_second(v, a, table):
    for name in ("mu_rkv", "w0", "a0", "k_k", "k_a", "lnx_g", "lnx_b", "conv_b", "b_rgate", "b_igate", "lam",
                 "g_mix", "g_ffn", "mu_wag", "r_k"):
        table.append((name, as_columns(v[f"{name}_2"][0])))
    table.append(("final_norm", as_columns(v["final_norm"])))
    table.append(("g_final", as_columns(v["g_final_2"])))
    table.append(("c", as_columns(v["c_2"])))
    table.append(("b_ada", np.concatenate([as_columns(v["b_ada_2"][0]), as_columns(v["b_ada_f_2"])], 1)))
    table.append(("conv_w", as_columns(v["conv_w_2"][0])))
    s, t = np.arange(CHUNK)[:, None], np.arange(CHUNK)[None, :]
    twice = lambda m: np.concatenate([m, m], 0).astype(np.float32)
    table.append(("eye", twice(s == t)))
    table.append(("tri", np.concatenate([twice(s < t), twice(s <= t)], 1)))
    table.append(("levels", np.concatenate([twice((s >> l + 1 == t >> l + 1) & (t >> l & 1 == 1) & (s >> l & 1 == 0))
                                            for l in range(6)], 1)))
    ada = side(v["w_ada_2"][0], v["w_ada_f_2"])
    a["modulation"] = ada.reshape(KT, P, 8, 1024).transpose(0, 2, 1, 3)
    w = v["w_in_2"][0]
    a["w_rec_in"] = columns_of(w[:, 0:2560], 256, 2)
    first = by_partition(side(v["w1_2"][0], v["a1_2"][0], v["g1_2"][0]))
    lower = lambda m: np.pad(m, ((0, P - m.shape[0]), (0, 0)))

    def diagonal(blocks):
        z = np.zeros((HALF, HALF), blocks.dtype)
        return side(*(np.block([[blocks[2 * m], z], [z, blocks[2 * m + 1]]]) for m in range(AT)))

    second = side(lower(v["w2_2"][0]), lower(v["a2_2"][0]), v["g2_2"][0], diagonal(v["w_rgate_2"][0]), diagonal(v["w_igate_2"][0]))
    a["w_low"] = np.stack([np.pad(first, ((0, 0), (0, second.shape[1] - first.shape[1]))), second])[None]
    a["w_merge"] = units_of([[w[:, 2560 + c:2560 + c + 256], w[:, 2560 + D + c:2560 + D + c + 256],
                              np.concatenate([v["p_a_2"][0][:, c:c + 256], v["p_b_2"][0][:, c:c + 256]], 0)]
                             for c in range(0, D, 256)])
    a["w_mix_out"] = rows_of(v["w_out_2"][0])


def lay_out_experts(v, a, table):
    table.append(("w_router", by_partition(side(v["w_rg_2"][0], v["w_re_2"][0]))))
    bias = np.concatenate([v["b_rg_2"][0], v["b_re_2"][0]])
    table.append(("b_router", np.broadcast_to(bias, (P, bias.size))))
    p = np.arange(P, dtype=np.float32)[:, None]
    table.append(("iota", np.broadcast_to(np.arange(P, dtype=np.float32), (P, P))))
    table.append(("pair_number", np.concatenate([2 * (P * t + p) + c + 1 for c in range(2) for t in range(TT)], 1)))
    table.append(("beyond", 8 * T + 2 * p))
    up = [side(v["w1e_2"][0][e], v["w3e_2"][0][e]) for e in range(EXPERTS)]
    down = v["w2e_2"][0]
    half = lambda e, s: np.concatenate([by_partition(up[e][s * T:(s + 1) * T]), down[e][s * P:(s + 1) * P]], 1)
    a["w_experts"] = np.stack([half(e, s) for e in range(EXPERTS) for s in range(2)]).reshape(
        EXPERTS // IN_FLIGHT, 2 * IN_FLIGHT, P, SLOT)


def lay_out_more(v, a, table):
    lay_out_mlstm(v, a, table)
    lay_out_second(v, a, table)
    lay_out_experts(v, a, table)


def build(nc, A, where, out):
    with ExitStack() as ctx:
        g = Core(nc, ctx, A, where)
        U = {name: Units(g.ring, A[name]) for name in A if name.startswith("w_") and name != "w_experts"}
        stage_setup(g, U["w_fox"])

        stage_attention(g, U["w_fox"], U["w_diff"], True)
        stage_attention(g, U["w_diff"], U["w_attn_out"], False)
        stage_dense_residual(g, U["w_attn_out"], U["w_xattn0"], g.mix)
        for layer in range(2):
            if layer == 1:
                stage_mlstm(g, U["w_mlstm"], U["w_mlstm_out"])
                stage_dense_residual(g, U["w_mlstm_out"], U["w_xattn1"], g.mix)
            stage_cross_attention(g, U[f"w_xattn{layer}"], U[f"w_xattn_out{layer}"], layer)
            stage_dense_residual(g, U[f"w_xattn_out{layer}"], U[f"w_up{layer}"], g.mix)
            with nc.sbuf_tensor(f"hidden{layer}", [P, FT, T], F32) as hidden:
                stage_ffn_up(g, U[f"w_up{layer}"], U[f"w_down{layer}"], layer, hidden)
                stage_dense_residual(g, U[f"w_down{layer}"], U[("w_mlstm", "w_rec_in")[layer]], hidden,
                                     modulation=(layer == 0))
        stage_norm(g, g.cols("final_norm", KT), None, out=g.x)

        with ExitStack() as inner:
            rec = Recurrent(nc, inner)
            stage_recurrent_in(g, rec, U["w_rec_in"], U["w_low"])
            stage_low_rank(g, rec, U["w_low"], None)
            stage_rg_lru(g, rec)
            rw = Rwkv(rec)
            stage_rwkv_prepare(g, rec, rw)
            stage_rwkv_chunks(g, rec, rw)
            stage_rwkv_finish(g, rec, rw, U["w_merge"])
        with nc.sbuf_tensor("merged", [P, KT, T], F32) as merged:
            stage_merge(g, U["w_merge"], U["w_mix_out"], merged)
            stage_dense_residual(g, U["w_mix_out"], None, merged, gate=g.mod[:, 16:24])
        with ExitStack() as inner:
            moe = Experts(nc, inner, g.ring)
            experts = Units(moe.ring, A["w_experts"])
            stage_router(g, moe, experts)
            stage_experts(g, moe, experts)
            stage_more_experts(g, moe, experts)
            stage_combine(g, moe)
        stage_store(g, out)


def kernel(**inputs):
    import concourse.bacc as bacc
    from concourse.bass_utils import run_bass_kernel_spmd

    arrays, where = lay_out(inputs)
    nc = bacc.Bacc("TRN2", target_bir_lowering=False, num_devices=1)
    A = {name: nc.dram_tensor(f"in_{name}", a.shape, mybir.dt.from_np(a.dtype), kind="ExternalInput").ap()
         for name, a in arrays.items()}
    out = nc.dram_tensor("out", [P, KT, T], F32, kind="ExternalOutput").ap()
    build(nc, A, where, out)
    if not nc.is_finalized():
        nc.finalize()
    r = run_bass_kernel_spmd(nc, [{f"in_{name}": a for name, a in arrays.items()}], core_ids=[0])
    return np.ascontiguousarray(np.asarray(r.results[0]["out"]).transpose(2, 1, 0).reshape(1, T, D))
```

```python
import math
from contextlib import ExitStack

import concourse.bass as bass
import numpy as np
from concourse import mybir

ACT = mybir.ActivationFunctionType
ALU = mybir.AluOpType
AX = mybir.AxisListType
F32 = mybir.dt.float32
F32R = mybir.dt.float32r
I32 = mybir.dt.int32

P = 128
T = 512
D = 1024
KT = D // P
TT = T // P
MEM = 256
HALF = P // 2
FF = 2816
FT = FF // P
SLOT = 3072
SLOTS = 3
RMS_EPS = 1e-6
NEG = -1e30
LAMBDA_INIT = 0.2
MASKED = -1e30

FOX_PAIRS = 4
DIFF_HEADS = 4
FOX_HEADS = 8
ML_HEADS = 4
X_HEADS = 4
AW = 512
AT = AW // P
CHUNK = 64
NCHUNK = T // CHUNK
GROUPS, PER_GROUP, EXPERTS, FE = 4, 8, 32, 256
IN_FLIGHT = 4
MORE = (2 * T - 1) // P
MOE_TILES = EXPERTS + MORE


def two_names(nc, ctx, name, shape):
    with nc.sbuf_tensor(name, shape, F32) as whole:
        pass
    return whole, ctx.enter_context(nc.sbuf_tensor(f"{name}_r", shape, F32R))


class WeightRing:

    def __init__(self, slots, slots_r, ready):
        self.slots, self.slots_r, self.ready, self.loads = slots, slots_r, ready, [0] * len(slots)


class Units:

    def __init__(self, ring, ap):
        self.ring, self.ap = ring, ap
        self.n, self.per, _, self.width = ap.shape
        self.base = None

    def begin(self):
        self.base = list(self.ring.loads)
        for s in range(self.per):
            self.ring.loads[s] += self.n

    def load(self, sp, i, s):
        sp.dma_start(self.ring.slots[s][:, 0:self.width], self.ap[i, s]).then_inc(self.ring.ready[s], 16)

    def wait(self, pe, i, s):
        pe.wait_ge(self.ring.ready[s], 16 * (self.base[s] + 1) + 16 * i)

    def tile(self, s, k, m, w):
        return self.ring.slots[s][:, k * w + m * P:k * w + (m + 1) * P]

    def rows(self, s, k, w, c0, c1):
        return self.ring.slots[s][:, k * w + c0:k * w + c1]

    def in_place(self, s, size):
        return self.ring.slots[s][:, 0:size], self.ring.slots_r[s][:, 0:size]


def first_loads(sp, units):
    if units is not None:
        for s in range(units.per):
            units.load(sp, 0, s)


class Own:

    def __init__(self, eng, sem, i=0, per=0):
        self.eng, self.sem, self.base, self.n = eng, sem, i * per, 0

    def did(self, ins):
        self.n += 1
        return ins.then_inc(self.sem, 1)

    def wait(self):
        self.eng.wait_ge(self.sem, self.base + self.n)


class Core:

    def __init__(self, nc, ctx, A, where):
        self.nc, self.A, self.where = nc, A, where
        self.signals_of = None

        def sb(name, shape, dt=F32):
            return ctx.enter_context(nc.sbuf_tensor(name, shape, dt))

        self.x = sb("x", [P, KT, T])
        self.xn, self.xn_r = two_names(nc, ctx, "xn", [P, KT, T])
        self.mix, self.mix_r = two_names(nc, ctx, "mix", [P, KT, T])
        self.memn = sb("memn", [P, KT, MEM])
        self.square = sb("square", [P, 2, T])
        self.std = sb("std", [P, T])
        self.rstd = sb("rstd", [P, T])
        self.vecs = sb("vecs", [P, where["width"]])
        self.mod = sb("mod", [P, 64])
        self.gains = sb("gains", [P, 3, KT])
        self.ident = sb("ident", [P, P])
        self.mean_all = sb("mean_all", [P, P])
        self.mean_256 = sb("mean_256", [P, P])
        self.mean_128 = sb("mean_128", [P, P])
        self.ones = sb("ones", [P, P])
        self.head_sum = sb("head_sum", [P, P])
        self.causal = sb("causal", [P, P])
        self.causal_T = sb("causal_T", [P, P])
        self.chunked = sb("chunked", [P, P])
        self.eps = sb("eps", [P, 3])
        self.neg_lam = sb("neg_lam", [P, 1])
        slots, slots_r = zip(*(two_names(nc, ctx, f"weights{s}", [P, SLOT]) for s in range(SLOTS)))
        self.ring = WeightRing(list(slots), list(slots_r), [ctx.enter_context(nc.semaphore(f"weights_ready{s}")) for s in range(SLOTS)])
        self.bank = [ctx.enter_context(nc.psum_tensor(f"bank{b}", [P, 512], F32)) for b in range(8)]

    def flag(self, ctx, name):
        s = ctx.enter_context(self.nc.semaphore(name))
        if self.signals_of is not ctx:
            self.signals_of, self.signals = ctx, []
            ctx.callback(self.clear, self.signals)
        self.signals.append(s.num)
        return s

    def clear(self, numbers):
        numbers = sorted(numbers)
        first = numbers[0]
        for a, b in zip(numbers, numbers[1:] + [None]):
            if b != a + 1:
                self.nc.gpsimd.sem_clear(range(first, a + 1))
                first = b

    def stage(self, ctx, tag):
        nc = self.nc
        sem = lambda name: self.flag(ctx, name)
        sb = lambda name, shape, dt=F32: ctx.enter_context(nc.sbuf_tensor(f"{tag}_{name}", shape, dt))
        return sem, sb

    def col(self, name, j=0, rows=P):
        c = self.where[name] + j
        return self.vecs[0:rows, c:c + 1]

    def cols(self, name, n, rows=P):
        c = self.where[name]
        return self.vecs[0:rows, c:c + n]

    def col_at(self, name, j, rows=P):
        return self.vecs[0:rows, bass.ds(j + self.where[name], 1)]


class Split:

    def __init__(self, hi, lo):
        self.hi, self.lo = hi, lo

    def cut(self, a, b):
        return Split(self.hi[:, a:b], self.lo[:, a:b])


def split_products(nc, out, left, right, first, last):
    nc.tensor.matmul(out, left.hi, right.hi, start=first, stop=False)
    nc.tensor.matmul(out, left.hi, right.lo, start=False, stop=False)
    return nc.tensor.matmul(out, left.lo, right.hi, start=False, stop=last)


def split_xn(g, lo):
    return [Split(g.xn_r[:, k, :], lo[1][:, k, :]) for k in range(KT)]


class Norm:

    def __init__(self, g, ctx, gain, shift=None, out=None, lo=None):
        nc = g.nc
        self.g, self.gain, self.shift, self.bank = g, gain, shift, g.bank[7]
        self.out = g.xn if out is None else out
        self.squared = g.flag(ctx, "squared")
        self.summed = g.flag(ctx, "summed")
        self.std_ready = g.flag(ctx, "std_ready")
        self.rstd_ready = g.flag(ctx, "rstd_ready")
        self.scaled = g.flag(ctx, "scaled")
        self.xn_ready = g.flag(ctx, "xn_ready") if shift is not None else self.scaled
        self.lo = None if lo is None else lo[0]
        if lo is not None:
            self.rounded, self.split_dve, self.split_pool = (g.flag(ctx, n) for n in ("rounded", "split_dve", "split_pool"))
            self.split = split_xn(g, lo)

    def scalar(self, act):
        self.scalar_squares(act)
        self.scalar_rest(act)

    def scalar_squares(self, act):
        g = self.g
        for k in range(KT):
            if k >= 2:
                act.wait_ge(self.summed, k - 1)
            g.nc.scalar.activation(g.square[:, k % 2, :], g.x[:, k, :], ACT.Square).then_inc(self.squared, 1)

    def scalar_rest(self, act):
        g = self.g
        act.wait_ge(self.summed, KT)
        g.nc.scalar.activation(g.std[:, :], self.bank[:, :], ACT.Sqrt, bias=g.eps[:, 0:1]).then_inc(self.std_ready, 1)
        if self.lo is not None:
            for k in range(KT):
                act.wait_ge(self.scaled, k + 1)
                g.nc.scalar.activation(self.split[k].hi, self.lo[:, k, :], ACT.Copy).then_inc(self.rounded, 1)
        if self.shift is not None:
            for k in range(KT):
                act.wait_ge(self.scaled, k + 1)
                g.nc.scalar.activation(self.out[:, k, :], self.out[:, k, :], ACT.Identity,
                                       bias=self.shift[:, k:k + 1]).then_inc(self.xn_ready, 1)

    def tensor(self, pe):
        g = self.g
        for k in range(KT):
            pe.wait_ge(self.squared, k + 1)
            g.nc.tensor.matmul(self.bank[:, :], g.mean_all[:, :], g.square[:, k % 2, :],
                               start=(k == 0), stop=(k == KT - 1)).then_inc(self.summed, 1)

    def vector(self, dve):
        g = self.g
        dve.wait_ge(self.std_ready, 1)
        g.nc.vector.reciprocal(g.rstd[:, :], g.std[:, :]).then_inc(self.rstd_ready, 1)
        dve.wait_ge(self.rstd_ready, 1)
        if self.lo is not None:
            for k in range(KT):
                g.nc.vector.scalar_tensor_tensor(self.lo[:, k, :], g.x[:, k, :], self.gain[:, k:k + 1], g.rstd[:, :],
                                                 ALU.mult, ALU.mult).then_inc(self.scaled, 1)
                if k % 2:
                    dve.wait_ge(self.rounded, k)
                    g.nc.vector.tensor_tensor(self.split[k - 1].lo, self.lo[:, k - 1, :], self.split[k - 1].hi,
                                              ALU.subtract).then_inc(self.split_dve, 1)
            return
        for k in range(KT):
            g.nc.vector.scalar_tensor_tensor(self.out[:, k, :], g.x[:, k, :], self.gain[:, k:k + 1], g.rstd[:, :],
                                             ALU.mult, ALU.mult).then_inc(self.scaled, 1)

    def gpsimd(self, pool):
        for k in range(1, KT, 2):
            pool.wait_ge(self.rounded, k + 1)
            self.g.nc.gpsimd.tensor_tensor(self.split[k].lo, self.lo[:, k, :], self.split[k].hi, ALU.subtract).then_inc(self.split_pool, 1)

    def wait_tile(self, eng, k):
        eng.wait_ge((self.split_dve, self.split_pool)[k % 2], k // 2 + 1)

    def wait(self, eng):
        if self.lo is not None:
            eng.wait_ge(self.split_dve, KT // 2)
            eng.wait_ge(self.split_pool, KT // 2)
        else:
            eng.wait_ge(self.xn_ready, KT)


def log1p_half(dve, own, nc, e, s, s2, p):
    own.did(nc.vector.tensor_scalar(s, e, 2.0, None, ALU.add))
    own.wait()
    own.did(nc.vector.reciprocal(s2, s))
    own.wait()
    own.did(nc.vector.tensor_tensor(s, e, s2, ALU.mult))
    own.wait()
    own.did(nc.vector.tensor_tensor(s2, s, s, ALU.mult))
    own.wait()
    own.did(nc.vector.tensor_scalar(p, s2, 1.0 / 15.0, None, ALU.mult))
    for odd in (13, 11, 9, 7, 5, 3):
        own.wait()
        own.did(nc.vector.scalar_tensor_tensor(p, p, 1.0 / odd, s2, ALU.add, ALU.mult))
    own.wait()
    own.did(nc.vector.scalar_tensor_tensor(p, p, 1.0, s, ALU.add, ALU.mult))
    own.wait()


def stage_setup(g, coming):
    nc = g.nc
    with ExitStack() as ctx:
        x_in, mem_in, vecs_in = (g.flag(ctx, n) for n in ("x_in", "mem_in", "vecs_in"))
        made, filled = g.flag(ctx, "made"), g.flag(ctx, "filled")
        squared, summed = g.flag(ctx, "squared"), g.flag(ctx, "summed")
        std_ready = g.flag(ctx, "std_ready")
        step = g.flag(ctx, "step")
        dots, dots_summed, dots_exp = (g.flag(ctx, n) for n in ("dots", "dots_summed", "dots_exp"))
        prod = ctx.enter_context(nc.sbuf_tensor("prod", [P, 2], F32))
        lam = ctx.enter_context(nc.sbuf_tensor("lam", [P, 2], F32))
        block = ctx.enter_context(nc.Block())

        @block.sync
        def _(sp):
            sp.dma_start(g.vecs[:, :], g.A["vecs"]).then_inc(vecs_in, 16)
            sp.dma_start(g.memn[:, :, :], g.A["mem"]).then_inc(mem_in, 16)
            sp.dma_start(g.x[:, :, :], g.A["x"]).then_inc(x_in, 16)
            first_loads(sp, coming)
            sp.wait_ge(x_in, 16)

        @block.gpsimd
        def _(pool):
            for t, value in ((g.ident, 0.0), (g.mean_all, 1.0 / D), (g.mean_256, 1.0 / 256), (g.mean_128, 1.0 / 128),
                             (g.ones, 1.0), (g.head_sum, 0.0), (g.causal, 0.0), (g.causal_T, 0.0), (g.chunked, 0.0)):
                nc.gpsimd.memset(t[:, :], value).then_inc(made, 1)
            for j, value in enumerate((RMS_EPS, 1e-12, 64e-5)):
                nc.gpsimd.memset(g.eps[:, j:j + 1], value).then_inc(made, 1)
            pool.wait_ge(made, 12)
            nc.gpsimd.affine_select(out=g.ident[:, :], in_=g.ident[:, :], compare_op=ALU.not_equal, fill=1.0, base=0,
                                    pattern=[[-1, P]], channel_multiplier=1).then_inc(made, 1)
            nc.gpsimd.affine_select(out=g.causal[:, :], in_=g.causal[:, :], compare_op=ALU.is_ge, fill=MASKED, base=0,
                                    pattern=[[-1, P]], channel_multiplier=1).then_inc(made, 1)
            nc.gpsimd.affine_select(out=g.causal_T[:, :], in_=g.causal_T[:, :], compare_op=ALU.is_ge, fill=MASKED, base=0,
                                    pattern=[[1, P]], channel_multiplier=-1).then_inc(made, 1)
            pool.wait_ge(made, 15)
            nc.gpsimd.memset(g.chunked[0:HALF, HALF:P], MASKED).then_inc(made, 1)
            for h in range(2):
                pool.wait_ge(made, 16 + h)
                nc.gpsimd.memset(g.head_sum[h * HALF:(h + 1) * HALF, h * HALF:(h + 1) * HALF], 1.0).then_inc(made, 1)
            pool.wait_ge(made, 18)
            nc.gpsimd.engine_nop().then_inc(filled, 1)

        @block.scalar
        def _(act):
            act.wait_ge(mem_in, 16)
            for k in range(KT):
                if k >= 2:
                    act.wait_ge(summed, k - 1)
                nc.scalar.activation(g.square[:, k % 2, 0:MEM], g.memn[:, k, :], ACT.Square).then_inc(squared, 1)
            act.wait_ge(summed, KT)
            nc.scalar.activation(g.std[:, 0:MEM], g.bank[0][:, 0:MEM], ACT.Sqrt, bias=g.eps[:, 0:1]).then_inc(std_ready, 1)
            act.wait_ge(dots_summed, 1)
            nc.scalar.activation(lam[:, :], g.bank[1][:, 0:2], ACT.Exp).then_inc(dots_exp, 1)

        @block.tensor
        def _(pe):
            pe.wait_ge(filled, 1)
            for k in range(KT):
                pe.wait_ge(squared, k + 1)
                nc.tensor.matmul(g.bank[0][:, 0:MEM], g.mean_all[:, :], g.square[:, k % 2, 0:MEM],
                                 start=(k == 0), stop=(k == KT - 1)).then_inc(summed, 1)
            pe.wait_ge(dots, 2)
            nc.tensor.matmul(g.bank[1][:, 0:2], g.ones[:, :], prod[:, :], start=True, stop=True).then_inc(dots_summed, 1)

        @block.vector
        def _(dve):
            dve.wait_ge(vecs_in, 16)
            for j in range(2):
                nc.vector.tensor_tensor(prod[:, j:j + 1], g.col("diff_l", 2 * j), g.col("diff_l", 2 * j + 1),
                                        ALU.mult).then_inc(dots, 1)
            own = Own(dve, step)
            dve.wait_ge(std_ready, 1)
            own.did(nc.vector.reciprocal(g.rstd[:, 0:MEM], g.std[:, 0:MEM]))
            own.wait()
            for k in range(KT):
                own.did(nc.vector.tensor_tensor(g.memn[:, k, :], g.memn[:, k, :], g.rstd[:, 0:MEM], ALU.mult))
            dve.wait_ge(dots_exp, 1)
            own.did(nc.vector.scalar_tensor_tensor(g.neg_lam[:, :], lam[:, 1:2], -LAMBDA_INIT, lam[:, 0:1],
                                                   ALU.add, ALU.subtract))


def stage_dense_residual(g, units, coming, src, gate=None, modulation=False):
    nc = g.nc
    units.begin()
    rounds = units.n
    with ExitStack() as ctx:
        sem, sb = g.stage(ctx, f"dense{units.base[0]}")
        w_rounded, s_rounded, w_split, s_split, used, done, read, passed = (
            sem(n) for n in ("w_rounded", "s_rounded", "w_split", "s_split", "used", "product_done", "bank_read", "passed"))
        w = [Split(sb(f"w_hi{b}", [P, D], F32R), sb(f"w_lo{b}", [P, D], F32R)) for b in range(2)]
        s = [Split(sb(f"s_hi{b}", [P, T], F32R), sb(f"s_lo{b}", [P, T], F32R)) for b in range(2)]
        beside = Modulation(g, ctx) if modulation else None
        block = ctx.enter_context(nc.Block())

        def steps(eng, step, cut=0):
            def alone(i):
                for b in range(2):
                    step(i, b, 2 * i + b, slice(2 * i + b, 2 * i + b + 1), i < cut or (i == cut and b == 0))

            def loop(start, end):
                with eng.Fori(start, end) as i:
                    for b in range(2):
                        step(i, b, 2 * i + b, bass.ds(2 * i + b, 1), start < cut)
            alone(0)
            if cut:
                loop(1, cut)
                alone(cut)
                loop(cut + 1, rounds - 1)
            else:
                loop(1, rounds - 1)
            alone(rounds - 1)

        @block.sync
        def _(sp):
            with sp.Fori(1, rounds) as i:
                for b in range(2):
                    sp.wait_ge(w_split, 2 * i + b - 1)
                    units.load(sp, i, b)
            sp.wait_ge(w_split, 2 * rounds)
            first_loads(sp, coming)

        @block.scalar
        def _(act):
            if beside:
                beside.scalar(act)

            def step(i, b, k, tile, early):
                if not isinstance(i, int) or i > 0:
                    act.wait_ge(used, k - 1)
                units.wait(act, i, b)
                nc.scalar.activation(w[b].hi[:, :], units.rows(b, 0, D, 0, D), ACT.Copy).then_inc(w_rounded, 1)
                nc.scalar.activation(s[b].hi[:, :], src[:, tile, :].rearrange("p a n -> p (a n)"), ACT.Copy).then_inc(s_rounded, 1)
                if beside and early:
                    beside.load(act, beside.PLACES * k + beside.PLACES)
            steps(act, step, beside.steps // 2 if beside else 0)

        @block.gpsimd
        def _(pool):
            def step(i, b, k, tile, early):
                pool.wait_ge(w_rounded, k + 1)
                pool.sem_inc(passed, 1)
                nc.gpsimd.tensor_tensor(w[b].lo[:, :], units.rows(b, 0, D, 0, D), w[b].hi[:, :], ALU.subtract).then_inc(w_split, 1)
                pool.wait_ge(s_rounded, k + 1)
                pool.sem_inc(passed, 1)
                nc.gpsimd.tensor_tensor(s[b].lo[:, :], src[:, tile, :].rearrange("p a n -> p (a n)"), s[b].hi[:, :],
                                        ALU.subtract).then_inc(s_split, 1)
            steps(pool, step)

        @block.tensor
        def _(pe):
            def step(i, b, k, tile, early):
                first = isinstance(i, int) and k == 0
                last = isinstance(i, int) and k == 2 * rounds - 1
                pe.wait_ge(w_split, k + 1)
                pe.wait_ge(s_split, k + 1)
                for m in range(KT):
                    mm = split_products(nc, g.bank[m][:, :], w[b].cut(m * P, (m + 1) * P), Split(s[b].hi[:, :], s[b].lo[:, :]), first, last)
                    if last:
                        mm.then_inc(done, 1)
                if not last:
                    mm.then_inc(used, 1)
            steps(pe, step)
            if beside:
                pe.wait_ge(read, KT)
                beside.tensor(pe)

        @block.vector
        def _(dve):
            if beside:
                beside.vector(dve)
            for m in range(KT):
                dve.wait_ge(done, m + 1)
                here = g.x[:, m, :]
                if gate is None:
                    nc.vector.tensor_tensor(here, g.bank[m][:, :], here, ALU.add).then_inc(read, 1)
                else:
                    nc.vector.scalar_tensor_tensor(here, g.bank[m][:, :], gate[:, m:m + 1], here, ALU.mult, ALU.add).then_inc(read, 1)
            if beside:
                beside.end(dve)


LOGITS = {3: [(0, 3, 0)], 4: [(0, 2, 0), (0, 0, 384)], 5: [(1, 3, 0)], 6: [(1, 2, 0), (1, 0, 384)],
          7: [(0, 1, 0)], 1: [(1, 1, 0)]}
NLOG = len(LOGITS)


def stage_attention(g, units, coming, fox, xn_lo):
    nc = g.nc
    units.begin()
    scale = HALF ** -0.5
    maps = 2 if fox else 1
    first = 0 if fox else FOX_PAIRS
    turned = 4 * maps
    with ExitStack() as ctx:
        sem, sb = g.stage(ctx, "fox" if fox else "diff")
        proj_done, q_ready, k_ready, vT_ready, vt_done, v_ready = (
            sem(n) for n in ("proj_done", "q_ready", "k_ready", "vT_ready", "vt_done", "v_ready"))
        logits_done, max_done, exp_done, p_ready = (sem(n) for n in ("logits_done", "max_done", "exp_done", "p_ready"))
        turned_done, turned_even, turned_odd = (sem(n) for n in ("turned_done", "turned_even", "turned_odd"))
        values_done, mixed = sem("values_done"), sem("mixed")
        step, rows_ready = sem("step"), sem("rows_ready")
        gate_done, gate_abs, gate_exp, forget_ready = (sem(n) for n in ("gate_done", "gate_abs", "gate_exp", "forget_ready"))
        head_squared, head_summed, head_std, head_rstd = (sem(n) for n in ("head_squared", "head_summed", "head_std", "head_rstd"))
        qT, kT, vT = sb("qT", [P, T]), sb("kT", [P, T]), sb("vT", [P, T])
        v = sb("v", [P, TT, P])
        probs = sb("probs", [P, 2, TT, T])
        probs_T = sb("probs_T", [P, 2, TT, T])
        neg_max, total, inv = sb("neg_max", [P, 8]), sb("total", [P, 8]), sb("inv", [P, 8])
        if fox:
            norm = Norm(g, ctx, g.cols("mix_norm0", KT), lo=xn_lo)
            forget_hi, forget_lo = sb("forget_hi", [P, KT * FOX_HEADS], F32R), sb("forget_lo", [P, KT * FOX_HEADS], F32R)
            w_forget = Split(forget_hi[:, :], forget_lo[:, :])
            forget_rounded, forget_split = sem("forget_rounded"), sem("forget_split")
            F = sb("F", [FOX_HEADS, T])
            tmp = [sb(f"gate_tmp{j}", [FOX_HEADS, T]) for j in range(5)]
            rows = sb("rows", [FOX_HEADS, 2, T])
            minus = sb("minus", [FOX_HEADS, P])
        else:
            sub_gain = sb("sub_gain", [P, 1])
        xn = split_xn(g, xn_lo)
        whole, whole_r = units.in_place(0, KT * 3 * P)
        w = Split(sb("w_hi", [P, KT * 3 * P], F32R)[:, :], whole_r)
        w_rounded, w_split, passed = sem("w_rounded"), sem("w_split"), sem("passed")
        last = units.n - 1
        block = ctx.enter_context(nc.Block())

        @block.sync
        def _(sp):
            with sp.Fori(1, units.n) as i:
                sp.wait_ge(proj_done, 3 * i)
                units.load(sp, i, 0)
            sp.wait_ge(proj_done, 3 * units.n)
            first_loads(sp, coming)

        @block.tensor
        def _(pe):
            pe.sem_inc(turned_even, 1)
            pe.sem_inc(turned_odd, 1)
            pe.sem_inc(mixed, 1)
            if fox:
                norm.tensor(pe)
                pe.wait_ge(forget_split, 1)
                for k in range(KT):
                    norm.wait_tile(pe, k)
                    mm = split_products(nc, g.bank[6][0:FOX_HEADS, :], w_forget.cut(k * FOX_HEADS, (k + 1) * FOX_HEADS), xn[k],
                                        k == 0, k == KT - 1)
                mm.then_inc(gate_done, 1)

            def project(i, before):
                pe.wait_ge(w_split, i + 1)
                for j in range(3):
                    if before:
                        pe.wait_ge(exp_done, NLOG * i - NLOG + j + 1)
                    for k in range(KT):
                        c = (k * 3 + j) * P
                        mm = split_products(nc, g.bank[3 + j][:, :], w.cut(c, c + P), xn[k], k == 0, k == KT - 1)
                    mm.then_inc(proj_done, 1)

            def step(i, later):
                pe.wait_ge(q_ready, i + 1)
                pe.wait_ge(k_ready, i + 1)
                pe.wait_ge(vT_ready, i + 1)
                if fox:
                    pe.wait_ge(rows_ready, 2 * i + 2)
                for b, places in LOGITS.items():
                    for m, qb, c in places:
                        keys = (qb + 1) * P
                        half = slice(m * HALF, (m + 1) * HALF)
                        out = g.bank[b][:, c:c + keys]
                        nc.tensor.matmul(out, qT[half, qb * P:(qb + 1) * P], kT[half, 0:keys], start=True, stop=False)
                        if fox:
                            nc.tensor.matmul(out, minus[:, :], rows[:, m, 0:keys], start=False, stop=False)
                        mm = nc.tensor.matmul(g.bank[b][:, c + keys - P:c + keys], g.ident[:, :],
                                              (g.causal if fox else g.chunked)[:, :], start=False, stop=True)
                    mm.then_inc(logits_done, 1)
                for t in range(TT):
                    mm = nc.tensor.transpose(g.bank[0][:, t * P:(t + 1) * P], vT[:, t * P:(t + 1) * P], g.ident[:, :])
                mm.then_inc(vt_done, 1)
                if later:
                    project(i + 1, True)
                pe.wait_ge(v_ready, i + 1)
                pe.wait_ge(mixed, i + 1)
                for m in range(maps):
                    for n, qb in enumerate((3, 2, 1, 0)):
                        pe.wait_ge(p_ready, 4 * maps * i + 4 * m + n + 1)
                        count = turned // 2 * i + (4 * m + n) // 2
                        if 4 * m + n >= 2:
                            pe.wait_ge((turned_even, turned_odd)[n % 2], count + 1)
                        for kb in range(qb + 1):
                            mm = nc.tensor.transpose(g.bank[n % 2][:, kb * P:(kb + 1) * P],
                                                     probs[:, m, qb, kb * P:(kb + 1) * P], g.ident[:, :])
                        mm.then_inc(turned_done, 1)
                    pe.wait_ge(turned_even, turned // 2 * i + 2 * (m + 1) + 1)
                    pe.wait_ge(turned_odd, turned // 2 * i + 2 * (m + 1) + 1)
                    own = slice(m * HALF, (m + 1) * HALF) if fox else slice(0, P)
                    for kb in range(TT):
                        mm = nc.tensor.matmul(g.bank[2][own, kb * P:T], v[:, kb, own], probs_T[:, m, kb, kb * P:T],
                                              start=(kb == 0), stop=(kb == TT - 1), skip_group_check=True)
                mm.then_inc(values_done, 1)
                if not fox:
                    pe.wait_ge(head_squared, i + 1)
                    nc.tensor.matmul(g.bank[0][:, :], g.mean_128[:, :], g.square[:, 0, :], start=True, stop=True)\
                      .then_inc(head_summed, 1)
                    pe.wait_ge(head_std, i + 1)
            project(0, False)
            with pe.Fori(0, last) as i:
                step(i, True)
            step(last, False)

        @block.scalar
        def _(act):
            def round_weights(i):
                units.wait(act, i, 0)
                nc.scalar.activation(w.hi, whole, ACT.Copy).then_inc(w_rounded, 1)

            def read_projections(i):
                act.wait_ge(proj_done, 3 * i + 1)
                nc.scalar.activation(qT[:, :], g.bank[3][:, :], ACT.Copy, scale=scale).then_inc(q_ready, 1)
                act.wait_ge(proj_done, 3 * i + 3)
                nc.scalar.activation(vT[:, :], g.bank[5][:, :], ACT.Copy).then_inc(vT_ready, 1)

            def step(i, later):
                if later:
                    round_weights(i + 1)
                for j, (b, places) in enumerate(LOGITS.items()):
                    act.wait_ge(max_done, NLOG * i + j + 1)
                    for m, qb, c in places:
                        keys, n = (qb + 1) * P, 4 * m + qb
                        e = nc.scalar.activation(probs[:, m, qb, 0:keys], g.bank[b][:, c:c + keys], ACT.Exp,
                                                 bias=neg_max[:, n:n + 1], accum_out=total[:, n:n + 1])
                    e.then_inc(exp_done, 1)
                if later:
                    read_projections(i + 1)
                for m in range(maps):
                    for n, qb in ((0, 3), (2, 1)):
                        act.wait_ge(turned_done, turned * i + 4 * m + n + 1)
                        nc.scalar.activation(probs_T[:, m, 0:qb + 1, qb * P:(qb + 1) * P],
                                             g.bank[0][:, 0:(qb + 1) * P].rearrange("p (a b) -> p a b", b=P),
                                             ACT.Copy).then_inc(turned_even, 1)
                act.wait_ge(values_done, i + 1)
                if fox:
                    nc.scalar.activation(g.mix[:, bass.ds(i + first, 1), :], g.bank[2][:, :], ACT.Copy).then_inc(mixed, 1)
                else:
                    nc.scalar.activation(g.square[:, 0, :], g.bank[2][:, :], ACT.Square).then_inc(head_squared, 1)
                    act.wait_ge(head_summed, i + 1)
                    nc.scalar.activation(g.std[:, :], g.bank[0][:, :], ACT.Sqrt, bias=g.eps[:, 0:1]).then_inc(head_std, 1)
            if fox:
                norm.scalar_squares(act)
                nc.scalar.activation(w_forget.hi, g.cols("w_forget", KT * FOX_HEADS), ACT.Copy).then_inc(forget_rounded, 1)
            round_weights(0)
            if fox:
                norm.scalar_rest(act)
                read_projections(0)
                act.wait_ge(gate_abs, 1)
                nc.scalar.activation(tmp[1][:, :], tmp[1][:, :], ACT.Exp, scale=-1.0).then_inc(gate_exp, 1)
            if not fox:
                read_projections(0)
            with act.Fori(0, last) as i:
                step(i, True)
            step(last, False)

        @block.gpsimd
        def _(pool):
            def rest(i):
                pool.wait_ge(w_rounded, i + 1)
                pool.sem_inc(passed, 1)
                nc.gpsimd.tensor_tensor(w.lo, whole, w.hi, ALU.subtract).then_inc(w_split, 1)
            if fox:
                pool.wait_ge(forget_rounded, 1)
                nc.gpsimd.tensor_tensor(w_forget.lo, g.cols("w_forget", KT * FOX_HEADS), w_forget.hi, ALU.subtract).then_inc(forget_split, 1)
            rest(0)
            if fox:
                norm.gpsimd(pool)
            with pool.Fori(1, units.n) as i:
                rest(i)

        @block.vector
        def _(dve):
            if fox:
                norm.vector(dve)
                z, e = tmp[0], tmp[1]
                own = Own(dve, step)
                dve.wait_ge(gate_done, 1)
                own.did(nc.vector.tensor_scalar(z[:, :], g.bank[6][0:FOX_HEADS, :], g.col("fox_bf", rows=FOX_HEADS), None, ALU.add))
                own.wait()
                nc.vector.scalar_tensor_tensor(e[:, :], z[:, :], -1.0, z[:, :], ALU.mult, ALU.max).then_inc(gate_abs, 1)
                own.did(nc.vector.memset(minus[:, :], -1.0))
                own.did(nc.vector.tensor_scalar(z[:, :], z[:, :], 0.0, None, ALU.min))
                dve.wait_ge(gate_exp, 1)
                log1p_half(dve, own, nc, e[:, :], tmp[2][:, :], tmp[3][:, :], tmp[4][:, :])
                own.did(nc.vector.scalar_tensor_tensor(z[:, :], tmp[4][:, :], -2.0, z[:, :], ALU.mult, ALU.add))
                own.did(nc.vector.memset(e[:, :], 1.0))
                own.wait()
                nc.vector.tensor_tensor_scan(F[:, :], e[:, :], z[:, :], 0.0, ALU.mult, ALU.add).then_inc(forget_ready, 1)
                dve.wait_ge(forget_ready, 1)
                opening = own.n
            else:
                own = Own(dve, step)
                own.did(nc.vector.tensor_scalar(sub_gain[:, :], g.col("subln"), 1.0 - LAMBDA_INIT, None, ALU.mult))
                own.wait()
                opening = own.n
            per = 1 if fox else 6

            def next_keys(i):
                if fox:
                    for m in range(2):
                        nc.vector.tensor_scalar(rows[:, m, :], F[:, :], g.ident[0:FOX_HEADS, bass.ds(2 * i + m, 1)],
                                                None, ALU.mult).then_inc(rows_ready, 1)
                dve.wait_ge(proj_done, 3 * i + 2)
                nc.vector.tensor_copy(kT[:, :], g.bank[4][:, :]).then_inc(k_ready, 1)

            def round_of(i, later):
                own = Own(dve, step, i, per)
                own.base = own.base + opening
                for j, (b, places) in enumerate(LOGITS.items()):
                    dve.wait_ge(logits_done, NLOG * i + j + 1)
                    for m, qb, c in places:
                        keys, n = (qb + 1) * P, 4 * m + qb
                        r = nc.vector.tensor_reduce(neg_max[:, n:n + 1], g.bank[b][:, c:c + keys], AX.X, ALU.max, negate=True)
                    r.then_inc(max_done, 1)
                dve.wait_ge(vt_done, i + 1)
                nc.vector.tensor_copy(v[:, :, :], g.bank[0][:, :].rearrange("p (a b) -> p a b", b=P)).then_inc(v_ready, 1)
                dve.wait_ge(exp_done, NLOG * i + NLOG)
                own.did(nc.vector.reciprocal(inv[:, :], total[:, :]))
                own.wait()
                if fox:
                    for m in range(2):
                        for qb in (3, 2, 1, 0):
                            here, n = probs[:, m, qb, 0:(qb + 1) * P], 4 * m + qb
                            nc.vector.tensor_scalar(here, here, inv[:, n:n + 1], None, ALU.mult).then_inc(p_ready, 1)
                else:
                    own.did(nc.vector.tensor_scalar(inv[:, 4:8], inv[:, 4:8], g.neg_lam[:, 0:1], None, ALU.mult))
                    for qb in (3, 2, 1, 0):
                        here = probs[:, 0, qb, 0:(qb + 1) * P]
                        own.did(nc.vector.tensor_scalar(here, here, inv[:, qb:qb + 1], None, ALU.mult))
                        own.wait()
                        nc.vector.scalar_tensor_tensor(here, probs[:, 1, qb, 0:(qb + 1) * P], inv[:, 4 + qb:5 + qb], here,
                                                       ALU.mult, ALU.add).then_inc(p_ready, 1)
                if later:
                    next_keys(i + 1)
                for m in range(maps):
                    for n, qb in ((1, 2), (3, 0)):
                        dve.wait_ge(turned_done, turned * i + 4 * m + n + 1)
                        nc.vector.tensor_copy(probs_T[:, m, 0:qb + 1, qb * P:(qb + 1) * P],
                                              g.bank[1][:, 0:(qb + 1) * P].rearrange("p (a b) -> p a b", b=P))\
                          .then_inc(turned_odd, 1)
                if not fox:
                    dve.wait_ge(head_std, i + 1)
                    nc.vector.reciprocal(g.rstd[:, :], g.std[:, :]).then_inc(head_rstd, 1)
                    dve.wait_ge(head_rstd, i + 1)
                    nc.vector.scalar_tensor_tensor(g.mix[:, bass.ds(i + first, 1), :], g.bank[2][:, :], sub_gain[:, 0:1],
                                                   g.rstd[:, :], ALU.mult, ALU.mult).then_inc(mixed, 1)
            next_keys(0)
            with dve.Fori(0, last) as i:
                round_of(i, True)
            round_of(last, False)


def stage_cross_attention(g, units, coming, layer):
    nc = g.nc
    units.begin()
    HD = D // X_HEADS
    KEY, VALUE, QUERY = range(3)
    scale = HD ** -0.5
    with ExitStack() as ctx:
        sem, sb = g.stage(ctx, f"cross{layer}")
        norm = Norm(g, ctx, g.cols(f"xattn_norm{layer}", KT), lo=two_names(nc, ctx, f"xattn{layer}_xn_lo", [P, KT, T]))
        mem_scaled, mem_rounded, mem_split = (sem(n) for n in ("mem_scaled", "mem_rounded", "mem_split"))
        w_rounded, w_split = [[sem(f"w_{what}{s}") for s in range(3)] for what in ("rounded", "split")]
        proj_done, q_ready, k_ready, v_ready, passed = (sem(n) for n in ("proj_done", "q_ready", "k_ready", "v_ready", "passed"))
        logits_done, max_done, exp_done, inv_ready, p_ready = (
            sem(n) for n in ("logits_done", "max_done", "exp_done", "inv_ready", "p_ready"))
        turned_done, pT_ready, values_done, mixed = (sem(n) for n in ("turned_done", "pT_ready", "values_done", "mixed"))
        mem_hi = sb("mem_hi", [P, KT, MEM], F32R)
        mem_lo, mem_lo_r = two_names(nc, ctx, f"xattn{layer}_mem_lo", [P, KT, MEM])
        mem = [Split(mem_hi[:, k, :], mem_lo_r[:, k, :]) for k in range(KT)]
        whole, whole_r = zip(*(units.in_place(s, KT * HD) for s in range(3)))
        w = [Split(sb(f"w_hi{s}", [P, KT * HD], F32R)[:, :], whole_r[s]) for s in range(3)]
        qT, kT = sb("qT", [P, 2, T]), sb("kT", [P, 2, MEM])
        v = sb("v", [P, 2, HD])
        probs, probs_T = sb("probs", [P, TT, MEM]), sb("probs_T", [P, 2, T])
        neg_max, total, inv = sb("neg_max", [P, TT]), sb("total", [P, TT]), sb("inv", [P, TT])
        block = ctx.enter_context(nc.Block())
        last = units.n - 1

        def heads(eng, step):
            with eng.Fori(0, last - 1) as i:
                step(i, 2)
            step(last - 1, 1)
            step(last, 0)

        @block.sync
        def _(sp):
            with sp.Fori(1, units.n) as i:
                for s, done in ((KEY, 1), (VALUE, 2), (QUERY, 4)):
                    sp.wait_ge(proj_done, 4 * i - 4 + done)
                    units.load(sp, i, s)
            sp.wait_ge(proj_done, 4 * units.n)
            first_loads(sp, coming)

        @block.tensor
        def _(pe):
            def keys_values(i, first=False):
                pe.wait_ge(w_split[KEY], i + 1)
                for m in range(2):
                    for k in range(KT):
                        c = k * HD + m * P
                        mm = split_products(nc, g.bank[2][:, m * MEM:(m + 1) * MEM], w[KEY].cut(c, c + P), mem[k], k == 0, k == KT - 1)
                mm.then_inc(proj_done, 1)
                pe.wait_ge(w_split[VALUE], i + 1)
                if not first:
                    pe.wait_ge(v_ready, i)
                for t in range(2):
                    for k in range(KT):
                        mm = split_products(nc, g.bank[3][:, t * HD:(t + 1) * HD], mem[k].cut(t * P, (t + 1) * P),
                                            w[VALUE].cut(k * HD, (k + 1) * HD), k == 0, k == KT - 1)
                mm.then_inc(proj_done, 1)

            def queries(i, first=False):
                pe.wait_ge(w_split[QUERY], i + 1)
                for m in range(2):
                    for k in range(KT):
                        c = k * HD + m * P
                        if first and m == 0:
                            norm.wait_tile(pe, k)
                        mm = split_products(nc, g.bank[m][:, :], w[QUERY].cut(c, c + P), norm.split[k], k == 0, k == KT - 1)
                    mm.then_inc(proj_done, 1)

            def step(i, later):
                pe.wait_ge(q_ready, 2 * i + 2)
                pe.wait_ge(k_ready, i + 1)
                pe.wait_ge(mixed, 2 * i + 1)
                for b in range(2):
                    for j in range(2):
                        qb = 2 * b + j
                        for m in range(2):
                            mm = nc.tensor.matmul(g.bank[4 + b][:, j * MEM:(j + 1) * MEM], qT[:, m, qb * P:(qb + 1) * P],
                                                  kT[:, m, :], start=(m == 0), stop=(m == 1))
                    mm.then_inc(logits_done, 1)
                if later:
                    keys_values(i + 1)
                    queries(i + 1)
                pe.wait_ge(p_ready, i + 1)
                for t in range(2):
                    for qb in range(TT):
                        mm = nc.tensor.transpose(g.bank[6 + t][:, qb * P:(qb + 1) * P], probs[:, qb, t * P:(t + 1) * P], g.ident[:, :])
                    mm.then_inc(turned_done, 1)
                pe.wait_ge(pT_ready, 2 * i + 2)
                pe.wait_ge(v_ready, i + 1)
                for m in range(2):
                    for t in range(2):
                        mm = nc.tensor.matmul(g.bank[4 + m][:, :], v[:, t, m * P:(m + 1) * P], probs_T[:, t, :],
                                              start=(t == 0), stop=(t == 1))
                    mm.then_inc(values_done, 1)
            pe.sem_inc(mixed, 1)
            norm.tensor(pe)
            pe.wait_ge(mem_split, KT)
            keys_values(0, first=True)
            queries(0, first=True)
            heads(pe, step)

        @block.scalar
        def _(act):
            def round_weights(i, s):
                units.wait(act, i, s)
                nc.scalar.activation(w[s].hi, whole[s], ACT.Copy).then_inc(w_rounded[s], 1)

            def read_queries(i):
                for m in range(2):
                    act.wait_ge(proj_done, 4 * i + m + 3)
                    nc.scalar.activation(qT[:, m, :], g.bank[m][:, :], ACT.Copy, scale=scale).then_inc(q_ready, 1)

            def step(i, later):
                for b in range(2):
                    act.wait_ge(max_done, 2 * i + b + 1)
                    for j in range(2):
                        qb = 2 * b + j
                        e = nc.scalar.activation(probs[:, qb, :], g.bank[4 + b][:, j * MEM:(j + 1) * MEM], ACT.Exp,
                                                 bias=neg_max[:, qb:qb + 1], accum_out=total[:, qb:qb + 1])
                    e.then_inc(exp_done, 1)
                if later:
                    round_weights(i + 1, QUERY)
                    if later == 2:
                        round_weights(i + 2, KEY)
                        round_weights(i + 2, VALUE)
                    read_queries(i + 1)
                for m in range(2):
                    act.wait_ge(values_done, 2 * i + m + 1)
                    nc.scalar.activation(g.mix[:, bass.ds(2 * i + m, 1), :], g.bank[4 + m][:, :], ACT.Copy).then_inc(mixed, 1)
            round_weights(0, KEY)
            for k in range(KT):
                act.wait_ge(mem_scaled, k + 1)
                nc.scalar.activation(mem[k].hi, mem_lo[:, k, :], ACT.Copy).then_inc(mem_rounded, 1)
            norm.scalar_squares(act)
            round_weights(0, VALUE)
            round_weights(0, QUERY)
            norm.scalar_rest(act)
            round_weights(1, KEY)
            round_weights(1, VALUE)
            read_queries(0)
            heads(act, step)

        @block.gpsimd
        def _(pool):
            def rest(i, s):
                pool.wait_ge(w_rounded[s], i + 1)
                pool.sem_inc(passed, 1)
                nc.gpsimd.tensor_tensor(w[s].lo, whole[s], w[s].hi, ALU.subtract).then_inc(w_split[s], 1)
            rest(0, KEY)
            rest(0, VALUE)
            norm.gpsimd(pool)
            with pool.Fori(1, units.n) as i:
                rest(i, KEY)
                rest(i, VALUE)

        @block.vector
        def _(dve):
            def rest(i):
                dve.wait_ge(w_rounded[QUERY], i + 1)
                nc.vector.tensor_tensor(w[QUERY].lo, whole[QUERY], w[QUERY].hi, ALU.subtract).then_inc(w_split[QUERY], 1)

            def read_keys(i):
                dve.wait_ge(proj_done, 4 * i + 1)
                nc.vector.tensor_copy(kT[:, :, :], g.bank[2][:, :].rearrange("p (a b) -> p a b", b=MEM)).then_inc(k_ready, 1)

            def read_values(i):
                dve.wait_ge(proj_done, 4 * i + 2)
                nc.vector.tensor_copy(v[:, :, :], g.bank[3][:, :].rearrange("p (a b) -> p a b", b=HD)).then_inc(v_ready, 1)

            def step(i, later):
                for b in range(2):
                    dve.wait_ge(logits_done, 2 * i + b + 1)
                    nc.vector.tensor_reduce(neg_max[:, 2 * b:2 * b + 2], g.bank[4 + b][:, :].rearrange("p (a b) -> p a b", b=MEM),
                                            AX.X, ALU.max, negate=True).then_inc(max_done, 1)
                dve.wait_ge(exp_done, 2 * i + 2)
                nc.vector.reciprocal(inv[:, :], total[:, :]).then_inc(inv_ready, 1)
                dve.wait_ge(inv_ready, i + 1)
                for qb in range(TT):
                    p = nc.vector.tensor_scalar(probs[:, qb, :], probs[:, qb, :], inv[:, qb:qb + 1], None, ALU.mult)
                p.then_inc(p_ready, 1)
                if later:
                    rest(i + 1)
                    read_keys(i + 1)
                for t in range(2):
                    dve.wait_ge(turned_done, 2 * i + t + 1)
                    nc.vector.tensor_copy(probs_T[:, t, :], g.bank[6 + t][:, :]).then_inc(pT_ready, 1)
                if later:
                    dve.wait_ge(values_done, 2 * i + 2)
                    read_values(i + 1)
            for k in range(KT):
                nc.vector.tensor_scalar(mem_lo[:, k, :], g.memn[:, k, :], g.col(f"mem_norm{layer}", k), None,
                                        ALU.mult).then_inc(mem_scaled, 1)
            for k in range(KT):
                dve.wait_ge(mem_rounded, k + 1)
                nc.vector.tensor_tensor(mem[k].lo, mem_lo[:, k, :], mem[k].hi, ALU.subtract).then_inc(mem_split, 1)
            rest(0)
            norm.vector(dve)
            read_keys(0)
            read_values(0)
            heads(dve, step)


def stage_ffn_up(g, units, coming, layer, h):
    nc = g.nc
    units.begin()
    W = 2 * P
    with ExitStack() as ctx:
        sem, sb = g.stage(ctx, f"up{layer}")
        y = sb("y", [P, 4, T])
        norm = Norm(g, ctx, g.cols(f"ffn_norm{layer}", KT), lo=two_names(nc, ctx, f"up{layer}_xn_lo", [P, KT, T]))
        done, now_done, tap1_done, conv_done, gelu_done, h_done = (
            sem(n) for n in ("product_done", "now_done", "tap1_done", "conv_done", "gelu_done", "h_done"))
        w_rounded, w_split, passed = (sem(n) for n in ("w_rounded", "w_split", "passed"))
        halves = [g.mix_r[:, 4 * j:4 * j + 4, :].rearrange("p a n -> p (a n)") for j in range(2)]
        w = [Split(*halves), Split(sb("w_hi", [P, KT * W], F32R)[:, :], sb("w_lo", [P, KT * W], F32R)[:, :])]
        block = ctx.enter_context(nc.Block())

        def tap(j, i, b):
            return g.col_at(f"ffn_conv{layer}", 2 * i + b // 2 + (b % 2) * FT + j * 2 * FT)

        @block.sync
        def _(sp):
            with sp.Fori(1, units.n) as i:
                for s in range(2):
                    sp.wait_ge(w_split, 2 * i + s - 1)
                    units.load(sp, i, s)
            sp.wait_ge(w_split, 2 * units.n)
            first_loads(sp, coming)

        @block.tensor
        def _(pe):
            norm.tensor(pe)
            with pe.Fori(0, units.n) as i:
                for b in range(4):
                    if b % 2 == 0:
                        pe.wait_ge(w_split, 2 * i + b // 2 + 1)
                    pe.wait_ge(conv_done, 4 * i - 4 + b + 1 + 4)
                    for k in range(KT):
                        c = k * W + b % 2 * P
                        if b == 0:
                            norm.wait_tile(pe, k)
                        mm = split_products(nc, g.bank[b][:, :], w[b // 2].cut(c, c + P), norm.split[k], k == 0, k == KT - 1)
                    mm.then_inc(done, 1)

        @block.scalar
        def _(act):
            act.sem_inc(h_done, 1)

            def round_weights(i, s):
                units.wait(act, i, s)
                nc.scalar.activation(w[s].hi, units.rows(s, 0, KT * W, 0, KT * W), ACT.Copy).then_inc(w_rounded, 1)

            def one(i, last):
                for b in range(4):
                    act.wait_ge(done, 4 * i + b + 1)
                    act.wait_ge(h_done, 2 * i + 1)
                    nc.scalar.activation(y[:, b, :], g.bank[b][:, :], ACT.Identity, scale=tap(2, i, b),
                                         bias=tap(3, i, b)).then_inc(now_done, 1)
                    if b % 2 == 1:
                        act.wait_ge(conv_done, 4 * i + b + 4)
                        if not last:
                            round_weights(i + 1, b // 2)
                        nc.scalar.activation(y[:, b - 1, :], y[:, b - 1, :], ACT.Gelu_apprx_tanh).then_inc(gelu_done, 1)
            norm.scalar_squares(act)
            for s in range(2):
                round_weights(0, s)
            norm.scalar_rest(act)
            with act.Fori(0, units.n - 1) as i:
                one(i, False)
            one(units.n - 1, True)

        @block.gpsimd
        def _(pool):
            def rest(i, s):
                pool.wait_ge(w_rounded, 2 * i + s + 1)
                pool.sem_inc(passed, 1)
                nc.gpsimd.tensor_tensor(w[s].lo, units.rows(s, 0, KT * W, 0, KT * W), w[s].hi, ALU.subtract).then_inc(w_split, 1)
            rest(0, 0)
            rest(0, 1)
            norm.gpsimd(pool)
            with pool.Fori(1, units.n) as i:
                for s in range(2):
                    rest(i, s)

        @block.vector
        def _(dve):
            norm.vector(dve)
            dve.sem_inc(conv_done, 4)
            with dve.Fori(0, units.n) as i:
                for b in range(4):
                    dve.wait_ge(now_done, 4 * i + b + 1)
                    nc.vector.scalar_tensor_tensor(y[:, b, 1:T], g.bank[b][:, 0:T - 1], tap(1, i, b), y[:, b, 1:T],
                                                   ALU.mult, ALU.add).then_inc(tap1_done, 1)
                    dve.wait_ge(tap1_done, 4 * i + b + 1)
                    nc.vector.scalar_tensor_tensor(y[:, b, 2:T], g.bank[b][:, 0:T - 2], tap(0, i, b), y[:, b, 2:T],
                                                   ALU.mult, ALU.add).then_inc(conv_done, 1)
                    if b % 2 == 1:
                        dve.wait_ge(gelu_done, 2 * i + b // 2 + 1)
                        dve.wait_ge(conv_done, 4 * i + b + 5)
                        nc.vector.tensor_tensor(h[:, bass.ds(2 * i + b // 2, 1), :], y[:, b - 1, :], y[:, b, :],
                                                ALU.mult).then_inc(h_done, 1)


def stage_mlstm(g, units, coming):
    nc = g.nc
    units.begin()
    H, VD, W = ML_HEADS, 2 * P, 2 * P
    scale = P ** -0.5
    with ExitStack() as ctx:
        sem, sb = g.stage(ctx, "mlstm")
        norm = Norm(g, ctx, g.cols("mix_norm1", KT), lo=two_names(nc, ctx, "mlstm_xn_lo", [P, KT, T]))
        w_rounded, w_split = [[sem(f"w_{what}{s}") for s in range(3)] for what in ("rounded", "split")]
        gate_rounded, gate_split, passed = (sem(n) for n in ("gate_rounded", "gate_split", "passed"))
        gate_done, gate_abs, gate_exp, neg_m_ready, em_ready, G_ready, G_turned, Gc_ready = (
            sem(n) for n in ("gate_done", "gate_abs", "gate_exp", "neg_m_ready", "em_ready", "G_ready", "G_turned", "Gc_ready"))
        proj_done, now_done, conv_done, qk_ready, og_ready, v_ready, rows_ready = (
            sem(n) for n in ("proj_done", "now_done", "conv_done", "qk_ready", "og_ready", "v_ready", "rows_ready"))
        scores_done, weights_done, p_ready, sums_done, den_abs, h_ready = (
            sem(n) for n in ("scores_done", "weights_done", "p_ready", "sums_done", "den_abs", "h_ready"))
        squared, mean_done, std_ready, mixed, step = (sem(n) for n in ("head_squared", "mean_done", "head_std", "mixed", "step"))
        ig, G, top = sb("ig", [H, T]), sb("G", [H, T]), sb("top", [H, T])
        em = sb("em", [H, T])
        rows = sb("rows", [H, 2, T])
        Gc = sb("Gc", [P, TT, H])
        y = sb("y", [P, 2, T])
        qk = sb("qk", [P, 2, T])
        og, h = sb("og", [P, 2, T]), sb("h", [P, 2, T])
        v = sb("v", [P, TT, VD])
        wts = sb("wts", [P, 2, T])
        probs_T = sb("probs_T", [P, TT, T])
        den = sb("den", [P, T])
        sq = g.square
        tmp = [t[0:H, j, :] for t in (y, og, h) for j in range(2)][0:5]
        gate_hi, gate_lo = sb("gate_hi", [P, KT * 2 * H], F32R), sb("gate_lo", [P, KT * 2 * H], F32R)
        w_gates = Split(gate_hi[:, :], gate_lo[:, :])
        whole, whole_r = zip(*(units.in_place(s, KT * W) for s in range(3)))
        w = [Split(sb(f"w_hi{s}", [P, KT * W], F32R)[:, :], whole_r[s]) for s in range(3)]
        block = ctx.enter_context(nc.Block())

        @block.sync
        def _(sp):
            with sp.Fori(1, units.n) as i:
                for s in range(3):
                    sp.wait_ge(proj_done, 6 * i - 6 + 2 * s + 2)
                    units.load(sp, i, s)
            sp.wait_ge(proj_done, 6 * units.n)
            first_loads(sp, coming)

        @block.tensor
        def _(pe):
            pe.sem_inc(h_ready, 1)
            pe.sem_inc(std_ready, 1)
            pe.sem_inc(p_ready, 1)
            norm.tensor(pe)
            pe.wait_ge(gate_split, 1)
            for j in range(2):
                for k in range(KT):
                    c = k * 2 * H + j * H
                    if j == 0:
                        norm.wait_tile(pe, k)
                    mm = split_products(nc, g.bank[6 - j][0:H, :], w_gates.cut(c, c + H), norm.split[k], k == 0, k == KT - 1)
                mm.then_inc(gate_done, 1)

            def head(i, first):
                pe.wait_ge(h_ready, 2 * i + 1)
                for j in range(2):
                    if j == 0:
                        pe.wait_ge(w_split[0], i + 1)
                    for k in range(KT):
                        c = k * W + j * P
                        mm = split_products(nc, g.bank[j][:, :], w[0].cut(c, c + P), norm.split[k], k == 0, k == KT - 1)
                    mm.then_inc(proj_done, 1)
                pe.wait_ge(w_split[1], i + 1)
                pe.wait_ge(std_ready, i + 1)
                for t in range(TT):
                    for k in range(KT):
                        mm = split_products(nc, g.bank[2 + t // 2][:, t % 2 * VD:(t % 2 + 1) * VD], norm.split[k].cut(t * P, (t + 1) * P),
                                            w[1].cut(k * W, k * W + VD), k == 0, k == KT - 1)
                    if t % 2 == 1:
                        mm.then_inc(proj_done, 1)
                if first:
                    pe.wait_ge(G_ready, 1)
                    for t in range(TT):
                        mm = nc.tensor.transpose(g.bank[4][:, t * H:(t + 1) * H], G[:, t * P:(t + 1) * P], g.ident[0:H, 0:H])
                    mm.then_inc(G_turned, 1)
                    pe.wait_ge(Gc_ready, 1)
                pe.wait_ge(w_split[2], i + 1)
                pe.wait_ge(p_ready, 4 * i + 1)
                for j in range(2):
                    for k in range(KT):
                        c = k * W + j * P
                        mm = split_products(nc, g.bank[4 + j][:, :], w[2].cut(c, c + P), norm.split[k], k == 0, k == KT - 1)
                    mm.then_inc(proj_done, 1)
                pe.wait_ge(qk_ready, 2 * i + 2)
                pe.wait_ge(rows_ready, 2 * i + 2)
                for kb in range(TT):
                    A, B = (g.bank[6], g.bank[7]) if kb % 2 == 0 else (g.bank[4], g.bank[5])
                    n = T - kb * P
                    if kb == 1:
                        pe.wait_ge(og_ready, 2 * i + 2)
                    if kb >= 2:
                        pe.wait_ge(p_ready, 4 * i + kb)
                    nc.tensor.matmul(A[:, 0:n], qk[:, 1, kb * P:(kb + 1) * P], qk[:, 0, kb * P:T], start=True, stop=True)
                    nc.tensor.matmul(B[:, 0:n], g.ones[0:H, :], rows[:, 0, kb * P:T], start=True, stop=False)
                    nc.tensor.matmul(B[:, 0:P], g.ident[:, :], g.causal_T[:, :], start=False, stop=True)\
                      .then_inc(scores_done, 1)
                pe.wait_ge(v_ready, 2 * i + 2)
                nc.tensor.matmul(g.bank[3][:, :], g.ones[0:H, :], rows[:, 1, :], start=True, stop=True)
                for kb in range(TT):
                    pe.wait_ge(p_ready, 4 * i + kb + 2)
                    for j in range(3):
                        left = v[:, kb, j * P:(j + 1) * P] if j < 2 else g.ones[:, :]
                        mm = nc.tensor.matmul(g.bank[j][:, kb * P:T], left, probs_T[:, kb, kb * P:T], start=(kb == 0),
                                              stop=(kb == TT - 1), skip_group_check=True)
                mm.then_inc(sums_done, 1)
                for j in range(2):
                    pe.wait_ge(squared, 2 * i + j + 1)
                    mm = nc.tensor.matmul(g.bank[3][:, :], g.mean_256[:, :], sq[:, j, :], start=(j == 0), stop=(j == 1))
                mm.then_inc(mean_done, 1)
            head(0, True)
            with pe.Fori(1, units.n) as i:
                head(i, False)

        @block.scalar
        def _(act):
            act.sem_inc(mixed, 1)

            def round_weights(i, s):
                units.wait(act, i, s)
                nc.scalar.activation(w[s].hi, whole[s], ACT.Copy).then_inc(w_rounded[s], 1)
            norm.scalar_squares(act)
            nc.scalar.activation(w_gates.hi, g.cols("w_gates", KT * 2 * H), ACT.Copy).then_inc(gate_rounded, 1)
            for s in range(3):
                round_weights(0, s)
            norm.scalar_rest(act)
            act.wait_ge(gate_abs, 1)
            nc.scalar.activation(tmp[1], tmp[1], ACT.Exp, scale=-1.0).then_inc(gate_exp, 1)
            act.wait_ge(neg_m_ready, 1)
            nc.scalar.activation(em[:, :], tmp[0], ACT.Exp).then_inc(em_ready, 1)
            act.wait_ge(em_ready, 1)

            def head(i, later):
                for j in range(2):
                    act.wait_ge(proj_done, 6 * i + j + 1)
                    nc.scalar.activation(y[:, j, :], g.bank[j][:, :], ACT.Copy,
                                         scale=g.col_at("conv_qk", i + 3 * 2 * H + j * H)).then_inc(now_done, 1)
                for j in range(2):
                    act.wait_ge(conv_done, 2 * i + j + 1)
                    nc.scalar.activation(qk[:, j, :], y[:, j, :], ACT.Silu).then_inc(qk_ready, 1)
                act.wait_ge(mixed, 2 * i + 1)
                for j in range(2):
                    act.wait_ge(proj_done, 6 * i + 5 + j)
                    nc.scalar.activation(og[:, j, :], g.bank[4 + j][:, :], ACT.Sigmoid).then_inc(og_ready, 1)
                for kb in range(TT):
                    act.wait_ge(scores_done, 4 * i + kb + 1)
                    if kb >= 2:
                        act.wait_ge(p_ready, 4 * i + kb)
                    nc.scalar.activation(wts[:, kb % 2, 0:T - kb * P], (g.bank[7] if kb % 2 == 0 else g.bank[5])[:, 0:T - kb * P],
                                         ACT.Exp, bias=Gc[:, kb, bass.ds(i, 1)]).then_inc(weights_done, 1)
                if later:
                    for s in range(3):
                        round_weights(i + 1, s)
                act.wait_ge(sums_done, i + 1)
                nc.scalar.activation(den[:, :], g.bank[2][:, :], ACT.Abs).then_inc(den_abs, 1)
                for j in range(2):
                    act.wait_ge(h_ready, 2 * i + j + 2)
                    nc.scalar.activation(sq[:, j, :], h[:, j, :], ACT.Square).then_inc(squared, 1)
                act.wait_ge(mean_done, i + 1)
                nc.scalar.activation(g.std[:, :], g.bank[3][:, :], ACT.Sqrt, bias=g.eps[:, 0:1]).then_inc(std_ready, 1)
            with act.Fori(0, units.n - 1) as i:
                head(i, True)
            head(units.n - 1, False)

        @block.gpsimd
        def _(pool):
            def rest(i, s):
                pool.wait_ge(w_rounded[s], i + 1)
                pool.sem_inc(passed, 1)
                nc.gpsimd.tensor_tensor(w[s].lo, whole[s], w[s].hi, ALU.subtract).then_inc(w_split[s], 1)
            pool.wait_ge(gate_rounded, 1)
            nc.gpsimd.tensor_tensor(w_gates.lo, g.cols("w_gates", KT * 2 * H), w_gates.hi, ALU.subtract).then_inc(gate_split, 1)
            rest(0, 0)
            norm.gpsimd(pool)
            for s in (1, 2):
                rest(0, s)
            with pool.Fori(1, units.n) as i:
                for s in range(3):
                    rest(i, s)

        @block.vector
        def _(dve):
            norm.vector(dve)
            z, e = tmp[0], tmp[1]
            own = Own(dve, step)
            dve.wait_ge(gate_done, 2)
            own.did(nc.vector.tensor_scalar(ig[:, :], g.bank[6][0:H, :], g.col("mlstm_b_i", rows=H), None, ALU.add))
            own.did(nc.vector.tensor_scalar(z, g.bank[5][0:H, :], g.col("mlstm_b_f", rows=H), None, ALU.add))
            own.wait()
            nc.vector.scalar_tensor_tensor(e, z, -1.0, z, ALU.mult, ALU.max).then_inc(gate_abs, 1)
            own.did(nc.vector.tensor_scalar(z, z, 0.0, None, ALU.min))
            dve.wait_ge(gate_exp, 1)
            log1p_half(dve, own, nc, e, tmp[2], tmp[3], tmp[4])
            own.did(nc.vector.scalar_tensor_tensor(z, tmp[4], -2.0, z, ALU.mult, ALU.add))
            own.did(nc.vector.memset(e, 1.0))
            own.wait()
            F = tmp[2]
            own.did(nc.vector.tensor_tensor_scan(F, e, z, 0.0, ALU.mult, ALU.add))
            own.wait()
            nc.vector.tensor_tensor(G[:, :], ig[:, :], F, ALU.subtract).then_inc(G_ready, 1)
            dve.wait_ge(G_ready, 1)
            own.did(nc.vector.tensor_tensor_scan(top[:, :], G[:, :], G[:, :], 0.0, ALU.max, ALU.max))
            own.wait()
            nc.vector.scalar_tensor_tensor(z, top[:, :], -1.0, F, ALU.mult, ALU.subtract).then_inc(neg_m_ready, 1)
            own.did(nc.vector.tensor_scalar(top[:, :], top[:, :], -1.0, None, ALU.mult))
            dve.wait_ge(G_turned, 1)
            nc.vector.tensor_copy(Gc[:, :, :], g.bank[4][:, 0:TT * H].rearrange("p (a b) -> p a b", b=H)).then_inc(Gc_ready, 1)
            dve.wait_ge(em_ready, 1)
            own.wait()
            opening = own.n
            per = 2 * 2 + 2 + 1 + 2
            with dve.Fori(0, units.n) as i:
                own = Own(dve, step, i, per)
                own.base = own.base + opening
                for j, row in enumerate((top, em)):
                    nc.vector.tensor_scalar(rows[:, j, :], row[:, :], g.ident[0:H, bass.ds(i, 1)], None,
                                            ALU.mult).then_inc(rows_ready, 1)
                for j in range(2):
                    dve.wait_ge(now_done, 2 * i + j + 1)
                    for back in (1, 2, 3):
                        tap = nc.vector.scalar_tensor_tensor(y[:, j, back:T], g.bank[j][:, 0:T - back],
                                                             g.col_at("conv_qk", i + (3 - back) * 2 * H + j * H), y[:, j, back:T],
                                                             ALU.mult, ALU.add)
                        if back < 3:
                            own.did(tap)
                            own.wait()
                        else:
                            tap.then_inc(conv_done, 1)
                for j in range(2):
                    dve.wait_ge(proj_done, 6 * i + 3 + j)
                    nc.vector.tensor_copy(v[:, 2 * j:2 * j + 2, :], g.bank[2 + j][:, :].rearrange("p (a b) -> p a b", b=VD))\
                      .then_inc(v_ready, 1)
                for kb in range(TT):
                    dve.wait_ge(weights_done, 4 * i + kb + 1)
                    n = T - kb * P
                    nc.vector.scalar_tensor_tensor(probs_T[:, kb, kb * P:T], (g.bank[6] if kb % 2 == 0 else g.bank[4])[:, 0:n],
                                                   scale, wts[:, kb % 2, 0:n], ALU.mult, ALU.mult).then_inc(p_ready, 1)
                dve.wait_ge(den_abs, i + 1)
                own.did(nc.vector.tensor_tensor(den[:, :], den[:, :], g.bank[3][:, :], ALU.max))
                own.wait()
                own.did(nc.vector.reciprocal(den[:, :], den[:, :]))
                own.wait()
                for j in range(2):
                    nc.vector.tensor_tensor(h[:, j, :], g.bank[j][:, :], den[:, :], ALU.mult).then_inc(h_ready, 1)
                dve.wait_ge(std_ready, i + 2)
                own.did(nc.vector.reciprocal(g.rstd[:, :], g.std[:, :]))
                own.wait()
                for j in range(2):
                    own.did(nc.vector.scalar_tensor_tensor(h[:, j, :], h[:, j, :], g.col_at("head_norm", 2 * i + j), g.rstd[:, :],
                                                           ALU.mult, ALU.mult))
                    own.wait()
                    nc.vector.tensor_tensor(g.mix[:, bass.ds(2 * i + j, 1), :], h[:, j, :], og[:, j, :], ALU.mult)\
                      .then_inc(mixed, 1)


def stage_norm(g, gain, coming, shift=None, out=None):
    nc = g.nc
    with ExitStack() as ctx:
        norm = Norm(g, ctx, gain, shift, out)
        block = ctx.enter_context(nc.Block())

        @block.sync
        def _(sp):
            first_loads(sp, coming)

        @block.tensor
        def _(pe):
            norm.tensor(pe)

        @block.scalar
        def _(act):
            norm.scalar(act)

        @block.vector
        def _(dve):
            norm.vector(dve)


class Modulation:
    PARTS, PLACES = 8, 4

    def __init__(self, g, ctx):
        sem, sb = g.stage(ctx, "modulation")
        self.g, self.ap = g, g.A["modulation"]
        self.W = self.ap.shape[3]
        self.units = self.ap.rearrange("k q p n -> (k q) p n")
        self.steps = self.PARTS * KT // self.PLACES - 1
        self.silu_ready, self.zeroed, self.used, self.summed, self.step = (
            sem(n) for n in ("silu_ready", "zeroed", "weighed", "summed", "modulation_step"))
        self.ready = [sem(f"rows_ready{s}") for s in range(self.PLACES)]
        pairs = lambda t: [t[:, 2 * s:2 * s + 2, :].rearrange("p a n -> p (a n)") for s in range(KT // 2)]
        more = sb("sums", [P, KT, T])
        self.rows, self.sums = pairs(g.mix), pairs(g.xn) + pairs(more)
        self.c = sb("c", [P, KT])

    def load(self, act, n):
        for b in range(self.PLACES):
            if not isinstance(n, int) or n > 0:
                act.wait_ge(self.used, n + b - self.PLACES + 1)
            act.dma_start(self.rows[b], self.units[bass.ds(n + b, 1)].rearrange("a p n -> (a p) n")).then_inc(self.ready[b], 16)

    def scalar(self, act):
        self.load(act, 0)
        self.g.nc.scalar.activation(self.c[:, :], self.g.cols("c", KT), ACT.Silu).then_inc(self.silu_ready, 1)

    def vector(self, dve):
        n, places = self.PARTS, self.PLACES
        for q in range(n):
            self.g.nc.vector.memset(self.sums[q], 0.0).then_inc(self.zeroed, 1)
        dve.wait_ge(self.zeroed, n)
        dve.wait_ge(self.silu_ready, 1)
        with dve.Fori(0, KT) as k:
            for q in range(n):
                dve.wait_ge(self.ready[q % places], 16 * (n // places) * k + 16 * (q // places) + 16)
                if q > 0:
                    dve.wait_ge(self.used, n * k + q)
                self.g.nc.vector.scalar_tensor_tensor(self.sums[q], self.rows[q % places], self.c[:, bass.ds(k, 1)], self.sums[q],
                                                      ALU.mult, ALU.add).then_inc(self.used, 1)

    def end(self, dve):
        g, own = self.g, Own(dve, self.step)
        dve.wait_ge(self.summed, 1)
        own.did(g.nc.vector.tensor_tensor(g.mod[:, :], g.bank[7][:, 0:64], g.cols("b_ada", 64), ALU.add))
        own.wait()
        for j, (name, scale) in enumerate((("g_mix", 8), ("g_ffn", 32), ("g_final", 56))):
            own.did(g.nc.vector.scalar_tensor_tensor(g.gains[:, j, :], g.mod[:, scale:scale + KT], 1.0, g.cols(name, KT),
                                                     ALU.add, ALU.mult))

    def tensor(self, pe):
        pe.wait_ge(self.used, self.PARTS * KT)
        for j in range(64):
            q, c = divmod(j * P, self.W)
            mm = self.g.nc.tensor.matmul(self.g.bank[7][:, j:j + 1], self.sums[q][:, c:c + P], self.g.ones[:, 0:1], start=True, stop=True)
        mm.then_inc(self.summed, 1)


class Recurrent:

    def __init__(self, nc, ctx):
        sb = lambda name, shape: ctx.enter_context(nc.sbuf_tensor(f"rec_{name}", shape, F32))
        self.rkv = sb("rkv", [P, 3 * AT, T])
        self.r, self.k, self.v = (self.rkv[:, j * AT:(j + 1) * AT, :] for j in range(3))
        self.xc = sb("xc", [P, AT, T])
        self.gelu_gate = sb("gelu_gate", [P, AT, T])
        self.keep = sb("keep", [P, 3 * AT])

    def add_gates(self, nc, ctx):
        sb = lambda name, shape: ctx.enter_context(nc.sbuf_tensor(f"rec_{name}", shape, F32))
        self.ell = sb("ell", [P, AT, T])
        self.a = sb("a", [P, AT, T])
        self.gate = sb("gate", [P, AT, T])
        self.gate_r, self.gate_i = sb("gate_r", [P, AT, T]), sb("gate_i", [P, AT, T])


def stage_recurrent_in(g, rec, units, coming):
    nc = g.nc
    units.begin()
    W = 2 * P
    with ExitStack() as ctx:
        sem, sb = g.stage(ctx, "recurrent_in")
        norm = Norm(g, ctx, g.gains[:, 0, :], g.mod[:, 0:KT])
        xn_lo = sb("xn_lo", [P, KT, T], F32R)
        xn = [Split(g.mix_r[:, k, :], xn_lo[:, k, :]) for k in range(KT)]
        whole = [units.in_place(s, KT * W)[0] for s in range(2)]
        w = [Split(sb("w_hi0", [P, KT * W], F32R)[:, :], units.in_place(2, KT * W)[1]),
             Split(sb("w_hi1", [P, KT * W], F32R)[:, :], sb("w_lo1", [P, KT * W], F32R)[:, :])]
        x_rounded, x_split, w_rounded, w_split, passed = (sem(n) for n in ("x_rounded", "x_split", "w_rounded", "w_split", "passed"))
        done, now_done, free, keep_ready, step = (sem(n) for n in ("product_done", "now_done", "bank_free", "keep_ready", "step"))
        block = ctx.enter_context(nc.Block())

        @block.sync
        def _(sp):
            with sp.Fori(1, units.n) as i:
                for s in range(2):
                    sp.wait_ge(w_split, 2 * i + s - 1)
                    units.load(sp, i, s)
            sp.wait_ge(w_split, 2 * units.n)
            first_loads(sp, coming)

        @block.tensor
        def _(pe):
            norm.tensor(pe)
            with pe.Fori(0, units.n) as i:
                for b in range(4):
                    if b % 2 == 0:
                        pe.wait_ge(w_split, 2 * i + b // 2 + 1)
                    pe.wait_ge(free, 4 * i + b + 1)
                    for k in range(KT):
                        c = k * W + b % 2 * P
                        if b == 0:
                            pe.wait_ge(x_split, k + 1)
                        mm = split_products(nc, g.bank[b][:, :], w[b // 2].cut(c, c + P), xn[k], k == 0, k == KT - 1)
                    mm.then_inc(done, 1)

        @block.scalar
        def _(act):
            def round_weights(i, s):
                units.wait(act, i, s)
                nc.scalar.activation(w[s].hi, whole[s], ACT.Copy).then_inc(w_rounded, 1)

            norm.scalar_squares(act)
            round_weights(0, 0)
            norm.scalar_rest(act)
            for k in range(KT):
                act.wait_ge(norm.xn_ready, k + 1)
                nc.scalar.activation(xn[k].hi, g.xn[:, k, :], ACT.Copy).then_inc(x_rounded, 1)
            round_weights(0, 1)
            act.wait_ge(keep_ready, 1)
            with act.Fori(0, 3) as i:
                for b in range(4):
                    act.wait_ge(done, 4 * i + b + 1)
                    nc.scalar.activation(rec.rkv[:, bass.ds(4 * i + b, 1), :], g.bank[b][:, :], ACT.Copy,
                                         scale=rec.keep[:, bass.ds(4 * i + b, 1)]).then_inc(now_done, 1)
                    if b % 2 == 1:
                        round_weights(i + 1, b // 2)
            for b in range(4):
                act.wait_ge(done, 12 + b + 1)
                nc.scalar.activation(rec.xc[:, b, :], g.bank[b][:, :], ACT.Identity, scale=g.col("conv_w", 3 * AT + b),
                                     bias=g.col("conv_b", b)).then_inc(now_done, 1)
                if b % 2 == 1:
                    round_weights(4, b // 2)
            for b in range(4):
                act.wait_ge(done, 16 + b + 1)
                nc.scalar.activation(rec.gelu_gate[:, b, :], g.bank[b][:, :], ACT.Gelu_apprx_tanh)

        @block.gpsimd
        def _(pool):
            def rest(i, s):
                pool.wait_ge(w_rounded, 2 * i + s + 1)
                pool.sem_inc(passed, 1)
                nc.gpsimd.tensor_tensor(w[s].lo, whole[s], w[s].hi, ALU.subtract).then_inc(w_split, 1)
            with pool.Fori(0, units.n) as i:
                for s in range(2):
                    rest(i, s)

        @block.vector
        def _(dve):
            nc.vector.tensor_scalar(rec.keep[:, :], g.cols("mu_rkv", 3 * AT), -1.0, 1.0, ALU.mult, ALU.add).then_inc(keep_ready, 1)
            norm.vector(dve)
            for k in range(KT):
                dve.wait_ge(x_rounded, k + 1)
                nc.vector.tensor_tensor(xn[k].lo, g.xn[:, k, :], xn[k].hi, ALU.subtract).then_inc(x_split, 1)
            dve.sem_inc(free, 4)
            with dve.Fori(0, 3) as i:
                for b in range(4):
                    dve.wait_ge(now_done, 4 * i + b + 1)
                    here = rec.rkv[:, bass.ds(4 * i + b, 1), 1:T]
                    nc.vector.scalar_tensor_tensor(here, g.bank[b][:, 0:T - 1], g.col_at("mu_rkv", 4 * i + b), here,
                                                   ALU.mult, ALU.add).then_inc(free, 1)
            own = Own(dve, step)
            for b in range(4):
                dve.wait_ge(now_done, 12 + b + 1)
                for back in (1, 2, 3):
                    here = rec.xc[:, b, back:T]
                    tap = nc.vector.scalar_tensor_tensor(here, g.bank[b][:, 0:T - back], g.col("conv_w", (3 - back) * AT + b), here,
                                                         ALU.mult, ALU.add)
                    if back < 3:
                        own.did(tap)
                        own.wait()
                    else:
                        tap.then_inc(free, 1)


def stage_low_rank(g, rec, units, coming):
    nc = g.nc
    units.begin()
    W = 2 * P
    RANK = (HALF, HALF, P)
    START = (0, HALF, P)
    with ExitStack() as ctx:
        sem, sb = g.stage(ctx, "low_rank")
        shifted, mixed, used, low_done, low_ready, up_done, up_read = (
            sem(n) for n in ("shifted", "mixed", "used", "low_done", "low_ready", "up_done", "up_read"))
        dx = g.mix
        mixes = sb("mixes", [P, 4, T])
        low = [sb(f"low{j}", [RANK[j], T]) for j in range(3)]
        block = ctx.enter_context(nc.Block())
        small = g.ring.slots[1]
        ups = [(rec.ell, m, small[0:HALF, m * P:(m + 1) * P], low[0][:, :], ACT.Sigmoid, "w0") for m in range(AT)]
        ups += [(rec.a, m, small[0:HALF, AW + m * P:AW + (m + 1) * P], low[1][:, :], ACT.Sigmoid, "a0") for m in range(AT)]
        ups += [(rec.gate, m, small[:, 2 * AW + m * P:2 * AW + (m + 1) * P], low[2][:, :], ACT.Copy, None) for m in range(AT)]
        ups += [(rec.gate_r, m, small[:, 3 * AW + m * P:3 * AW + (m + 1) * P], rec.xc[:, m, :], ACT.Sigmoid, "b_rgate") for m in range(AT)]
        ups += [(rec.gate_i, m, small[:, 4 * AW + m * P:4 * AW + (m + 1) * P], rec.xc[:, m, :], ACT.Sigmoid, "b_igate") for m in range(AT)]

        @block.sync
        def _(sp):
            sp.wait_ge(up_done, len(ups))
            first_loads(sp, coming)

        @block.vector
        def _(dve):
            nc.vector.tensor_scalar(dx[:, :, 0:1], g.xn[:, :, 0:1], -1.0, None, ALU.mult).then_inc(shifted, 1)
            for k in range(KT):
                nc.vector.tensor_tensor(dx[:, k, 1:T], g.xn[:, k, 0:T - 1], g.xn[:, k, 1:T], ALU.subtract).then_inc(shifted, 1)
            for j in range(3):
                for k in range(KT):
                    n = j * KT + k
                    if j == 0:
                        dve.wait_ge(shifted, k + 2)
                    if n >= 4:
                        dve.wait_ge(used, n - 3)
                    nc.vector.scalar_tensor_tensor(mixes[:, n % 4, :], dx[:, k, :], g.col("mu_wag", n), g.xn[:, k, :],
                                                   ALU.mult, ALU.add).then_inc(mixed, 1)

        @block.tensor
        def _(pe):
            units.wait(pe, 0, 0)
            units.wait(pe, 0, 1)
            for j in range(3):
                for k in range(KT):
                    pe.wait_ge(mixed, j * KT + k + 1)
                    mm = nc.tensor.matmul(g.bank[j][0:RANK[j], :], g.ring.slots[0][:, k * W + START[j]:k * W + START[j] + RANK[j]],
                                          mixes[:, (j * KT + k) % 4, :], start=(k == 0), stop=(k == KT - 1))
                    mm.then_inc(used, 1)
            for n, (_, _, weights, source, _, _) in enumerate(ups):
                if n % AT == 0 and n < 3 * AT:
                    pe.wait_ge(low_ready, n // AT + 1)
                if n >= 4:
                    pe.wait_ge(up_read, n - 3)
                nc.tensor.matmul(g.bank[3 + n % 4][:, :], weights, source, start=True, stop=True).then_inc(up_done, 1)

        @block.scalar
        def _(act):
            for j, f in enumerate((ACT.Tanh, ACT.Copy, ACT.Sigmoid)):
                act.wait_ge(used, (j + 1) * KT)
                nc.scalar.activation(low[j][:, :], g.bank[j][0:RANK[j], :], f).then_inc(low_ready, 1)
            for n, (out, m, _, _, f, bias) in enumerate(ups):
                act.wait_ge(up_done, n + 1)
                more = {} if bias is None else {"bias": g.col(bias, m)}
                nc.scalar.activation(out[:, m, :], g.bank[3 + n % 4][:, :], f, **more).then_inc(up_read, 1)


def stage_rg_lru(g, rec):
    nc = g.nc
    with ExitStack() as ctx:
        sem, sb = g.stage(ctx, "rg_lru")
        lam_abs, lam_exp, rate_ready, tanh_done, root_in, root_done, input_ready, h_ready, step = (
            sem(n) for n in ("lam_abs", "lam_exp", "rate_ready", "tanh_done", "root_in", "root_done", "input_ready", "h_ready", "step"))
        small = [sb(f"small{j}", [P, AT]) for j in range(5)]
        t = rec.gate_r
        u = g.mix[:, 0:AT, :]
        d = sb("d", [P, AT, T])
        block = ctx.enter_context(nc.Block())
        lam = g.cols("lam", AT)
        all_of = lambda b: b[:, :, :].rearrange("p a b -> p (a b)")

        @block.scalar
        def _(act):
            act.wait_ge(lam_abs, 1)
            nc.scalar.activation(small[0][:, :], small[0][:, :], ACT.Exp, scale=-1.0).then_inc(lam_exp, 1)
            act.wait_ge(rate_ready, 1)
            for m in range(AT):
                nc.scalar.activation(t[:, m, :], rec.gate_r[:, m, :], ACT.Tanh, scale=small[4][:, m:m + 1]).then_inc(tanh_done, 1)
            act.wait_ge(root_in, 1)
            nc.scalar.activation(all_of(d), all_of(d), ACT.Sqrt).then_inc(root_done, 1)

        @block.gpsimd
        def _(pool):
            nc.gpsimd.tensor_tensor(all_of(u), all_of(rec.gate_i), all_of(rec.xc), ALU.mult).then_inc(input_ready, 1)

        @block.vector
        def _(dve):
            own = Own(dve, step)
            nc.vector.scalar_tensor_tensor(small[0][:, :], lam, -1.0, lam, ALU.mult, ALU.max).then_inc(lam_abs, 1)
            dve.wait_ge(lam_exp, 1)
            log1p_half(dve, own, nc, *(s[:, :] for s in small[0:4]))
            own.did(nc.vector.tensor_scalar(small[1][:, :], lam, 0.0, -4.0, ALU.min, ALU.mult))
            own.wait()
            nc.vector.scalar_tensor_tensor(small[4][:, :], small[3][:, :], 8.0, small[1][:, :], ALU.mult, ALU.add).then_inc(rate_ready, 1)
            dve.wait_ge(tanh_done, AT)
            own.did(nc.vector.tensor_scalar(all_of(d), all_of(t), 1.0, None, ALU.add))
            own.wait()
            own.did(nc.vector.reciprocal(all_of(d), all_of(d)))
            own.wait()
            own.did(nc.vector.scalar_tensor_tensor(all_of(d), all_of(t), 2.0, all_of(d), ALU.mult, ALU.mult))
            own.wait()
            own.did(nc.vector.tensor_scalar(all_of(t), all_of(d), -1.0, 1.0, ALU.mult, ALU.add))
            own.wait()
            nc.vector.scalar_tensor_tensor(all_of(d), all_of(t), 1.0, all_of(d), ALU.add, ALU.mult).then_inc(root_in, 1)
            dve.wait_ge(root_done, 1)
            dve.wait_ge(input_ready, 1)
            own.did(nc.vector.tensor_tensor(all_of(u), all_of(u), all_of(d), ALU.mult))
            own.wait()
            for m in range(AT):
                own.did(nc.vector.tensor_tensor_scan(d[:, m, :], t[:, m, :], u[:, m, :], 0.0, ALU.mult, ALU.add))
            own.wait()
            nc.vector.tensor_tensor(g.mix[:, AT:2 * AT, :].rearrange("p a b -> p (a b)"), all_of(d), all_of(rec.gelu_gate),
                                    ALU.mult).then_inc(h_ready, 1)


class Rwkv:

    def __init__(self, rec):
        self.nkk = rec.xc
        self.b = rec.gelu_gate
        self.L = rec.gate_r
        self.y = rec.gate_i


def stage_rwkv_prepare(g, rec, rw):
    nc = g.nc
    with ExitStack() as ctx:
        sem, sb = g.stage(ctx, "prepare")
        kk_ready, squared, summed, norm_ready, step, rates_ready = (
            sem(n) for n in ("kk_ready", "squared", "summed", "norm_ready", "step", "rates_ready"))
        kk = rw.nkk
        sq, one = sb("sq", [P, AT, T]), sb("one", [P, T])
        inv = sq
        block = ctx.enter_context(nc.Block())

        @block.vector
        def _(dve):
            own = Own(dve, step)
            for m in range(AT):
                nc.vector.tensor_scalar(kk[:, m, :], rec.k[:, m, :], g.col("k_k", m), None, ALU.mult).then_inc(kk_ready, 1)
            own.did(nc.vector.memset(one[:, :], 1.0))
            own.wait()
            own.did(nc.vector.memset(one[:, 0:T:CHUNK], 0.0))
            own.wait()
            decay = -math.exp(-0.5)
            for m in range(AT):
                own.did(nc.vector.tensor_scalar(rec.ell[:, m, :], rec.ell[:, m, :], decay, None, ALU.mult))
            own.wait()
            for m in range(AT):
                own.did(nc.vector.tensor_tensor_scan(rw.L[:, m, :], one[:, :], rec.ell[:, m, :], 0.0, ALU.mult, ALU.add))
            dve.wait_ge(rates_ready, AT)
            for m in range(AT):
                own.did(nc.vector.scalar_tensor_tensor(rec.k[:, m, :], rw.y[:, m, :], 1.0, rec.k[:, m, :], ALU.add, ALU.mult))
            for m in range(AT):
                dve.wait_ge(norm_ready, m + 1)
                own.did(nc.vector.reciprocal(inv[:, m, :], inv[:, m, :]))
                own.wait()
                own.did(nc.vector.scalar_tensor_tensor(rw.nkk[:, m, :], kk[:, m, :], -1.0, inv[:, m, :], ALU.mult, ALU.mult))
                own.wait()
                own.did(nc.vector.scalar_tensor_tensor(rw.b[:, m, :], rw.nkk[:, m, :], -1.0, rec.a[:, m, :], ALU.mult, ALU.mult))

        @block.gpsimd
        def _(pool):
            pool.wait_ge(kk_ready, AT)
            for m in range(AT):
                nc.gpsimd.tensor_scalar(rw.y[:, m, :], rec.a[:, m, :], -1.0, g.col("k_a", m), ALU.add, ALU.mult).then_inc(rates_ready, 1)

        @block.scalar
        def _(act):
            for m in range(AT):
                act.wait_ge(kk_ready, m + 1)
                nc.scalar.activation(sq[:, m, :], kk[:, m, :], ACT.Square).then_inc(squared, 1)
            for m in range(AT):
                act.wait_ge(summed, m + 1)
                nc.scalar.activation(inv[:, m, :], g.bank[m][:, :], ACT.Sqrt, bias=g.eps[:, 1:2]).then_inc(norm_ready, 1)

        @block.tensor
        def _(pe):
            for m in range(AT):
                pe.wait_ge(squared, m + 1)
                nc.tensor.matmul(g.bank[m][:, :], g.head_sum[:, :], sq[:, m, :], start=True, stop=True).then_inc(summed, 1)


def stage_rwkv_chunks(g, rec, rw):
    nc = g.nc
    C, PAIRS = CHUNK, AT
    LEVELS = int(math.log2(C))
    UNIT = PAIRS * C
    TWO = range(2)
    ROUNDS = NCHUNK // 2
    both = [slice(h * HALF, (h + 1) * HALF) for h in range(2)]
    with ExitStack() as ctx:
        sem, sb = g.stage(ctx, "chunks")
        S = [sb(f"S{p}", [P, PAIRS, C]) for p in TWO]
        flat = lambda t: t[:, :, :].rearrange("p a n -> p (a n)")
        places = [slot[:, :] for slot in g.ring.slots] + [flat(g.memn), flat(g.square), g.std[:, :], g.rstd[:, :],
                                                          sb("own", [P, 6 * UNIT])[:, :]]

        class Chunk:
            pass

        def carve(*shape):
            n = int(np.prod(shape))
            i = next(i for i, place in enumerate(places) if place.shape[1] >= n)
            here, places[i] = places[i][:, 0:n], places[i][:, n:]
            if len(shape) == 2:
                return here.rearrange("p (a n) -> p a n", n=C)
            return here.rearrange("p (a b n) -> p a b n", b=shape[1], n=C)

        chunks = []
        for p in TWO:
            w = Chunk()
            w.al = carve(LEVELS, PAIRS, C)
            w.ar = carve(PAIRS, 2, C)
            w.Mb, w.Mk = carve(PAIRS, 2, C), carve(PAIRS, 2, C)
            w.bk = carve(2, PAIRS, C)
            w.dl, w.en, w.ep, w.epv = (carve(PAIRS, C) for _ in range(4))
            w.bt, w.kt, w.vt = (carve(PAIRS, C) for _ in range(3))
            w.vs = carve(PAIRS, C)
            w.M, w.MT, w.Wt = (carve(PAIRS, C) for _ in range(3))
            w.rhs, w.U = (carve(PAIRS, C) for _ in range(2))
            w.w_bank, w.z_bank, w.zt_bank = ((4, 5, 6), (0, 1, 2))[p]
            w.diff_ready, w.exps_ready, w.scaled, w.v_copied, w.pairs_done, w.pairs_read, w.tokens_read = (
                sem(f"{n}{p}") for n in ("diff_ready", "exps_ready", "scaled", "v_copied", "pairs_done", "pairs_read", "tokens_read"))
            w.level_ready, w.w_done, w.w_ready, w.z_done, w.zt_done, w.inverse_step = (
                sem(f"{n}{p}") for n in ("level_ready", "w_done", "w_ready", "z_done", "zt_done", "inverse_step"))
            w.rhs_done, w.rhs_ready, w.u_done, w.u_ready, w.y_done, w.y_ready, w.s_done = (
                sem(f"{n}{p}") for n in ("rhs_done", "rhs_ready", "u_done", "u_ready", "y_done", "y_ready", "s_done"))
            chunks.append(w)
        s_added, s_ready, passed = sem("s_added"), sem("s_ready"), sem("passed")
        block = ctx.enter_context(nc.Block())
        eye = g.cols("eye", C)
        tri = g.cols("tri", 2 * C).rearrange("p (a b) -> p a b", b=C)
        level = lambda l: g.cols("levels", LEVELS * C)[:, l * C:(l + 1) * C]
        spread = lambda m: m.unsqueeze(1).broadcast_to([P, PAIRS, *m.shape[1:]])
        wide = lambda b: g.bank[b][:, 0:UNIT].rearrange("p (a b) -> p a b", b=C)
        now = lambda a, i, p: a[:, :, bass.ds(i * 2 * C + p * C, C)]
        steps = 2 * LEVELS - 1

        @block.scalar
        def _(act):
            with act.Fori(0, ROUNDS) as i:
                for p, w in enumerate(chunks):
                    act.wait_ge(s_ready, 2 * i + p)
                    nc.scalar.activation(w.en, now(rw.L, i, p), ACT.Exp, scale=-1.0).then_inc(w.exps_ready, 1)
                    nc.scalar.activation(w.ep, now(rw.L, i, p), ACT.Exp).then_inc(w.exps_ready, 1)
                    act.wait_ge(w.diff_ready, i + 1)
                    nc.scalar.activation(w.epv, w.dl, ACT.Exp).then_inc(w.exps_ready, 1)
                for p, w in enumerate(chunks):
                    act.wait_ge(w.pairs_done, 4 * i + 3)
                    nc.scalar.activation(w.bk.rearrange("p a b n -> p (a b n)"), g.bank[(2, 7)[p]][:, :], ACT.Copy).then_inc(w.tokens_read, 1)
                    act.wait_ge(w.pairs_done, 4 * i + 4)
                    nc.scalar.activation(w.vs, wide(3), ACT.Copy).then_inc(w.tokens_read, 1)
                for l in range(1, LEVELS):
                    for w in chunks:
                        act.wait_ge(w.w_done, LEVELS * i + l + 1)
                        nc.scalar.activation(w.Wt, wide(w.w_bank), ACT.Copy).then_inc(w.w_ready, 1)
                for p, w in enumerate(chunks):
                    act.wait_ge(w.rhs_done, i + 1)
                    nc.scalar.activation(w.rhs, wide(7), ACT.Copy).then_inc(w.rhs_ready, 1)
                    act.wait_ge(w.u_done, i + 1)
                    nc.scalar.activation(w.U, wide(4), ACT.Copy).then_inc(w.u_ready, 1)
                    act.wait_ge(w.y_done, i + 2)
                    nc.scalar.activation(now(rw.y, i, p), wide((5, 3)[p]), ACT.Copy).then_inc(w.y_ready, 1)

        @block.gpsimd
        def _(pool):
            with pool.Fori(0, ROUNDS) as i:
                for p, w in enumerate(chunks):
                    pool.wait_ge(s_ready, 2 * i + p)
                    nc.gpsimd.tensor_copy(w.vt, now(rec.v, i, p)).then_inc(w.v_copied, 1)
                for w in chunks:
                    pool.wait_ge(w.pairs_read, 2 * i + 1)
                    nc.gpsimd.tensor_tensor(w.al[:, 0, :, :], w.Mb[:, :, 0, :], spread(level(0)), ALU.mult).then_inc(w.level_ready, 1)
                for l in range(1, LEVELS):
                    for w in chunks:
                        nc.gpsimd.tensor_tensor(w.al[:, l, :, :], w.Mb[:, :, 0, :], spread(level(l)), ALU.mult).then_inc(w.level_ready, 1)

        @block.vector
        def _(dve):
            nc.vector.memset(S[0][:, :, :], 0.0).then_inc(s_added, 1)
            dve.sem_inc(s_ready, 1)
            for w in chunks:
                dve.sem_inc(w.y_done, 1)
                dve.sem_inc(w.y_ready, 1)
            with dve.Fori(0, ROUNDS) as i:
                for p, w in enumerate(chunks):
                    dve.wait_ge(s_ready, 2 * i + p)
                    nc.vector.tensor_tensor(w.dl, now(rw.L, i, p), now(rec.ell, i, p), ALU.subtract).then_inc(w.diff_ready, 1)
                for p, w in enumerate(chunks):
                    dve.wait_ge(w.exps_ready, 3 * i + 2)
                    dve.wait_ge(w.y_done, i + 1)
                    nc.vector.tensor_tensor(w.bt, now(rw.b, i, p), w.en, ALU.mult).then_inc(w.scaled, 1)
                    nc.vector.tensor_tensor(w.kt, now(rec.k, i, p), w.en, ALU.mult).then_inc(w.scaled, 1)
                    nc.vector.tensor_tensor(w.ar[:, :, 1, :], now(rec.r, i, p), w.ep, ALU.mult).then_inc(w.scaled, 1)
                    dve.wait_ge(w.exps_ready, 3 * i + 3)
                    nc.vector.tensor_tensor(w.ar[:, :, 0, :], now(rw.nkk, i, p), w.epv, ALU.mult).then_inc(w.scaled, 1)
                for w in chunks:
                    for j, m in enumerate((w.Mb, w.Mk)):
                        dve.wait_ge(w.pairs_done, 4 * i + j + 1)
                        nc.vector.tensor_tensor(m, g.bank[j][:, :].rearrange("p (a b n) -> p a b n", b=2, n=C),
                                                spread(tri), ALU.mult).then_inc(w.pairs_read, 1)
                for w in chunks:
                    dve.wait_ge(w.level_ready, LEVELS * i + 1)
                    nc.vector.tensor_tensor(w.MT, w.al[:, 0, :, :], spread(eye), ALU.add).then_inc(w.inverse_step, 1)
                    dve.wait_ge(w.w_done, LEVELS * i + 1)
                    nc.vector.tensor_tensor(w.M, wide(w.w_bank), spread(eye), ALU.add).then_inc(w.inverse_step, 1)
                for l in range(1, LEVELS):
                    for w in chunks:
                        if l < LEVELS - 1:
                            dve.wait_ge(w.z_done, (LEVELS - 2) * i + l)
                            dve.wait_ge(w.inverse_step, steps * i + 2 * l)
                            nc.vector.tensor_tensor(w.M, wide(w.z_bank), w.M, ALU.add).then_inc(w.inverse_step, 1)
                        dve.wait_ge(w.zt_done, (LEVELS - 1) * i + l)
                        nc.vector.tensor_tensor(w.MT, wide(w.zt_bank), w.MT, ALU.add).then_inc(w.inverse_step, 1)
                for p, w in enumerate(chunks):
                    dve.wait_ge(w.s_done, i + 1)
                    dve.wait_ge(s_added, 2 * i + p + 1)
                    after = S[1 - p][:, :, :]
                    nc.vector.tensor_tensor(after, wide(6), S[p][:, :, :], ALU.add).then_inc(s_added, 1)
                    dve.wait_ge(s_added, 2 * i + p + 2)
                    nc.vector.tensor_tensor(after, after, w.ep[:, :, C - 1:C].broadcast_to([P, PAIRS, C]), ALU.mult).then_inc(s_ready, 1)

        @block.tensor
        def _(pe):
            def product(bank, left, right, width=C):
                for n in range(PAIRS):
                    for h in both:
                        mm = nc.tensor.matmul(g.bank[bank][h, n * width:(n + 1) * width], left(h, n), right(h, n), start=True, stop=True)
                return mm

            with pe.Fori(0, ROUNDS) as i:
                for w in chunks:
                    pe.wait_ge(w.y_ready, i + 1)
                for p, w in enumerate(chunks):
                    pe.wait_ge(w.scaled, 4 * i + 4)
                    pe.wait_ge(w.v_copied, i + 1)
                    pe.wait_ge(s_added, 2 * i + 1)
                    pe.sem_inc(passed, 1)
                    for j, left in enumerate((w.bt, w.kt)):
                        if p == 1:
                            pe.wait_ge(chunks[0].pairs_read, 2 * i + j + 1)
                            pe.sem_inc(passed, 1)
                        product(j, lambda h, n: left[h, n, :], lambda h, n: w.ar[h, n, :, :].rearrange("p a b -> p (a b)"), 2 * C)\
                            .then_inc(w.pairs_done, 1)
                    for j, src in enumerate((w.bt, w.kt)):
                        for n in range(PAIRS):
                            for h in both:
                                mm = nc.tensor.matmul(g.bank[(2, 7)[p]][h, (j * PAIRS + n) * C:(j * PAIRS + n + 1) * C], src[h, n, :],
                                                      g.ident[h, h], start=True, stop=True)
                    mm.then_inc(w.pairs_done, 1)
                    if p == 1:
                        pe.wait_ge(chunks[0].tokens_read, 2 * i + 2)
                        pe.sem_inc(passed, 1)
                    product(3, lambda h, n: w.vt[h, n, :], lambda h, n: g.ident[h, h]).then_inc(w.pairs_done, 1)
                for p, w in enumerate(chunks):
                    pe.wait_ge(w.level_ready, LEVELS * i + 1)
                    if p == 1:
                        pe.wait_ge(w.pairs_read, 2 * i + 2)
                        pe.wait_ge(w.tokens_read, 2 * i + 2)
                    pe.sem_inc(passed, 1)
                    product(w.w_bank, lambda h, n: w.al[h, 0, n, :], lambda h, n: eye[h, :]).then_inc(w.w_done, 1)
                for l in range(1, LEVELS):
                    for w in chunks:
                        pe.wait_ge(w.level_ready, LEVELS * i + l + 1)
                        pe.wait_ge(w.inverse_step, steps * i + 2 * l)
                        pe.sem_inc(passed, 1)
                        product(w.w_bank, lambda h, n: w.al[h, l, n, :], lambda h, n: w.M[h, n, :]).then_inc(w.w_done, 1)
                    for w in chunks:
                        pe.wait_ge(w.w_ready, (LEVELS - 1) * i + l)
                        pe.sem_inc(passed, 1)
                        if l < LEVELS - 1:
                            product(w.z_bank, lambda h, n: w.MT[h, n, :], lambda h, n: w.Wt[h, n, :]).then_inc(w.z_done, 1)
                        product(w.zt_bank, lambda h, n: w.Wt[h, n, :], lambda h, n: w.MT[h, n, :]).then_inc(w.zt_done, 1)
                for p, w in enumerate(chunks):
                    pe.wait_ge(w.tokens_read, 2 * i + 2)
                    pe.wait_ge(w.pairs_read, 2 * i + 2)
                    pe.wait_ge(s_ready, 2 * i + p + 1)
                    pe.sem_inc(passed, 1)
                    for n in range(PAIRS):
                        for h in both:
                            out = g.bank[7][h, n * C:(n + 1) * C]
                            nc.tensor.matmul(out, w.Mk[h, n, 0, :], w.vs[h, n, :], start=True, stop=False)
                            mm = nc.tensor.matmul(out, w.ar[h, n, 0, :], S[p][h, n, :], start=False, stop=True)
                    mm.then_inc(w.rhs_done, 1)
                    pe.wait_ge(w.rhs_ready, i + 1)
                    pe.wait_ge(w.inverse_step, steps * (i + 1))
                    pe.sem_inc(passed, 1)
                    product(4, lambda h, n: w.MT[h, n, :], lambda h, n: w.rhs[h, n, :]).then_inc(w.u_done, 1)
                    pe.wait_ge(w.u_ready, i + 1)
                    pe.sem_inc(passed, 1)
                    for n in range(PAIRS):
                        for h in both:
                            out = g.bank[6][h, n * C:(n + 1) * C]
                            nc.tensor.matmul(out, w.bk[h, 0, n, :], w.U[h, n, :], start=True, stop=False)
                            mm = nc.tensor.matmul(out, w.bk[h, 1, n, :], w.vs[h, n, :], start=False, stop=True)
                    mm.then_inc(w.s_done, 1)
                    for n in range(PAIRS):
                        for h in both:
                            out = g.bank[(5, 3)[p]][h, n * C:(n + 1) * C]
                            nc.tensor.matmul(out, S[p][h, n, :], w.ar[h, n, 1, :], start=True, stop=False)
                            nc.tensor.matmul(out, w.U[h, n, :], w.Mb[h, n, 1, :], start=False, stop=False)
                            mm = nc.tensor.matmul(out, w.vs[h, n, :], w.Mk[h, n, 1, :], start=False, stop=True)
                    mm.then_inc(w.y_done, 1)


def stage_rwkv_finish(g, rec, rw, coming):
    nc = g.nc
    with ExitStack() as ctx:
        sem, sb = g.stage(ctx, "finish")
        rk_ready, bonus_done, mean_done, centred, squared, var_done, std_ready, step = (
            sem(n) for n in ("rk_ready", "bonus_done", "mean_done", "centred", "squared", "var_done", "std_ready", "step"))
        rk, sq, std = rw.nkk, rw.b, rw.L
        block = ctx.enter_context(nc.Block())

        @block.sync
        def _(sp):
            first_loads(sp, coming)

        @block.vector
        def _(dve):
            own = Own(dve, step)
            for m in range(AT):
                nc.vector.scalar_tensor_tensor(rk[:, m, :], rec.r[:, m, :], g.col("r_k", m), rec.k[:, m, :],
                                               ALU.mult, ALU.mult).then_inc(rk_ready, 1)
            for m in range(AT):
                dve.wait_ge(mean_done, m + 1)
                nc.vector.scalar_tensor_tensor(rw.y[:, m, :], g.bank[m][:, :], -1.0 / HALF, rw.y[:, m, :], ALU.mult, ALU.add)\
                  .then_inc(centred, 1)
            dve.wait_ge(bonus_done, AT)
            for m in range(AT):
                own.did(nc.vector.tensor_tensor(rk[:, m, :], g.bank[4 + m][:, :], rec.v[:, m, :], ALU.mult))
            for m in range(AT):
                dve.wait_ge(std_ready, m + 1)
                own.did(nc.vector.reciprocal(std[:, m, :], std[:, m, :]))
                own.wait()
                own.did(nc.vector.scalar_tensor_tensor(rw.y[:, m, :], rw.y[:, m, :], g.col("lnx_g", m), std[:, m, :], ALU.mult, ALU.mult))
                own.wait()
                own.did(nc.vector.scalar_tensor_tensor(rw.y[:, m, :], rw.y[:, m, :], g.col("lnx_b", m), rk[:, m, :], ALU.add, ALU.add))
                own.wait()
                own.did(nc.vector.tensor_tensor(g.mix[:, m, :], rw.y[:, m, :], rec.gate[:, m, :], ALU.mult))

        @block.scalar
        def _(act):
            for m in range(AT):
                act.wait_ge(centred, m + 1)
                nc.scalar.activation(sq[:, m, :], rw.y[:, m, :], ACT.Square).then_inc(squared, 1)
            for m in range(AT):
                act.wait_ge(var_done, m + 1)
                nc.scalar.activation(std[:, m, :], g.bank[m][:, :], ACT.Sqrt, scale=1.0 / HALF, bias=g.eps[:, 2:3]).then_inc(std_ready, 1)

        @block.tensor
        def _(pe):
            for m in range(AT):
                nc.tensor.matmul(g.bank[m][:, :], g.head_sum[:, :], rw.y[:, m, :], start=True, stop=True).then_inc(mean_done, 1)
            for m in range(AT):
                pe.wait_ge(rk_ready, m + 1)
                nc.tensor.matmul(g.bank[4 + m][:, :], g.head_sum[:, :], rk[:, m, :], start=True, stop=True).then_inc(bonus_done, 1)
            for m in range(AT):
                pe.wait_ge(squared, m + 1)
                nc.tensor.matmul(g.bank[m][:, :], g.head_sum[:, :], sq[:, m, :], start=True, stop=True).then_inc(var_done, 1)


def stage_merge(g, units, coming, merged):
    nc = g.nc
    units.begin()
    W = 2 * P
    with ExitStack() as ctx:
        sem, sb = g.stage(ctx, "merge")
        done, gated, read, merged_done, step = (sem(n) for n in ("product_done", "gated", "read", "merged_done", "step"))
        sig = sb("sig", [P, 4, T])
        x_rounded, x_split, passed = sem("x_rounded"), sem("x_split"), sem("passed")
        w_rounded, w_split = [sem(f"w_rounded{s}") for s in range(3)], [sem(f"w_split{s}") for s in range(3)]
        xn_hi, mix_hi = sb("xn_hi", [P, KT, T], F32R), sb("mix_hi", [P, KT, T], F32R)
        inputs = [(g.xn[:, k, :], Split(xn_hi[:, k, :], g.xn_r[:, k, :])) for k in range(KT)]
        inputs += [(g.mix[:, k, :], Split(mix_hi[:, k, :], g.mix_r[:, k, :])) for k in range(KT)]
        whole, whole_r = zip(*(units.in_place(s, KT * W) for s in range(3)))
        w = [Split(sb(f"w_hi{s}", [P, KT * W], F32R)[:, :], whole_r[s]) for s in range(3)]
        last = units.n - 1
        block = ctx.enter_context(nc.Block())

        @block.sync
        def _(sp):
            with sp.Fori(1, units.n) as i:
                for s, last in enumerate((2, 4, 8)):
                    sp.wait_ge(done, 8 * i - 8 + last)
                    units.load(sp, i, s)
            sp.wait_ge(done, 8 * units.n)
            first_loads(sp, coming)

        @block.tensor
        def _(pe):
            pe.sem_inc(gated, 1)
            pe.sem_inc(read, 1)
            with pe.Fori(0, units.n) as i:
                pe.wait_ge(gated, 4 * i + 1)
                for b in range(4):
                    if b % 2 == 0:
                        pe.wait_ge(w_split[b // 2], i + 1)
                    for k in range(KT):
                        c = k * W + b % 2 * P
                        if b == 0:
                            pe.wait_ge(x_split, k + 1)
                        mm = split_products(nc, g.bank[b][:, :], w[b // 2].cut(c, c + P), inputs[k][1], k == 0, k == KT - 1)
                    mm.then_inc(done, 1)
                pe.wait_ge(w_split[2], i + 1)
                pe.wait_ge(read, 4 * i + 1)
                for b in range(4):
                    for k in range(AT):
                        j = b // 2 * AT + k
                        c = j * W + b % 2 * P
                        if b % 2 == 0:
                            pe.wait_ge(x_split, KT + j + 1)
                        mm = split_products(nc, g.bank[4 + b][:, :], w[2].cut(c, c + P), inputs[KT + j][1], k == 0, k == AT - 1)
                    mm.then_inc(done, 1)

        @block.scalar
        def _(act):
            act.sem_inc(merged_done, 1)

            def round_weights(i, s):
                units.wait(act, i, s)
                nc.scalar.activation(w[s].hi, whole[s], ACT.Copy).then_inc(w_rounded[s], 1)

            def step(i, later):
                act.wait_ge(merged_done, 2 * i + 1)
                for b in range(4):
                    act.wait_ge(done, 8 * i + b + 1)
                    nc.scalar.activation(sig[:, b, :], g.bank[b][:, :], ACT.Sigmoid).then_inc(gated, 1)
                    if b == 1:
                        round_weights(i, 2)
                    if b % 2 == 1 and later:
                        round_weights(i + 1, b // 2)
            round_weights(0, 0)
            for j, (x, halves) in enumerate(inputs):
                nc.scalar.activation(halves.hi, x, ACT.Copy).then_inc(x_rounded, 1)
                if j == KT // 2:
                    round_weights(0, 1)
            with act.Fori(0, last) as i:
                step(i, True)
            step(last, False)

        @block.gpsimd
        def _(pool):
            def rest(i, s):
                pool.wait_ge(w_rounded[s], i + 1)
                pool.sem_inc(passed, 1)
                nc.gpsimd.tensor_tensor(w[s].lo, whole[s], w[s].hi, ALU.subtract).then_inc(w_split[s], 1)
            rest(0, 0)
            rest(0, 1)
            with pool.Fori(1, units.n) as i:
                rest(i - 1, 2)
                rest(i, 0)
                rest(i, 1)
            rest(last, 2)

        @block.vector
        def _(dve):
            for j, (x, halves) in enumerate(inputs):
                dve.wait_ge(x_rounded, j + 1)
                nc.vector.tensor_tensor(halves.lo, x, halves.hi, ALU.subtract).then_inc(x_split, 1)
            with dve.Fori(0, units.n) as i:
                for b in range(4):
                    dve.wait_ge(done, 8 * i + 4 + b + 1)
                    dve.wait_ge(gated, 4 * i + b + 2)
                    nc.vector.tensor_tensor(sig[:, b, :], g.bank[4 + b][:, :], sig[:, b, :], ALU.mult).then_inc(read, 1)
                    if b >= 2:
                        dve.wait_ge(read, 4 * i + b + 2)
                        nc.vector.tensor_tensor(merged[:, bass.ds(2 * i + b - 2, 1), :], sig[:, b - 2, :], sig[:, b, :], ALU.add)\
                          .then_inc(merged_done, 1)


class Experts:

    def __init__(self, nc, ctx, ring):
        sb = lambda name, shape, dt=F32: ctx.enter_context(nc.sbuf_tensor(f"moe_{name}", shape, dt))
        dram = lambda name, rows: nc.dram_tensor(name, [rows, D], F32, kind="Internal").ap()
        self.weight = sb("weight", [P, 2, TT])
        self.pair = sb("pair", [P, MOE_TILES], I32)
        self.token = sb("token", [P, MOE_TILES], I32)
        self.more_expert = sb("more_expert", [1, MORE], I32)
        self.more_tiles = sb("more_tiles", [1, 1], I32)
        self.rows = dram("moe_rows", T)
        self.pair_rows = dram("moe_pair_rows", 2 * T)
        extra = 2 * IN_FLIGHT - SLOTS
        slots, slots_r = zip(*(two_names(nc, ctx, f"moe_weights{s}", [P, SLOT]) for s in range(extra)))
        self.ring = WeightRing(ring.slots + list(slots), ring.slots_r + list(slots_r),
                               ring.ready + [ctx.enter_context(nc.semaphore(f"expert_ready{s}")) for s in range(extra)])
        self.ring.loads = ring.loads + [0] * extra


def stage_router(g, moe, units):
    nc = g.nc
    LOGITS = GROUPS + EXPERTS
    with ExitStack() as ctx:
        sem, sb = g.stage(ctx, "router")
        norm = Norm(g, ctx, g.gains[:, 1, :], g.mod[:, 24:24 + KT])
        turned, row_read, stored, logits_done, step, to_exp, exp_done = (
            sem(n) for n in ("turned", "row_read", "stored", "logits_done", "step", "to_exp", "exp_done"))
        chosen, counted, sorted_, placed, table_done = (sem(n) for n in ("chosen", "counted", "sorted", "placed", "table_done"))
        rows = g.mix[:, :, :].rearrange("p (t h) n -> p t (h n)", h=2)
        logits = sb("logits", [P, TT, LOGITS])
        top, first, total = sb("top", [P, TT]), sb("first", [P, TT]), sb("total", [P, TT])
        exps = sb("exps", [P, TT, GROUPS])
        group, group_weight = sb("group", [P, TT, GROUPS]), sb("group_weight", [P, TT])
        parts = sb("parts", [P, TT, GROUPS, PER_GROUP])
        inside = sb("inside", [P, TT, PER_GROUP])
        best = sb("best", [P, 2, TT])
        here = sb("here", [P, 2, TT, PER_GROUP])
        second = sb("second", [P, TT])
        hot = sb("hot", [P, 2, TT, EXPERTS])
        both = sb("both", [P, TT, EXPERTS])
        earlier = sb("earlier", [P, P])
        rank, count = sb("rank", [P, TT, EXPERTS]), sb("count", [P, EXPERTS])
        more, more_end, more_start = sb("more", [P, EXPERTS]), sb("more_end", [P, EXPERTS]), sb("more_start", [P, EXPERTS])
        picked = sb("picked", [P, 2, TT, EXPERTS])
        slot, expert, start, past = (sb(n, [P, 2, TT]) for n in ("slot", "expert", "start", "past"))
        by_slot = sb("by_slot", [P, 2 * TT, P])
        by_tile = sb("by_tile", [P, 2 * TT, MOE_TILES])
        place = sb("place", [P, MOE_TILES])
        empty = sb("empty", [P, MOE_TILES])
        ended = sb("ended", [1, MORE, EXPERTS])
        which = sb("which", [1, MORE])
        block = ctx.enter_context(nc.Block())
        iota = lambda n, rows=P: g.cols("iota", n, rows)
        w_router = g.cols("w_router", KT * LOGITS)

        @block.sync
        def _(sp):
            for s in range(units.per):
                units.load(sp, 0, s)
            for t in range(TT):
                sp.wait_ge(row_read, 2 * t + 2)
                sp.dma_start(moe.rows[t * P:(t + 1) * P, :], rows[:, t, :]).then_inc(stored, 16)
            sp.wait_ge(stored, 16 * TT)

        @block.tensor
        def _(pe):
            norm.tensor(pe)
            norm.wait(pe)
            for t in range(TT):
                for k in range(KT):
                    mm = nc.tensor.matmul(g.bank[0][:, t * LOGITS:(t + 1) * LOGITS], g.xn[:, k, t * P:(t + 1) * P],
                                          w_router[:, k * LOGITS:(k + 1) * LOGITS], start=(k == 0), stop=(k == KT - 1))
            mm.then_inc(logits_done, 1)
            for t in range(TT):
                for h in range(2):
                    n = 2 * t + h
                    if n >= 4:
                        pe.wait_ge(row_read, n - 3)
                    for j in range(TT):
                        mm = nc.tensor.matmul(g.bank[2 + n % 4][:, j * P:(j + 1) * P], g.xn[:, h * 4 + j, t * P:(t + 1) * P],
                                              g.ident[:, :], start=True, stop=True)
                    mm.then_inc(turned, 1)
            pe.wait_ge(chosen, 1)
            for t in range(TT):
                for s in range(t + 1):
                    nc.tensor.matmul(g.bank[1][:, t * EXPERTS:(t + 1) * EXPERTS], (earlier if s == t else g.ones)[:, :],
                                     both[:, s, :], start=(s == 0), stop=(s == t))
            for t in range(TT):
                mm = nc.tensor.matmul(g.bank[1][:, TT * EXPERTS:(TT + 1) * EXPERTS], g.ones[:, :], both[:, t, :],
                                      start=(t == 0), stop=(t == TT - 1))
            mm.then_inc(counted, 1)
            pe.wait_ge(placed, 1)
            for n in range(2 * TT):
                mm = nc.tensor.matmul(g.bank[6][:, 0:MOE_TILES], by_slot[:, n, :], by_tile[:, n, :],
                                      start=(n == 0), stop=(n == 2 * TT - 1))
            mm.then_inc(table_done, 1)

        @block.scalar
        def _(act):
            norm.scalar(act)
            for n in range(2 * TT):
                act.wait_ge(turned, n + 1)
                nc.scalar.activation(rows[:, n // 2, n % 2 * T:(n % 2 + 1) * T], g.bank[2 + n % 4][:, :], ACT.Copy).then_inc(row_read, 1)
            act.wait_ge(to_exp, 1)
            nc.scalar.activation(exps[:, :, :], exps[:, :, :], ACT.Exp).then_inc(exp_done, 1)
            act.wait_ge(to_exp, 2)
            nc.scalar.activation(second[:, :], second[:, :], ACT.Exp).then_inc(exp_done, 1)

        @block.vector
        def _(dve):
            norm.vector(dve)
            own = Own(dve, step)
            v = nc.vector

            def do(ins):
                own.did(ins)
                own.wait()

            def last(a, n):
                return a.unsqueeze(len(a.shape)).broadcast_to([*a.shape, n])

            def one_hot_max(values, top, out, n):
                do(v.tensor_reduce(top, values, AX.X, ALU.max))
                do(v.tensor_tensor(out, values, last(top, n), ALU.is_ge))
                do(v.tensor_scalar(out, out, -float(n), float(n), ALU.mult, ALU.add))
                do(v.tensor_tensor(out, out, iota(n).unsqueeze(1).broadcast_to([P, TT, n]), ALU.add))
                do(v.tensor_reduce(first[:, :], out, AX.X, ALU.min))
                do(v.tensor_tensor(out, iota(n).unsqueeze(1).broadcast_to([P, TT, n]), last(first[:, :], n), ALU.is_equal))

            do(v.scalar_tensor_tensor(earlier[:, :], g.causal_T[:, :], 0.0, g.ident[:, :], ALU.is_equal, ALU.subtract))
            dve.wait_ge(logits_done, 1)
            do(v.tensor_tensor(logits[:, :, :], g.bank[0][:, 0:TT * LOGITS].rearrange("p (t n) -> p t n", n=LOGITS),
                               g.cols("b_router", LOGITS).unsqueeze(1).broadcast_to([P, TT, LOGITS]), ALU.add))
            groups = logits[:, :, 0:GROUPS]
            one_hot_max(groups, top[:, :], group[:, :, :], GROUPS)
            v.tensor_tensor(exps[:, :, :], groups, last(top[:, :], GROUPS), ALU.subtract).then_inc(to_exp, 1)
            do(v.tensor_tensor(parts[:, :, :, :], logits[:, :, GROUPS:LOGITS].rearrange("p t (g e) -> p t g e", e=PER_GROUP),
                               last(group[:, :, :], PER_GROUP), ALU.mult))
            do(v.tensor_reduce(inside[:, :, :], parts[:, :, :, :].rearrange("p t g e -> p t e g"), AX.X, ALU.add))
            one_hot_max(inside[:, :, :], best[:, 0, :], here[:, 0, :, :], PER_GROUP)
            do(v.scalar_tensor_tensor(inside[:, :, :], here[:, 0, :, :], -3e38, inside[:, :, :], ALU.mult, ALU.add))
            one_hot_max(inside[:, :, :], best[:, 1, :], here[:, 1, :, :], PER_GROUP)
            v.tensor_tensor(second[:, :], best[:, 1, :], best[:, 0, :], ALU.subtract).then_inc(to_exp, 1)
            for c in range(2):
                do(v.tensor_tensor(hot[:, c, :, :].rearrange("p t (g e) -> p t g e", e=PER_GROUP), last(group[:, :, :], PER_GROUP),
                                   here[:, c, :, :].unsqueeze(2).broadcast_to([P, TT, GROUPS, PER_GROUP]), ALU.mult))
            v.tensor_tensor(both[:, :, :], hot[:, 0, :, :], hot[:, 1, :, :], ALU.add).then_inc(chosen, 1)
            dve.wait_ge(exp_done, 2)
            do(v.tensor_reduce(total[:, :], exps[:, :, :], AX.X, ALU.add))
            do(v.scalar_tensor_tensor(total[:, :], second[:, :], 1.0, total[:, :], ALU.add, ALU.mult))
            do(v.reciprocal(moe.weight[:, 0, :], total[:, :]))
            do(v.tensor_tensor(moe.weight[:, 1, :], moe.weight[:, 0, :], second[:, :], ALU.mult))
            dve.wait_ge(counted, 1)
            do(v.tensor_copy(rank[:, :, :], g.bank[1][:, 0:TT * EXPERTS].rearrange("p (t e) -> p t e", e=EXPERTS)))
            do(v.tensor_copy(count[:, :], g.bank[1][:, TT * EXPERTS:(TT + 1) * EXPERTS]))
            do(v.tensor_scalar(more[:, :], count[:, :], float(P), None, ALU.is_gt))
            for j in range(2, TT):
                do(v.scalar_tensor_tensor(more[:, :], count[:, :], float(j * P), more[:, :], ALU.is_gt, ALU.add))
            do(v.tensor_tensor_scan(more_end[:, :], g.ones[:, 0:EXPERTS], more[:, :], 0.0, ALU.mult, ALU.add))
            do(v.tensor_tensor(more_start[:, :], more_end[:, :], more[:, :], ALU.subtract))
            over_pairs = lambda a: a.unsqueeze(1).broadcast_to([P, 2, TT, EXPERTS])
            spread = lambda a: a.unsqueeze(1).broadcast_to([P, TT, EXPERTS])
            for out, of in ((slot, rank[:, :, :]), (expert, spread(iota(EXPERTS))), (start, spread(more_start[:, :]))):
                for c in range(2):
                    do(v.tensor_tensor(picked[:, c, :, :], hot[:, c, :, :], of, ALU.mult))
                do(v.tensor_reduce(out[:, :, :], picked[:, :, :, :], AX.X, ALU.add))
            do(v.tensor_scalar(past[:, :, :], slot[:, :, :], float(P), None, ALU.is_ge))
            for j in range(2, TT):
                do(v.scalar_tensor_tensor(past[:, :, :], slot[:, :, :], float(j * P), past[:, :, :], ALU.is_ge, ALU.add))
            do(v.scalar_tensor_tensor(slot[:, :, :], past[:, :, :], -float(P), slot[:, :, :], ALU.mult, ALU.add))
            do(v.scalar_tensor_tensor(start[:, :, :], start[:, :, :], EXPERTS - 1.0, past[:, :, :], ALU.add, ALU.add))
            do(v.tensor_tensor(start[:, :, :], start[:, :, :], expert[:, :, :], ALU.subtract))
            do(v.scalar_tensor_tensor(start[:, :, :], past[:, :, :], 0.0, start[:, :, :], ALU.is_gt, ALU.mult))
            do(v.tensor_tensor(expert[:, :, :], expert[:, :, :], start[:, :, :], ALU.add))
            for c in range(2):
                for t in range(TT):
                    n = c * TT + t
                    own.did(v.tensor_scalar(by_slot[:, n, :], iota(P), slot[:, c, t:t + 1], None, ALU.is_equal))
                    own.did(v.tensor_scalar(by_tile[:, n, :], iota(MOE_TILES), expert[:, c, t:t + 1], g.col("pair_number", n),
                                            ALU.is_equal, ALU.mult))
            own.wait()
            dve.sem_inc(placed, 1)
            do(v.tensor_tensor(ended[:, :, :], more_end[0:1, :].unsqueeze(1).broadcast_to([1, MORE, EXPERTS]),
                               last(iota(MORE, 1), EXPERTS), ALU.is_le))
            do(v.tensor_reduce(which[:, :], ended[:, :, :], AX.X, ALU.add))
            do(v.tensor_scalar(which[:, :], which[:, :], EXPERTS - 1.0, None, ALU.min))
            do(v.tensor_copy(moe.more_expert[:, :], which[:, :]))
            do(v.tensor_copy(moe.more_tiles[:, :], more_end[0:1, EXPERTS - 1:EXPERTS]))
            dve.wait_ge(table_done, 1)
            do(v.tensor_scalar(empty[:, :], g.bank[6][:, 0:MOE_TILES], 0.0, g.col("beyond"), ALU.is_equal, ALU.mult))
            do(v.scalar_tensor_tensor(place[:, :], g.bank[6][:, 0:MOE_TILES], -1.0, empty[:, :], ALU.add, ALU.add))
            do(v.tensor_copy(moe.pair[:, :], place[:, :]))
            do(v.tensor_scalar(moe.token[:, :], moe.pair[:, :], 1, None, ALU.logical_shift_right))



def after(eng, semaphore, count):
    if not isinstance(count, int) or count > 0:
        eng.wait_ge(semaphore, count)


class Tile:

    def __init__(self, g, ctx, moe, tag, split=False):
        sem, sb = g.stage(ctx, tag)
        self.g, self.moe, self.split = g, moe, split
        if split:
            self.split_up(sem, sb)
        self.cleared, self.passed = sem("cleared"), sem("passed")
        self.token_copied, self.pair_copied = sem("token_copied"), sem("pair_copied")
        self.gathered, self.scattered = [sem(f"gathered{b}") for b in range(IN_FLIGHT)], [sem("scattered0"), sem("scattered1")]
        self.turned, self.turn_read_act, self.turn_read_dve = sem("turned"), sem("turn_read_act"), sem("turn_read_dve")
        self.up_done, self.silu_done, self.product_done = sem("up_done"), sem("silu_done"), sem("product_done")
        self.back_turned, self.back_read = sem("back_turned"), sem("back_read")
        self.down_done, self.out_read_act, self.out_read_dve = sem("down_done"), sem("out_read_act"), sem("out_read_dve")
        self.rows = [t.rearrange("p a n -> p (a n)") for t in (g.mix[:, 0:2, :], g.mix[:, 2:4, :], g.square[:, :, :],
                                                               sb("rows", [P, 2, T])[:, :, :])]
        self.xt = g.mix[:, 4:6, :].rearrange("p a (k n) -> p (a k) n", n=P)
        self.out = [g.memn[:, 4 * b:4 * b + 4, :].rearrange("p a n -> p (a n)") for b in range(2)]
        self.silu, self.act, self.back = sb("silu", [P, FE]), sb("act", [P, FE]), sb("back", [P, 2, P])
        self.token, self.pair = sb("token", [P, IN_FLIGHT], I32), sb("pair", [P, 2], I32)


    def clear(self, pool):
        for rows in self.rows:
            self.g.nc.gpsimd.memset(rows, 0.0).then_inc(self.cleared, 1)
        pool.wait_ge(self.cleared, len(self.rows))

    def gather(self, pool, n, tile, b):
        nc, moe, here = self.g.nc, self.moe, slice(b, b + 1)
        nc.gpsimd.tensor_copy(self.token[:, here], moe.token[:, tile]).then_inc(self.token_copied, 1)
        pool.wait_ge(self.token_copied, n + 1)
        pool.sem_inc(self.passed, 1)
        nc.gpsimd.indirect_dma_start(out=self.rows[b], out_offset=None, in_=moe.rows,
                                     in_offset=bass.IndirectOffsetOnAxis(ap=self.token[:, here], axis=0),
                                     bounds_check=T - 1, oob_is_err=False).then_inc(self.gathered[b], 16)

    def scatter(self, pool, n, tile, b):
        nc, moe, here = self.g.nc, self.moe, slice(b, b + 1)
        pool.wait_ge(self.out_read_act, n + 1)
        pool.wait_ge(self.out_read_dve, n + 1)
        pool.sem_inc(self.passed, 1)
        nc.gpsimd.tensor_copy(self.pair[:, here], moe.pair[:, tile]).then_inc(self.pair_copied, 1)
        pool.wait_ge(self.pair_copied, n + 1)
        pool.sem_inc(self.passed, 1)
        nc.gpsimd.indirect_dma_start(out=moe.pair_rows, out_offset=bass.IndirectOffsetOnAxis(ap=self.pair[:, here], axis=0),
                                     in_=self.out[b], in_offset=None,
                                     bounds_check=2 * T - 1, oob_is_err=False).then_inc(self.scattered[b], 16)


    def turn(self, pe, n, b, uses):
        pe.wait_ge(self.gathered[b], 16 * uses + 16)
        if self.split:
            after(pe, self.xt_done, 2 * n)
        else:
            after(pe, self.turn_read_act, n)
            after(pe, self.turn_read_dve, n)
        for k in range(KT):
            mm = self.g.nc.tensor.matmul(self.g.bank[k // 4][:, k % 4 * P:(k % 4 + 1) * P], self.rows[b][:, k * P:(k + 1) * P],
                                         self.g.ident[:, :], start=True, stop=True)
            if k % 4 == 3:
                mm.then_inc(self.turned, 1)

    def up(self, pe, n, b, weights):
        pe.wait_ge(self.turn_read_act, n + 1)
        pe.wait_ge(self.turn_read_dve, n + 1)
        for k in range(KT):
            mm = self.g.nc.tensor.matmul(self.g.bank[2 + b][:, :], self.xt[:, k, :], weights[k // 4][:, k % 4 * 2 * FE:(k % 4 + 1) * 2 * FE],
                                         start=(k == 0), stop=(k == KT - 1))
        mm.then_inc(self.up_done, 1)

    def turn_back(self, pe, n):
        pe.wait_ge(self.product_done, n + 1)
        for j in range(2):
            mm = self.g.nc.tensor.matmul(self.g.bank[4][:, j * P:(j + 1) * P], self.act[:, j * P:(j + 1) * P], self.g.ident[:, :],
                                         start=True, stop=True)
        mm.then_inc(self.back_turned, 1)

    def down(self, pe, n, weights):
        pe.wait_ge(self.back_read, n + 1)
        after(pe, self.out_read_act, n)
        after(pe, self.out_read_dve, n)
        for h in range(2):
            for j in range(2):
                c = 4 * 2 * FE + h * T
                mm = self.g.nc.tensor.matmul(self.g.bank[5 + h][:, :], self.back[:, j, :], weights[j][:, c:c + T],
                                             start=(j == 0), stop=(j == 1))
            mm.then_inc(self.down_done, 1)


    def act_turn(self, act, n):
        act.wait_ge(self.turned, 2 * n + 1)
        self.g.nc.scalar.activation(self.xt[:, 0:4, :].rearrange("p k n -> p (k n)"), self.g.bank[0][:, :], ACT.Copy)\
            .then_inc(self.turn_read_act, 1)

    def act_silu(self, act, n, b):
        act.wait_ge(self.up_done, n + 1)
        after(act, self.product_done, n)
        self.g.nc.scalar.activation(self.silu[:, :], self.g.bank[2 + b][:, 0:FE], ACT.Silu).then_inc(self.silu_done, 1)

    def act_out(self, act, n, b, uses):
        act.wait_ge(self.down_done, 2 * n + 1)
        after(act, self.scattered[b], 16 * uses)
        self.g.nc.scalar.activation(self.out[b][:, 0:T], self.g.bank[5][:, :], ACT.Copy).then_inc(self.out_read_act, 1)


    def dve_turn(self, dve, n):
        dve.wait_ge(self.turned, 2 * n + 2)
        self.g.nc.vector.tensor_copy(self.xt[:, 4:8, :].rearrange("p k n -> p (k n)"), self.g.bank[1][:, :])\
            .then_inc(self.turn_read_dve, 1)


    def split_up(self, sem, sb):
        self.xt_split = [Split(self.g.mix_r[:, 4 + k // 4, k % 4 * P:(k % 4 + 1) * P], self.g.mix_r[:, 6 + k // 4, k % 4 * P:(k % 4 + 1) * P])
                         for k in range(KT)]
        self.xt_half = [Split(self.g.mix_r[:, 4 + h, :], self.g.mix_r[:, 6 + h, :]) for h in range(2)]
        self.w_hi = [self.g.xn_r[:, :, :].rearrange("p k n -> p (k n)"), sb("w_hi", [P, KT * 2 * FE], F32R)[:, :]]
        self.w_rounded, self.w_split_dve, self.w_split_pool = sem("w_rounded"), sem("w_split_dve"), sem("w_split_pool")
        self.xt_rounded, self.xt_done = sem("xt_rounded"), sem("xt_done")

    def half(self, b, h):
        n = KT // 2 * 2 * FE
        return self.w_hi[b][:, h * n:(h + 1) * n]

    def round_weights(self, act, b, h, slot):
        self.g.nc.scalar.activation(self.half(b, h), slot[:, 0:KT // 2 * 2 * FE], ACT.Copy).then_inc(self.w_rounded, 1)

    def round_turned(self, act, n):
        for h in range(2):
            act.wait_ge(self.turned, 2 * n + h + 1)
            self.g.nc.scalar.activation(self.xt_half[h].hi, self.g.bank[h][:, :], ACT.Copy).then_inc(self.xt_rounded, 1)

    def rest_turned(self, dve, n):
        for h in range(2):
            dve.wait_ge(self.xt_rounded, 2 * n + h + 1)
            self.g.nc.vector.tensor_tensor(self.xt_half[h].lo, self.g.bank[h][:, :], self.xt_half[h].hi, ALU.subtract)\
                .then_inc(self.xt_done, 1)

    def up_products(self, pe, n, b, rests):
        for h, ready in enumerate((self.w_split_dve, self.w_split_pool)):
            pe.wait_ge(ready, n + 1)
            pe.wait_ge(self.xt_done, 2 * n + h + 1)
            for k in range(4 * h, 4 * h + 4):
                c = k % 4 * 2 * FE
                w = Split(self.w_hi[b][:, k * 2 * FE:(k + 1) * 2 * FE], rests[h][:, c:c + 2 * FE])
                mm = split_products(self.g.nc, self.g.bank[2 + b][:, :], self.xt_split[k], w, k == 0, k == KT - 1)
        mm.then_inc(self.up_done, 1)

    def dve_product(self, dve, n, b):
        dve.wait_ge(self.silu_done, n + 1)
        after(dve, self.back_turned, n)
        self.g.nc.vector.tensor_tensor(self.act[:, :], self.silu[:, :], self.g.bank[2 + b][:, FE:2 * FE], ALU.mult)\
            .then_inc(self.product_done, 1)

    def dve_back(self, dve, n):
        dve.wait_ge(self.back_turned, n + 1)
        after(dve, self.down_done, 2 * n)
        self.g.nc.vector.tensor_copy(self.back[:, :, :].rearrange("p a n -> p (a n)"), self.g.bank[4][:, 0:2 * P])\
            .then_inc(self.back_read, 1)

    def dve_out(self, dve, n, b, uses):
        dve.wait_ge(self.down_done, 2 * n + 2)
        after(dve, self.scattered[b], 16 * uses)
        self.g.nc.vector.tensor_copy(self.out[b][:, T:D], self.g.bank[6][:, :]).then_inc(self.out_read_dve, 1)


def stage_experts(g, moe, units):
    nc = g.nc
    units.begin()
    ROUNDS = EXPERTS // IN_FLIGHT
    HALF_UP = KT // 2 * 2 * FE
    weights = [[moe.ring.slots[2 * u], moe.ring.slots[2 * u + 1]] for u in range(IN_FLIGHT)]
    with ExitStack() as ctx:
        w = Tile(g, ctx, moe, "experts", split=True)
        block = ctx.enter_context(nc.Block())

        def rounds(eng, step):
            for u in range(IN_FLIGHT):
                step(0, u, IN_FLIGHT)
            with eng.Fori(1, ROUNDS - 1) as i:
                for u in range(IN_FLIGHT):
                    step(i, u, IN_FLIGHT)
            for u in range(IN_FLIGHT):
                step(ROUNDS - 1, u, IN_FLIGHT - 1 - u)

        @block.sync
        def _(sp):
            with sp.Fori(1, ROUNDS) as i:
                for u in range(IN_FLIGHT):
                    sp.wait_ge(w.down_done, 2 * IN_FLIGHT * i - 2 * IN_FLIGHT + 2 * u + 2)
                    units.load(sp, i, 2 * u)
                    units.load(sp, i, 2 * u + 1)

        @block.gpsimd
        def _(pool):
            w.clear(pool)
            for u in range(IN_FLIGHT):
                w.gather(pool, u, slice(u, u + 1), u)

            def rest(i, u):
                n, slot = IN_FLIGHT * i + u, 2 * (u % IN_FLIGHT) + 1
                pool.wait_ge(w.w_rounded, 2 * n + 2)
                pool.sem_inc(w.passed, 1)
                nc.gpsimd.tensor_tensor(moe.ring.slots_r[slot][:, 0:HALF_UP], moe.ring.slots[slot][:, 0:HALF_UP], w.half(u % 2, 1),
                                        ALU.subtract).then_inc(w.w_split_pool, 1)
            rest(0, 0)
            rest(0, 1)

            def step(i, u, later):
                n, b = IN_FLIGHT * i + u, u % 2
                if later >= IN_FLIGHT:
                    pool.wait_ge(w.turned, 2 * n + 2)
                    pool.sem_inc(w.passed, 1)
                    w.gather(pool, n + IN_FLIGHT, bass.ds(n + IN_FLIGHT, 1), u)
                if later >= 2:
                    rest(i, u + 2)
                w.scatter(pool, n, bass.ds(n, 1), b)
            rounds(pool, step)
            for b in range(2):
                pool.wait_ge(w.scattered[b], 16 * EXPERTS // 2)

        @block.tensor
        def _(pe):
            def load_up(i, u):
                v = u % IN_FLIGHT
                w.up_products(pe, IN_FLIGHT * i + u, u % 2, moe.ring.slots_r[2 * v:2 * v + 2])

            def step(i, u, later):
                n = IN_FLIGHT * i + u
                if later >= 1:
                    w.turn(pe, n + 1, (u + 1) % IN_FLIGHT, i + (u + 1) // IN_FLIGHT)
                w.turn_back(pe, n)
                if later >= 1:
                    load_up(i, u + 1)
                w.down(pe, n, weights[u])
            w.turn(pe, 0, 0, 0)
            load_up(0, 0)
            rounds(pe, step)

        @block.scalar
        def _(act):
            def round_weights(i, u):
                v = u % IN_FLIGHT
                for s in range(2):
                    units.wait(act, i + u // IN_FLIGHT, 2 * v + s)
                    w.round_weights(act, u % 2, s, weights[v][s])

            def step(i, u, later):
                n = IN_FLIGHT * i + u
                if later >= 1:
                    w.round_turned(act, n + 1)
                if later >= 2:
                    round_weights(i, u + 2)
                if later >= 1:
                    w.act_silu(act, n + 1, (u + 1) % 2)
                w.act_out(act, n, u % 2, IN_FLIGHT // 2 * i + u // 2)
            round_weights(0, 0)
            w.round_turned(act, 0)
            round_weights(0, 1)
            w.act_silu(act, 0, 0)
            rounds(act, step)

        @block.vector
        def _(dve):
            def rest(i, u):
                n, slot = IN_FLIGHT * i + u, 2 * (u % IN_FLIGHT)
                dve.wait_ge(w.w_rounded, 2 * n + 1)
                nc.vector.tensor_tensor(moe.ring.slots_r[slot][:, 0:HALF_UP], moe.ring.slots[slot][:, 0:HALF_UP], w.half(u % 2, 0),
                                        ALU.subtract).then_inc(w.w_split_dve, 1)

            def step(i, u, later):
                n = IN_FLIGHT * i + u
                if later >= 1:
                    w.rest_turned(dve, n + 1)
                w.dve_back(dve, n)
                if later >= 2:
                    rest(i, u + 2)
                if later >= 1:
                    w.dve_product(dve, n + 1, (u + 1) % 2)
                w.dve_out(dve, n, u % 2, IN_FLIGHT // 2 * i + u // 2)
            rest(0, 0)
            w.rest_turned(dve, 0)
            rest(0, 1)
            w.dve_product(dve, 0, 0)
            rounds(dve, step)


def stage_more_experts(g, moe, units):
    nc = g.nc
    of_expert = units.ap.rearrange("i (u s) p n -> (i u) s p n", s=2)
    weights = moe.ring.slots[0:2]
    with ExitStack() as ctx:
        w = Tile(g, ctx, moe, "more")
        ready = [g.flag(ctx, f"more_ready{s}") for s in range(2)]
        block = ctx.enter_context(nc.Block())

        def any_more(eng):
            return eng.If(eng.value_load(moe.more_tiles[0:1, 0:1], min_val=0, max_val=MORE) > 0)

        def tiles(eng, tile):
            tile(0)
            with eng.Fori(1, MORE) as n:
                tile(n)

        @block.sync
        def _(sp):
            with any_more(sp):
                def tile(n):
                    expert = sp.value_load(moe.more_expert[0:1, bass.ds(n, 1)], min_val=0, max_val=EXPERTS - 1)
                    after(sp, w.down_done, 2 * n)
                    sp.sem_inc(w.passed, 1)
                    for s in range(2):
                        sp.dma_start(weights[s][:, :], of_expert[expert, s]).then_inc(ready[s], 16)
                tiles(sp, tile)

        @block.gpsimd
        def _(pool):
            with any_more(pool):
                def tile(n):
                    after(pool, w.turned, 2 * n)
                    pool.sem_inc(w.passed, 1)
                    w.gather(pool, n, bass.ds(n + EXPERTS, 1), 0)
                    w.scatter(pool, n, bass.ds(n + EXPERTS, 1), 0)
                tiles(pool, tile)
                pool.wait_ge(w.scattered[0], 16 * MORE)

        @block.tensor
        def _(pe):
            with any_more(pe):
                def tile(n):
                    w.turn(pe, n, 0, n)
                    for s in range(2):
                        pe.wait_ge(ready[s], 16 * n + 16)
                    w.up(pe, n, 0, weights)
                    w.turn_back(pe, n)
                    w.down(pe, n, weights)
                tiles(pe, tile)

        @block.scalar
        def _(act):
            with any_more(act):
                def tile(n):
                    w.act_turn(act, n)
                    w.act_silu(act, n, 0)
                    w.act_out(act, n, 0, n)
                tiles(act, tile)

        @block.vector
        def _(dve):
            with any_more(dve):
                def tile(n):
                    w.dve_turn(dve, n)
                    w.dve_product(dve, n, 0)
                    w.dve_back(dve, n)
                    w.dve_out(dve, n, 0, n)
                tiles(dve, tile)


def stage_combine(g, moe):
    nc = g.nc
    with ExitStack() as ctx:
        sem, sb = g.stage(ctx, "combine")
        loaded = [sem("loaded0"), sem("loaded1")]
        weighed, summed, turned, added = (sem(n) for n in ("weighed", "summed", "turned", "added"))
        two = [sb(f"two{b}", [P, 2, D]) for b in range(2)]
        out = [sb(f"sum{b}", [P, D]) for b in range(2)]
        block = ctx.enter_context(nc.Block())
        pairs = moe.pair_rows.rearrange("(t p c) n -> t p (c n)", p=P, c=2)

        @block.sync
        def _(sp):
            for t in range(TT):
                if t >= 2:
                    sp.wait_ge(summed, t - 1)
                sp.dma_start(two[t % 2][:, :, :].rearrange("p c n -> p (c n)"), pairs[t]).then_inc(loaded[t % 2], 16)
            sp.wait_ge(loaded[0], 32)
            sp.wait_ge(loaded[1], 32)

        @block.scalar
        def _(act):
            for t in range(TT):
                act.wait_ge(loaded[t % 2], 16 * (t // 2 + 1))
                if t >= 2:
                    act.wait_ge(turned, 2 * t - 2)
                nc.scalar.activation(out[t % 2][:, :], two[t % 2][:, 0, :], ACT.Copy, scale=moe.weight[:, 0, t:t + 1]).then_inc(weighed, 1)

        @block.vector
        def _(dve):
            def add(t):
                for h in range(2):
                    dve.wait_ge(turned, 2 * t + h + 1)
                    for j in range(4):
                        here = g.x[:, 4 * h + j, t * P:(t + 1) * P]
                        ins = nc.vector.scalar_tensor_tensor(here, g.bank[2 * (t % 2) + h][:, j * P:(j + 1) * P],
                                                             g.mod[:, 40 + 4 * h + j:41 + 4 * h + j], here, ALU.mult, ALU.add)
                    ins.then_inc(added, 1)
            for t in range(TT):
                dve.wait_ge(weighed, t + 1)
                nc.vector.scalar_tensor_tensor(out[t % 2][:, :], two[t % 2][:, 1, :], moe.weight[:, 1, t:t + 1], out[t % 2][:, :],
                                               ALU.mult, ALU.add).then_inc(summed, 1)
                if t > 0:
                    add(t - 1)
            add(TT - 1)

        @block.tensor
        def _(pe):
            for t in range(TT):
                pe.wait_ge(summed, t + 1)
                for h in range(2):
                    if t >= 2:
                        pe.wait_ge(added, 2 * (t - 2) + h + 1)
                    for j in range(4):
                        k = 4 * h + j
                        mm = nc.tensor.matmul(g.bank[2 * (t % 2) + h][:, j * P:(j + 1) * P], out[t % 2][:, k * P:(k + 1) * P],
                                              g.ident[:, :], start=True, stop=True)
                    mm.then_inc(turned, 1)


def stage_store(g, out):
    nc = g.nc
    with ExitStack() as ctx:
        norm = Norm(g, ctx, g.gains[:, 2, :], g.mod[:, 48:48 + KT])
        stored = g.flag(ctx, "stored")
        block = ctx.enter_context(nc.Block())

        @block.sync
        def _(sp):
            for k in range(KT):
                sp.wait_ge(norm.xn_ready, k + 1)
                sp.dma_start(out[:, k, :], g.xn[:, k, :]).then_inc(stored, 16)
            sp.wait_ge(stored, 16 * KT)

        @block.tensor
        def _(pe):
            norm.tensor(pe)

        @block.scalar
        def _(act):
            norm.scalar(act)

        @block.vector
        def _(dve):
            norm.vector(dve)



def as_columns(a):
    return np.asarray(a).reshape(-1, P).T


def padded_column(a):
    a = np.asarray(a).reshape(-1)
    return np.pad(a, (0, P - a.size)).reshape(P, 1)


def by_partition(w):
    w = np.asarray(w)
    return w.reshape(-1, P, w.shape[1]).transpose(1, 0, 2).reshape(P, -1)


def units_of(pieces):
    return np.stack([np.stack([by_partition(p) for p in one]) for one in pieces])


def columns_of(w, width, per):
    w = np.asarray(w)
    cut = [w[:, c:c + width] for c in range(0, w.shape[1], width)]
    return units_of([cut[n:n + per] for n in range(0, len(cut), per)])


def rows_of(w):
    w = np.asarray(w)
    return w.reshape(-1, 2, P, w.shape[1])


def side(*pieces):
    return np.concatenate([np.asarray(p) for p in pieces], axis=1)


def lay_out(v):
    a, table = {}, []
    v = {k: np.asarray(x) for k, x in v.items()}
    feature_major = lambda t: t.reshape(-1, KT, P).transpose(2, 1, 0)
    a["x"], a["mem"] = feature_major(v["x"][0]), feature_major(v["mem"][0])
    for l in range(2):
        for n in ("mix", "xattn", "mem", "ffn"):
            table.append((f"{n}_norm{l}", as_columns(v[f"{n}_norm"][l])))
        table.append((f"ffn_conv{l}", as_columns(np.concatenate([v["ffn_conv_w"][l].reshape(-1), v["ffn_conv_b"][l]]))))
    w = v["attn_w_in"][0]
    table.append(("w_forget", by_partition(w[:, 1536:1544])))
    table.append(("fox_bf", padded_column(v["attn_fox_bf"][0])))
    table.append(("diff_l", np.concatenate([padded_column(v[n][0]) for n in ("diff_lq1", "diff_lk1", "diff_lq2", "diff_lk2")], 1)))
    table.append(("subln", as_columns(v["diff_subln"][0])))
    a["w_fox"] = units_of([[side(*(w[:, c + P * h:c + P * h + P] for c in (0, 512, 1024)))] for h in range(4)])
    a["w_diff"] = units_of([[side(*(w[:, 1544 + c + P * h:1544 + c + P * h + P] for c in (0, 512, 1024)))] for h in range(4)])
    a["w_attn_out"] = rows_of(v["attn_w_out"][0])
    for l in range(2):
        q, kv = v["xattn_wq"][l], v["xattn_wkv"][l]
        a[f"w_xattn{l}"] = units_of([[m[:, c + 256 * h:c + 256 * h + 256] for m, c in ((kv, 0), (kv, D), (q, 0))] for h in range(X_HEADS)])
        a[f"w_xattn_out{l}"] = rows_of(v["xattn_wo"][l])
        up = v["ffn_w_up"][l]
        cut = [side(up[:, P * u:P * u + P], up[:, FF + P * u:FF + P * u + P]) for u in range(FT)]
        a[f"w_up{l}"] = units_of([cut[n:n + 2] for n in range(0, FT, 2)])
        a[f"w_down{l}"] = rows_of(v["ffn_w_down"][l])
    lay_out_more(v, a, table)
    where, at = {}, 0
    for name, c in table:
        where[name], at = at, at + c.shape[1]
    where["width"] = at
    a["vecs"] = np.concatenate([c for _, c in table], axis=1)
    return {k: np.ascontiguousarray(x) for k, x in a.items()}, where


def lay_out_mlstm(v, a, table):
    w = v["mlstm_w_in"][0]
    table.append(("w_gates", by_partition(w[:, 2048:2056])))
    table.append(("mlstm_b_i", padded_column(v["mlstm_b_i"][0])))
    table.append(("mlstm_b_f", padded_column(v["mlstm_b_f"][0])))
    table.append(("conv_qk", as_columns(v["mlstm_conv_qk"][0])))
    table.append(("head_norm", as_columns(v["mlstm_head_norm"][0])))
    a["w_mlstm"] = units_of([[side(w[:, P * h:P * h + P], w[:, 512 + P * h:512 + P * h + P]),
                              w[:, 1024 + 256 * h:1024 + 256 * h + 256], w[:, 2056 + 256 * h:2056 + 256 * h + 256]]
                             for h in range(ML_HEADS)])
    a["w_mlstm_out"] = rows_of(v["mlstm_w_out"][0])


def lay_out_second(v, a, table):
    for name in ("mu_rkv", "w0", "a0", "k_k", "k_a", "lnx_g", "lnx_b", "conv_b", "b_rgate", "b_igate", "lam",
                 "g_mix", "g_ffn", "mu_wag", "r_k"):
        table.append((name, as_columns(v[f"{name}_2"][0])))
    table.append(("final_norm", as_columns(v["final_norm"])))
    table.append(("g_final", as_columns(v["g_final_2"])))
    table.append(("c", as_columns(v["c_2"])))
    table.append(("b_ada", np.concatenate([as_columns(v["b_ada_2"][0]), as_columns(v["b_ada_f_2"])], 1)))
    table.append(("conv_w", as_columns(v["conv_w_2"][0])))
    s, t = np.arange(CHUNK)[:, None], np.arange(CHUNK)[None, :]
    twice = lambda m: np.concatenate([m, m], 0).astype(np.float32)
    table.append(("eye", twice(s == t)))
    table.append(("tri", np.concatenate([twice(s < t), twice(s <= t)], 1)))
    table.append(("levels", np.concatenate([twice((s >> l + 1 == t >> l + 1) & (t >> l & 1 == 1) & (s >> l & 1 == 0))
                                            for l in range(6)], 1)))
    ada = side(v["w_ada_2"][0], v["w_ada_f_2"])
    a["modulation"] = ada.reshape(KT, P, 8, 1024).transpose(0, 2, 1, 3)
    w = v["w_in_2"][0]
    a["w_rec_in"] = columns_of(w[:, 0:2560], 256, 2)
    first = by_partition(side(v["w1_2"][0], v["a1_2"][0], v["g1_2"][0]))
    lower = lambda m: np.pad(m, ((0, P - m.shape[0]), (0, 0)))

    def diagonal(blocks):
        z = np.zeros((HALF, HALF), blocks.dtype)
        return side(*(np.block([[blocks[2 * m], z], [z, blocks[2 * m + 1]]]) for m in range(AT)))

    second = side(lower(v["w2_2"][0]), lower(v["a2_2"][0]), v["g2_2"][0], diagonal(v["w_rgate_2"][0]), diagonal(v["w_igate_2"][0]))
    a["w_low"] = np.stack([np.pad(first, ((0, 0), (0, second.shape[1] - first.shape[1]))), second])[None]
    a["w_merge"] = units_of([[w[:, 2560 + c:2560 + c + 256], w[:, 2560 + D + c:2560 + D + c + 256],
                              np.concatenate([v["p_a_2"][0][:, c:c + 256], v["p_b_2"][0][:, c:c + 256]], 0)]
                             for c in range(0, D, 256)])
    a["w_mix_out"] = rows_of(v["w_out_2"][0])


def lay_out_experts(v, a, table):
    table.append(("w_router", by_partition(side(v["w_rg_2"][0], v["w_re_2"][0]))))
    bias = np.concatenate([v["b_rg_2"][0], v["b_re_2"][0]])
    table.append(("b_router", np.broadcast_to(bias, (P, bias.size))))
    p = np.arange(P, dtype=np.float32)[:, None]
    table.append(("iota", np.broadcast_to(np.arange(P, dtype=np.float32), (P, P))))
    table.append(("pair_number", np.concatenate([2 * (P * t + p) + c + 1 for c in range(2) for t in range(TT)], 1)))
    table.append(("beyond", 8 * T + 2 * p))
    up = [side(v["w1e_2"][0][e], v["w3e_2"][0][e]) for e in range(EXPERTS)]
    down = v["w2e_2"][0]
    half = lambda e, s: np.concatenate([by_partition(up[e][s * T:(s + 1) * T]), down[e][s * P:(s + 1) * P]], 1)
    a["w_experts"] = np.stack([half(e, s) for e in range(EXPERTS) for s in range(2)]).reshape(
        EXPERTS // IN_FLIGHT, 2 * IN_FLIGHT, P, SLOT)


def lay_out_more(v, a, table):
    lay_out_mlstm(v, a, table)
    lay_out_second(v, a, table)
    lay_out_experts(v, a, table)


def build(nc, A, where, out):
    with ExitStack() as ctx:
        g = Core(nc, ctx, A, where)
        U = {name: Units(g.ring, A[name]) for name in A if name.startswith("w_") and name != "w_experts"}
        stage_setup(g, U["w_fox"])

        with ExitStack() as attention:
            xn_lo = two_names(nc, attention, "attention_xn_lo", [P, KT, T])
            stage_attention(g, U["w_fox"], U["w_diff"], True, xn_lo)
            stage_attention(g, U["w_diff"], U["w_attn_out"], False, xn_lo)
        stage_dense_residual(g, U["w_attn_out"], U["w_xattn0"], g.mix)
        for layer in range(2):
            if layer == 1:
                stage_mlstm(g, U["w_mlstm"], U["w_mlstm_out"])
                stage_dense_residual(g, U["w_mlstm_out"], U["w_xattn1"], g.mix)
            stage_cross_attention(g, U[f"w_xattn{layer}"], U[f"w_xattn_out{layer}"], layer)
            stage_dense_residual(g, U[f"w_xattn_out{layer}"], U[f"w_up{layer}"], g.mix)
            with nc.sbuf_tensor(f"hidden{layer}", [P, FT, T], F32) as hidden:
                stage_ffn_up(g, U[f"w_up{layer}"], U[f"w_down{layer}"], layer, hidden)
                stage_dense_residual(g, U[f"w_down{layer}"], U[("w_mlstm", "w_rec_in")[layer]], hidden,
                                     modulation=(layer == 0))
        stage_norm(g, g.cols("final_norm", KT), None, out=g.x)

        with ExitStack() as inner:
            rec = Recurrent(nc, inner)
            stage_recurrent_in(g, rec, U["w_rec_in"], U["w_low"])
            rec.add_gates(nc, inner)
            stage_low_rank(g, rec, U["w_low"], None)
            stage_rg_lru(g, rec)
            rw = Rwkv(rec)
            stage_rwkv_prepare(g, rec, rw)
            stage_rwkv_chunks(g, rec, rw)
            stage_rwkv_finish(g, rec, rw, U["w_merge"])
        with nc.sbuf_tensor("merged", [P, KT, T], F32) as merged:
            stage_merge(g, U["w_merge"], U["w_mix_out"], merged)
            stage_dense_residual(g, U["w_mix_out"], None, merged, gate=g.mod[:, 16:24])
        with ExitStack() as inner:
            moe = Experts(nc, inner, g.ring)
            experts = Units(moe.ring, A["w_experts"])
            stage_router(g, moe, experts)
            stage_experts(g, moe, experts)
            stage_more_experts(g, moe, experts)
            stage_combine(g, moe)
        stage_store(g, out)


def kernel(**inputs):
    import concourse.bacc as bacc
    from concourse.bass_utils import run_bass_kernel_spmd

    arrays, where = lay_out(inputs)
    nc = bacc.Bacc("TRN2", target_bir_lowering=False, num_devices=1)
    A = {name: nc.dram_tensor(f"in_{name}", a.shape, mybir.dt.from_np(a.dtype), kind="ExternalInput").ap()
         for name, a in arrays.items()}
    out = nc.dram_tensor("out", [P, KT, T], F32, kind="ExternalOutput").ap()
    build(nc, A, where, out)
    if not nc.is_finalized():
        nc.finalize()
    r = run_bass_kernel_spmd(nc, [{f"in_{name}": a for name, a in arrays.items()}], core_ids=[0])
    return np.ascontiguousarray(np.asarray(r.results[0]["out"]).transpose(2, 1, 0).reshape(1, T, D))
```
